# Optimizing a Trainium2 kernel written in Bass

```python
import math
import jax
import jax.numpy as jnp
from jax import lax
import numpy as np
import jax, jax.numpy as jnp

D_MODEL = 1024
BATCH = 1
SEQ = 1024
DEPTH = 1

N_MEM = 256
Q_BLOCK = 128
RMS_EPS = 1e-6
NEG_INF = -1e30
ROPE_THETA = 10000.0
POS_OFFSET_MAX = 1024

DIFF_HEADS = 8
DIFF_HALF_DIM = 32
DIFF_V_DIM = 2 * DIFF_HALF_DIM
DIFF_QK_WIDTH = DIFF_HEADS * 2 * DIFF_HALF_DIM
DIFF_WIDTH = DIFF_HEADS * DIFF_V_DIM

MLA_HEADS = 8
MLA_Q_RANK = 256
MLA_KV_RANK = 128
MLA_NOPE_DIM = 64
MLA_ROPE_DIM = 32
MLA_QK_DIM = MLA_NOPE_DIM + MLA_ROPE_DIM
MLA_V_DIM = 64
MLA_WIDTH = MLA_HEADS * MLA_V_DIM

MIX_WIDTH = DIFF_WIDTH + MLA_WIDTH
IN_SPLITS = (DIFF_QK_WIDTH,
             2 * DIFF_QK_WIDTH,
             2 * DIFF_QK_WIDTH + DIFF_WIDTH,
             2 * DIFF_QK_WIDTH + DIFF_WIDTH + MLA_Q_RANK,
             2 * DIFF_QK_WIDTH + DIFF_WIDTH + MLA_Q_RANK + MLA_KV_RANK)
IN_PROJ_WIDTH = IN_SPLITS[-1] + MLA_ROPE_DIM

MEM_HEADS = 4
MEM_HEAD_DIM = 128
MEM_WIDTH = MEM_HEADS * MEM_HEAD_DIM

N_GROUPS = 4
EXPERTS_PER_GROUP = 8
N_EXPERTS = N_GROUPS * EXPERTS_PER_GROUP
TOP_K_IN_GROUP = 2
EXPERT_FF = 256
EXPERT_BLOCK = 128


def _rms_norm(x, gain):
    xf = x.astype(jnp.float32)
    y = xf * lax.rsqrt(jnp.mean(xf * xf, axis=-1, keepdims=True) + RMS_EPS)
    return (y * gain.astype(jnp.float32)).astype(x.dtype)

def _alibi_slopes(n_heads):
    return 2.0 ** (-8.0 * jnp.arange(1, n_heads + 1, dtype=jnp.float32) / n_heads)

def _rope_angles(positions, dim):
    inv_freq = ROPE_THETA ** (-jnp.arange(0, dim, 2, dtype=jnp.float32) / dim)
    ang = positions.astype(jnp.float32)[..., None] * inv_freq
    return jnp.cos(ang), jnp.sin(ang)

def _apply_rope(x, cos, sin):
    half = x.shape[-1] // 2
    x1 = x[..., :half].astype(jnp.float32)
    x2 = x[..., half:].astype(jnp.float32)
    return jnp.concatenate([x1 * cos - x2 * sin, x2 * cos + x1 * sin], axis=-1).astype(x.dtype)

def _causal_mask(start, seq_len):
    q_idx = start + jnp.arange(Q_BLOCK)
    k_idx = jnp.arange(seq_len)
    return k_idx[None, :] <= q_idx[:, None]

def _query_block_sweep(block_fn, seq_len):
    n_blocks = seq_len // Q_BLOCK
    out = lax.map(block_fn, jnp.arange(n_blocks))
    nb, b, qb, w = out.shape
    return out.transpose(1, 0, 2, 3).reshape(b, nb * qb, w)

def _differential_attention(q, k, v, positions, lam, lambda_init, out_gain):
    b, s, h, _ = q.shape
    q = q.transpose(0, 2, 1, 3)
    k = k.transpose(0, 2, 1, 3)
    v = v.transpose(0, 2, 1, 3)
    q1, q2 = q[..., :DIFF_HALF_DIM], q[..., DIFF_HALF_DIM:]
    k1, k2 = k[..., :DIFF_HALF_DIM], k[..., DIFF_HALF_DIM:]
    slopes = _alibi_slopes(h)
    scale = DIFF_HALF_DIM ** -0.5
    pos_f = positions.astype(jnp.float32)
    gain = out_gain.astype(jnp.float32) * (1.0 - lambda_init)

    def block_fn(i):
        start = i * Q_BLOCK
        qb1 = lax.dynamic_slice_in_dim(q1, start, Q_BLOCK, axis=2)
        qb2 = lax.dynamic_slice_in_dim(q2, start, Q_BLOCK, axis=2)
        pos_q = lax.dynamic_slice_in_dim(pos_f, start, Q_BLOCK, axis=1)
        dist = jnp.abs(pos_q[:, :, None] - pos_f[:, None, :])
        bias = -slopes[None, :, None, None] * dist[:, None]
        mask = _causal_mask(start, s)

        def attn_map(qb, kk):
            sc = jnp.einsum('bhqd,bhkd->bhqk', qb, kk, preferred_element_type=jnp.float32) * scale + bias
            return jax.nn.softmax(jnp.where(mask, sc, NEG_INF), axis=-1)

        a = attn_map(qb1, k1) - lam * attn_map(qb2, k2)
        o = jnp.einsum('bhqk,bhkd->bhqd', a.astype(v.dtype), v, preferred_element_type=jnp.float32)
        o = o * lax.rsqrt(jnp.mean(o * o, axis=-1, keepdims=True) + RMS_EPS) * gain
        return o.transpose(0, 2, 1, 3).reshape(b, Q_BLOCK, h * DIFF_V_DIM).astype(v.dtype)

    return _query_block_sweep(block_fn, s)

def _latent_attention(q, k, v):
    b, s, h, _ = q.shape
    q = q.transpose(0, 2, 1, 3)
    k = k.transpose(0, 2, 1, 3)
    v = v.transpose(0, 2, 1, 3)
    scale = MLA_QK_DIM ** -0.5

    def block_fn(i):
        start = i * Q_BLOCK
        qb = lax.dynamic_slice_in_dim(q, start, Q_BLOCK, axis=2)
        sc = jnp.einsum('bhqd,bhkd->bhqk', qb, k, preferred_element_type=jnp.float32) * scale
        p = jax.nn.softmax(jnp.where(_causal_mask(start, s), sc, NEG_INF), axis=-1)
        o = jnp.einsum('bhqk,bhkd->bhqd', p.astype(v.dtype), v, preferred_element_type=jnp.float32)
        return o.transpose(0, 2, 1, 3).reshape(b, Q_BLOCK, h * MLA_V_DIM).astype(v.dtype)

    return _query_block_sweep(block_fn, s)

def _memory_cross_attention(h, mem_n, w_q, w_kv, w_o):
    b, s, _ = h.shape
    n_mem = mem_n.shape[1]
    q = (h @ w_q).reshape(b, s, MEM_HEADS, MEM_HEAD_DIM)
    kv = (mem_n @ w_kv).reshape(b, n_mem, 2, MEM_HEADS, MEM_HEAD_DIM)
    k, v = kv[:, :, 0], kv[:, :, 1]
    sc = jnp.einsum('bshd,bmhd->bhsm', q, k, preferred_element_type=jnp.float32) * MEM_HEAD_DIM ** -0.5
    p = jax.nn.softmax(sc, axis=-1)
    o = jnp.einsum('bhsm,bmhd->bshd', p.astype(v.dtype), v).reshape(b, s, MEM_WIDTH)
    return o @ w_o

def _hierarchical_moe(h, w_group_router, b_group_router, w_expert_router, b_expert_router,
                      w_gate, w_up, w_down):
    b, s, d = h.shape
    n_tok = b * s
    hf = h.reshape(n_tok, d)
    g_logits = jnp.einsum('td,dg->tg', hf, w_group_router, preferred_element_type=jnp.float32) \
        + b_group_router.astype(jnp.float32)
    g_probs = jax.nn.softmax(g_logits, axis=-1)
    g_gate, g_sel = lax.top_k(g_probs, 1)
    e_logits = jnp.einsum('td,de->te', hf, w_expert_router, preferred_element_type=jnp.float32) \
        + b_expert_router.astype(jnp.float32)
    e_logits = e_logits.reshape(n_tok, N_GROUPS, EXPERTS_PER_GROUP)
    e_logits = jnp.take_along_axis(e_logits, g_sel[:, :, None], axis=1)[:, 0]
    e_probs = jax.nn.softmax(e_logits, axis=-1)
    e_gate, e_sel = lax.top_k(e_probs, TOP_K_IN_GROUP)
    e_gate = e_gate / jnp.sum(e_gate, axis=-1, keepdims=True)
    weights = (g_gate * e_gate).reshape(-1)
    expert_ids = (g_sel * EXPERTS_PER_GROUP + e_sel).reshape(-1)
    token_ids = jnp.repeat(jnp.arange(n_tok, dtype=jnp.int32), TOP_K_IN_GROUP)

    n_assign = n_tok * TOP_K_IN_GROUP
    n_blocks = -(-(n_assign + N_EXPERTS * (EXPERT_BLOCK - 1)) // EXPERT_BLOCK)
    n_slots = n_blocks * EXPERT_BLOCK
    order = jnp.argsort(expert_ids)
    sorted_e = expert_ids[order]
    counts = jnp.bincount(expert_ids, length=N_EXPERTS)
    padded = ((counts + EXPERT_BLOCK - 1) // EXPERT_BLOCK) * EXPERT_BLOCK
    seg_start = jnp.cumsum(counts) - counts
    padded_end = jnp.cumsum(padded)
    padded_start = padded_end - padded
    dest = padded_start[sorted_e] + (jnp.arange(n_assign) - seg_start[sorted_e])
    slot_token = jnp.full((n_slots,), n_tok, jnp.int32).at[dest].set(token_ids[order])
    slot_weight = jnp.zeros((n_slots,), jnp.float32).at[dest].set(weights[order])
    block_expert = jnp.minimum(
        jnp.searchsorted(padded_end, jnp.arange(n_blocks) * EXPERT_BLOCK, side='right'), N_EXPERTS - 1)
    h_pad = jnp.concatenate([hf, jnp.zeros((1, d), hf.dtype)], axis=0)

    def block_fn(args):
        tok, wt, e = args
        xb = h_pad[tok]
        hidden = jax.nn.silu(xb @ w_gate[e]) * (xb @ w_up[e])
        return (hidden @ w_down[e]) * wt[:, None].astype(hf.dtype)

    y = lax.map(block_fn, (slot_token.reshape(n_blocks, EXPERT_BLOCK),
                           slot_weight.reshape(n_blocks, EXPERT_BLOCK),
                           block_expert))
    out = jnp.zeros((n_tok + 1, d), hf.dtype).at[slot_token].add(y.reshape(n_slots, d))[:n_tok]
    return out.reshape(b, s, d)

def first_inputs(seed: int = 0) -> dict:
    key = jax.random.key(seed)
    ks = jax.random.split(key, 30)

    def w(k, shape, fan_in):
        return jax.random.normal(k, shape, jnp.float32) * fan_in ** -0.5

    def gain(k, shape):
        return 1.0 + 0.02 * jax.random.normal(k, shape, jnp.float32)

    x = jax.random.normal(ks[0], (BATCH, SEQ, D_MODEL), jnp.float32)
    mem = jax.random.normal(ks[1], (BATCH, N_MEM, D_MODEL), jnp.float32)
    offset = jax.random.randint(ks[2], (BATCH, 1), 0, POS_OFFSET_MAX, jnp.int32)
    positions = (offset + jnp.arange(SEQ, dtype=jnp.int32)[None, :]).astype(jnp.int32)
    return {
        'x': x,
        'mem': mem,
        'positions': positions,
        'norm_mix_g': gain(ks[3], (DEPTH, D_MODEL)),
        'w_in': w(ks[4], (DEPTH, D_MODEL, IN_PROJ_WIDTH), D_MODEL),
        'diff_lambda_q1': 0.1 * jax.random.normal(ks[5], (DEPTH, DIFF_HALF_DIM), jnp.float32),
        'diff_lambda_k1': 0.1 * jax.random.normal(ks[6], (DEPTH, DIFF_HALF_DIM), jnp.float32),
        'diff_lambda_q2': 0.1 * jax.random.normal(ks[7], (DEPTH, DIFF_HALF_DIM), jnp.float32),
        'diff_lambda_k2': 0.1 * jax.random.normal(ks[8], (DEPTH, DIFF_HALF_DIM), jnp.float32),
        'diff_out_g': gain(ks[9], (DEPTH, DIFF_V_DIM)),
        'mla_q_norm_g': gain(ks[10], (DEPTH, MLA_Q_RANK)),
        'w_mla_uq': w(ks[11], (DEPTH, MLA_Q_RANK, MLA_HEADS * MLA_QK_DIM), MLA_Q_RANK),
        'mla_kv_norm_g': gain(ks[12], (DEPTH, MLA_KV_RANK)),
        'w_mla_ukv': w(ks[13], (DEPTH, MLA_KV_RANK, MLA_HEADS * (MLA_NOPE_DIM + MLA_V_DIM)), MLA_KV_RANK),
        'mla_out_g': gain(ks[14], (DEPTH, MLA_WIDTH)),
        'w_out': w(ks[15], (DEPTH, MIX_WIDTH, D_MODEL), MIX_WIDTH),
        'norm_cross_g': gain(ks[16], (DEPTH, D_MODEL)),
        'norm_mem_g': gain(ks[17], (DEPTH, D_MODEL)),
        'w_mem_q': w(ks[18], (DEPTH, D_MODEL, MEM_WIDTH), D_MODEL),
        'w_mem_kv': w(ks[19], (DEPTH, D_MODEL, 2 * MEM_WIDTH), D_MODEL),
        'w_mem_o': w(ks[20], (DEPTH, MEM_WIDTH, D_MODEL), MEM_WIDTH),
        'norm_ffn_g': gain(ks[21], (DEPTH, D_MODEL)),
        'w_group_router': w(ks[22], (DEPTH, D_MODEL, N_GROUPS), D_MODEL),
        'b_group_router': 0.01 * jax.random.normal(ks[23], (DEPTH, N_GROUPS), jnp.float32),
        'w_expert_router': w(ks[24], (DEPTH, D_MODEL, N_EXPERTS), D_MODEL),
        'b_expert_router': 0.01 * jax.random.normal(ks[25], (DEPTH, N_EXPERTS), jnp.float32),
        'w_expert_gate': w(ks[26], (DEPTH, N_EXPERTS, D_MODEL, EXPERT_FF), D_MODEL),
        'w_expert_up': w(ks[27], (DEPTH, N_EXPERTS, D_MODEL, EXPERT_FF), D_MODEL),
        'w_expert_down': w(ks[28], (DEPTH, N_EXPERTS, EXPERT_FF, D_MODEL), EXPERT_FF),
        'norm_final_g': gain(ks[29], (D_MODEL,)),
    }

def first_block(x, mem, positions, norm_mix_g, w_in, diff_lambda_q1, diff_lambda_k1,
              diff_lambda_q2, diff_lambda_k2, diff_out_g, mla_q_norm_g, w_mla_uq,
              mla_kv_norm_g, w_mla_ukv, mla_out_g, w_out, norm_cross_g, norm_mem_g,
              w_mem_q, w_mem_kv, w_mem_o, norm_ffn_g, w_group_router, b_group_router,
              w_expert_router, b_expert_router, w_expert_gate, w_expert_up, w_expert_down,
              norm_final_g):
    b, s, _ = x.shape
    cos, sin = _rope_angles(positions, MLA_ROPE_DIM)
    for l in range(DEPTH):
        h = _rms_norm(x, norm_mix_g[l])
        proj = h @ w_in[l]
        q_d, k_d, v_d, c_q, c_kv, k_pe = jnp.split(proj, IN_SPLITS, axis=-1)

        lambda_init = 0.8 - 0.6 * math.exp(-0.3 * l)
        lam = (jnp.exp(jnp.sum(diff_lambda_q1[l].astype(jnp.float32) * diff_lambda_k1[l].astype(jnp.float32)))
               - jnp.exp(jnp.sum(diff_lambda_q2[l].astype(jnp.float32) * diff_lambda_k2[l].astype(jnp.float32)))
               + lambda_init)
        diff_out = _differential_attention(
            q_d.reshape(b, s, DIFF_HEADS, 2 * DIFF_HALF_DIM),
            k_d.reshape(b, s, DIFF_HEADS, 2 * DIFF_HALF_DIM),
            v_d.reshape(b, s, DIFF_HEADS, DIFF_V_DIM),
            positions, lam, lambda_init, diff_out_g[l])

        q_m = (_rms_norm(c_q, mla_q_norm_g[l]) @ w_mla_uq[l]).reshape(b, s, MLA_HEADS, MLA_QK_DIM)
        q_nope, q_pe = q_m[..., :MLA_NOPE_DIM], q_m[..., MLA_NOPE_DIM:]
        q_pe = _apply_rope(q_pe, cos[:, :, None, :], sin[:, :, None, :])
        q_m = jnp.concatenate([q_nope, q_pe], axis=-1)
        kv_m = (_rms_norm(c_kv, mla_kv_norm_g[l]) @ w_mla_ukv[l]).reshape(
            b, s, MLA_HEADS, MLA_NOPE_DIM + MLA_V_DIM)
        k_nope, v_m = kv_m[..., :MLA_NOPE_DIM], kv_m[..., MLA_NOPE_DIM:]
        k_pe = _apply_rope(k_pe, cos, sin)
        k_m = jnp.concatenate(
            [k_nope, jnp.broadcast_to(k_pe[:, :, None, :], (b, s, MLA_HEADS, MLA_ROPE_DIM))], axis=-1)
        mla_out = _rms_norm(_latent_attention(q_m, k_m, v_m), mla_out_g[l])

        x = x + jnp.concatenate([diff_out, mla_out], axis=-1) @ w_out[l]

        x = x + _memory_cross_attention(_rms_norm(x, norm_cross_g[l]), _rms_norm(mem, norm_mem_g[l]),
                                        w_mem_q[l], w_mem_kv[l], w_mem_o[l])

        x = x + _hierarchical_moe(_rms_norm(x, norm_ffn_g[l]), w_group_router[l], b_group_router[l],
                                  w_expert_router[l], b_expert_router[l],
                                  w_expert_gate[l], w_expert_up[l], w_expert_down[l])
    return _rms_norm(x, norm_final_g)


HEAD_DIM = 64
FOX_HEADS = 4
FOX_W = FOX_HEADS * HEAD_DIM
CONV_W = 256
CONV_K = 3
MLSTM_HEADS = 4
MLSTM_W = MLSTM_HEADS * HEAD_DIM
MLSTM_CHUNK = 64
SWA_Q_HEADS = 8
SWA_KV_HEADS = 2
SWA_W = SWA_Q_HEADS * HEAD_DIM
SWA_KV_W = SWA_KV_HEADS * HEAD_DIM
WINDOW = 128
REL_BUCKETS = 32
REL_MAX_DIST = 128
N_BRANCH = 4
D_FF = -(-8 * D_MODEL // (3 * 256)) * 256
EPS = 1e-6

SPLIT_SIZES = (FOX_W, FOX_W, FOX_W, FOX_HEADS,
               CONV_W, CONV_W, CONV_W,
               MLSTM_W, MLSTM_W, MLSTM_W, MLSTM_HEADS, MLSTM_HEADS, MLSTM_W,
               SWA_W, SWA_KV_W, SWA_KV_W,
               N_BRANCH * D_MODEL)
IN_COLS = sum(SPLIT_SIZES)


def rms_norm(x, gain):
    xf = x.astype(jnp.float32)
    y = xf * lax.rsqrt(jnp.mean(xf * xf, axis=-1, keepdims=True) + EPS)
    return (y * gain.astype(jnp.float32)).astype(x.dtype)

def t5_bucket(n):
    max_exact = REL_BUCKETS // 2
    nf = jnp.maximum(n, 1).astype(jnp.float32)
    large = max_exact + (jnp.log(nf / max_exact) / math.log(REL_MAX_DIST / max_exact)
                         * (REL_BUCKETS - max_exact)).astype(jnp.int32)
    large = jnp.minimum(large, REL_BUCKETS - 1)
    return jnp.where(n < max_exact, n, large)

def fox_attention(q, k, v, f_logit):
    B, S, H, d = q.shape
    nblk = S // Q_BLOCK
    c = jnp.cumsum(jax.nn.log_sigmoid(f_logit.astype(jnp.float32)), axis=1)
    c_t = c.transpose(0, 2, 1)
    qb = q.reshape(B, nblk, Q_BLOCK, H, d).transpose(1, 0, 2, 3, 4)
    cb = c.reshape(B, nblk, Q_BLOCK, H).transpose(1, 0, 3, 2)
    key_pos = jnp.arange(S)
    scale = d ** -0.5

    def block(args):
        qi, ci, bi = args
        s = jnp.einsum('bqhd,bkhd->bhqk', qi, k).astype(jnp.float32) * scale
        s = s + (ci[..., :, None] - c_t[..., None, :])
        q_pos = bi * Q_BLOCK + jnp.arange(Q_BLOCK)
        s = jnp.where(key_pos[None, :] <= q_pos[:, None], s, -jnp.inf)
        p = jax.nn.softmax(s, axis=-1).astype(v.dtype)
        return jnp.einsum('bhqk,bkhd->bqhd', p, v)

    out = lax.map(block, (qb, cb, jnp.arange(nblk)))
    return out.transpose(1, 0, 2, 3, 4).reshape(B, S, H * d)

def short_conv_mixer(u, b_gate, c_gate, w):
    z = c_gate * u
    y = lax.conv_general_dilated(z, w[:, None, :], window_strides=(1,),
                                 padding=[(CONV_K - 1, 0)],
                                 dimension_numbers=('NWC', 'WIO', 'NWC'),
                                 feature_group_count=z.shape[-1])
    return b_gate * y

def mlstm_chunkwise(q, k, v, i_pre, f_pre):
    out_dtype = q.dtype
    f32 = jnp.float32
    B, S, H, d = q.shape
    L = MLSTM_CHUNK
    nc = S // L
    q = q.astype(f32).reshape(B, nc, L, H, d) * d ** -0.5
    k = k.astype(f32).reshape(B, nc, L, H, d)
    v = v.astype(f32).reshape(B, nc, L, H, d)
    log_i = i_pre.astype(f32).reshape(B, nc, L, H)
    log_f = jax.nn.log_sigmoid(f_pre.astype(f32)).reshape(B, nc, L, H)
    b = jnp.cumsum(log_f, axis=2)
    b_last = b[:, :, -1]

    a = b_last[:, :, None] - b + log_i
    m_loc = a.max(axis=2)
    w_state = jnp.exp(a - m_loc[:, :, None])
    c_loc = jnp.einsum('bclh,bclhd,bclhe->bchde', w_state, k, v)
    n_loc = jnp.einsum('bclh,bclhd->bchd', w_state, k)

    def step(carry, xs):
        c_st, n_st, m_st = carry
        bl, ml, cl, nl = xs
        m_new = jnp.maximum(bl + m_st, ml)
        decay = jnp.exp(bl + m_st - m_new)
        wl = jnp.exp(ml - m_new)
        c_new = decay[..., None, None] * c_st + wl[..., None, None] * cl
        n_new = decay[..., None] * n_st + wl[..., None] * nl
        return (c_new, n_new, m_new), (c_st, n_st, m_st)

    init = (jnp.zeros((B, H, d, d), f32), jnp.zeros((B, H, d), f32), jnp.zeros((B, H), f32))
    xs = (jnp.moveaxis(b_last, 1, 0), jnp.moveaxis(m_loc, 1, 0),
          jnp.moveaxis(c_loc, 1, 0), jnp.moveaxis(n_loc, 1, 0))
    _, (c_prev, n_prev, m_prev) = lax.scan(step, init, xs)
    c_prev = jnp.moveaxis(c_prev, 0, 1)
    n_prev = jnp.moveaxis(n_prev, 0, 1)
    m_prev = jnp.moveaxis(m_prev, 0, 1)

    g = b + m_prev[:, :, None, :]
    dmat = b[:, :, :, None, :] - b[:, :, None, :, :] + log_i[:, :, None, :, :]
    causal = jnp.tril(jnp.ones((L, L), dtype=bool))
    dmat = jnp.where(causal[None, None, :, :, None], dmat, -jnp.inf)
    m_t = jnp.maximum(g, dmat.max(axis=3))
    s_w = jnp.einsum('bcthd,bcshd->bctsh', q, k) * jnp.exp(dmat - m_t[:, :, :, None, :])
    inter = jnp.exp(g - m_t)
    num = (jnp.einsum('bctsh,bcshe->bcthe', s_w, v)
           + inter[..., None] * jnp.einsum('bcthd,bchde->bcthe', q, c_prev))
    den = s_w.sum(axis=3) + inter * jnp.einsum('bcthd,bchd->bcth', q, n_prev)
    h = num / jnp.maximum(jnp.abs(den), jnp.exp(-m_t))[..., None]
    return h.reshape(B, S, H, d).astype(out_dtype)

def swa_attention(q, k, v, sinks, bias):
    B, S, Hq, d = q.shape
    Hkv = k.shape[2]
    G = Hq // Hkv
    W = WINDOW
    nb = S // W
    qb = q.reshape(B, nb, W, Hkv, G, d)

    def band(t):
        tp = jnp.pad(t, ((0, 0), (W, 0), (0, 0), (0, 0))).reshape(B, nb + 1, W, Hkv, d)
        return jnp.concatenate([tp[:, :-1], tp[:, 1:]], axis=2)

    kb, vb = band(k), band(v)
    s = jnp.einsum('bnqhgd,bnjhd->bnhgqj', qb, kb).astype(jnp.float32) * d ** -0.5
    s = s + bias.astype(jnp.float32).reshape(Hkv, G, W, 2 * W)
    qi = jnp.arange(W)[:, None]
    kj = jnp.arange(2 * W)[None, :]
    dist = qi + W - kj
    in_window = (dist >= 0) & (dist < WINDOW)
    key_pos = jnp.arange(nb)[:, None, None] * W - W + kj[None]
    valid = in_window[None] & (key_pos >= 0)
    s = jnp.where(valid[None, :, None, None], s, -jnp.inf)
    sink = jnp.broadcast_to(sinks.astype(jnp.float32).reshape(1, 1, Hkv, G, 1, 1),
                            s.shape[:-1] + (1,))
    p = jax.nn.softmax(jnp.concatenate([s, sink], axis=-1), axis=-1)[..., :-1]
    out = jnp.einsum('bnhgqj,bnjhd->bnqhgd', p.astype(v.dtype), vb)
    return out.reshape(B, S, Hq * d)

def second_inputs(seed: int = 0) -> dict:
    key = jax.random.key(seed)
    ks = jax.random.split(key, 24)

    def nrm(k, shape, scale):
        return jax.random.normal(k, shape, jnp.float32) * scale

    return {
        'x': nrm(ks[0], (BATCH, SEQ, D_MODEL), 1.0),
        'rel_bias': nrm(ks[1], (REL_BUCKETS, SWA_Q_HEADS), 0.5),
        'attn_norm': 1.0 + nrm(ks[2], (DEPTH, D_MODEL), 0.05),
        'w_in': nrm(ks[3], (DEPTH, D_MODEL, IN_COLS), D_MODEL ** -0.5),
        'fox_f_bias': 3.0 + nrm(ks[4], (DEPTH, FOX_HEADS), 1.0),
        'fox_q_gain': 1.0 + nrm(ks[5], (DEPTH, HEAD_DIM), 0.05),
        'fox_k_gain': 1.0 + nrm(ks[6], (DEPTH, HEAD_DIM), 0.05),
        'conv_w': nrm(ks[7], (DEPTH, CONV_K, CONV_W), CONV_K ** -0.5),
        'mlstm_i_bias': nrm(ks[8], (DEPTH, MLSTM_HEADS), 0.1),
        'mlstm_f_bias': 4.0 + nrm(ks[9], (DEPTH, MLSTM_HEADS), 1.0),
        'mlstm_h_gain': 1.0 + nrm(ks[10], (DEPTH, MLSTM_W), 0.05),
        'swa_q_gain': 1.0 + nrm(ks[11], (DEPTH, HEAD_DIM), 0.05),
        'swa_k_gain': 1.0 + nrm(ks[12], (DEPTH, HEAD_DIM), 0.05),
        'swa_sinks': nrm(ks[13], (DEPTH, SWA_Q_HEADS), 1.0),
        'w_fox_out': nrm(ks[14], (DEPTH, FOX_W, D_MODEL), FOX_W ** -0.5),
        'w_conv_out': nrm(ks[15], (DEPTH, CONV_W, D_MODEL), CONV_W ** -0.5),
        'w_mlstm_out': nrm(ks[16], (DEPTH, MLSTM_W, D_MODEL), MLSTM_W ** -0.5),
        'w_swa_out': nrm(ks[17], (DEPTH, SWA_W, D_MODEL), SWA_W ** -0.5),
        'w_merge_out': nrm(ks[18], (DEPTH, D_MODEL, D_MODEL), D_MODEL ** -0.5),
        'ffn_norm': 1.0 + nrm(ks[19], (DEPTH, D_MODEL), 0.05),
        'w_gate': nrm(ks[20], (DEPTH, D_MODEL, D_FF), D_MODEL ** -0.5),
        'w_up': nrm(ks[21], (DEPTH, D_MODEL, D_FF), D_MODEL ** -0.5),
        'w_down': nrm(ks[22], (DEPTH, D_FF, D_MODEL), D_FF ** -0.5),
    }

def second_block(x, rel_bias, attn_norm, w_in, fox_f_bias, fox_q_gain, fox_k_gain, conv_w,
              mlstm_i_bias, mlstm_f_bias, mlstm_h_gain, swa_q_gain, swa_k_gain, swa_sinks,
              w_fox_out, w_conv_out, w_mlstm_out, w_swa_out, w_merge_out, ffn_norm,
              w_gate, w_up, w_down):
    B, S, _ = x.shape
    split_points = np.cumsum(SPLIT_SIZES)[:-1].tolist()

    dist = jnp.arange(WINDOW)[:, None] + WINDOW - jnp.arange(2 * WINDOW)[None, :]
    swa_bias = rel_bias[t5_bucket(jnp.maximum(dist, 0))].transpose(2, 0, 1)

    for l in range(DEPTH):
        h = rms_norm(x, attn_norm[l])
        proj = jnp.einsum('bsd,dc->bsc', h, w_in[l])
        (fq, fk, fv, ff, cu, cb, cc, mq, mk, mv, mi, mf, mo, sq, sk, sv,
         gates) = jnp.split(proj, split_points, axis=-1)

        fq = rms_norm(fq.reshape(B, S, FOX_HEADS, HEAD_DIM), fox_q_gain[l])
        fk = rms_norm(fk.reshape(B, S, FOX_HEADS, HEAD_DIM), fox_k_gain[l])
        fv = fv.reshape(B, S, FOX_HEADS, HEAD_DIM)
        y_fox = fox_attention(fq, fk, fv, ff + fox_f_bias[l])

        y_conv = short_conv_mixer(cu, cb, cc, conv_w[l])

        hm = mlstm_chunkwise(mq.reshape(B, S, MLSTM_HEADS, HEAD_DIM),
                             mk.reshape(B, S, MLSTM_HEADS, HEAD_DIM),
                             mv.reshape(B, S, MLSTM_HEADS, HEAD_DIM),
                             mi + mlstm_i_bias[l], mf + mlstm_f_bias[l])
        hm = rms_norm(hm, mlstm_h_gain[l].reshape(MLSTM_HEADS, HEAD_DIM))
        y_mlstm = jax.nn.sigmoid(mo) * hm.reshape(B, S, MLSTM_W)

        sq = rms_norm(sq.reshape(B, S, SWA_Q_HEADS, HEAD_DIM), swa_q_gain[l])
        sk = rms_norm(sk.reshape(B, S, SWA_KV_HEADS, HEAD_DIM), swa_k_gain[l])
        sv = sv.reshape(B, S, SWA_KV_HEADS, HEAD_DIM)
        y_swa = swa_attention(sq, sk, sv, swa_sinks[l], swa_bias)

        g = jax.nn.sigmoid(gates.reshape(B, S, N_BRANCH, D_MODEL))
        merged = (g[:, :, 0] * jnp.einsum('bsw,wd->bsd', y_fox, w_fox_out[l])
                  + g[:, :, 1] * jnp.einsum('bsw,wd->bsd', y_conv, w_conv_out[l])
                  + g[:, :, 2] * jnp.einsum('bsw,wd->bsd', y_mlstm, w_mlstm_out[l])
                  + g[:, :, 3] * jnp.einsum('bsw,wd->bsd', y_swa, w_swa_out[l]))
        x = x + jnp.einsum('bsd,de->bse', merged, w_merge_out[l])

        h = rms_norm(x, ffn_norm[l])
        act = jax.nn.silu(jnp.einsum('bsd,df->bsf', h, w_gate[l])) * jnp.einsum('bsd,df->bsf', h, w_up[l])
        x = x + jnp.einsum('bsf,fd->bsd', act, w_down[l])
    return x


def setup_inputs(seed=0):
    out = dict(first_inputs(seed))
    for name, value in second_inputs(seed + 1).items():
        if name != "x":
            out[name + "_2"] = value
    return out


def reference(
    x, mem, positions, norm_mix_g, w_in, diff_lambda_q1, diff_lambda_k1, diff_lambda_q2,
    diff_lambda_k2, diff_out_g, mla_q_norm_g, w_mla_uq, mla_kv_norm_g, w_mla_ukv, mla_out_g,
    w_out, norm_cross_g, norm_mem_g, w_mem_q, w_mem_kv, w_mem_o, norm_ffn_g, w_group_router,
    b_group_router, w_expert_router, b_expert_router, w_expert_gate, w_expert_up, w_expert_down,
    norm_final_g, rel_bias_2, attn_norm_2, w_in_2, fox_f_bias_2, fox_q_gain_2, fox_k_gain_2,
    conv_w_2, mlstm_i_bias_2, mlstm_f_bias_2, mlstm_h_gain_2, swa_q_gain_2, swa_k_gain_2,
    swa_sinks_2, w_fox_out_2, w_conv_out_2, w_mlstm_out_2, w_swa_out_2, w_merge_out_2,
    ffn_norm_2, w_gate_2, w_up_2, w_down_2,
):
    x = first_block(
        x, mem, positions, norm_mix_g, w_in, diff_lambda_q1, diff_lambda_k1, diff_lambda_q2,
        diff_lambda_k2, diff_out_g, mla_q_norm_g, w_mla_uq, mla_kv_norm_g, w_mla_ukv, mla_out_g,
        w_out, norm_cross_g, norm_mem_g, w_mem_q, w_mem_kv, w_mem_o, norm_ffn_g, w_group_router,
        b_group_router, w_expert_router, b_expert_router, w_expert_gate, w_expert_up,
        w_expert_down, norm_final_g,
    )
    return second_block(
        x, rel_bias_2, attn_norm_2, w_in_2, fox_f_bias_2, fox_q_gain_2, fox_k_gain_2, conv_w_2,
        mlstm_i_bias_2, mlstm_f_bias_2, mlstm_h_gain_2, swa_q_gain_2, swa_k_gain_2, swa_sinks_2,
        w_fox_out_2, w_conv_out_2, w_mlstm_out_2, w_swa_out_2, w_merge_out_2, ffn_norm_2,
        w_gate_2, w_up_2, w_down_2,
    )


_drawn_inputs = setup_inputs


def setup_inputs(seed=0):
    import zlib

    import numpy as np

    out = dict(_drawn_inputs(seed))
    spreads = {}
    factors = {'diff_lambda_k2': 7.369,
     'norm_cross_g': 5.804,
     'norm_mem_g': 4.333,
     'b_group_router': 11.488,
     'b_expert_router': 3.342,
     'fox_q_gain_2': 7.179,
     'fox_k_gain_2': 8.0,
     'mlstm_i_bias_2': 200.0,
     'mlstm_h_gain_2': 4.057,
     'swa_q_gain_2': 8.0,
     'swa_k_gain_2': 8.0,
     'swa_sinks_2': 200.0,
     'rel_bias_2': 3.206}
    for name, (base, spread) in spreads.items():
        noise = np.random.default_rng([zlib.crc32(name.encode()), seed]).standard_normal(out[name].shape)
        drawn = base * np.exp(spread * noise) if base else spread * noise
        out[name] = jnp.asarray(drawn.astype(out[name].dtype))
    for name, factor in factors.items():
        out[name] = (out[name] * factor).astype(out[name].dtype)
    return out
```

```python
from contextlib import ExitStack

import numpy as np

import concourse.bass as bass
from concourse import mybir

F32 = mybir.dt.float32
I32 = mybir.dt.int32
U32 = mybir.dt.uint32
ALU = mybir.AluOpType
ACT = mybir.ActivationFunctionType
AX = mybir.AxisListType.X

P = 128
S = 1024
D = 1024
ST = S // P
KD = D // P
HALF = 512
EPS = 1e-6
NEG = -1e30

DIFF_HEADS, DIFF_HALF, DIFF_V = 8, 32, 64
DIFF_QK = DIFF_HEADS * 2 * DIFF_HALF
DIFF_W = DIFF_HEADS * DIFF_V
MLA_HEADS, MLA_QR, MLA_KVR, NOPE, ROPE, MLA_V = 8, 256, 128, 64, 32, 64
MLA_QK = NOPE + ROPE
MLA_W = MLA_HEADS * MLA_V
COL_VD = 2 * DIFF_QK
COL_CQ = COL_VD + DIFF_W
COL_KPE = COL_CQ + MLA_QR + MLA_KVR
LAMBDA_INIT = 0.8 - 0.6
MEM_T, MEM_HEADS, MEM_HD = 256, 4, 128
MEM_W = MEM_HEADS * MEM_HD

GROUPS, PER_GROUP = 4, 8
EXPERTS = GROUPS * PER_GROUP
FF = 256
BLK = 128
N_BLOCKS = -(-(2 * S + EXPERTS * (BLK - 1)) // BLK)

HD = 64
C_FQ, C_FF, C_CU, C_MQ, C_MI, C_MO, C_SQ = 0, 768, 772, 1540, 2308, 2316, 2572
C_FV, C_MV, C_SV, C_GATES = 512, 2052, 3212, 3340
D_FF = 2816
FFC = D_FF // P
WINDOW = 128

GAIN_ROWS = {}
_row = 0
for _name, _count in (("norm_mix_g", 8), ("norm_cross_g", 8), ("norm_mem_g", 8), ("norm_ffn_g", 8),
                      ("attn_norm_2", 8), ("ffn_norm_2", 8), ("mla_out_g", 4), ("mla_q_norm_g", 2),
                      ("mla_kv_norm_g", 1), ("mlstm_h_gain_2", 2), ("conv_w_2", 6)):
    GAIN_ROWS[_name] = (_row, _count)
    _row += _count
for _name in ("diff_out_g", "fox_q_gain_2", "fox_k_gain_2", "swa_q_gain_2", "swa_k_gain_2"):
    GAIN_ROWS[_name] = (_row, 1)
    _row += 1
N_GAINS = _row


SEMS = 24


class Chain:

    def __init__(self, sem):
        self.sem, self.total, self.start, self.count = sem, 0, 0, 0

    def enter(self, i, per):
        self.start, self.count, self.per = self.total + i * per, 0, per

    def leave(self, rounds):
        assert self.count == self.per, (self.count, self.per)
        self.total += rounds * self.per
        self.start, self.count = self.total, 0

    def step(self):
        self.count += 1
        return self.start + self.count

    def settle(self):
        self.total += self.count
        self.start, self.count = self.total, 0


class Core:

    def __init__(self, nc, ctx, dram, out, scratch):
        self.nc, self.ctx, self.dram, self.out = nc, ctx, dram, out
        self.scratch = scratch
        self.chains, self.names = {}, {}
        sb = self.sb
        self.banks = [[ctx.enter_context(nc.semaphore(f"bank{n}_{i}")) for i in range(SEMS)] for n in range(2)]
        self.bank, self.taken = 0, 0
        self.soft = {n: ctx.enter_context(nc.semaphore(n)) for n in (
            "token_numbers_scattered", "rows_gathered0", "rows_gathered1", "outputs_gathered0", "outputs_gathered1")}
        self.X = sb("X", [P, ST, D])
        self.HT = sb("HT", [P, KD, S])
        self.ident = sb("ident", [P, P])
        self.ones = sb("ones", [P, P])
        self.ones64 = sb("ones64", [P, P])
        self.gains = sb("gains", [P, N_GAINS])
        self.ssq = sb("ssq", [P, ST])
        self.mean = sb("mean", [P, ST])
        self.root = sb("root", [P, ST])
        self.rstd = sb("rstd", [P, ST])
        for e in ("dve", "act", "pool"):
            self.chains[e] = Chain(ctx.enter_context(nc.semaphore(f"{e}_own")))

    def unused(self, name):
        self.names[name] = self.names.get(name, 0) + 1
        return name if self.names[name] == 1 else f"{name}_{self.names[name]}"

    def sb(self, name, shape, dt=F32, ctx=None):
        return (ctx or self.ctx).enter_context(self.nc.sbuf_tensor(self.unused(name), shape, dt))

    def ps(self, name, shape, ctx):
        return ctx.enter_context(self.nc.psum_tensor(self.unused(name), shape, F32))

    def phase(self):
        self.bank, self.taken = 1 - self.bank, 0
        other = [s.num for s in self.banks[1 - self.bank]]
        self.nc.gpsimd.sem_clear(range(min(other), max(other) + 1))
        return ExitStack()

    def sems(self, phase, names):
        n = len(names.split())
        got = self.banks[self.bank][self.taken:self.taken + n]
        assert len(got) == n, phase
        self.taken += n
        return got

    def gain(self, name, extra=0, count=None):
        row, n = GAIN_ROWS[name]
        return self.gains[:, row + extra:row + extra + (count or n)]

    def own(self, engine_name, engine):
        chain = self.chains[engine_name]

        def link(ins):
            value = chain.step()
            ins.then_inc(chain.sem, 1)
            engine.wait_ge(chain.sem, value)
        return link


def setup(k):
    nc = k.nc
    with k.phase() as ctx:
        rows = k.sb("gain_rows", [N_GAINS, P], ctx=ctx)
        turned = k.ps("turned", [P, N_GAINS], ctx)
        x_in, gains_in, ident_made, gains_turned = k.sems("setup", "x_in gains_in ident_made gains_turned")
        block = ctx.enter_context(nc.Block())
        doubled = ("diff_out_g", "fox_q_gain_2", "fox_k_gain_2", "swa_q_gain_2", "swa_k_gain_2")
        n_loads = len(GAIN_ROWS) + len(doubled)

        @block.sync
        def _(sp):
            for name, (row, count) in GAIN_ROWS.items():
                if name in doubled:
                    for half in range(2):
                        sp.dma_start(rows[row:row + 1, half * 64:half * 64 + 64],
                                     k.dram[name]).then_inc(gains_in, 16)
                else:
                    flat = "l k c -> (l k c)" if name == "conv_w_2" else "l c -> (l c)"
                    src = k.dram[name].rearrange(flat).rearrange("(r c) -> r c", c=P)
                    sp.dma_start(rows[row:row + count, :], src).then_inc(gains_in, 16)

        @block.scalar
        def _(act):
            x = k.dram["x"].rearrange("a (t p) d -> p (a t) d", p=P)
            with act.Fori(0, ST) as t:
                act.dma_start(k.X[:, bass.ds(t, 1), :], x[:, bass.ds(t, 1), :]).then_inc(x_in, 16)
            act.wait_ge(x_in, 16 * ST)

        @block.gpsimd
        def _(pool):
            link = k.own("pool", pool)
            link(nc.gpsimd.memset(k.ident[:], 0.0))
            nc.gpsimd.affine_select(out=k.ident[:], in_=k.ident[:], compare_op=ALU.not_equal, fill=1.0,
                                    base=0, pattern=[[-1, P]], channel_multiplier=1).then_inc(ident_made, 1)
            link(nc.gpsimd.memset(k.ones64[:], 0.0))
            link(nc.gpsimd.memset(k.ones[:], 1.0))

        @block.vector
        def _(dve):
            link = k.own("dve", dve)
            dve.wait_ge(k.chains["pool"].sem, 3)
            link(nc.vector.memset(k.ones64[0:64, 0:64], 1.0))
            link(nc.vector.memset(k.ones64[64:128, 64:128], 1.0))
            dve.wait_ge(gains_turned, 1)
            link(nc.vector.tensor_copy(k.gains[:], turned[:, :]))

        @block.tensor
        def _(pe):
            pe.wait_ge(ident_made, 1)
            pe.wait_ge(gains_in, 16 * n_loads)
            nc.tensor.transpose(turned[:, :], rows[:, :], k.ident[0:N_GAINS, 0:N_GAINS]).then_inc(gains_turned, 1)

        for e in ("dve", "pool"):
            k.chains[e].settle()


def norm_turn(k, phase, X, tiles, gain, HT, rows_out=None):
    nc = k.nc
    pairs = tiles // 2
    with k.phase() as ctx:
        junk = [k.sb(f"{phase}_junk{b}", [P, D], ctx=ctx) for b in range(2)]
        scaled = [k.sb(f"{phase}_scaled{b}", [P, D], ctx=ctx) for b in range(2)]
        turned = [k.ps(f"{phase}_turned{b}", [P, KD, P], ctx) for b in range(2)]
        even_squares, odd_squares, mean_ready, root_ready, rstd_ready, scaled_ready, turns, stored, kept0, kept1 = k.sems(
            phase, "even_squares odd_squares mean_ready root_ready rstd_ready scaled_ready turns stored kept0 kept1")
        kept = (kept0, kept1)
        block = ctx.enter_context(nc.Block())

        @block.scalar
        def _(act):
            act.sem_inc(kept0, 16)
            act.sem_inc(kept1, 16)
            for i in range(pairs):
                if i:
                    act.wait_ge(even_squares, i)
                nc.scalar.activation(junk[0][:], X[:, 2 * i, :], ACT.Square,
                                     accum_out=k.ssq[:, 2 * i:2 * i + 1]).then_inc(even_squares, 1)
            act.wait_ge(mean_ready, 1)
            nc.scalar.activation(k.root[:, 0:tiles], k.mean[:, 0:tiles], ACT.Sqrt).then_inc(root_ready, 1)
            act.wait_ge(rstd_ready, 1)
            with act.Fori(0, pairs) as i:
                for b in range(2):
                    act.wait_ge(turns, 2 * i + b + 1)
                    if rows_out is not None:
                        act.wait_ge(kept[b], 16 * i + 16)
                    nc.scalar.activation(scaled[b][:], row_of(X, 2 * i + b), ACT.Copy,
                                         scale=k.rstd[:, bass.ds(2 * i + b, 1)]).then_inc(scaled_ready, 1)

        @block.vector
        def _(dve):
            dve.sem_inc(stored, 1)
            link = k.own("dve", dve)
            for i in range(pairs):
                if i:
                    dve.wait_ge(odd_squares, i)
                nc.vector.tensor_tensor_reduce(out=junk[1][:], in0=X[:, 2 * i + 1, :], in1=X[:, 2 * i + 1, :],
                                               scale=1.0, scalar=0.0, op0=ALU.mult, op1=ALU.add,
                                               accum_out=k.ssq[:, 2 * i + 1:2 * i + 2]).then_inc(odd_squares, 1)
            dve.wait_ge(odd_squares, pairs)
            dve.wait_ge(even_squares, pairs)
            nc.vector.tensor_scalar(k.mean[:, 0:tiles], k.ssq[:, 0:tiles], 1.0 / D, EPS,
                                    ALU.mult, ALU.add).then_inc(mean_ready, 1)
            dve.wait_ge(root_ready, 1)
            nc.vector.reciprocal(k.rstd[:, 0:tiles], k.root[:, 0:tiles]).then_inc(rstd_ready, 1)
            with dve.Fori(0, pairs) as i:
                for b in range(2):
                    dve.wait_ge(turns, 2 * i + b + 1 + 2)
                    nc.vector.tensor_tensor(HT[:, :, bass.ds((2 * i + b) * P, P)], turned[b][:, :, :],
                                            gain.rearrange("p (c o) -> p c o", o=1).broadcast_to([P, KD, P]), ALU.mult).then_inc(stored, 1)

        if rows_out is not None:
            @block.sync
            def _(sp):
                with sp.Fori(0, pairs) as i:
                    for b in range(2):
                        sp.wait_ge(scaled_ready, 2 * i + b + 1)
                        sp.dma_start(rows_out[bass.ds((2 * i + b) * P, P), :], scaled[b][:]).then_inc(kept[b], 16)
                sp.wait_ge(kept0, 16 * pairs + 16)
                sp.wait_ge(kept1, 16 * pairs + 16)

        @block.tensor
        def _(pe):
            pe.sem_inc(turns, 2)
            with pe.Fori(0, pairs) as i:
                for b in range(2):
                    pe.wait_ge(scaled_ready, 2 * i + b + 1)
                    if b == 0:
                        pe.wait_ge(stored, 2 * i + 1)
                    for c in range(KD):
                        last = nc.tensor.transpose(turned[b][:, c, :], scaled[b][:, c * P:(c + 1) * P], k.ident[:])
                    last.then_inc(turns, 1)


def row_of(X, t):
    return X[:, bass.ds(t, 1), :].rearrange("p a d -> p (a d)")


def project_rows(k, phase, w, n_chunks, src, kc, dest, scale=1.0, gain=None, tokens=S):
    nc = k.nc
    to_dram = not isinstance(dest, tuple)
    with k.phase() as ctx:
        weights = [k.sb(f"{phase}_w{b}", [P, kc, P], ctx=ctx) for b in range(2)]
        stage = [k.sb(f"{phase}_stage{b}", [P, tokens], ctx=ctx) for b in range(2)]
        acc = [k.ps(f"{phase}_acc{b}", [P, max(tokens, HALF)], ctx) for b in range(2)]
        if gain is not None:
            square = k.sb(f"{phase}_square", [P, S], ctx=ctx)
            norm = k.sb(f"{phase}_norm", [P, S], ctx=ctx)
            sums = k.ps(f"{phase}_sums", [P, S], ctx)
            squared, summed, meaned, rooted = k.sems(phase, "squared summed meaned rooted")
        w_in0, w_in1, products, evacuated, stored0, stored1 = k.sems(
            phase, "w_in0 w_in1 products evacuated stored0 stored1")
        w_in, stored = (w_in0, w_in1), (stored0, stored1)
        block = ctx.enter_context(nc.Block())
        pairs, tail = n_chunks // 2, n_chunks % 2
        w_view = w.rearrange("(c p) n -> p c n", p=P)

        def chunks(engine, body):
            with engine.Fori(0, pairs) as i:
                for b in range(2):
                    body(i * 2 + b, b, i)
            if tail:
                body(pairs * 2, 0, pairs)

        @block.sync
        def _(sp):
            def load(j, b, r):
                sp.wait_ge(products, j + 1)
                sp.dma_start(weights[b][:, :, :], w_view[:, :, bass.ds(j * P, P)]).then_inc(w_in[b], 16)
            chunks(sp, load)

        @block.tensor
        def _(pe):
            if gain is not None:
                pe.sem_inc(summed, 1)
            pe.sem_inc(products, 2)

            def multiply(j, b, r):
                pe.wait_ge(w_in[b], 16 * r + 16)
                pe.wait_ge(evacuated, j + 1)
                for c in range(kc):
                    for at in range(0, tokens, HALF):
                        to = min(at + HALF, tokens)
                        last = nc.tensor.matmul(acc[b][:, at:to], weights[b][:, c, :], src[:, c, at:to],
                                                start=(c == 0), stop=(c == kc - 1))
                last.then_inc(products, 1)
                if gain is not None:
                    pe.wait_ge(squared, j + 1)
                    pe.wait_ge(meaned, j + 1)
                    for h in range(2):
                        last = nc.tensor.matmul(sums[:, h * HALF:(h + 1) * HALF], k.ones64[:],
                                                square[:, h * HALF:(h + 1) * HALF], start=True, stop=True)
                    last.then_inc(summed, 1)
            chunks(pe, multiply)

        @block.scalar
        def _(act):
            act.sem_inc(stored0, 16)
            act.sem_inc(stored1, 16)
            if gain is None:
                act.sem_inc(evacuated, 2)

            def leave(j, b, r):
                act.wait_ge(products, j + 1 + 2)
                if gain is not None:
                    act.wait_ge(summed, j + 1)
                    nc.scalar.activation(square[:], acc[b][:], ACT.Square).then_inc(squared, 1)
                    act.wait_ge(meaned, j + 1 + 1)
                    nc.scalar.activation(norm[:], norm[:], ACT.Sqrt).then_inc(rooted, 1)
                elif to_dram:
                    act.wait_ge(stored[b], 16 * r + 16)
                    nc.scalar.activation(stage[b][:], acc[b][:, 0:tokens], ACT.Copy, scale=scale).then_inc(evacuated, 1)
                else:
                    nc.scalar.activation(dest[0][:, bass.ds(j, 1), :].rearrange("p a s -> p (a s)"),
                                         acc[b][:, 0:tokens], ACT.Copy, scale=scale).then_inc(evacuated, 1)
                if to_dram:
                    act.wait_ge(evacuated, j + 1 + 2)
                    act.dma_start(dest.rearrange("(c p) s -> p c s", p=P)[:, bass.ds(j, 1), :].rearrange(
                        "p a s -> p (a s)"), stage[b][:]).then_inc(stored[b], 16)
            chunks(act, leave)
            if to_dram:
                act.wait_ge(stored0, 16 * (pairs + tail) + 16)
                act.wait_ge(stored1, 16 * pairs + 16)

        if gain is not None:
            @block.vector
            def _(dve):
                dve.sem_inc(meaned, 1)
                dve.sem_inc(evacuated, 2)
                link = k.own("dve", dve)
                chain = k.chains["dve"]

                def normalise(j, b, r):
                    dve.wait_ge(summed, j + 1 + 1)
                    nc.vector.tensor_scalar(norm[:], sums[:], 1.0 / HD, EPS, ALU.mult, ALU.add).then_inc(meaned, 1)
                    dve.wait_ge(rooted, j + 1)
                    link(nc.vector.reciprocal(norm[:], norm[:]))
                    dve.wait_ge(stored[b], 16 * r + 16)
                    nc.vector.scalar_tensor_tensor(out=stage[b][:], in0=acc[b][:], scalar=gain[:, bass.ds(j, 1)],
                                                   in1=norm[:], op0=ALU.mult, op1=ALU.mult).then_inc(evacuated, 1)
                with dve.Fori(0, pairs) as i:
                    chain.enter(i, 2)
                    for b in range(2):
                        normalise(i * 2 + b, b, i)
                    chain.leave(pairs)
                if tail:
                    normalise(pairs * 2, 0, pairs)
                    chain.settle()


def project_tokens(k, phase, loads, n_cols, src, kc, dest, tiles=ST):
    nc = k.nc
    pieces = [(c, min(HALF, n_cols - c)) for c in range(0, n_cols, HALF)]
    with k.phase() as ctx:
        weights = k.sb(f"{phase}_w", [P, kc, n_cols], ctx=ctx)
        tokens = [k.sb(f"{phase}_tokens{b}", [P, kc, P], ctx=ctx) for b in range(2)]
        acc = [k.ps(f"{phase}_acc{b}", [P, 2 * HALF], ctx) for b in range(2)]
        w_in, copied, products, evacuated = k.sems(phase, "w_in copied products evacuated")
        block = ctx.enter_context(nc.Block())

        @block.sync
        def _(sp):
            for view, col, n in loads:
                into = weights[:, :, col:col + n]
                if kc == 1:
                    into = into.rearrange("p c (h n) -> p (c h) n", n=view.shape[-1])
                sp.dma_start(into, view).then_inc(w_in, 16)

        @block.scalar
        def _(act):
            with act.Fori(0, tiles // 2) as i:
                for b in range(2):
                    act.wait_ge(products, i * 2 + b + 1)
                    nc.scalar.activation(tokens[b][:, :, :], src[:, 0:kc, bass.ds((i * 2 + b) * P, P)],
                                         ACT.Copy).then_inc(copied, 1)

        @block.tensor
        def _(pe):
            pe.sem_inc(products, 2)
            pe.wait_ge(w_in, 16 * len(loads))
            with pe.Fori(0, tiles // 2) as i:
                for b in range(2):
                    pe.wait_ge(copied, i * 2 + b + 1)
                    pe.wait_ge(evacuated, i * 2 + b + 1)
                    for c in range(kc):
                        for at, n in pieces:
                            last = nc.tensor.matmul(acc[b][:, at:at + n], tokens[b][:, c, :],
                                                    weights[:, c, at:at + n], start=(c == 0), stop=(c == kc - 1))
                    last.then_inc(products, 1)

        @block.vector
        def _(dve):
            dve.sem_inc(evacuated, 2)
            with dve.Fori(0, tiles // 2) as i:
                for b in range(2):
                    dve.wait_ge(products, i * 2 + b + 1 + 2)
                    nc.vector.tensor_copy(row_of(dest, i * 2 + b), acc[b][:, 0:n_cols]).then_inc(evacuated, 1)


def project_residual(k, phase, w, src, kc):
    nc = k.nc
    with k.phase() as ctx:
        weights = [k.sb(f"{phase}_w{b}", [P, kc, P], ctx=ctx) for b in range(2)]
        rows = [k.sb(f"{phase}_rows{b}", [P, S], ctx=ctx) for b in range(2)]
        acc = [k.ps(f"{phase}_acc{b}", [P, S], ctx) for b in range(2)]
        turned = [k.ps(f"{phase}_turned{b}", [P, ST, P], ctx) for b in range(2)]
        w_in0, w_in1, products, evacuated, turns, added = k.sems(phase, "w_in0 w_in1 products evacuated turns added")
        w_in = (w_in0, w_in1)
        block = ctx.enter_context(nc.Block())
        w_view = w.rearrange("(c p) n -> p c n", p=P)

        @block.sync
        def _(sp):
            with sp.Fori(0, KD // 2) as i:
                for b in range(2):
                    sp.wait_ge(products, i * 2 + b + 1)
                    sp.dma_start(weights[b][:, :, :], w_view[:, :, bass.ds((i * 2 + b) * P, P)]).then_inc(w_in[b], 16)

        @block.tensor
        def _(pe):
            pe.sem_inc(turns, 1)
            pe.sem_inc(products, 2)
            with pe.Fori(0, KD // 2) as i:
                for b in range(2):
                    pe.wait_ge(w_in[b], 16 * i + 16)
                    pe.wait_ge(evacuated, i * 2 + 1)
                    for c in range(kc):
                        for h in range(2):
                            last = nc.tensor.matmul(acc[b][:, h * HALF:(h + 1) * HALF], weights[b][:, c, :],
                                                    src[:, c, h * HALF:(h + 1) * HALF],
                                                    start=(c == 0), stop=(c == kc - 1))
                    last.then_inc(products, 1)
                for b in range(2):
                    pe.wait_ge(evacuated, i * 2 + b + 1 + 1)
                    pe.wait_ge(added, i * 2 + b + 1)
                    for t in range(ST):
                        last = nc.tensor.transpose(turned[b][:, t, :], rows[b][:, t * P:(t + 1) * P], k.ident[:])
                    last.then_inc(turns, 1)

        @block.scalar
        def _(act):
            act.sem_inc(evacuated, 1)
            with act.Fori(0, KD // 2) as i:
                for b in range(2):
                    act.wait_ge(products, i * 2 + b + 1 + 2)
                    act.wait_ge(turns, i * 2 + 1)
                    nc.scalar.activation(rows[b][:], acc[b][:], ACT.Copy).then_inc(evacuated, 1)

        @block.vector
        def _(dve):
            dve.sem_inc(added, 2)
            with dve.Fori(0, KD // 2) as i:
                for b in range(2):
                    dve.wait_ge(turns, i * 2 + b + 1 + 1)
                    x = k.X[:, :, bass.ds((i * 2 + b) * P, P)]
                    nc.vector.tensor_tensor(x, x, turned[b][:, :, :], ALU.add).then_inc(added, 1)



def tables(k):
    nc = k.nc
    with k.phase() as ctx:
        scale = MLA_QK ** -0.5
        pos_row_i = k.sb("pos_row_i", [P, S], I32, ctx=ctx)
        pos_row = k.sb("pos_row", [P, S], ctx=ctx)
        lams = k.sb("lams", [P, 4, DIFF_HALF], ctx=ctx)
        lam_junk = k.sb("lam_junk", [P, 2, DIFF_HALF], ctx=ctx)
        lam_dot = k.sb("lam_dot", [P, 4], ctx=ctx)
        consts = k.sb("consts", [1, 4, P], ctx=ctx)
        cols = k.sb("cols", [P, 4], ctx=ctx)
        turns = k.sb("turns", [P, S], ctx=ctx)
        angle = k.rot
        cols_ps = k.ps("cols_ps", [P, 4], ctx)
        pos_in, lams_in, consts_made, cols_turned, dots, lam_exp, angle_made = k.sems(
            "tables", "pos_in lams_in consts_made cols_turned dots lam_exp angle_made")
        block = ctx.enter_context(nc.Block())

        @block.sync
        def _(sp):
            sp.dma_start(pos_row_i[:], k.dram["positions"].broadcast_to([P, S])).then_inc(pos_in, 16)
            for n, name in enumerate(("diff_lambda_q1", "diff_lambda_k1", "diff_lambda_q2", "diff_lambda_k2")):
                sp.dma_start(lams[:, n, :], k.dram[name].broadcast_to([P, DIFF_HALF])).then_inc(lams_in, 16)

        @block.gpsimd
        def _(pool):
            link = k.own("pool", pool)
            quarters = consts[:, :, :].rearrange("a n (q c) -> a n q c", q=4)
            for f in range(ROPE // 2):
                inv = float(np.float32(10000.0) ** np.float32(-2.0 * f / ROPE))
                nc.gpsimd.memset(consts[:, 0, :].rearrange("a (q f) -> a q f", f=ROPE // 2)[:, :, f:f + 1],
                                 inv).then_inc(consts_made, 1)
            for q, (turn, radian) in enumerate(((0.25, np.pi / 2), (0.0, 0.0)) * 2):
                nc.gpsimd.memset(quarters[:, 1, q, :], turn).then_inc(consts_made, 1)
                nc.gpsimd.memset(quarters[:, 2, q, :], float(radian)).then_inc(consts_made, 1)
            for q, (low, high) in enumerate(((1.0, 1.0), (-1.0, 1.0), (scale, scale), (-scale, scale))):
                nc.gpsimd.memset(quarters[:, 3, q, 0:16], low).then_inc(consts_made, 1)
                nc.gpsimd.memset(quarters[:, 3, q, 16:32], high).then_inc(consts_made, 1)
            for h in range(DIFF_HEADS):
                nc.gpsimd.memset(k.slopes[:, h:h + 1], -(2.0 ** (-8.0 * (h + 1) / DIFF_HEADS)) * DIFF_HALF ** 0.5).then_inc(consts_made, 1)
            link(nc.gpsimd.memset(k.causal[:], 0.0))
            link(nc.gpsimd.affine_select(out=k.causal[:, S - P:S], in_=k.causal[:, S - P:S], compare_op=ALU.is_ge,
                                         fill=NEG, base=0, pattern=[[-1, P]], channel_multiplier=1))

        @block.tensor
        def _(pe):
            pe.wait_ge(consts_made, 32 + DIFF_HEADS)
            for n in range(4):
                last = nc.tensor.transpose(cols_ps[:, n:n + 1], consts[0:1, n, :], k.ident[0:1, 0:1])
            last.then_inc(cols_turned, 1)

        @block.vector
        def _(dve):
            link = k.own("dve", dve)
            dve.wait_ge(lams_in, 64)
            for n in range(2):
                nc.vector.tensor_tensor_reduce(out=lam_junk[:, n, :], in0=lams[:, 2 * n, :], in1=lams[:, 2 * n + 1, :],
                                               scale=1.0, scalar=0.0, op0=ALU.mult, op1=ALU.add,
                                               accum_out=lam_dot[:, n:n + 1]).then_inc(dots, 1)
            dve.wait_ge(pos_in, 16)
            link(nc.vector.tensor_copy(pos_row[:], pos_row_i[:]))
            dve.wait_ge(lam_exp, 1)
            link(nc.vector.tensor_tensor(lam_dot[:, 3:4], lam_dot[:, 3:4], lam_dot[:, 2:3], ALU.subtract))
            link(nc.vector.tensor_scalar(k.neg_lambda[:], lam_dot[:, 3:4], -LAMBDA_INIT, None, ALU.add))
            dve.wait_ge(cols_turned, 1)
            link(nc.vector.tensor_copy(cols[:], cols_ps[:]))
            link(nc.vector.tensor_scalar(angle[:], pos_row[:], cols[:, 0:1], None, ALU.mult))
            link(nc.vector.tensor_scalar(turns[:], angle[:], 1.0 / (2 * np.pi), cols[:, 1:2], ALU.mult, ALU.add))
            link(nc.vector.tensor_scalar(turns[:], turns[:], 12582912.0, None, ALU.add))
            link(nc.vector.tensor_scalar(turns[:], turns[:], -12582912.0, None, ALU.add))
            c1 = 6.28125
            c2 = float(np.float32(np.round((2 * np.pi - c1) * 2 ** 20) / 2 ** 20))
            c3 = float(2 * np.pi - c1 - c2)
            for part in (c1, c2, c3):
                link(nc.vector.scalar_tensor_tensor(out=angle[:], in0=turns[:], scalar=-part, in1=angle[:],
                                                    op0=ALU.mult, op1=ALU.add))
            link(nc.vector.tensor_scalar(angle[:], angle[:], cols[:, 2:3], 3.1415925, ALU.add, ALU.min))
            nc.vector.tensor_scalar(angle[:], angle[:], -3.1415925, None, ALU.max).then_inc(angle_made, 1)
            dve.wait_ge(angle_made, 2)
            link(nc.vector.tensor_scalar(k.rot[:], k.rot[:], cols[:, 3:4], None, ALU.mult))

        @block.scalar
        def _(act):
            act.wait_ge(dots, 2)
            nc.scalar.activation(lam_dot[:, 2:4], lam_dot[:, 0:2], ACT.Exp).then_inc(lam_exp, 1)
            act.wait_ge(angle_made, 1)
            nc.scalar.activation(k.rot[:], angle[:], ACT.Sin).then_inc(angle_made, 1)

        for e in ("dve", "pool"):
            k.chains[e].settle()


def distances(k):
    nc = k.nc
    with k.phase() as ctx:
        pos_row_i = k.sb("pos_row_i", [P, S], I32, ctx=ctx)
        pos_row = k.sb("pos_row", [P, S], ctx=ctx)
        pos_col_i = k.sb("pos_col_i", [P, ST], I32, ctx=ctx)
        pos_col = k.sb("pos_col", [P, ST], ctx=ctx)
        pos_in, dist_made, masked = k.sems("distances", "pos_in dist_made masked")
        block = ctx.enter_context(nc.Block())

        @block.sync
        def _(sp):
            sp.dma_start(pos_row_i[:], k.dram["positions"].broadcast_to([P, S])).then_inc(pos_in, 16)
            with nc.allow_non_contiguous_dma(reason="1024 positions, one to a descriptor"):
                sp.dma_start(pos_col_i[:], k.dram["positions"].rearrange("a (t p) -> p (a t)", p=P)).then_inc(pos_in, 16)

        @block.vector
        def _(dve):
            link = k.own("dve", dve)
            dve.wait_ge(pos_in, 32)
            link(nc.vector.tensor_copy(pos_row[:], pos_row_i[:]))
            link(nc.vector.tensor_copy(pos_col[:], pos_col_i[:]))
            for t in range(ST):
                link(nc.vector.tensor_scalar(k.dist[:, t, :], pos_row[:], pos_col[:, t:t + 1], None, ALU.subtract))
                nc.vector.scalar_tensor_tensor(out=k.dist[:, t, :], in0=k.dist[:, t, :], scalar=-1.0, in1=k.dist[:, t, :],
                                               op0=ALU.mult, op1=ALU.max).then_inc(dist_made, 1)

        @block.gpsimd
        def _(pool):
            for t in range(ST):
                pool.wait_ge(dist_made, t + 1)
                diag = k.dist[:, t, t * P:(t + 1) * P]
                nc.gpsimd.affine_select(out=diag, in_=diag, compare_op=ALU.is_ge, fill=-NEG, base=0,
                                        pattern=[[-1, P]], channel_multiplier=1).then_inc(masked, 1)
        k.chains["dve"].settle()


def latent_up(k, cq):
    nc = k.nc
    with k.phase() as ctx:
        scale = MLA_QK ** -0.5
        wk = k.sb("kpe_w", [P, KD, 2 * ROPE], ctx=ctx)
        sq = k.sb("lat_sq", [P, 3, S], ctx=ctx)
        norm = k.sb("lat_norm", [P, 2, S], ctx=ctx)
        wq = [k.sb(f"lat_wq{b}", [P, 2, P], ctx=ctx) for b in range(2)]
        wn = [k.sb(f"lat_wn{b}", [P, NOPE], ctx=ctx) for b in range(2)]
        turned = [k.sb(f"lat_rot{b}", [P, S], ctx=ctx) for b in range(2)]
        qs = [k.sb(f"lat_q{b}", [P, S], ctx=ctx) for b in range(2)]
        ks = [k.sb(f"lat_k{b}", [NOPE, S], ctx=ctx) for b in range(2)]
        kpe = k.sb("kpe", [ROPE, S], ctx=ctx)
        qp = [k.ps(f"lat_qp{b}", [P, S], ctx) for b in range(2)]
        kp = [k.ps(f"lat_kp{b}", [P, S], ctx) for b in range(2)]
        (wk_in, kpe_made, kpe_read, sq_made, sums_made, mean_made, root_made, lat_made, wq_in0, wq_in1, heads,
         nopes, q_made, turned_made, stored) = k.sems("lat", "wk_in kpe_made kpe_read sq_made sums_made mean_made root_made lat_made "
                                         "wq_in0 wq_in1 heads nopes q_made turned_made stored")
        w_in = (wq_in0, wq_in1)
        block = ctx.enter_context(nc.Block())
        w_uq = k.dram["w_mla_uq"].rearrange("l (c p) (h n) -> p (l c) h n", p=P, n=MLA_QK)
        w_ukv = k.dram["w_mla_ukv"].rearrange("l p (h n) -> p (l h) n", n=NOPE + MLA_V)
        w_pe = k.dram["w_in"][0].rearrange("(c p) n -> p c n", p=P)
        half = ROPE // 2

        def head(i, b):
            return i * 2 + b

        @block.sync
        def _(sp):
            for at, col, n in ((0, COL_KPE, ROPE), (ROPE, COL_KPE + half, half), (ROPE + half, COL_KPE, half)):
                sp.dma_start(wk[:, :, at:at + n], w_pe[:, :, col:col + n]).then_inc(wk_in, 16)
            with sp.Fori(0, MLA_HEADS // 2) as i:
                for b in range(2):
                    sp.wait_ge(heads, head(i, b) + 1)
                    for at, col, n in ((0, 0, MLA_QK), (MLA_QK, NOPE + half, half), (MLA_QK + half, NOPE, half)):
                        sp.dma_start(wq[b][:, :, at:at + n],
                                     w_uq[:, :, bass.ds(head(i, b), 1), col:col + n].rearrange(
                                         "p c h n -> p c (h n)")).then_inc(w_in[b], 16)
                    sp.dma_start(wn[b][:], w_ukv[:, bass.ds(head(i, b), 1), 0:NOPE].rearrange(
                        "p h n -> p (h n)")).then_inc(w_in[b], 16)

        @block.tensor
        def _(pe):
            pe.sem_inc(heads, 2)
            pe.wait_ge(wk_in, 48)
            for c in range(KD):
                for h in range(2):
                    last = nc.tensor.matmul(qp[0][0:2 * ROPE, h * HALF:(h + 1) * HALF], wk[:, c, :],
                                            k.HT[:, c, h * HALF:(h + 1) * HALF], start=(c == 0), stop=(c == KD - 1))
            last.then_inc(kpe_made, 1)
            pe.wait_ge(sq_made, 1)
            for n, chunks in ((0, (0, 1)), (1, (2,))):
                for c in chunks:
                    for h in range(2):
                        last = nc.tensor.matmul(kp[n][:, h * HALF:(h + 1) * HALF], k.ones[:],
                                                sq[:, c, h * HALF:(h + 1) * HALF],
                                                start=(c == chunks[0]), stop=(c == chunks[-1]))
            last.then_inc(sums_made, 1)
            pe.wait_ge(lat_made, 3)
            pe.wait_ge(kpe_read, 1)
            with pe.Fori(0, MLA_HEADS // 2) as i:
                for b in range(2):
                    pe.wait_ge(w_in[b], 64 * i + 64)
                    pe.wait_ge(q_made, head(i, b) + 1)
                    for c in range(2):
                        for h in range(2):
                            last = nc.tensor.matmul(qp[b][:, h * HALF:(h + 1) * HALF], wq[b][:, c, :],
                                                    cq[:, c, h * HALF:(h + 1) * HALF], start=(c == 0), stop=(c == 1))
                    for h in range(2):
                        last = nc.tensor.matmul(kp[b][0:NOPE, h * HALF:(h + 1) * HALF], wn[b][:],
                                                cq[:, 2, h * HALF:(h + 1) * HALF], start=True, stop=True)
                    last.then_inc(heads, 1)

        @block.scalar
        def _(act):
            act.sem_inc(stored, 16)
            nc.scalar.activation(sq[:, :, :], cq[:, :, :], ACT.Square).then_inc(sq_made, 1)
            act.wait_ge(mean_made, 2)
            nc.scalar.activation(norm[:, :, :], norm[:, :, :], ACT.Sqrt).then_inc(root_made, 1)
            act.sem_inc(nopes, 2 * 2)
            with act.Fori(0, MLA_HEADS // 2) as i:
                for b in range(2):
                    h = head(i, b)
                    act.wait_ge(heads, h + 1 + 2)
                    act.wait_ge(stored, 32 * h + 16)
                    nc.scalar.activation(qs[b][0:NOPE, :], qp[b][0:NOPE, :], ACT.Copy, scale=scale).then_inc(nopes, 1)
                    nc.scalar.activation(ks[b][:], kp[b][0:NOPE, :], ACT.Copy).then_inc(nopes, 1)
                    act.wait_ge(nopes, 2 * h + 2 + 4)
                    act.wait_ge(q_made, h + 1 + 2)
                    act.dma_start(k.scratch["qm"][bass.ds(h * MLA_QK, MLA_QK), :], qs[b][0:MLA_QK, :]).then_inc(stored, 16)
                    act.dma_start(k.scratch["km"][bass.ds(h * NOPE, NOPE), :], ks[b][:]).then_inc(stored, 16)
            act.dma_start(k.scratch["kpe"], kpe[:]).then_inc(stored, 16)
            act.wait_ge(stored, 32 * MLA_HEADS + 16 + 16)

        @block.vector
        def _(dve):
            link = k.own("dve", dve)
            dve.wait_ge(kpe_made, 1)
            link(nc.vector.tensor_tensor(turned[0][0:ROPE, :], qp[0][ROPE:2 * ROPE, :], k.rot[ROPE:2 * ROPE, :], ALU.mult))
            link(nc.vector.tensor_tensor(kpe[:], qp[0][0:ROPE, :], k.rot[0:ROPE, :], ALU.mult))
            nc.vector.tensor_tensor(kpe[:], kpe[:], turned[0][0:ROPE, :], ALU.add).then_inc(kpe_read, 1)
            dve.wait_ge(sums_made, 1)
            for n, width in ((0, MLA_QR), (1, MLA_KVR)):
                nc.vector.tensor_scalar(norm[:, n, :], kp[n][:], 1.0 / width, EPS, ALU.mult, ALU.add).then_inc(mean_made, 1)
            dve.wait_ge(root_made, 1)
            link(nc.vector.reciprocal(norm[:, :, :], norm[:, :, :]))
            gains = (k.gain("mla_q_norm_g", 0, 1), k.gain("mla_q_norm_g", 1, 1), k.gain("mla_kv_norm_g"))
            for c in range(3):
                nc.vector.scalar_tensor_tensor(out=cq[:, c, :], in0=cq[:, c, :], scalar=gains[c], in1=norm[:, c // 2, :],
                                               op0=ALU.mult, op1=ALU.mult).then_inc(lat_made, 1)
            dve.sem_inc(q_made, 2)
            dve.wait_ge(kpe_read, 1)
            pe_rows, swapped_rows = slice(NOPE, MLA_QK), slice(MLA_QK, P)
            chain = k.chains["dve"]
            chain.settle()
            with dve.Fori(0, MLA_HEADS // 2) as i:
                chain.enter(i, 4)
                for b in range(2):
                    h = head(i, b)
                    dve.wait_ge(heads, h + 1 + 2)
                    dve.wait_ge(stored, 32 * h + 16)
                    link(nc.vector.tensor_tensor(turned[b][pe_rows, :], qp[b][swapped_rows, :], k.rot[swapped_rows, :], ALU.mult))
                    link(nc.vector.tensor_tensor(qs[b][pe_rows, :], qp[b][pe_rows, :], k.rot[pe_rows, :], ALU.mult))
                    dve.wait_ge(nopes, 2 * h + 2 + 4)
                    nc.vector.tensor_tensor(qs[b][pe_rows, :], qs[b][pe_rows, :], turned[b][pe_rows, :],
                                            ALU.add).then_inc(q_made, 1)
                chain.leave(MLA_HEADS // 2)


def attention(k, phase, heads, loads, rows, V, out, out_col, maps=1, alibi=False, scale=1.0,
              window=None):
    nc = k.nc
    with k.phase() as ctx:
        q = [k.sb(f"{phase}_q{b}", [P, S], ctx=ctx) for b in range(2)]
        kk = [k.sb(f"{phase}_k{b}", [P, S], ctx=ctx) for b in range(2)]
        probs = [[k.sb(f"{phase}_p{m}{b}", [P, S], ctx=ctx) for b in range(2)] for m in range(maps)]
        turned_sb = [k.sb(f"{phase}_pt{b}", [P, ST, P], ctx=ctx) for b in range(2)]
        slope = [k.sb(f"{phase}_slope{b}", [P, 1], ctx=ctx) for b in range(2)]
        bias = [k.sb(f"{phase}_bias{b}", [P, S], ctx=ctx) for b in range(2)] if alibi else None
        head_bias = [k.sb(f"{phase}_hbias{b}", [P, 2 * P], ctx=ctx) for b in range(2)] if window else None
        sink = [k.sb(f"{phase}_sink{b}", [P, 1], ctx=ctx) for b in range(2)] if window else None
        stats = [k.sb(f"{phase}_stats{n}", [P, 9], ctx=ctx) for n in range(4)]
        scores = [k.ps(f"{phase}_scores{n}", [P, S], ctx) for n in range(2)]
        turned = k.ps(f"{phase}_turned", [P, ST, P], ctx)
        outs = [k.ps(f"{phase}_out{b}", [P, HD], ctx) for b in range(2)]
        (head_in0, head_in1, products, biased, scored, maxed, exps, mixed, turns, copied, values, done, passed) = k.sems(
            phase, "head_in0 head_in1 products biased scored maxed exps mixed turns copied values done passed")
        head_in = (head_in0, head_in1)
        block = ctx.enter_context(nc.Block())
        per_round = 2 * ST
        n_loads = len(loads(0, 0))
        rounds = heads // 2
        ready = mixed if maps == 2 else exps

        def first(t):
            return max(t - 1, 0) if window else 0

        def parts(width):
            return [(c, min(HALF, width - c)) for c in range(0, width, HALF)]

        def value_cols(i, b):
            return slice(window[1], window[1] + HD) if window else bass.ds((i * 2 + b) * HD, HD)

        @block.sync
        def _(sp):
            with sp.Fori(0, rounds) as i:
                for b in range(2):
                    sp.wait_ge(products, (i * 2 + b) * ST * maps + 1)
                    for which, row, src in loads(b, i * 2 + b):
                        tile = q[b] if which == "q" else kk[b]
                        sp.dma_start(tile[row:row + src.shape[0], :], src).then_inc(head_in[b], 16)

        @block.tensor
        def _(pe):
            pe.sem_inc(products, 1)
            pe.sem_inc(products, ST * maps)
            pe.sem_inc(turns, 2)
            pe.sem_inc(values, 2)
            with pe.Fori(0, rounds) as i:
                for n in range(per_round + 2):
                    g = i * per_round + n
                    if n < per_round:
                        b, t = n // ST, n % ST
                        if t == 0:
                            pe.wait_ge(head_in[b], 16 * n_loads * i + 16 * n_loads)
                        for m in range(maps):
                            pe.wait_ge(scored, g * maps + m + 1 + 1)
                            ps = scores[m if maps == 2 else n % 2]
                            r = slice(rows * m, rows * (m + 1))
                            for at, w in parts((t + 1 - first(t)) * P):
                                key = first(t) * P + at
                                last = nc.tensor.matmul(ps[:, at:at + w], q[b][r, t * P:(t + 1) * P],
                                                        kk[b][r, key:key + w], start=True, stop=True)
                            last.then_inc(products, 1)
                    if n >= 2:
                        b, t = (n - 2) // ST, (n - 2) % ST
                        pe.wait_ge(copied, g - 1 + 1)
                        pe.wait_ge(done, g - 1)
                        for c in range(first(t), t + 1):
                            last = nc.tensor.matmul(outs[n % 2][:], turned_sb[n % 2][:, c - first(t), :],
                                                    V[:, c, value_cols(i, b)], start=(c == first(t)), stop=(c == t))
                        last.then_inc(values, 1)
                    if 1 <= n <= per_round:
                        t = (n - 1) % ST
                        pe.wait_ge(ready, g + (maps == 1))
                        pe.wait_ge(copied, g - 1 + 1)
                        for c in range(t + 1 - first(t)):
                            last = nc.tensor.transpose(turned[:, c, :], probs[0][(n - 1) % 2][:, c * P:(c + 1) * P], k.ident[:])
                        last.then_inc(turns, 1)

        @block.vector
        def _(dve):
            dve.sem_inc(scored, 1)
            link = k.own("dve", dve)
            chain = k.chains["dve"]
            dve.sem_inc(scored, 2)
            dve.sem_inc(done, 2)
            with dve.Fori(0, rounds) as i:
                chain.enter(i, per_round * (2 if maps == 2 or window else 1))
                for n in range(per_round + 3):
                    g = i * per_round + n
                    if n < per_round:
                        t = n % ST
                        w = (t + 1 - first(t)) * P
                        st = stats[n % 4]
                        dve.wait_ge(turns, g + 1)
                        if alibi:
                            dve.wait_ge(biased, g + 2)
                        if window and t == 0:
                            dve.wait_ge(biased, 2 * (i * 2 + n // ST) + 2)
                        for m in range(maps):
                            dve.wait_ge(products, g * maps + m + 1 + ST * maps + 1)
                            dve.sem_inc(passed, 1)
                            ps = scores[m if maps == 2 else n % 2]
                            b_ap = (bias[n % 2][:, 0:w] if alibi else head_bias[n // ST][:, 2 * P - w:2 * P] if window
                                    else k.causal[:, S - w:S])
                            least = sink[n // ST][:, 0:1] if window else -3e38
                            nc.vector.tensor_tensor_reduce(out=probs[m][n % 2][:, 0:w], in0=ps[:, 0:w], in1=b_ap,
                                                           scale=scale, scalar=least, op0=ALU.add, op1=ALU.max,
                                                           accum_out=st[:, m:m + 1]).then_inc(scored, 1)
                        dve.wait_ge(scored, (g + 1) * maps + 2 + 1)
                        nc.vector.tensor_scalar(st[:, 2:2 + maps], st[:, 0:maps], -1.0, None, ALU.mult).then_inc(maxed, 1)
                    if 1 <= n <= per_round:
                        t, par, st = (n - 1) % ST, (n - 1) % 2, stats[(n - 1) % 4]
                        w = (t + 1 - first(t)) * P
                        dve.wait_ge(exps, g + 1)
                        if window:
                            link(nc.vector.tensor_tensor(st[:, 4:5], st[:, 4:5], st[:, 8:9], ALU.add))
                        link(nc.vector.reciprocal(st[:, 6:6 + maps], st[:, 4:4 + maps]))
                        if maps == 2:
                            link(nc.vector.scalar_tensor_tensor(out=st[:, 8:9], in0=st[:, 4:5], scalar=k.neg_lambda[:, 0:1],
                                                                in1=st[:, 7:8], op0=ALU.mult, op1=ALU.mult))
                            nc.vector.scalar_tensor_tensor(out=probs[0][par][:, 0:w], in0=probs[1][par][:, 0:w],
                                                           scalar=st[:, 8:9], in1=probs[0][par][:, 0:w],
                                                           op0=ALU.mult, op1=ALU.add).then_inc(mixed, 1)
                    if n >= 3:
                        b, t = (n - 3) // ST, (n - 3) % ST
                        dve.wait_ge(values, g - 3 + 1 + 2)
                        nc.vector.tensor_scalar(out[:, t, bass.ds((i * 2 + b) * HD + out_col, HD)], outs[(n - 3 + 2) % 2][:],
                                                stats[(n - 3) % 4][:, 6:7], None, ALU.mult).then_inc(done, 1)
                chain.leave(rounds)

        @block.scalar
        def _(act):
            act.sem_inc(exps, 1)
            act.sem_inc(copied, 1)
            with act.Fori(0, rounds) as i:
                for n in range(per_round + 1):
                    g = i * per_round + n
                    if n < per_round:
                        w, st = (n % ST + 1 - first(n % ST)) * P, stats[n % 4]
                        act.wait_ge(maxed, g + 1)
                        if window:
                            nc.scalar.activation(st[:, 8:9], sink[n // ST][:], ACT.Exp, bias=st[:, 2:3])
                        for m in range(maps):
                            last = nc.scalar.activation(probs[m][n % 2][:, 0:w], probs[m][n % 2][:, 0:w], ACT.Exp,
                                                        bias=st[:, 2 + m:3 + m], accum_out=st[:, 4 + m:5 + m])
                        last.then_inc(exps, 1)
                    if n >= 1:
                        t = (n - 1) % ST
                        act.wait_ge(turns, g + 2)
                        act.wait_ge(values, g)
                        nc.scalar.activation(turned_sb[(n - 1) % 2][:, 0:t + 1 - first(t), :],
                                             turned[:, 0:t + 1 - first(t), :], ACT.Copy).then_inc(copied, 1)

        if window:
            @block.gpsimd
            def _(pool):
                with pool.Fori(0, rounds) as i:
                    pool.wait_ge(scored, i * per_round + 2 + 1)
                    pool.wait_ge(exps, i * per_round + 1)
                    for b in range(2):
                        head = bass.ds(i * 2 + b + window[0], 1)
                        nc.gpsimd.tensor_copy(head_bias[b][:], window[2][:, head, :].rearrange("p h c -> p (h c)")
                                              ).then_inc(biased, 1)
                        nc.gpsimd.tensor_copy(sink[b][:], window[3][:, head]).then_inc(biased, 1)

        if alibi:
            @block.gpsimd
            def _(pool):
                pool.sem_inc(biased, 1)
                chain = k.chains["pool"]
                link = k.own("pool", pool)
                with pool.Fori(0, rounds) as i:
                    chain.enter(i, 2)
                    for n in range(per_round):
                        b, t = n // ST, n % ST
                        w = (t + 1) * P
                        if t == 0:
                            pool.wait_ge(biased, i * per_round + n + 1)
                            pool.sem_inc(passed, 1)
                            link(nc.gpsimd.tensor_copy(slope[b][:], k.slopes[:, bass.ds(i * 2 + b, 1)]))
                        pool.wait_ge(scored, (i * per_round + n) * 2 + 1)
                        pool.sem_inc(passed, 1)
                        nc.gpsimd.tensor_scalar(bias[n % 2][:, 0:w], k.dist[:, t, 0:w], slope[b][:], 1.0,
                                                ALU.mult, ALU.mult).then_inc(biased, 1)
                    chain.leave(rounds)


def head_norm(k, phase, Y, heads, width, factor):
    nc = k.nc
    with k.phase() as ctx:
        sq = k.sb(f"{phase}_sq", [P, ST, heads * width], ctx=ctx)
        norm = k.sb(f"{phase}_norm", [P, ST, heads], ctx=ctx)
        squared, mean_made, root_made, norm_made = k.sems(phase, "squared mean_made root_made norm_made")
        block = ctx.enter_context(nc.Block())
        n = ST * heads

        @block.scalar
        def _(act):
            nc.scalar.activation(sq[:, :, :], Y, ACT.Square).then_inc(squared, 1)
            act.wait_ge(mean_made, 1)
            nc.scalar.activation(norm[:, :, :], norm[:, :, :], ACT.Sqrt).then_inc(root_made, 1)

        @block.vector
        def _(dve):
            link = k.own("dve", dve)
            dve.wait_ge(squared, 1)
            link(nc.vector.tensor_reduce(norm[:, :, :], sq[:, :, :].rearrange("p t (h w) -> p t h w", w=width), AX, ALU.add))
            nc.vector.tensor_scalar(norm[:, :, :], norm[:, :, :], 1.0 / width / factor ** 2, EPS / factor ** 2,
                                    ALU.mult, ALU.add).then_inc(mean_made, 1)
            dve.wait_ge(root_made, 1)
            link(nc.vector.reciprocal(norm[:, :, :], norm[:, :, :]))
            for t in range(ST):
                link(nc.vector.tensor_tensor(Y[:, t, :].rearrange("p (h w) -> p h w", w=width),
                                             Y[:, t, :].rearrange("p (h w) -> p h w", w=width),
                                             norm[:, t, :].rearrange("p (h o) -> p h o", o=1).broadcast_to([P, heads, width]),
                                             ALU.mult))
        k.chains["dve"].settle()


def turn(k, phase, Y, gain, dest, chunks):
    nc = k.nc
    with k.phase() as ctx:
        tiles = [k.sb(f"{phase}_tile{b}", [P, chunks * P], ctx=ctx) for b in range(2)]
        turned = [k.ps(f"{phase}_turned{b}", [P, chunks, P], ctx) for b in range(2)]
        copied, turns, stored = k.sems(phase, "copied turns stored")
        block = ctx.enter_context(nc.Block())

        @block.scalar
        def _(act):
            with act.Fori(0, ST // 2) as i:
                for b in range(2):
                    act.wait_ge(turns, 2 * i + b + 1)
                    nc.scalar.activation(tiles[b][:], row_of(Y, 2 * i + b), ACT.Copy).then_inc(copied, 1)

        @block.tensor
        def _(pe):
            pe.sem_inc(turns, 2)
            with pe.Fori(0, ST // 2) as i:
                for b in range(2):
                    pe.wait_ge(copied, 2 * i + b + 1)
                    pe.wait_ge(stored, 2 * i + 1)
                    for c in range(chunks):
                        last = nc.tensor.transpose(turned[b][:, c, :], tiles[b][:, c * P:(c + 1) * P], k.ident[:])
                    last.then_inc(turns, 1)

        @block.vector
        def _(dve):
            dve.sem_inc(stored, 1)
            with dve.Fori(0, ST // 2) as i:
                for b in range(2):
                    dve.wait_ge(turns, 2 * i + b + 1 + 2)
                    nc.vector.tensor_tensor(dest[:, 0:chunks, bass.ds((2 * i + b) * P, P)], turned[b][:, :, :],
                                            gain.rearrange("p (c o) -> p c o", o=1).broadcast_to([P, chunks, P]), ALU.mult).then_inc(stored, 1)


def first_mixer(k):
    nc = k.nc
    w_in = k.dram["w_in"][0]
    with ExitStack() as ctx:
        mix = k.sb("mix", [P, ST, D], ctx=ctx)
        vd = k.sb("vd", [P, ST, DIFF_W], ctx=ctx)
        vm = k.sb("vm", [P, ST, MLA_W], ctx=ctx)
        k.causal = k.sb("causal", [P, S], ctx=ctx)
        k.slopes = k.sb("slopes", [P, DIFF_HEADS], ctx=ctx)
        k.neg_lambda = k.sb("neg_lambda", [P, 1], ctx=ctx)
        with ExitStack() as early:
            cq = k.sb("cq", [P, 3, S], ctx=early)
            with ExitStack() as tab:
                k.rot = k.sb("rot", [P, S], ctx=tab)
                tables(k)
                norm_turn(k, "mix_norm", k.X, ST, k.gain("norm_mix_g"), k.HT)
                project_rows(k, "diff_qk", w_in[:, 0:2 * DIFF_QK], 2 * DIFF_QK // P, k.HT, KD, k.scratch["qk1"])
                project_rows(k, "latents", w_in[:, COL_CQ:COL_KPE], 3, k.HT, KD, (cq,))
                project_tokens(k, "diff_v", [(w_in[:, COL_VD:COL_CQ].rearrange("(c p) n -> p c n", p=P), 0, DIFF_W)],
                               DIFF_W, k.HT, KD, vd)
                latent_up(k, cq)
            w_ukv = k.dram["w_mla_ukv"].rearrange("l p (h n) -> p (l h) n", n=NOPE + MLA_V)
            project_tokens(k, "latent_v", [(w_ukv[:, :, NOPE:], 0, MLA_W)], MLA_W, cq[:, 2:3, :], 1, vm)
        k.dist = k.HT
        distances(k)
        attention(k, "diff", DIFF_HEADS,
                  lambda b, h: [("q", 0, k.scratch["qk1"][bass.ds(h * HD, HD), :]),
                                ("k", 0, k.scratch["qk1"][bass.ds(h * HD + DIFF_QK, HD), :])],
                  DIFF_HALF, vd, mix, 0, maps=2, alibi=True, scale=DIFF_HALF ** -0.5)
        attention(k, "latent", MLA_HEADS,
                  lambda b, h: [("q", 0, k.scratch["qm"][bass.ds(h * MLA_QK, MLA_QK), :]),
                                ("k", 0, k.scratch["km"][bass.ds(h * NOPE, NOPE), :]),
                                ("k", NOPE, k.scratch["kpe"])],
                  MLA_QK, vm, mix, DIFF_W)
        head_norm(k, "diff_rms", mix[:, :, 0:DIFF_W], DIFF_HEADS, DIFF_V, 1.0 - LAMBDA_INIT)
        head_norm(k, "latent_rms", mix[:, :, DIFF_W:D], 1, MLA_W, 1.0)
        diff_gain, latent_gain = k.gain("diff_out_g"), k.gain("mla_out_g")
        turn(k, "diff_turn", mix[:, :, 0:DIFF_W], diff_gain, k.HT[:, 0:4, :], 4)
        turn(k, "latent_turn", mix[:, :, DIFF_W:D], latent_gain, k.HT[:, 4:8, :], 4)
    project_residual(k, "mix_out", k.dram["w_out"][0], k.HT, KD)


def memory_attention(k, q, km, vm, out):
    nc = k.nc
    with k.phase() as ctx:
        qt = [k.sb(f"mem_qt{b}", [P, MEM_HEADS, P], ctx=ctx) for b in range(2)]
        probs = [k.sb(f"mem_p{b}", [P, MEM_HEADS, MEM_T], ctx=ctx) for b in range(2)]
        turned_sb = [k.sb(f"mem_pt{b}", [P, 2 * MEM_HEADS, P], ctx=ctx) for b in range(2)]
        stats = [k.sb(f"mem_stats{b}", [P, 3, MEM_HEADS], ctx=ctx) for b in range(2)]
        scores = [k.ps(f"mem_scores{b}", [P, MEM_HEADS, MEM_T], ctx) for b in range(2)]
        turned = k.ps("mem_turned", [P, 2 * MEM_HEADS, P], ctx)
        outs = [k.ps(f"mem_out{b}", [P, MEM_HEADS, P], ctx) for b in range(2)]
        q_copied, products, shifted, exps, probs_ready, turns, copied, values, done = k.sems(
            "mem", "q_copied products shifted exps probs_ready turns copied values done")
        block = ctx.enter_context(nc.Block())

        def across(column):
            return column.rearrange("p (h o) -> p h o", o=1).broadcast_to([P, MEM_HEADS, MEM_T])

        @block.tensor
        def _(pe):
            pe.sem_inc(values, 1)
            pe.sem_inc(products, 1)
            pe.sem_inc(turns, 1)
            with pe.Fori(0, ST // 2) as i:
                for b in range(2):
                    pe.wait_ge(q_copied, 2 * i + b + 1)
                    pe.wait_ge(shifted, 2 * i + 1)
                    for h in range(MEM_HEADS):
                        last = nc.tensor.matmul(scores[b][:, h, :], qt[b][:, h, :], km[:, h, :], start=True, stop=True)
                    last.then_inc(products, 1)
                for b in range(2):
                    pe.wait_ge(probs_ready, 2 * i + b + 1)
                    pe.wait_ge(copied, 2 * i + b + 1)
                    for n in range(2 * MEM_HEADS):
                        last = nc.tensor.transpose(turned[:, n, :], probs[b][:, n // 2, (n % 2) * P:(n % 2 + 1) * P],
                                                   k.ident[:])
                    last.then_inc(turns, 1)
                for b in range(2):
                    pe.wait_ge(copied, 2 * i + b + 1 + 1)
                    pe.wait_ge(done, 2 * i + 1)
                    for h in range(MEM_HEADS):
                        for c in range(2):
                            last = nc.tensor.matmul(outs[b][:, h, :], vm[:, c, h * MEM_HD:(h + 1) * MEM_HD],
                                                    turned_sb[b][:, 2 * h + c, :], start=(c == 0), stop=(c == 1))
                    last.then_inc(values, 1)

        @block.vector
        def _(dve):
            dve.sem_inc(done, 1)
            dve.sem_inc(shifted, 1)
            link = k.own("dve", dve)
            chain = k.chains["dve"]
            with dve.Fori(0, ST // 2) as i:
                chain.enter(i, 6)
                for b in range(2):
                    dve.wait_ge(products, 2 * i + b + 1 + 1)
                    dve.wait_ge(turns, 2 * i + 1)
                    link(nc.vector.tensor_reduce(stats[b][:, 0, :], scores[b][:, :, :], AX, ALU.max))
                    nc.vector.tensor_tensor(probs[b][:, :, :], scores[b][:, :, :], across(stats[b][:, 0, :]),
                                            ALU.subtract).then_inc(shifted, 1)
                for b in range(2):
                    dve.wait_ge(exps, 2 * i + b + 1)
                    link(nc.vector.tensor_reduce(stats[b][:, 1, :], probs[b][:, :, :], AX, ALU.add))
                    link(nc.vector.reciprocal(stats[b][:, 2, :], stats[b][:, 1, :]))
                    nc.vector.tensor_tensor(probs[b][:, :, :], probs[b][:, :, :], across(stats[b][:, 2, :]),
                                            ALU.mult).then_inc(probs_ready, 1)
                for b in range(2):
                    dve.wait_ge(values, 2 * i + b + 1 + 1)
                    nc.vector.tensor_copy(out[:, :, bass.ds((2 * i + b) * P, P)], outs[b][:, :, :]).then_inc(done, 1)
                chain.leave(ST // 2)

        @block.scalar
        def _(act):
            act.sem_inc(copied, 1)
            with act.Fori(0, ST // 2) as i:
                for b in range(2):
                    act.wait_ge(products, 2 * i + 1)
                    nc.scalar.activation(qt[b][:, :, :], q[:, :, bass.ds((2 * i + b) * P, P)], ACT.Copy).then_inc(q_copied, 1)
                for b in range(2):
                    act.wait_ge(shifted, 2 * i + b + 1 + 1)
                    nc.scalar.activation(probs[b][:, :, :], probs[b][:, :, :], ACT.Exp).then_inc(exps, 1)
                for b in range(2):
                    act.wait_ge(turns, 2 * i + b + 1 + 1)
                    act.wait_ge(values, 2 * i + 1)
                    nc.scalar.activation(turned_sb[b][:, :, :], turned[:, :, :], ACT.Copy).then_inc(copied, 1)


def cross_mixer(k):
    nc = k.nc
    norm_turn(k, "cross_norm", k.X, ST, k.gain("norm_cross_g"), k.HT)
    with ExitStack() as ctx:
        out = k.sb("mem_mixed", [P, MEM_HEADS, S], ctx=ctx)
        with ExitStack() as inner:
            q = k.sb("mem_q", [P, MEM_HEADS, S], ctx=inner)
            km = k.sb("mem_k", [P, MEM_HEADS, MEM_T], ctx=inner)
            vm = k.sb("mem_v", [P, MEM_T // P, MEM_W], ctx=inner)
            mem = k.sb("mem_x", [P, MEM_T // P, D], ctx=inner)
            mem_t = k.sb("mem_t", [P, KD, MEM_T], ctx=inner)
            load_rows(k, k.dram["mem"].rearrange("a (t p) d -> p (a t) d", p=P), mem)
            norm_turn(k, "mem_norm", mem, MEM_T // P, k.gain("norm_mem_g"), mem_t)
            w_kv = k.dram["w_mem_kv"][0]
            project_rows(k, "mem_k", w_kv[:, 0:MEM_W], MEM_HEADS, mem_t, KD, (km,), tokens=MEM_T)
            project_tokens(k, "mem_v", [(w_kv[:, MEM_W:].rearrange("(c p) n -> p c n", p=P), 0, MEM_W)],
                           MEM_W, mem_t, KD, vm, tiles=MEM_T // P)
            project_rows(k, "mem_q", k.dram["w_mem_q"][0], MEM_HEADS, k.HT, KD, (q,), scale=MEM_HD ** -0.5)
            memory_attention(k, q, km, vm, out)
        project_residual(k, "mem_out", k.dram["w_mem_o"][0], out, MEM_HEADS)


def load_rows(k, view, tile):
    nc = k.nc
    with k.phase() as ctx:
        (loaded,) = k.sems("load", "loaded")
        block = ctx.enter_context(nc.Block())

        @block.sync
        def _(sp):
            sp.dma_start(tile[:, :, :], view).then_inc(loaded, 16)
            sp.wait_ge(loaded, 16)


def route(k, logits, slots, weights, experts, slot_of_block):
    nc = k.nc
    E, G = EXPERTS, GROUPS
    with k.phase() as ctx:
        sb = lambda name, shape, dt=F32: k.sb(f"route_{name}", shape, dt, ctx=ctx)
        bias = sb("bias", [P, G + E])
        groups = sb("groups", [P, ST, 8])
        group_max, group_idx = sb("group_max", [P, ST, 8]), sb("group_idx", [P, ST, 8], U32)
        group_f, gate = sb("group_f", [P, ST]), sb("gate", [P, ST])
        e_sum = sb("e_sum", [P, ST, G])
        picked = sb("picked", [P, ST, E])
        top, top_idx = sb("top", [P, ST, 8]), sb("top_idx", [P, ST, 8], U32)
        choice = sb("choice", [P, 2, ST])
        ratio, total = sb("ratio", [P, ST]), sb("total", [P, ST])
        numbers, group_of = sb("numbers", [P, ST, E]), sb("group_of", [P, ST, E])
        hot = [sb(f"hot{c}", [P, ST, E]) for c in range(2)]
        both, before = sb("both", [P, ST, E]), sb("before", [P, ST + 1, E])
        earlier = sb("earlier", [P, P])
        steps, over = sb("steps", [P, E, ST]), sb("over", [P, E, ST])
        n_blocks, ends, starts = sb("n_blocks", [P, E]), sb("ends", [P, E]), sb("starts", [P, E])
        place = sb("place", [P, ST, E])
        slot_f = sb("slot_f", [P, 2, ST])
        block_no, passed = sb("block_no", [P, N_BLOCKS, E]), sb("passed", [P, N_BLOCKS, E])
        expert_f = sb("expert_f", [P, N_BLOCKS])
        tokens, clear = sb("tokens", [P, ST]), sb("clear", [N_BLOCKS, BLK])
        rows = sb("rows", [N_BLOCKS, BLK])
        ranks = k.ps("route_ranks", [P, ST, E], ctx)
        counts = k.ps("route_counts", [P, E], ctx)
        turned = k.ps("route_turned", [P, N_BLOCKS], ctx)
        bias_in, made, shifted, exped, hot_made, ranked, slots_made, cleared, rows_in, rows_turned = k.sems(
            "route", "bias_in made shifted exped hot_made ranked slots_made cleared rows_in rows_turned")
        scattered = k.soft["token_numbers_scattered"]
        block = ctx.enter_context(nc.Block())
        table = k.scratch["slot_token"]
        row_table = table.rearrange("(b s) o -> b (s o)", s=BLK)

        def over_experts(x):
            return x.rearrange("p (t o) -> p t o", o=1).broadcast_to([P, ST, E])

        def over_tiles(x):
            return x.rearrange("p (o e) -> p o e", o=1).broadcast_to([P, ST, x.shape[-1]])

        @block.sync
        def _(sp):
            sp.dma_start(bias[:, 0:G], k.dram["b_group_router"].broadcast_to([P, G])).then_inc(bias_in, 16)
            sp.dma_start(bias[:, G:], k.dram["b_expert_router"].broadcast_to([P, E])).then_inc(bias_in, 16)
            sp.wait_ge(made, 9)
            sp.dma_start(row_table, clear[:]).then_inc(cleared, 16)
            sp.wait_ge(scattered, 16 * 2 * ST)
            sp.dma_start(rows[:], row_table).then_inc(rows_in, 16)

        @block.gpsimd
        def _(pool):
            iota = dict(allow_small_or_imprecise_dtypes=True)
            nc.gpsimd.iota(numbers[:, :, :], [[0, ST], [1, E]], 0, 0, **iota).then_inc(made, 1)
            nc.gpsimd.iota(group_of[:, :, :], [[0, ST], [1, G], [0, PER_GROUP]], 0, 0, **iota).then_inc(made, 1)
            nc.gpsimd.iota(steps[:, :, :], [[0, E], [BLK, ST]], 0, 0, **iota).then_inc(made, 1)
            nc.gpsimd.iota(block_no[:, :, :], [[1, N_BLOCKS], [0, E]], 0, 0, **iota).then_inc(made, 1)
            nc.gpsimd.iota(tokens[:, :], [[P, ST]], 0, 1, **iota).then_inc(made, 1)
            nc.gpsimd.memset(earlier[:], 1.0).then_inc(made, 1)
            nc.gpsimd.memset(groups[:, :, :], -3e38).then_inc(made, 1)
            nc.gpsimd.memset(clear[:], 0.0).then_inc(made, 1)
            pool.wait_ge(made, 8)
            nc.gpsimd.affine_select(out=earlier[:], in_=earlier[:], compare_op=ALU.is_gt, fill=0.0, base=0,
                                    pattern=[[1, P]], channel_multiplier=-1).then_inc(made, 1)
            pool.wait_ge(slots_made, 2)
            pool.wait_ge(cleared, 16)
            for c in range(2):
                for t in range(ST):
                    nc.gpsimd.indirect_dma_start(
                        out=table, out_offset=bass.IndirectOffsetOnAxis(ap=slots[c][:, t:t + 1], axis=0),
                        in_=tokens[:, t:t + 1], in_offset=None).then_inc(scattered, 16)
            pool.wait_ge(scattered, 16 * 2 * ST)

        @block.scalar
        def _(act):
            act.wait_ge(shifted, 1)
            nc.scalar.activation(e_sum[:, :, :], e_sum[:, :, :], ACT.Exp).then_inc(exped, 1)
            act.wait_ge(shifted, 2)
            nc.scalar.activation(ratio[:], ratio[:], ACT.Exp).then_inc(exped, 1)

        @block.vector
        def _(dve):
            link = k.own("dve", dve)
            v = nc.vector
            dve.wait_ge(bias_in, 32)
            dve.wait_ge(made, 9)
            link(v.tensor_tensor(logits, logits, over_tiles(bias[:, :]), ALU.add))
            link(v.tensor_copy(groups[:, :, 0:G], logits[:, :, 0:G]))
            for t in range(ST):
                link(v.max(group_max[:, t, :], groups[:, t, :]))
                link(v.max_index(group_idx[:, t, :], group_max[:, t, :], groups[:, t, :]))
            v.tensor_tensor(e_sum[:, :, :], logits[:, :, 0:G], group_max[:, :, 0:1].broadcast_to([P, ST, G]),
                            ALU.subtract).then_inc(shifted, 1)
            link(v.tensor_copy(group_f[:], group_idx[:, :, 0:1].rearrange("p t o -> p (t o)")))
            dve.wait_ge(exped, 1)
            link(v.tensor_reduce(total[:], e_sum[:, :, :], AX, ALU.add))
            link(v.reciprocal(gate[:], total[:]))
            link(v.tensor_tensor(hot[0][:, :, :], group_of[:, :, :], over_experts(group_f[:]), ALU.is_equal))
            link(v.tensor_tensor(picked[:, :, :], logits[:, :, G:], hot[0][:, :, :], ALU.mult))
            link(v.tensor_scalar(hot[0][:, :, :], hot[0][:, :, :], -1.0, 3e38, ALU.add, ALU.mult))
            link(v.tensor_tensor(picked[:, :, :], picked[:, :, :], hot[0][:, :, :], ALU.add))
            for t in range(ST):
                link(v.max(top[:, t, :], picked[:, t, :]))
                link(v.max_index(top_idx[:, t, :], top[:, t, :], picked[:, t, :]))
            v.tensor_tensor(ratio[:], top[:, :, 1:2].rearrange("p t o -> p (t o)"),
                            top[:, :, 0:1].rearrange("p t o -> p (t o)"), ALU.subtract).then_inc(shifted, 1)
            for c in range(2):
                link(v.tensor_copy(choice[:, c, :], top_idx[:, :, c:c + 1].rearrange("p t o -> p (t o)")))
                link(v.tensor_tensor(hot[c][:, :, :], numbers[:, :, :], over_experts(choice[:, c, :]), ALU.is_equal))
            link(v.tensor_tensor(both[:, :, :], hot[0][:, :, :], hot[1][:, :, :], ALU.add))
            link(v.memset(before[:, 0, :], 0.0))
            for t in range(ST):
                link(v.tensor_tensor(before[:, t + 1, :], before[:, t, :], both[:, t, :], ALU.add))
            dve.sem_inc(hot_made, 1)
            dve.wait_ge(exped, 2)
            link(v.tensor_scalar(total[:], ratio[:], 1.0, None, ALU.add))
            link(v.reciprocal(total[:], total[:]))
            link(v.tensor_tensor(weights[:, 0, :], gate[:], total[:], ALU.mult))
            link(v.tensor_tensor(weights[:, 1, :], weights[:, 0, :], ratio[:], ALU.mult))
            dve.wait_ge(ranked, 1)
            link(v.tensor_tensor(over[:, :, :], counts[:, :].rearrange("p (e o) -> p e o", o=1).broadcast_to([P, E, ST]),
                                 steps[:, :, :], ALU.is_gt))
            link(v.tensor_reduce(n_blocks[:], over[:, :, :], AX, ALU.add))
            link(v.tensor_tensor_scan(ends[:], k.ones[:, 0:E], n_blocks[:], 0.0, ALU.mult, ALU.add))
            link(v.tensor_tensor(starts[:], ends[:], n_blocks[:], ALU.subtract))
            link(v.tensor_scalar(starts[:], starts[:], float(BLK), None, ALU.mult))
            link(v.tensor_tensor(place[:, :, :], ranks[:, :, :], over_tiles(starts[:, :]), ALU.add))
            for c in range(2):
                link(v.tensor_tensor(hot[c][:, :, :], hot[c][:, :, :], place[:, :, :], ALU.mult))
                link(v.tensor_reduce(slot_f[:, c, :], hot[c][:, :, :], AX, ALU.add))
                v.tensor_copy(slots[c][:], slot_f[:, c, :]).then_inc(slots_made, 1)
            link(v.tensor_tensor(passed[:, :, :], block_no[:, :, :],
                                 ends[:, :].rearrange("p (o e) -> p o e", o=1).broadcast_to([P, N_BLOCKS, E]), ALU.is_ge))
            link(v.tensor_reduce(expert_f[:], passed[:, :, :], AX, ALU.add))
            link(v.tensor_scalar(expert_f[:], expert_f[:], float(E - 1), None, ALU.min))
            link(v.tensor_copy(experts[:], expert_f[:]))
            dve.wait_ge(rows_turned, 1)
            link(v.tensor_copy(slot_of_block[:], turned[:]))

        @block.tensor
        def _(pe):
            pe.wait_ge(hot_made, 1)
            pe.wait_ge(made, 9)
            for t in range(ST):
                nc.tensor.matmul(ranks[:, t, :], earlier[:], both[:, t, :], start=True, stop=False)
                nc.tensor.matmul(ranks[:, t, :], k.ones[:], before[:, t, :], start=False, stop=True)
            nc.tensor.matmul(counts[:, :], k.ones[:], before[:, ST, :], start=True, stop=True).then_inc(ranked, 1)
            pe.wait_ge(rows_in, 16)
            nc.tensor.transpose(turned[:], rows[:], k.ident[0:N_BLOCKS, 0:N_BLOCKS]).then_inc(rows_turned, 1)
        k.chains["dve"].settle()


def run_experts(k, experts, slot_of_block):
    nc = k.nc
    with k.phase() as ctx:
        idx = [k.sb(f"moe_idx{b}", [P, 1], U32, ctx=ctx) for b in range(2)]
        rows = [k.sb(f"moe_rows{b}", [P, D], ctx=ctx) for b in range(2)]
        xt = [k.sb(f"moe_xt{b}", [P, KD, BLK], ctx=ctx) for b in range(2)]
        wgu = [k.sb(f"moe_wgu{b}", [P, 2, KD, FF], ctx=ctx) for b in range(2)]
        wd = [k.sb(f"moe_wd{b}", [P, FF // P, D], ctx=ctx) for b in range(2)]
        silu = [k.sb(f"moe_silu{b}", [P, 2, BLK], ctx=ctx) for b in range(2)]
        hidden = [k.sb(f"moe_hidden{b}", [P, 2, BLK], ctx=ctx) for b in range(2)]
        y = [k.sb(f"moe_y{b}", [P, D], ctx=ctx) for b in range(2)]
        turned = k.ps("moe_turned", [P, KD, BLK], ctx)
        up = [k.ps(f"moe_up{b}", [P, 2, 2, BLK], ctx) for b in range(2)]
        down = [k.ps(f"moe_down{b}", [P, D], ctx) for b in range(2)]
        (w_in0, w_in1, indexed, turns, x_ready, ups, silus, hiddens, downs, y_ready, stored0,
         stored1, passed) = k.sems("moe", "w_in0 w_in1 indexed turns x_ready ups silus hiddens downs "
                                  "y_ready stored0 stored1 passed")
        gathered = (k.soft["rows_gathered0"], k.soft["rows_gathered1"])
        w_in, stored = (w_in0, w_in1), (stored0, stored1)
        block = ctx.enter_context(nc.Block())
        rounds = N_BLOCKS // 2
        gate_w = k.dram["w_expert_gate"][0].rearrange("e (c p) f -> p e c f", p=P)
        up_w = k.dram["w_expert_up"][0].rearrange("e (c p) f -> p e c f", p=P)
        down_w = k.dram["w_expert_down"][0].rearrange("e (c p) d -> p e c d", p=P)
        y_out = k.scratch["expert_rows"].rearrange("(n s) d -> s n d", s=BLK)
        ffn_gain = k.gain("norm_ffn_g")

        @block.sync
        def _(sp):
            with sp.Fori(0, rounds) as i:
                for b in range(2):
                    sp.wait_ge(downs, 2 * i + b + 1)
                    e = sp.value_load(experts[0:1, bass.ds(2 * i + b, 1)], min_val=0, max_val=EXPERTS - 1)
                    sp.dma_start(wgu[b][:, 0, :, :], gate_w[:, bass.ds(e, 1), :, :].rearrange("p e c f -> p (e c) f")
                                 ).then_inc(w_in[b], 16)
                    sp.dma_start(wgu[b][:, 1, :, :], up_w[:, bass.ds(e, 1), :, :].rearrange("p e c f -> p (e c) f")
                                 ).then_inc(w_in[b], 16)
                    sp.dma_start(wd[b][:, :, :], down_w[:, bass.ds(e, 1), :, :].rearrange("p e c d -> p (e c) d")
                                 ).then_inc(w_in[b], 16)

        @block.gpsimd
        def _(pool):
            with pool.Fori(0, rounds) as i:
                for b in range(2):
                    pool.wait_ge(turns, 2 * i + b + 1)
                    nc.gpsimd.tensor_copy(idx[b][:], slot_of_block[:, bass.ds(2 * i + b, 1)]).then_inc(indexed, 1)
                    pool.wait_ge(indexed, 2 * i + b + 1)
                    pool.sem_inc(passed, 1)
                    nc.gpsimd.indirect_dma_start(out=rows[b][:], out_offset=None, in_=k.scratch["ffn_rows"],
                                                 in_offset=bass.IndirectOffsetOnAxis(ap=idx[b][:, 0:1], axis=0)
                                                 ).then_inc(gathered[b], 16)

        @block.tensor
        def _(pe):
            pe.sem_inc(ups, 1)
            pe.sem_inc(downs, 2)
            pe.sem_inc(turns, 2)
            with pe.Fori(0, rounds) as i:
                for b in range(2):
                    pe.wait_ge(gathered[b], 16 * i + 16)
                    pe.wait_ge(x_ready, 2 * i + b + 1)
                    for c in range(KD):
                        last = nc.tensor.transpose(turned[:, c, :], rows[b][:, c * P:(c + 1) * P], k.ident[:])
                    last.then_inc(turns, 1)
                for b in range(2):
                    pe.wait_ge(w_in[b], 48 * i + 48)
                    pe.wait_ge(x_ready, 2 * i + b + 1 + 1)
                    pe.wait_ge(hiddens, 2 * i + 1)
                    for m in range(2):
                        for f in range(2):
                            for c in range(KD):
                                last = nc.tensor.matmul(up[b][:, m, f, :], wgu[b][:, m, c, f * P:(f + 1) * P],
                                                        xt[b][:, c, :], start=(c == 0), stop=(c == KD - 1))
                    last.then_inc(ups, 1)
                for b in range(2):
                    pe.wait_ge(hiddens, 2 * i + b + 1 + 1)
                    pe.wait_ge(y_ready, 2 * i + 1)
                    for h in range(2):
                        for c in range(FF // P):
                            last = nc.tensor.matmul(down[b][:, h * HALF:(h + 1) * HALF], hidden[b][:, c, :],
                                                    wd[b][:, c, h * HALF:(h + 1) * HALF],
                                                    start=(c == 0), stop=(c == FF // P - 1))
                    last.then_inc(downs, 1)

        @block.vector
        def _(dve):
            dve.sem_inc(hiddens, 1)
            dve.sem_inc(x_ready, 1)
            with dve.Fori(0, rounds) as i:
                for b in range(2):
                    dve.wait_ge(turns, 2 * i + b + 1 + 2)
                    dve.wait_ge(ups, 2 * i + 1)
                    nc.vector.tensor_tensor(xt[b][:, :, :], turned[:, :, :],
                                            ffn_gain.rearrange("p (c o) -> p c o", o=1).broadcast_to([P, KD, BLK]),
                                            ALU.mult).then_inc(x_ready, 1)
                for b in range(2):
                    dve.wait_ge(silus, 2 * i + b + 1)
                    dve.wait_ge(downs, 2 * i + 2)
                    nc.vector.tensor_tensor(hidden[b][:, :, :], up[b][:, 1, :, :], silu[b][:, :, :],
                                            ALU.mult).then_inc(hiddens, 1)

        @block.scalar
        def _(act):
            act.sem_inc(stored0, 16)
            act.sem_inc(stored1, 16)
            act.sem_inc(y_ready, 1)
            with act.Fori(0, rounds) as i:
                for b in range(2):
                    act.wait_ge(ups, 2 * i + b + 1 + 1)
                    act.wait_ge(hiddens, 2 * i + 1)
                    nc.scalar.activation(silu[b][:, :, :], up[b][:, 0, :, :], ACT.Silu).then_inc(silus, 1)
                for b in range(2):
                    act.wait_ge(downs, 2 * i + b + 1 + 2)
                    act.wait_ge(stored[b], 16 * i + 16)
                    nc.scalar.activation(y[b][:], down[b][:], ACT.Copy).then_inc(y_ready, 1)
                    act.wait_ge(y_ready, 2 * i + b + 1 + 1)
                    act.dma_start(y_out[:, bass.ds(2 * i + b, 1), :].rearrange("s n d -> s (n d)"),
                                  y[b][:]).then_inc(stored[b], 16)
            act.wait_ge(stored0, 16 * rounds + 16)
            act.wait_ge(stored1, 16 * rounds + 16)


def combine(k, slots, weights):
    nc = k.nc
    with k.phase() as ctx:
        idx = [[k.sb(f"comb_idx{c}{b}", [P, 1], U32, ctx=ctx) for b in range(2)] for c in range(2)]
        rows = [[k.sb(f"comb_rows{c}{b}", [P, D], ctx=ctx) for b in range(2)] for c in range(2)]
        indexed, added, passed = k.sems("comb", "indexed added passed")
        gathered = (k.soft["outputs_gathered0"], k.soft["outputs_gathered1"])
        block = ctx.enter_context(nc.Block())

        @block.gpsimd
        def _(pool):
            with pool.Fori(0, ST // 2) as i:
                for b in range(2):
                    pool.wait_ge(added, 4 * i + 1)
                    for c in range(2):
                        nc.gpsimd.tensor_copy(idx[c][b][:], slots[c][:, bass.ds(2 * i + b, 1)]).then_inc(indexed, 1)
                        pool.wait_ge(indexed, 2 * (2 * i + b) + c + 1)
                        pool.sem_inc(passed, 1)
                        nc.gpsimd.indirect_dma_start(out=rows[c][b][:], out_offset=None, in_=k.scratch["expert_rows"],
                                                     in_offset=bass.IndirectOffsetOnAxis(ap=idx[c][b][:, 0:1], axis=0)
                                                     ).then_inc(gathered[b], 16)

        @block.vector
        def _(dve):
            dve.sem_inc(added, 1)
            with dve.Fori(0, ST // 2) as i:
                for b in range(2):
                    dve.wait_ge(gathered[b], 32 * i + 32)
                    x = row_of(k.X, 2 * i + b)
                    for c in range(2):
                        nc.vector.scalar_tensor_tensor(out=x, in0=rows[c][b][:], scalar=weights[:, c, bass.ds(2 * i + b, 1)],
                                                       in1=x, op0=ALU.mult, op1=ALU.add).then_inc(added, 1)
                        dve.wait_ge(added, 2 * (2 * i + b) + c + 1 + 1)


def expert_layer(k):
    nc = k.nc
    norm_turn(k, "ffn_norm", k.X, ST, k.gain("norm_ffn_g"), k.HT, rows_out=k.scratch["ffn_rows"])
    with ExitStack() as ctx:
        logits = k.sb("logits", [P, ST, GROUPS + EXPERTS], ctx=ctx)
        slots = [k.sb(f"slots{c}", [P, ST], U32, ctx=ctx) for c in range(2)]
        weights = k.sb("route_w", [P, 2, ST], ctx=ctx)
        experts = k.sb("experts", [P, N_BLOCKS], I32, ctx=ctx)
        slot_of_block = k.sb("slot_of_block", [P, N_BLOCKS], U32, ctx=ctx)
        w_g = k.dram["w_group_router"][0].rearrange("(c p) n -> p c n", p=P)
        w_e = k.dram["w_expert_router"][0].rearrange("(c p) n -> p c n", p=P)
        project_tokens(k, "router", [(w_g, 0, GROUPS), (w_e, GROUPS, EXPERTS)], GROUPS + EXPERTS, k.HT, KD, logits)
        route(k, logits[:, :, :], slots, weights, experts, slot_of_block)
        run_experts(k, experts, slot_of_block)
        combine(k, slots, weights)


def final_norm(k):
    nc = k.nc
    with k.phase() as ctx:
        gain = k.sb("final_gain", [P, D], ctx=ctx)
        junk = [k.sb(f"final_junk{b}", [P, D], ctx=ctx) for b in range(2)]
        gain_in, even, odd, mean_made, root_made, normed = k.sems("final", "gain_in even odd mean_made root_made normed")
        block = ctx.enter_context(nc.Block())

        @block.sync
        def _(sp):
            sp.dma_start(gain[:], k.dram["norm_final_g"].rearrange("(o d) -> o d", o=1).broadcast_to([P, D])
                         ).then_inc(gain_in, 16)

        @block.scalar
        def _(act):
            for t in range(0, ST, 2):
                if t:
                    act.wait_ge(even, t // 2)
                nc.scalar.activation(junk[0][:], k.X[:, t, :], ACT.Square, accum_out=k.ssq[:, t:t + 1]).then_inc(even, 1)
            act.wait_ge(mean_made, 1)
            nc.scalar.activation(k.root[:], k.mean[:], ACT.Sqrt).then_inc(root_made, 1)

        @block.vector
        def _(dve):
            link = k.own("dve", dve)
            for t in range(1, ST, 2):
                if t > 1:
                    dve.wait_ge(odd, t // 2)
                nc.vector.tensor_tensor_reduce(out=junk[1][:], in0=k.X[:, t, :], in1=k.X[:, t, :], scale=1.0, scalar=0.0,
                                               op0=ALU.mult, op1=ALU.add, accum_out=k.ssq[:, t:t + 1]).then_inc(odd, 1)
            dve.wait_ge(odd, ST // 2)
            dve.wait_ge(even, ST // 2)
            nc.vector.tensor_scalar(k.mean[:], k.ssq[:], 1.0 / D, EPS, ALU.mult, ALU.add).then_inc(mean_made, 1)
            dve.wait_ge(root_made, 1)
            link(nc.vector.reciprocal(k.rstd[:], k.root[:]))
            dve.wait_ge(gain_in, 16)
            with dve.Fori(0, ST) as t:
                nc.vector.scalar_tensor_tensor(out=row_of(k.X, t), in0=row_of(k.X, t), scalar=k.rstd[:, bass.ds(t, 1)],
                                               in1=gain[:], op0=ALU.mult, op1=ALU.mult).then_inc(normed, 1)
        k.chains["dve"].settle()


def gate_rows(k, vm):
    nc = k.nc
    H = 4
    with k.phase() as ctx:
        w = k.sb("gr_w", [P, KD, 96], ctx=ctx)
        bias = k.sb("gr_bias", [H, 3], ctx=ctx)
        raw = [k.sb(f"gr_raw{n}", [H, S], ctx=ctx) for n in range(3)]
        logs = [k.sb(f"gr_logs{n}", [H, S], ctx=ctx) for n in range(2)]
        sums = [k.sb(f"gr_sums{n}", [H, S], ctx=ctx) for n in range(2)]
        ones = k.sb("gr_ones", [H, S], ctx=ctx)
        a, top, floor, neg = (k.sb(f"gr_{n}", [H, S], ctx=ctx) for n in ("a", "top", "floor", "neg"))
        acc = k.ps("gr_acc", [P, S], ctx)
        cols = k.ps("gr_cols", [P, 2, ST, H], ctx)
        w_in, bias_in, cleared, products, copied, absed, logged, rows_made, turned, stored = k.sems(
            "gr", "w_in bias_in cleared products copied absed logged rows_made turned stored")
        block = ctx.enter_context(nc.Block())
        w_view = k.dram["w_in_2"][0].rearrange("(c p) n -> p c n", p=P)

        @block.sync
        def _(sp):
            sp.wait_ge(cleared, 2)
            for n, col in enumerate((C_FF, C_MI, C_MI + H)):
                sp.dma_start(w[:, :, 32 * n:32 * n + H], w_view[:, :, col:col + H]).then_inc(w_in, 16)
            for n, name in enumerate(("fox_f_bias_2", "mlstm_i_bias_2", "mlstm_f_bias_2")):
                sp.dma_start(bias[:, n:n + 1], k.dram[name].rearrange("l h -> h l")).then_inc(bias_in, 16)
            fox_q = k.scratch["fox_q"].rearrange("(h n) s -> h n s", n=2)
            fox_k = k.scratch["fox_k"].rearrange("(h n) s -> h n s", n=2)
            sp.dma_start(fox_q[:, 0, :], ones[:]).then_inc(stored, 16)
            sp.dma_start(fox_k[:, 1, :], ones[:]).then_inc(stored, 16)
            sp.wait_ge(rows_made, 1)
            sp.dma_start(fox_q[:, 1, :], sums[0][:]).then_inc(stored, 16)
            sp.wait_ge(rows_made, 2)
            sp.dma_start(fox_k[:, 0, :], neg[:]).then_inc(stored, 16)
            sp.wait_ge(rows_made, 4)
            sp.dma_start(k.scratch["mlstm_row"], top[:]).then_inc(stored, 16)
            sp.wait_ge(stored, 16 * 5)

        @block.gpsimd
        def _(pool):
            nc.gpsimd.memset(w[:, :, :], 0.0).then_inc(cleared, 1)
            nc.gpsimd.memset(ones[:], 1.0).then_inc(cleared, 1)
            nc.gpsimd.memset(vm[:, :, :, HD:HD + 1], 1.0).then_inc(cleared, 1)

        @block.tensor
        def _(pe):
            pe.wait_ge(w_in, 48)
            for c in range(KD):
                for h in range(2):
                    last = nc.tensor.matmul(acc[0:96, h * HALF:(h + 1) * HALF], w[:, c, :],
                                            k.HT[:, c, h * HALF:(h + 1) * HALF], start=(c == 0), stop=(c == KD - 1))
            last.then_inc(products, 1)
            pe.wait_ge(rows_made, 5)
            for n, row in enumerate((a, floor)):
                for t in range(ST):
                    last = nc.tensor.transpose(cols[:, n, t, :], row[:, t * P:(t + 1) * P], k.ident[0:H, 0:H])
            last.then_inc(turned, 1)

        @block.scalar
        def _(act):
            act.wait_ge(products, 1)
            for n in range(3):
                nc.scalar.activation(raw[n][:], acc[32 * n:32 * n + H, :], ACT.Copy).then_inc(copied, 1)
            for n, x in enumerate((raw[0], raw[2])):
                act.wait_ge(absed, n + 1)
                nc.scalar.activation(logs[n][:], x[:], ACT.Abs).then_inc(logged, 1)
                act.wait_ge(logged, 3 * n + 1)
                nc.scalar.activation(logs[n][:], logs[n][:], ACT.Exp, scale=-1.0).then_inc(logged, 1)
                act.wait_ge(logged, 3 * n + 2)
                nc.scalar.activation(logs[n][:], logs[n][:], ACT.Ln, bias=1.0).then_inc(logged, 1)
            act.wait_ge(turned, 1)
            nc.scalar.activation(k.a_col[:, :, :], cols[:, 0, :, :], ACT.Copy)
            nc.scalar.activation(k.floor_col[:, :, :], cols[:, 1, :, :], ACT.Exp, scale=-1.0)

        @block.vector
        def _(dve):
            link = k.own("dve", dve)
            v = nc.vector
            dve.wait_ge(bias_in, 48)
            dve.wait_ge(copied, 3)
            dve.wait_ge(cleared, 3)
            for n in (0, 2):
                v.tensor_scalar(raw[n][:], raw[n][:], bias[:, n:n + 1], None, ALU.add).then_inc(absed, 1)
            link(v.tensor_scalar(raw[1][:], raw[1][:], bias[:, 1:2], None, ALU.add))
            for n, x in enumerate((raw[0], raw[2])):
                dve.wait_ge(logged, 3 * n + 3)
                link(v.scalar_tensor_tensor(out=logs[n][:], in0=x[:], scalar=0.0, in1=logs[n][:],
                                            op0=ALU.min, op1=ALU.subtract))
                ins = v.tensor_tensor_scan(sums[n][:], ones[:], logs[n][:], 0.0, ALU.mult, ALU.add)
                if n == 0:
                    ins.then_inc(rows_made, 1)
                    dve.wait_ge(rows_made, 1)
                    v.tensor_scalar(neg[:], sums[0][:], -1.0, None, ALU.mult).then_inc(rows_made, 1)
                else:
                    link(ins)
            link(v.tensor_tensor(a[:], raw[1][:], sums[1][:], ALU.subtract))
            link(v.tensor_tensor_scan(top[:], ones[:], a[:], 0.0, ALU.mult, ALU.max))
            v.tensor_tensor(floor[:], top[:], sums[1][:], ALU.add).then_inc(rows_made, 1)
            dve.wait_ge(rows_made, 3)
            v.tensor_scalar(top[:], top[:], -1.0, None, ALU.mult).then_inc(rows_made, 1)
            dve.wait_ge(rows_made, 4)
            dve.sem_inc(rows_made, 1)
        k.chains["dve"].settle()


def matrix_lstm(k, V, out):
    nc = k.nc
    H = 4
    with k.phase() as ctx:
        q = [k.sb(f"ml_q{b}", [HD, S], ctx=ctx) for b in range(2)]
        kk = [k.sb(f"ml_k{b}", [HD, S], ctx=ctx) for b in range(2)]
        row = [k.sb(f"ml_row{b}", [P, S], ctx=ctx) for b in range(2)]
        a_col = [k.sb(f"ml_a{b}", [P, ST], ctx=ctx) for b in range(2)]
        decay = [k.sb(f"ml_decay{b}", [P, S], ctx=ctx) for b in range(2)]
        w = [[k.sb(f"ml_w{b}{t}", [P, S - t * P], ctx=ctx) for t in range(ST)] for b in range(2)]
        stats = [k.sb(f"ml_stats{b}", [P, ST, 2], ctx=ctx) for b in range(2)]
        values = [k.sb(f"ml_v{b}", [P, ST, HD + 1], ctx=ctx) for b in range(2)]
        before_mask = k.sb("ml_mask", [P, P], ctx=ctx)
        scores = [k.ps(f"ml_scores{b}", [P, S], ctx) for b in range(2)]
        acc = [k.ps(f"ml_acc{b}", [P, 2, HALF], ctx) for b in range(2)]
        (head_in0, head_in1, mask_made, a_ready, masked, decays, products, weighted, sums_made, done) = k.sems(
            "ml", "head_in0 head_in1 mask_made a_ready masked decays products weighted sums_made done")
        head_in = (head_in0, head_in1)
        block = ctx.enter_context(nc.Block())
        rounds = H // 2
        plain = k.scratch["plain"]
        q_row, k_row = C_MQ - C_CU, C_MQ + H * HD - C_CU

        def at(b, t):
            return acc[b][:, t // 4, (t % 4) * (HD + 1):(t % 4 + 1) * (HD + 1)]

        @block.sync
        def _(sp):
            with sp.Fori(0, rounds) as i:
                for b in range(2):
                    sp.wait_ge(done, 2 * i + 1)
                    h = i * 2 + b
                    sp.dma_start(q[b][:], plain[bass.ds(h * HD + q_row, HD), :]).then_inc(head_in[b], 16)
                    sp.dma_start(kk[b][:], plain[bass.ds(h * HD + k_row, HD), :]).then_inc(head_in[b], 16)
                    sp.dma_start(row[b][:], k.scratch["mlstm_row"][bass.ds(h, 1), :].broadcast_to([P, S])
                                 ).then_inc(head_in[b], 16)

        @block.gpsimd
        def _(pool):
            nc.gpsimd.memset(before_mask[:], 0.0).then_inc(mask_made, 1)
            pool.wait_ge(mask_made, 1)
            nc.gpsimd.affine_select(out=before_mask[:], in_=before_mask[:], compare_op=ALU.is_ge, fill=NEG, base=0,
                                    pattern=[[1, P]], channel_multiplier=-1).then_inc(mask_made, 1)
            with pool.Fori(0, rounds) as i:
                for b in range(2):
                    pool.wait_ge(done, 2 * i + 1)
                    h = i * 2 + b
                    nc.gpsimd.tensor_copy(a_col[b][:], k.a_col[:, :, bass.ds(h, 1)].rearrange("p t h -> p (t h)")
                                          ).then_inc(a_ready, 1)
                    nc.gpsimd.tensor_copy(values[b][:, :, :], V[:, :, bass.ds(h, 1), :].rearrange(
                        "p t h n -> p (t h) n")).then_inc(a_ready, 1)

        @block.tensor
        def _(pe):
            pe.sem_inc(sums_made, 1)
            with pe.Fori(0, rounds) as i:
                for b in range(2):
                    pe.wait_ge(head_in[b], 48 * i + 48)
                    for t in range(ST):
                        g = (i * 2 + b) * ST + t
                        pe.wait_ge(weighted, g + 1)
                        width = S - t * P
                        for c in range(0, width, HALF):
                            n = min(HALF, width - c)
                            last = nc.tensor.matmul(scores[t % 2][:, c:c + n], kk[b][:, t * P:(t + 1) * P],
                                                    q[b][:, t * P + c:t * P + c + n], start=True, stop=True)
                        last.then_inc(products, 1)
                for b in range(2):
                    pe.wait_ge(weighted, (i * 2 + b + 1) * ST + 2)
                    pe.wait_ge(a_ready, (i * 2 + b) * 2 + 2)
                    pe.wait_ge(done, 2 * i + 1)
                    for t in range(ST):
                        for c in range(t + 1):
                            last = nc.tensor.matmul(at(b, t), w[b][c][:, (t - c) * P:(t - c + 1) * P],
                                                    values[b][:, c, :], start=(c == 0), stop=(c == t))
                    last.then_inc(sums_made, 1)

        @block.scalar
        def _(act):
            with act.Fori(0, rounds) as i:
                for b in range(2):
                    act.wait_ge(head_in[b], 48 * i + 48)
                    act.wait_ge(a_ready, (i * 2 + b) * 2 + 2)
                    for t in range(ST):
                        g = (i * 2 + b) * ST + t
                        act.wait_ge(weighted, g + 1)
                        act.wait_ge(masked, g + 1)
                        nc.scalar.activation(decay[t % 2][:, 0:P], decay[t % 2][:, 0:P], ACT.Exp,
                                             bias=a_col[b][:, t:t + 1]).then_inc(decays, 1)
                        if t < ST - 1:
                            nc.scalar.activation(decay[t % 2][:, P:S - t * P], row[b][:, (t + 1) * P:S], ACT.Exp,
                                                 bias=a_col[b][:, t:t + 1]).then_inc(decays, 1)

        @block.vector
        def _(dve):
            dve.sem_inc(done, 1)
            link = k.own("dve", dve)
            chain = k.chains["dve"]
            dve.sem_inc(weighted, 2)
            dve.wait_ge(mask_made, 2)
            per = 2 * ST - 1
            with dve.Fori(0, rounds) as i:
                chain.enter(i, 2 * 3)
                for b in range(2):
                    dve.wait_ge(head_in[b], 48 * i + 48)
                    for t in range(ST + 1):
                        g = (i * 2 + b) * ST + t
                        if t < ST:
                            dve.wait_ge(weighted, g + 1)
                            nc.vector.tensor_tensor(decay[t % 2][:, 0:P], row[b][:, t * P:(t + 1) * P], before_mask[:],
                                                    ALU.add).then_inc(masked, 1)
                        if t:
                            dve.wait_ge(products, g)
                            dve.wait_ge(decays, (i * 2 + b) * per + min(2 * t, per))
                            dve.wait_ge(sums_made, 2 * i + 1)
                            width = S - (t - 1) * P
                            nc.vector.scalar_tensor_tensor(out=w[b][t - 1][:], in0=scores[(t - 1) % 2][:, 0:width],
                                                           scalar=HD ** -0.5, in1=decay[(t - 1) % 2][:, 0:width],
                                                           op0=ALU.mult, op1=ALU.mult).then_inc(weighted, 1)
                for b in range(2):
                    dve.wait_ge(sums_made, i * 2 + b + 1 + 1)
                    h = i * 2 + b
                    st = stats[b]
                    den = acc[b][:, :, 0:4 * (HD + 1)].rearrange("p a (t n) -> p a t n", n=HD + 1)[:, :, :, HD:HD + 1]
                    den = den.rearrange("p a t n -> p a (t n)")
                    one, two = (st[:, :, n:n + 1].rearrange("p (a t) n -> p a (t n)", a=2) for n in range(2))
                    link(nc.vector.tensor_copy(one, den))
                    link(nc.vector.scalar_tensor_tensor(
                        out=st[:, :, 1:2], in0=st[:, :, 0:1], scalar=-1.0, in1=k.floor_col[:, :, bass.ds(h, 1)],
                        op0=ALU.mult, op1=ALU.max))
                    link(nc.vector.tensor_tensor(st[:, :, 0:1], st[:, :, 0:1], st[:, :, 1:2], ALU.max))
                    nc.vector.reciprocal(st[:, :, 1:2], st[:, :, 0:1]).then_inc(mask_made, 1)
                    dve.wait_ge(mask_made, 2 + 5 * h + 1)
                    for t in range(ST):
                        ins = nc.vector.tensor_scalar(out[:, t, bass.ds(h * HD, HD)], at(b, t)[:, 0:HD], st[:, t, 1:2],
                                                      None, ALU.mult)
                    ins.then_inc(mask_made, 4)
                    dve.wait_ge(mask_made, 2 + 5 * h + 5)
                    dve.sem_inc(done, 1)
                chain.leave(rounds)


def short_conv(k, conv_out, ml_rows):
    nc = k.nc
    CH = 2
    with k.phase() as ctx:
        u, bg, cg, mo = (k.sb(f"conv_{n}", [P, CH, S], ctx=ctx) for n in ("u", "b", "c", "mo"))
        loaded, gated, chain_c = k.sems("conv", "loaded gated chain_c")
        block = ctx.enter_context(nc.Block())
        plain = k.scratch["plain"]

        @block.sync
        def _(sp):
            for n, tile in enumerate((u, bg, cg)):
                sp.dma_start(tile[:, :, :], plain[n * CH * P:(n + 1) * CH * P, :].rearrange("(c p) s -> p c s", p=P)
                             ).then_inc(loaded, 16)
            sp.dma_start(mo[:, :, :], k.scratch["mo"].rearrange("(c p) s -> p c s", p=P)).then_inc(gated, 16)

        @block.scalar
        def _(act):
            act.wait_ge(gated, 16)
            nc.scalar.activation(mo[:, :, :], mo[:, :, :], ACT.Sigmoid).then_inc(gated, 1)

        @block.vector
        def _(dve):
            link = k.own("dve", dve)
            dve.wait_ge(loaded, 48)
            link(nc.vector.tensor_tensor(u[:, :, :], u[:, :, :], cg[:, :, :], ALU.mult))
            for c in range(CH):
                taps = [k.gain("conv_w_2", n * CH + c, 1) for n in range(3)]
                link(nc.vector.tensor_scalar(conv_out[:, c, :], u[:, c, :], taps[2], None, ALU.mult))
                for back, tap in ((1, taps[1]), (2, taps[0])):
                    link(nc.vector.scalar_tensor_tensor(out=conv_out[:, c, back:], in0=u[:, c, 0:S - back], scalar=tap,
                                                        in1=conv_out[:, c, back:], op0=ALU.mult, op1=ALU.add))
            link(nc.vector.tensor_tensor(conv_out[:, :, :], conv_out[:, :, :], bg[:, :, :], ALU.mult))
            dve.wait_ge(gated, 17)
            link(nc.vector.tensor_tensor(ml_rows[:, :, :], ml_rows[:, :, :], mo[:, :, :], ALU.mult))
        k.chains["dve"].settle()


def t5_buckets(n):
    exact, most, buckets = 16, 128, 32
    out = []
    for d in range(n):
        if d < exact:
            out.append(d)
        else:
            large = exact + int(np.log(d / exact) / np.log(most / exact) * (buckets - exact))
            out.append(min(large, buckets - 1))
    return out


def window_bias(k, biases, sinks):
    nc = k.nc
    H, B, W2 = 8, 32, 3 * P
    with k.phase() as ctx:
        rel = k.sb("wb_rel", [B, H], ctx=ctx)
        hot = k.sb("wb_hot", [B, W2], ctx=ctx)
        index = k.sb("wb_index", [B, 1], ctx=ctx)
        bucket = k.sb("wb_bucket", [B, W2], ctx=ctx)
        rows = k.sb("wb_rows", [H, W2], ctx=ctx)
        flipped = k.sb("wb_flipped", [P, H, 2 * P], ctx=ctx)
        flip = k.sb("wb_flip", [P, P], ctx=ctx)
        acc = k.ps("wb_acc", [H, W2], ctx)
        turned = k.ps("wb_turned", [P, H, 2 * P], ctx)
        rel_in, bucketed, made, hot_made, product, rows_made, stored, loaded, upright = k.sems(
            "wb", "rel_in bucketed made hot_made product rows_made stored loaded upright")
        block = ctx.enter_context(nc.Block())
        buckets = t5_buckets(WINDOW)
        runs = []
        for j in range(P, 2 * P):
            value = buckets[2 * P - 1 - j]
            if runs and runs[-1][2] == value:
                runs[-1][1] = j + 1
            else:
                runs.append([j, j + 1, value])

        @block.sync
        def _(sp):
            sp.dma_start(rel[:], k.dram["rel_bias_2"]).then_inc(rel_in, 16)
            sp.dma_start(sinks[:], k.dram["swa_sinks_2"].broadcast_to([P, H])).then_inc(loaded, 16)
            sp.wait_ge(rows_made, 3)
            sp.dma_start(k.scratch["window_rows"], rows[:]).then_inc(stored, 16)
            sp.wait_ge(stored, 16)
            view = k.scratch["window_rows"]
            for h in range(H):
                skewed = bass.AP(view.tensor, view.offset + h * W2, [[1, P], [1, 2 * P]])
                sp.dma_start(flipped[:, h, :], skewed).then_inc(loaded, 16)

        @block.gpsimd
        def _(pool):
            nc.gpsimd.memset(bucket[:], -1.0).then_inc(made, 1)
            nc.gpsimd.iota(index[:], [[0, 1]], 0, 1, allow_small_or_imprecise_dtypes=True).then_inc(made, 1)
            nc.gpsimd.memset(flip[:], 0.0).then_inc(made, 1)
            pool.wait_ge(made, 3)
            nc.gpsimd.affine_select(out=flip[:], in_=flip[:], compare_op=ALU.not_equal, fill=1.0, base=1 - P,
                                    pattern=[[1, P]], channel_multiplier=1).then_inc(made, 1)
            for at, to, value in runs:
                nc.gpsimd.memset(bucket[:, at:to], float(value)).then_inc(bucketed, 1)

        @block.vector
        def _(dve):
            dve.wait_ge(bucketed, len(runs))
            nc.vector.tensor_scalar(hot[:], bucket[:], index[:], None, ALU.is_equal).then_inc(hot_made, 1)
            nc.vector.memset(rows[:, 0:P], NEG).then_inc(rows_made, 1)
            nc.vector.memset(rows[:, 2 * P:], NEG).then_inc(rows_made, 1)
            dve.wait_ge(product, 1)
            nc.vector.tensor_copy(rows[:, P:2 * P], acc[:, P:2 * P]).then_inc(rows_made, 1)
            dve.wait_ge(upright, 1)
            nc.vector.tensor_copy(biases[:, :, :], turned[:, :, :])

        @block.tensor
        def _(pe):
            pe.wait_ge(hot_made, 1)
            pe.wait_ge(rel_in, 16)
            nc.tensor.matmul(acc[:], rel[:], hot[:], start=True, stop=True).then_inc(product, 1)
            pe.wait_ge(made, 4)
            pe.wait_ge(loaded, 16 * (H + 1))
            for h in range(0, H, 2):
                last = nc.tensor.matmul(turned[:, h:h + 2, :], flip[:], flipped[:, h:h + 2, :], start=True, stop=True)
            last.then_inc(upright, 1)


def gated_merge(k, branches, merged):
    nc = k.nc
    NB = len(branches)
    with k.phase() as ctx:
        wg = [k.sb(f"gm_wg{b}", [P, KD, P], ctx=ctx) for b in range(2)]
        wo = [k.sb(f"gm_wo{b}", [P, 4, P], ctx=ctx) for b in range(2)]
        gate = [k.sb(f"gm_gate{b}", [P, S], ctx=ctx) for b in range(2)]
        part = k.sb("gm_part", [P, S], ctx=ctx)
        total = k.sb("gm_total", [P, S], ctx=ctx)
        gate_ps = [k.ps(f"gm_gate_ps{b}", [P, S], ctx) for b in range(2)]
        out_ps = [k.ps(f"gm_out_ps{b}", [P, S], ctx) for b in range(2)]
        w_in0, w_in1, products, gates, gated, parts, totals = k.sems("gm", "w_in0 w_in1 products gates gated parts totals")
        w_in = (w_in0, w_in1)
        block = ctx.enter_context(nc.Block())
        w_view = k.dram["w_in_2"][0].rearrange("(c p) n -> p c n", p=P)
        outs = [k.dram[name][0].rearrange("(c p) n -> p c n", p=P) for name, _, _ in branches]

        @block.sync
        def _(sp):
            with sp.Fori(0, KD) as i:
                for n in range(NB):
                    sp.wait_ge(products, i * NB + n + 1)
                    col = bass.ds(i * P + C_GATES + n * D, P)
                    sp.dma_start(wg[n % 2][:, :, :], w_view[:, :, col]).then_inc(w_in[n % 2], 16)
                    sp.dma_start(wo[n % 2][:, 0:branches[n][2], :], outs[n][:, :, bass.ds(i * P, P)]).then_inc(w_in[n % 2], 16)

        @block.tensor
        def _(pe):
            pe.sem_inc(products, 2)
            with pe.Fori(0, KD) as i:
                for n in range(NB):
                    b = n % 2
                    y, chunks = branches[n][1], branches[n][2]
                    pe.wait_ge(w_in[b], 32 * (i * (NB // 2) + n // 2) + 32)
                    pe.wait_ge(gated, i * NB + n + 1)
                    for c in range(KD):
                        for h in range(2):
                            nc.tensor.matmul(gate_ps[b][:, h * HALF:(h + 1) * HALF], wg[b][:, c, :],
                                             k.HT[:, c, h * HALF:(h + 1) * HALF], start=(c == 0), stop=(c == KD - 1))
                    for c in range(chunks):
                        for h in range(2):
                            last = nc.tensor.matmul(out_ps[b][:, h * HALF:(h + 1) * HALF], wo[b][:, c, :],
                                                    y[:, c, h * HALF:(h + 1) * HALF], start=(c == 0), stop=(c == chunks - 1))
                    last.then_inc(products, 1)

        @block.scalar
        def _(act):
            with act.Fori(0, KD) as i:
                for n in range(NB):
                    g = i * NB + n
                    act.wait_ge(products, g + 1 + 2)
                    act.wait_ge(gated, g + 1)
                    nc.scalar.activation(gate[n % 2][:], gate_ps[n % 2][:], ACT.Sigmoid).then_inc(gates, 1)

        @block.vector
        def _(dve):
            dve.sem_inc(totals, 1)
            dve.sem_inc(gated, 2)
            with dve.Fori(0, KD) as i:
                for n in range(NB):
                    g = i * NB + n
                    dve.wait_ge(gates, g + 1)
                    if n == 0:
                        dve.wait_ge(totals, i * NB + 1)
                        nc.vector.tensor_tensor(total[:], gate[0][:], out_ps[0][:], ALU.mult).then_inc(gated, 1)
                        dve.wait_ge(gated, g + 1 + 2)
                        dve.sem_inc(totals, 1)
                        continue
                    dve.wait_ge(totals, g + 1)
                    nc.vector.tensor_tensor(part[:], gate[n % 2][:], out_ps[n % 2][:], ALU.mult).then_inc(gated, 1)
                    dve.wait_ge(gated, g + 1 + 2)
                    target = merged[:, bass.ds(i, 1), :].rearrange("p c s -> p (c s)") if n == NB - 1 else total[:]
                    nc.vector.tensor_tensor(target, total[:], part[:], ALU.add).then_inc(totals, 1)


def swiglu_up(k, hidden):
    nc = k.nc
    with k.phase() as ctx:
        w = [k.sb(f"up_w{b}", [P, 2, KD, P], ctx=ctx) for b in range(2)]
        silu = [k.sb(f"up_silu{b}", [P, S], ctx=ctx) for b in range(2)]
        acc = [k.ps(f"up_acc{b}", [P, 2, S], ctx) for b in range(2)]
        w_in0, w_in1, products, silus, done = k.sems("up", "w_in0 w_in1 products silus done")
        w_in = (w_in0, w_in1)
        block = ctx.enter_context(nc.Block())
        views = [k.dram[name][0].rearrange("(c p) n -> p c n", p=P) for name in ("w_gate_2", "w_up_2")]

        @block.sync
        def _(sp):
            with sp.Fori(0, FFC // 2) as i:
                for b in range(2):
                    sp.wait_ge(products, 2 * i + b + 1)
                    for m in range(2):
                        sp.dma_start(w[b][:, m, :, :], views[m][:, :, bass.ds((2 * i + b) * P, P)]).then_inc(w_in[b], 16)

        @block.tensor
        def _(pe):
            pe.sem_inc(products, 2)
            with pe.Fori(0, FFC // 2) as i:
                for b in range(2):
                    pe.wait_ge(w_in[b], 32 * i + 32)
                    pe.wait_ge(done, 2 * i + b + 1)
                    for m in range(2):
                        for c in range(KD):
                            for h in range(2):
                                last = nc.tensor.matmul(acc[b][:, m, h * HALF:(h + 1) * HALF], w[b][:, m, c, :],
                                                        k.HT[:, c, h * HALF:(h + 1) * HALF],
                                                        start=(c == 0), stop=(c == KD - 1))
                    last.then_inc(products, 1)

        @block.scalar
        def _(act):
            with act.Fori(0, FFC // 2) as i:
                for b in range(2):
                    act.wait_ge(products, 2 * i + b + 1 + 2)
                    act.wait_ge(done, 2 * i + b + 1)
                    nc.scalar.activation(silu[b][:], acc[b][:, 0, :], ACT.Silu).then_inc(silus, 1)

        @block.vector
        def _(dve):
            dve.sem_inc(done, 2)
            with dve.Fori(0, FFC // 2) as i:
                for b in range(2):
                    dve.wait_ge(silus, 2 * i + b + 1)
                    nc.vector.tensor_tensor(hidden[:, bass.ds(2 * i + b, 1), :].rearrange("p c s -> p (c s)"),
                                            silu[b][:], acc[b][:, 1, :], ALU.mult).then_inc(done, 1)


def scaled_gains(k):
    nc = k.nc
    with k.phase() as ctx:
        (made,) = k.sems("gains", "made")
        block = ctx.enter_context(nc.Block())

        @block.vector
        def _(dve):
            for col, name, factor in (((0, 2), "fox_q_gain_2", HD ** -0.5), ((2, 4), "fox_k_gain_2", 1.0),
                                      ((4, 8), "swa_q_gain_2", HD ** -0.5), ((8, 9), "swa_k_gain_2", 1.0)):
                n = col[1] - col[0]
                nc.vector.tensor_scalar(k.head_gains[:, col[0]:col[1]], k.gain(name).broadcast_to([P, n]), factor, None,
                                        ALU.mult).then_inc(made, 1)


def second_mixer(k):
    nc = k.nc
    w_in = k.dram["w_in_2"][0]
    H = 4
    norm_turn(k, "attn_norm", k.X, ST, k.gain("attn_norm_2"), k.HT)
    with ExitStack() as ctx:
        fox_y = k.sb("fox_y", [P, 2, S], ctx=ctx)
        conv_y = k.sb("conv_y", [P, 2, S], ctx=ctx)
        ml_y = k.sb("ml_y", [P, 2, S], ctx=ctx)
        swa_y = k.sb("swa_y", [P, 4, S], ctx=ctx)
        with ExitStack() as inner:
            k.head_gains = k.sb("head_gains", [P, 9], ctx=inner)
            k.a_col = k.sb("a_col", [P, ST, H], ctx=inner)
            k.floor_col = k.sb("floor_col", [P, ST, H], ctx=inner)
            v2 = k.sb("v2", [P, ST, 5 * P], ctx=inner)
            vm = k.sb("vm", [P, ST, H, HD + 1], ctx=inner)
            scaled_gains(k)
            project_rows(k, "fox_qk", w_in[:, 0:512], 4, k.HT, KD, k.scratch["fox_qk"], gain=k.head_gains[:, 0:4])
            project_rows(k, "swa_qk", w_in[:, C_SQ:C_SQ + 640], 5, k.HT, KD, k.scratch["swa_qk"], gain=k.head_gains[:, 4:9])
            project_rows(k, "plain", w_in[:, C_CU:C_MV], 10, k.HT, KD, k.scratch["plain"])
            project_rows(k, "mo", w_in[:, C_MO:C_SQ], 2, k.HT, KD, k.scratch["mo"])
            views = [w_in[:, c:c + n].rearrange("(c p) n -> p c n", p=P) for c, n in ((C_FV, 256), (C_MV, 256), (C_SV, 128))]
            project_tokens(k, "v2", [(views[0], 0, 256), (views[1], 256, 256), (views[2], 512, 128)], 5 * P, k.HT, KD, v2)
            gate_rows(k, vm)
            y = swa_y[:, :, :].rearrange("p c (x n) -> p (c x) n", n=512)
            with ExitStack() as fox:
                k.causal = k.sb("causal", [P, S], ctx=fox)
                split_values(k, v2, vm)
                attention(k, "fox", H,
                          lambda b, h: [("q", 0, k.scratch["fox_qk"][bass.ds(h * HD, HD), :]),
                                        ("q", HD, k.scratch["fox_q"][bass.ds(h * 2, 2), :]),
                                        ("k", 0, k.scratch["fox_qk"][bass.ds(h * HD + 256, HD), :]),
                                        ("k", HD, k.scratch["fox_k"][bass.ds(h * 2, 2), :])],
                          HD + 2, v2, y, 0)
                turn(k, "fox_turn", y[:, :, 0:256], k.ones[:, 0:2], fox_y, 2)
            matrix_lstm(k, vm, y)
            head_norm(k, "ml_rms", y[:, :, 0:256], H, HD, 1.0)
            turn(k, "ml_turn", y[:, :, 0:256], k.gain("mlstm_h_gain_2"), ml_y, 2)
            short_conv(k, conv_y, ml_y)
            biases = k.sb("biases", [P, 8, 2 * P], ctx=inner)
            sinks = k.sb("sinks", [P, 8], ctx=inner)
            window_bias(k, biases, sinks)
            y = k.sb("y_rows", [P, ST, 512], ctx=inner)
            for kv in range(2):
                attention(k, f"swa{kv}", 4,
                          lambda b, h: [("q", 0, k.scratch["swa_qk"][bass.ds(h * HD + kv * 4 * HD, HD), :]),
                                        ("k", 0, k.scratch["swa_qk"][512 + kv * HD:512 + (kv + 1) * HD, :])],
                          HD, v2, y, kv * 256, window=(kv * 4, 512 + kv * HD, biases, sinks))
            turn(k, "swa_turn", y[:, :, 0:512], k.ones[:, 0:4], swa_y, 4)
        merged = k.sb("merged", [P, KD, S], ctx=ctx)
        gated_merge(k, [("w_fox_out_2", fox_y, 2), ("w_conv_out_2", conv_y, 2), ("w_mlstm_out_2", ml_y, 2),
                        ("w_swa_out_2", swa_y, 4)], merged)
        project_residual(k, "merge_out", k.dram["w_merge_out_2"][0], merged, KD)


def split_values(k, v2, vm):
    nc = k.nc
    with k.phase() as ctx:
        (made,) = k.sems("split", "made")
        block = ctx.enter_context(nc.Block())

        @block.gpsimd
        def _(pool):
            link = k.own("pool", pool)
            link(nc.gpsimd.memset(k.causal[:], 0.0))
            link(nc.gpsimd.affine_select(out=k.causal[:, S - P:S], in_=k.causal[:, S - P:S], compare_op=ALU.is_ge,
                                         fill=NEG, base=0, pattern=[[-1, P]], channel_multiplier=1))

        @block.vector
        def _(dve):
            for t in range(ST):
                nc.vector.tensor_copy(vm[:, t, :, 0:HD], v2[:, t, 256:512].rearrange("p (h n) -> p h n", n=HD)
                                      ).then_inc(made, 1)
        k.chains["pool"].settle()


def store(k, view, tile):
    nc = k.nc
    with k.phase() as ctx:
        (stored,) = k.sems("store", "stored")
        block = ctx.enter_context(nc.Block())

        @block.sync
        def _(sp):
            sp.dma_start(view, tile).then_inc(stored, 16)
            sp.wait_ge(stored, 16)


def swiglu(k):
    norm_turn(k, "ffn2_norm", k.X, ST, k.gain("ffn_norm_2"), k.HT)
    with ExitStack() as ctx:
        hidden = k.sb("hidden", [P, FFC, S], ctx=ctx)
        swiglu_up(k, hidden)
        project_residual(k, "down", k.dram["w_down_2"][0], hidden, FFC)


def gate_rows(k, vm):
    nc = k.nc
    H = 4
    with k.phase() as ctx:
        w = k.sb("gr_w", [P, KD, 96], ctx=ctx)
        bias = k.sb("gr_bias", [H, 3], ctx=ctx)
        raw = [k.sb(f"gr_raw{n}", [H, S], ctx=ctx) for n in range(3)]
        logs = [k.sb(f"gr_logs{n}", [H, S], ctx=ctx) for n in range(2)]
        sums = [k.sb(f"gr_sums{n}", [H, S], ctx=ctx) for n in range(2)]
        ones = k.sb("gr_ones", [H, S], ctx=ctx)
        a, top, floor, neg = (k.sb(f"gr_{n}", [H, S], ctx=ctx) for n in ("a", "top", "floor", "neg"))
        acc = k.ps("gr_acc", [P, S], ctx)
        cols = k.ps("gr_cols", [P, 2, ST, H], ctx)
        w_in, bias_in, cleared, products, copied, absed, logged, rows_made, turned, stored = k.sems(
            "gr", "w_in bias_in cleared products copied absed logged rows_made turned stored")
        block = ctx.enter_context(nc.Block())
        w_view = k.dram["w_in_2"][0].rearrange("(c p) n -> p c n", p=P)

        @block.sync
        def _(sp):
            sp.wait_ge(cleared, 2)
            for n, col in enumerate((C_FF, C_MI, C_MI + H)):
                sp.dma_start(w[:, :, 32 * n:32 * n + H], w_view[:, :, col:col + H]).then_inc(w_in, 16)
            for n, name in enumerate(("fox_f_bias_2", "mlstm_i_bias_2", "mlstm_f_bias_2")):
                sp.dma_start(bias[:, n:n + 1], k.dram[name].rearrange("l h -> h l")).then_inc(bias_in, 16)
            fox_q = k.scratch["fox_q"].rearrange("(h n) s -> h n s", n=2)
            fox_k = k.scratch["fox_k"].rearrange("(h n) s -> h n s", n=2)
            sp.dma_start(fox_q[:, 0, :], ones[:]).then_inc(stored, 16)
            sp.dma_start(fox_k[:, 1, :], ones[:]).then_inc(stored, 16)
            sp.wait_ge(rows_made, 1)
            sp.dma_start(fox_q[:, 1, :], sums[0][:]).then_inc(stored, 16)
            sp.wait_ge(rows_made, 2)
            sp.dma_start(fox_k[:, 0, :], neg[:]).then_inc(stored, 16)
            sp.wait_ge(rows_made, 4)
            sp.dma_start(k.scratch["mlstm_row"], top[:]).then_inc(stored, 16)
            sp.wait_ge(stored, 16 * 5)

        @block.gpsimd
        def _(pool):
            nc.gpsimd.memset(w[:, :, :], 0.0).then_inc(cleared, 1)
            nc.gpsimd.memset(ones[:], 1.0).then_inc(cleared, 1)
            nc.gpsimd.memset(vm[:, :, :, HD:HD + 1], 1.0).then_inc(cleared, 1)

        @block.tensor
        def _(pe):
            pe.wait_ge(w_in, 48)
            for c in range(KD):
                for h in range(2):
                    last = nc.tensor.matmul(acc[0:96, h * HALF:(h + 1) * HALF], w[:, c, :],
                                            k.HT[:, c, h * HALF:(h + 1) * HALF], start=(c == 0), stop=(c == KD - 1))
            last.then_inc(products, 1)
            pe.wait_ge(rows_made, 5)
            for n, row in enumerate((a, floor)):
                for t in range(ST):
                    last = nc.tensor.transpose(cols[:, n, t, :], row[:, t * P:(t + 1) * P], k.ident[0:H, 0:H])
            last.then_inc(turned, 1)

        @block.scalar
        def _(act):
            act.wait_ge(products, 1)
            for n in range(3):
                nc.scalar.activation(raw[n][:], acc[32 * n:32 * n + H, :], ACT.Copy).then_inc(copied, 1)
            for n, x in enumerate((raw[0], raw[2])):
                act.wait_ge(absed, n + 1)
                nc.scalar.activation(logs[n][:], x[:], ACT.Abs).then_inc(logged, 1)
                act.wait_ge(logged, 3 * n + 1)
                nc.scalar.activation(logs[n][:], logs[n][:], ACT.Exp, scale=-1.0).then_inc(logged, 1)
                act.wait_ge(logged, 3 * n + 2)
                nc.scalar.activation(logs[n][:], logs[n][:], ACT.Ln, bias=1.0).then_inc(logged, 1)
            act.wait_ge(turned, 1)
            nc.scalar.activation(k.a_col[:, :, :], cols[:, 0, :, :], ACT.Copy)
            nc.scalar.activation(k.floor_col[:, :, :], cols[:, 1, :, :], ACT.Exp, scale=-1.0)

        @block.vector
        def _(dve):
            link = k.own("dve", dve)
            v = nc.vector
            dve.wait_ge(bias_in, 48)
            dve.wait_ge(copied, 3)
            dve.wait_ge(cleared, 3)
            for n in (0, 2):
                v.tensor_scalar(raw[n][:], raw[n][:], bias[:, n:n + 1], None, ALU.add).then_inc(absed, 1)
            link(v.tensor_scalar(raw[1][:], raw[1][:], bias[:, 1:2], None, ALU.add))
            for n, x in enumerate((raw[0], raw[2])):
                dve.wait_ge(logged, 3 * n + 3)
                link(v.scalar_tensor_tensor(out=logs[n][:], in0=x[:], scalar=0.0, in1=logs[n][:],
                                            op0=ALU.min, op1=ALU.subtract))
                ins = v.tensor_tensor_scan(sums[n][:], ones[:], logs[n][:], 0.0, ALU.mult, ALU.add)
                if n == 0:
                    ins.then_inc(rows_made, 1)
                    dve.wait_ge(rows_made, 1)
                    v.tensor_scalar(neg[:], sums[0][:], -1.0, None, ALU.mult).then_inc(rows_made, 1)
                else:
                    link(ins)
            link(v.tensor_tensor(a[:], raw[1][:], sums[1][:], ALU.subtract))
            link(v.tensor_tensor_scan(top[:], ones[:], a[:], 0.0, ALU.mult, ALU.max))
            v.tensor_tensor(floor[:], top[:], sums[1][:], ALU.add).then_inc(rows_made, 1)
            dve.wait_ge(rows_made, 3)
            v.tensor_scalar(top[:], top[:], -1.0, None, ALU.mult).then_inc(rows_made, 1)
            dve.wait_ge(rows_made, 4)
            dve.sem_inc(rows_made, 1)
        k.chains["dve"].settle()


def matrix_lstm(k, V, out):
    nc = k.nc
    H = 4
    with k.phase() as ctx:
        q = [k.sb(f"ml_q{b}", [HD, S], ctx=ctx) for b in range(2)]
        kk = [k.sb(f"ml_k{b}", [HD, S], ctx=ctx) for b in range(2)]
        row = [k.sb(f"ml_row{b}", [P, S], ctx=ctx) for b in range(2)]
        a_col = [k.sb(f"ml_a{b}", [P, ST], ctx=ctx) for b in range(2)]
        decay = [k.sb(f"ml_decay{b}", [P, S], ctx=ctx) for b in range(2)]
        w = [[k.sb(f"ml_w{b}{t}", [P, S - t * P], ctx=ctx) for t in range(ST)] for b in range(2)]
        stats = [k.sb(f"ml_stats{b}", [P, ST, 2], ctx=ctx) for b in range(2)]
        values = [k.sb(f"ml_v{b}", [P, ST, HD + 1], ctx=ctx) for b in range(2)]
        before_mask = k.sb("ml_mask", [P, P], ctx=ctx)
        scores = [k.ps(f"ml_scores{b}", [P, S], ctx) for b in range(2)]
        acc = [k.ps(f"ml_acc{b}", [P, 2, HALF], ctx) for b in range(2)]
        (head_in0, head_in1, mask_made, a_ready, masked, decays, products, weighted, sums_made, done) = k.sems(
            "ml", "head_in0 head_in1 mask_made a_ready masked decays products weighted sums_made done")
        head_in = (head_in0, head_in1)
        block = ctx.enter_context(nc.Block())
        rounds = H // 2
        plain = k.scratch["plain"]
        q_row, k_row = C_MQ - C_CU, C_MQ + H * HD - C_CU

        def at(b, t):
            return acc[b][:, t // 4, (t % 4) * (HD + 1):(t % 4 + 1) * (HD + 1)]

        @block.sync
        def _(sp):
            with sp.Fori(0, rounds) as i:
                for b in range(2):
                    sp.wait_ge(done, 2 * i + 1)
                    h = i * 2 + b
                    sp.dma_start(q[b][:], plain[bass.ds(h * HD + q_row, HD), :]).then_inc(head_in[b], 16)
                    sp.dma_start(kk[b][:], plain[bass.ds(h * HD + k_row, HD), :]).then_inc(head_in[b], 16)
                    sp.dma_start(row[b][:], k.scratch["mlstm_row"][bass.ds(h, 1), :].broadcast_to([P, S])
                                 ).then_inc(head_in[b], 16)

        @block.gpsimd
        def _(pool):
            nc.gpsimd.memset(before_mask[:], 0.0).then_inc(mask_made, 1)
            pool.wait_ge(mask_made, 1)
            nc.gpsimd.affine_select(out=before_mask[:], in_=before_mask[:], compare_op=ALU.is_ge, fill=NEG, base=0,
                                    pattern=[[1, P]], channel_multiplier=-1).then_inc(mask_made, 1)
            with pool.Fori(0, rounds) as i:
                for b in range(2):
                    pool.wait_ge(done, 2 * i + 1)
                    h = i * 2 + b
                    nc.gpsimd.tensor_copy(a_col[b][:], k.a_col[:, :, bass.ds(h, 1)].rearrange("p t h -> p (t h)")
                                          ).then_inc(a_ready, 1)
                    nc.gpsimd.tensor_copy(values[b][:, :, :], V[:, :, bass.ds(h, 1), :].rearrange(
                        "p t h n -> p (t h) n")).then_inc(a_ready, 1)

        @block.tensor
        def _(pe):
            pe.sem_inc(sums_made, 1)
            with pe.Fori(0, rounds) as i:
                for b in range(2):
                    pe.wait_ge(head_in[b], 48 * i + 48)
                    for t in range(ST):
                        g = (i * 2 + b) * ST + t
                        pe.wait_ge(weighted, g + 1)
                        width = S - t * P
                        for c in range(0, width, HALF):
                            n = min(HALF, width - c)
                            last = nc.tensor.matmul(scores[t % 2][:, c:c + n], kk[b][:, t * P:(t + 1) * P],
                                                    q[b][:, t * P + c:t * P + c + n], start=True, stop=True)
                        last.then_inc(products, 1)
                for b in range(2):
                    pe.wait_ge(weighted, (i * 2 + b + 1) * ST + 2)
                    pe.wait_ge(a_ready, (i * 2 + b) * 2 + 2)
                    pe.wait_ge(done, 2 * i + 1)
                    for t in range(ST):
                        for c in range(t + 1):
                            last = nc.tensor.matmul(at(b, t), w[b][c][:, (t - c) * P:(t - c + 1) * P],
                                                    values[b][:, c, :], start=(c == 0), stop=(c == t))
                    last.then_inc(sums_made, 1)

        @block.scalar
        def _(act):
            with act.Fori(0, rounds) as i:
                for b in range(2):
                    act.wait_ge(head_in[b], 48 * i + 48)
                    act.wait_ge(a_ready, (i * 2 + b) * 2 + 2)
                    for t in range(ST):
                        g = (i * 2 + b) * ST + t
                        act.wait_ge(weighted, g + 1)
                        act.wait_ge(masked, g + 1)
                        nc.scalar.activation(decay[t % 2][:, 0:P], decay[t % 2][:, 0:P], ACT.Exp,
                                             bias=a_col[b][:, t:t + 1]).then_inc(decays, 1)
                        if t < ST - 1:
                            nc.scalar.activation(decay[t % 2][:, P:S - t * P], row[b][:, (t + 1) * P:S], ACT.Exp,
                                                 bias=a_col[b][:, t:t + 1]).then_inc(decays, 1)

        @block.vector
        def _(dve):
            dve.sem_inc(done, 1)
            link = k.own("dve", dve)
            chain = k.chains["dve"]
            dve.sem_inc(weighted, 2)
            dve.wait_ge(mask_made, 2)
            per = 2 * ST - 1
            with dve.Fori(0, rounds) as i:
                chain.enter(i, 2 * 3)
                for b in range(2):
                    dve.wait_ge(head_in[b], 48 * i + 48)
                    for t in range(ST + 1):
                        g = (i * 2 + b) * ST + t
                        if t < ST:
                            dve.wait_ge(weighted, g + 1)
                            nc.vector.tensor_tensor(decay[t % 2][:, 0:P], row[b][:, t * P:(t + 1) * P], before_mask[:],
                                                    ALU.add).then_inc(masked, 1)
                        if t:
                            dve.wait_ge(products, g)
                            dve.wait_ge(decays, (i * 2 + b) * per + min(2 * t, per))
                            dve.wait_ge(sums_made, 2 * i + 1)
                            width = S - (t - 1) * P
                            nc.vector.scalar_tensor_tensor(out=w[b][t - 1][:], in0=scores[(t - 1) % 2][:, 0:width],
                                                           scalar=HD ** -0.5, in1=decay[(t - 1) % 2][:, 0:width],
                                                           op0=ALU.mult, op1=ALU.mult).then_inc(weighted, 1)
                for b in range(2):
                    dve.wait_ge(sums_made, i * 2 + b + 1 + 1)
                    h = i * 2 + b
                    st = stats[b]
                    den = acc[b][:, :, 0:4 * (HD + 1)].rearrange("p a (t n) -> p a t n", n=HD + 1)[:, :, :, HD:HD + 1]
                    den = den.rearrange("p a t n -> p a (t n)")
                    one, two = (st[:, :, n:n + 1].rearrange("p (a t) n -> p a (t n)", a=2) for n in range(2))
                    link(nc.vector.tensor_copy(one, den))
                    link(nc.vector.scalar_tensor_tensor(
                        out=st[:, :, 1:2], in0=st[:, :, 0:1], scalar=-1.0, in1=k.floor_col[:, :, bass.ds(h, 1)],
                        op0=ALU.mult, op1=ALU.max))
                    link(nc.vector.tensor_tensor(st[:, :, 0:1], st[:, :, 0:1], st[:, :, 1:2], ALU.max))
                    nc.vector.reciprocal(st[:, :, 1:2], st[:, :, 0:1]).then_inc(mask_made, 1)
                    dve.wait_ge(mask_made, 2 + 5 * h + 1)
                    for t in range(ST):
                        ins = nc.vector.tensor_scalar(out[:, t, bass.ds(h * HD, HD)], at(b, t)[:, 0:HD], st[:, t, 1:2],
                                                      None, ALU.mult)
                    ins.then_inc(mask_made, 4)
                    dve.wait_ge(mask_made, 2 + 5 * h + 5)
                    dve.sem_inc(done, 1)
                chain.leave(rounds)


def short_conv(k, conv_out, ml_rows):
    nc = k.nc
    CH = 2
    with k.phase() as ctx:
        u, bg, cg, mo = (k.sb(f"conv_{n}", [P, CH, S], ctx=ctx) for n in ("u", "b", "c", "mo"))
        loaded, gated, chain_c = k.sems("conv", "loaded gated chain_c")
        block = ctx.enter_context(nc.Block())
        plain = k.scratch["plain"]

        @block.sync
        def _(sp):
            for n, tile in enumerate((u, bg, cg)):
                sp.dma_start(tile[:, :, :], plain[n * CH * P:(n + 1) * CH * P, :].rearrange("(c p) s -> p c s", p=P)
                             ).then_inc(loaded, 16)
            sp.dma_start(mo[:, :, :], k.scratch["mo"].rearrange("(c p) s -> p c s", p=P)).then_inc(gated, 16)

        @block.scalar
        def _(act):
            act.wait_ge(gated, 16)
            nc.scalar.activation(mo[:, :, :], mo[:, :, :], ACT.Sigmoid).then_inc(gated, 1)

        @block.vector
        def _(dve):
            link = k.own("dve", dve)
            dve.wait_ge(loaded, 48)
            link(nc.vector.tensor_tensor(u[:, :, :], u[:, :, :], cg[:, :, :], ALU.mult))
            for c in range(CH):
                taps = [k.gain("conv_w_2", n * CH + c, 1) for n in range(3)]
                link(nc.vector.tensor_scalar(conv_out[:, c, :], u[:, c, :], taps[2], None, ALU.mult))
                for back, tap in ((1, taps[1]), (2, taps[0])):
                    link(nc.vector.scalar_tensor_tensor(out=conv_out[:, c, back:], in0=u[:, c, 0:S - back], scalar=tap,
                                                        in1=conv_out[:, c, back:], op0=ALU.mult, op1=ALU.add))
            link(nc.vector.tensor_tensor(conv_out[:, :, :], conv_out[:, :, :], bg[:, :, :], ALU.mult))
            dve.wait_ge(gated, 17)
            link(nc.vector.tensor_tensor(ml_rows[:, :, :], ml_rows[:, :, :], mo[:, :, :], ALU.mult))
        k.chains["dve"].settle()


def t5_buckets(n):
    exact, most, buckets = 16, 128, 32
    out = []
    for d in range(n):
        if d < exact:
            out.append(d)
        else:
            large = exact + int(np.log(d / exact) / np.log(most / exact) * (buckets - exact))
            out.append(min(large, buckets - 1))
    return out


def window_bias(k, biases, sinks):
    nc = k.nc
    H, B, W2 = 8, 32, 3 * P
    with k.phase() as ctx:
        rel = k.sb("wb_rel", [B, H], ctx=ctx)
        hot = k.sb("wb_hot", [B, W2], ctx=ctx)
        index = k.sb("wb_index", [B, 1], ctx=ctx)
        bucket = k.sb("wb_bucket", [B, W2], ctx=ctx)
        rows = k.sb("wb_rows", [H, W2], ctx=ctx)
        flipped = k.sb("wb_flipped", [P, H, 2 * P], ctx=ctx)
        flip = k.sb("wb_flip", [P, P], ctx=ctx)
        acc = k.ps("wb_acc", [H, W2], ctx)
        turned = k.ps("wb_turned", [P, H, 2 * P], ctx)
        rel_in, bucketed, made, hot_made, product, rows_made, stored, loaded, upright = k.sems(
            "wb", "rel_in bucketed made hot_made product rows_made stored loaded upright")
        block = ctx.enter_context(nc.Block())
        buckets = t5_buckets(WINDOW)
        runs = []
        for j in range(P, 2 * P):
            value = buckets[2 * P - 1 - j]
            if runs and runs[-1][2] == value:
                runs[-1][1] = j + 1
            else:
                runs.append([j, j + 1, value])

        @block.sync
        def _(sp):
            sp.dma_start(rel[:], k.dram["rel_bias_2"]).then_inc(rel_in, 16)
            sp.dma_start(sinks[:], k.dram["swa_sinks_2"].broadcast_to([P, H])).then_inc(loaded, 16)
            sp.wait_ge(rows_made, 3)
            sp.dma_start(k.scratch["window_rows"], rows[:]).then_inc(stored, 16)
            sp.wait_ge(stored, 16)
            view = k.scratch["window_rows"]
            for h in range(H):
                skewed = bass.AP(view.tensor, view.offset + h * W2, [[1, P], [1, 2 * P]])
                sp.dma_start(flipped[:, h, :], skewed).then_inc(loaded, 16)

        @block.gpsimd
        def _(pool):
            nc.gpsimd.memset(bucket[:], -1.0).then_inc(made, 1)
            nc.gpsimd.iota(index[:], [[0, 1]], 0, 1, allow_small_or_imprecise_dtypes=True).then_inc(made, 1)
            nc.gpsimd.memset(flip[:], 0.0).then_inc(made, 1)
            pool.wait_ge(made, 3)
            nc.gpsimd.affine_select(out=flip[:], in_=flip[:], compare_op=ALU.not_equal, fill=1.0, base=1 - P,
                                    pattern=[[1, P]], channel_multiplier=1).then_inc(made, 1)
            for at, to, value in runs:
                nc.gpsimd.memset(bucket[:, at:to], float(value)).then_inc(bucketed, 1)

        @block.vector
        def _(dve):
            dve.wait_ge(bucketed, len(runs))
            nc.vector.tensor_scalar(hot[:], bucket[:], index[:], None, ALU.is_equal).then_inc(hot_made, 1)
            nc.vector.memset(rows[:, 0:P], NEG).then_inc(rows_made, 1)
            nc.vector.memset(rows[:, 2 * P:], NEG).then_inc(rows_made, 1)
            dve.wait_ge(product, 1)
            nc.vector.tensor_copy(rows[:, P:2 * P], acc[:, P:2 * P]).then_inc(rows_made, 1)
            dve.wait_ge(upright, 1)
            nc.vector.tensor_copy(biases[:, :, :], turned[:, :, :])

        @block.tensor
        def _(pe):
            pe.wait_ge(hot_made, 1)
            pe.wait_ge(rel_in, 16)
            nc.tensor.matmul(acc[:], rel[:], hot[:], start=True, stop=True).then_inc(product, 1)
            pe.wait_ge(made, 4)
            pe.wait_ge(loaded, 16 * (H + 1))
            for h in range(0, H, 2):
                last = nc.tensor.matmul(turned[:, h:h + 2, :], flip[:], flipped[:, h:h + 2, :], start=True, stop=True)
            last.then_inc(upright, 1)


def gated_merge(k, branches, merged):
    nc = k.nc
    NB = len(branches)
    with k.phase() as ctx:
        wg = [k.sb(f"gm_wg{b}", [P, KD, P], ctx=ctx) for b in range(2)]
        wo = [k.sb(f"gm_wo{b}", [P, 4, P], ctx=ctx) for b in range(2)]
        gate = [k.sb(f"gm_gate{b}", [P, S], ctx=ctx) for b in range(2)]
        part = k.sb("gm_part", [P, S], ctx=ctx)
        total = k.sb("gm_total", [P, S], ctx=ctx)
        gate_ps = [k.ps(f"gm_gate_ps{b}", [P, S], ctx) for b in range(2)]
        out_ps = [k.ps(f"gm_out_ps{b}", [P, S], ctx) for b in range(2)]
        w_in0, w_in1, products, gates, gated, parts, totals = k.sems("gm", "w_in0 w_in1 products gates gated parts totals")
        w_in = (w_in0, w_in1)
        block = ctx.enter_context(nc.Block())
        w_view = k.dram["w_in_2"][0].rearrange("(c p) n -> p c n", p=P)
        outs = [k.dram[name][0].rearrange("(c p) n -> p c n", p=P) for name, _, _ in branches]

        @block.sync
        def _(sp):
            with sp.Fori(0, KD) as i:
                for n in range(NB):
                    sp.wait_ge(products, i * NB + n + 1)
                    col = bass.ds(i * P + C_GATES + n * D, P)
                    sp.dma_start(wg[n % 2][:, :, :], w_view[:, :, col]).then_inc(w_in[n % 2], 16)
                    sp.dma_start(wo[n % 2][:, 0:branches[n][2], :], outs[n][:, :, bass.ds(i * P, P)]).then_inc(w_in[n % 2], 16)

        @block.tensor
        def _(pe):
            pe.sem_inc(products, 2)
            with pe.Fori(0, KD) as i:
                for n in range(NB):
                    b = n % 2
                    y, chunks = branches[n][1], branches[n][2]
                    pe.wait_ge(w_in[b], 32 * (i * (NB // 2) + n // 2) + 32)
                    pe.wait_ge(gated, i * NB + n + 1)
                    for c in range(KD):
                        for h in range(2):
                            nc.tensor.matmul(gate_ps[b][:, h * HALF:(h + 1) * HALF], wg[b][:, c, :],
                                             k.HT[:, c, h * HALF:(h + 1) * HALF], start=(c == 0), stop=(c == KD - 1))
                    for c in range(chunks):
                        for h in range(2):
                            last = nc.tensor.matmul(out_ps[b][:, h * HALF:(h + 1) * HALF], wo[b][:, c, :],
                                                    y[:, c, h * HALF:(h + 1) * HALF], start=(c == 0), stop=(c == chunks - 1))
                    last.then_inc(products, 1)

        @block.scalar
        def _(act):
            with act.Fori(0, KD) as i:
                for n in range(NB):
                    g = i * NB + n
                    act.wait_ge(products, g + 1 + 2)
                    act.wait_ge(gated, g + 1)
                    nc.scalar.activation(gate[n % 2][:], gate_ps[n % 2][:], ACT.Sigmoid).then_inc(gates, 1)

        @block.vector
        def _(dve):
            dve.sem_inc(totals, 1)
            dve.sem_inc(gated, 2)
            with dve.Fori(0, KD) as i:
                for n in range(NB):
                    g = i * NB + n
                    dve.wait_ge(gates, g + 1)
                    if n == 0:
                        dve.wait_ge(totals, i * NB + 1)
                        nc.vector.tensor_tensor(total[:], gate[0][:], out_ps[0][:], ALU.mult).then_inc(gated, 1)
                        dve.wait_ge(gated, g + 1 + 2)
                        dve.sem_inc(totals, 1)
                        continue
                    dve.wait_ge(totals, g + 1)
                    nc.vector.tensor_tensor(part[:], gate[n % 2][:], out_ps[n % 2][:], ALU.mult).then_inc(gated, 1)
                    dve.wait_ge(gated, g + 1 + 2)
                    target = merged[:, bass.ds(i, 1), :].rearrange("p c s -> p (c s)") if n == NB - 1 else total[:]
                    nc.vector.tensor_tensor(target, total[:], part[:], ALU.add).then_inc(totals, 1)


def swiglu_up(k, hidden):
    nc = k.nc
    with k.phase() as ctx:
        w = [k.sb(f"up_w{b}", [P, 2, KD, P], ctx=ctx) for b in range(2)]
        silu = [k.sb(f"up_silu{b}", [P, S], ctx=ctx) for b in range(2)]
        acc = [k.ps(f"up_acc{b}", [P, 2, S], ctx) for b in range(2)]
        w_in0, w_in1, products, silus, done = k.sems("up", "w_in0 w_in1 products silus done")
        w_in = (w_in0, w_in1)
        block = ctx.enter_context(nc.Block())
        views = [k.dram[name][0].rearrange("(c p) n -> p c n", p=P) for name in ("w_gate_2", "w_up_2")]

        @block.sync
        def _(sp):
            with sp.Fori(0, FFC // 2) as i:
                for b in range(2):
                    sp.wait_ge(products, 2 * i + b + 1)
                    for m in range(2):
                        sp.dma_start(w[b][:, m, :, :], views[m][:, :, bass.ds((2 * i + b) * P, P)]).then_inc(w_in[b], 16)

        @block.tensor
        def _(pe):
            pe.sem_inc(products, 2)
            with pe.Fori(0, FFC // 2) as i:
                for b in range(2):
                    pe.wait_ge(w_in[b], 32 * i + 32)
                    pe.wait_ge(done, 2 * i + b + 1)
                    for m in range(2):
                        for c in range(KD):
                            for h in range(2):
                                last = nc.tensor.matmul(acc[b][:, m, h * HALF:(h + 1) * HALF], w[b][:, m, c, :],
                                                        k.HT[:, c, h * HALF:(h + 1) * HALF],
                                                        start=(c == 0), stop=(c == KD - 1))
                    last.then_inc(products, 1)

        @block.scalar
        def _(act):
            with act.Fori(0, FFC // 2) as i:
                for b in range(2):
                    act.wait_ge(products, 2 * i + b + 1 + 2)
                    act.wait_ge(done, 2 * i + b + 1)
                    nc.scalar.activation(silu[b][:], acc[b][:, 0, :], ACT.Silu).then_inc(silus, 1)

        @block.vector
        def _(dve):
            dve.sem_inc(done, 2)
            with dve.Fori(0, FFC // 2) as i:
                for b in range(2):
                    dve.wait_ge(silus, 2 * i + b + 1)
                    nc.vector.tensor_tensor(hidden[:, bass.ds(2 * i + b, 1), :].rearrange("p c s -> p (c s)"),
                                            silu[b][:], acc[b][:, 1, :], ALU.mult).then_inc(done, 1)


def scaled_gains(k):
    nc = k.nc
    with k.phase() as ctx:
        (made,) = k.sems("gains", "made")
        block = ctx.enter_context(nc.Block())

        @block.vector
        def _(dve):
            for col, name, factor in (((0, 2), "fox_q_gain_2", HD ** -0.5), ((2, 4), "fox_k_gain_2", 1.0),
                                      ((4, 8), "swa_q_gain_2", HD ** -0.5), ((8, 9), "swa_k_gain_2", 1.0)):
                n = col[1] - col[0]
                nc.vector.tensor_scalar(k.head_gains[:, col[0]:col[1]], k.gain(name).broadcast_to([P, n]), factor, None,
                                        ALU.mult).then_inc(made, 1)


def second_mixer(k):
    nc = k.nc
    w_in = k.dram["w_in_2"][0]
    H = 4
    norm_turn(k, "attn_norm", k.X, ST, k.gain("attn_norm_2"), k.HT)
    with ExitStack() as ctx:
        fox_y = k.sb("fox_y", [P, 2, S], ctx=ctx)
        conv_y = k.sb("conv_y", [P, 2, S], ctx=ctx)
        ml_y = k.sb("ml_y", [P, 2, S], ctx=ctx)
        swa_y = k.sb("swa_y", [P, 4, S], ctx=ctx)
        with ExitStack() as inner:
            k.head_gains = k.sb("head_gains", [P, 9], ctx=inner)
            k.a_col = k.sb("a_col", [P, ST, H], ctx=inner)
            k.floor_col = k.sb("floor_col", [P, ST, H], ctx=inner)
            v2 = k.sb("v2", [P, ST, 5 * P], ctx=inner)
            vm = k.sb("vm", [P, ST, H, HD + 1], ctx=inner)
            scaled_gains(k)
            project_rows(k, "fox_qk", w_in[:, 0:512], 4, k.HT, KD, k.scratch["fox_qk"], gain=k.head_gains[:, 0:4])
            project_rows(k, "swa_qk", w_in[:, C_SQ:C_SQ + 640], 5, k.HT, KD, k.scratch["swa_qk"], gain=k.head_gains[:, 4:9])
            project_rows(k, "plain", w_in[:, C_CU:C_MV], 10, k.HT, KD, k.scratch["plain"])
            project_rows(k, "mo", w_in[:, C_MO:C_SQ], 2, k.HT, KD, k.scratch["mo"])
            views = [w_in[:, c:c + n].rearrange("(c p) n -> p c n", p=P) for c, n in ((C_FV, 256), (C_MV, 256), (C_SV, 128))]
            project_tokens(k, "v2", [(views[0], 0, 256), (views[1], 256, 256), (views[2], 512, 128)], 5 * P, k.HT, KD, v2)
            gate_rows(k, vm)
            y = swa_y[:, :, :].rearrange("p c (x n) -> p (c x) n", n=512)
            with ExitStack() as fox:
                k.causal = k.sb("causal", [P, S], ctx=fox)
                split_values(k, v2, vm)
                attention(k, "fox", H,
                          lambda b, h: [("q", 0, k.scratch["fox_qk"][bass.ds(h * HD, HD), :]),
                                        ("q", HD, k.scratch["fox_q"][bass.ds(h * 2, 2), :]),
                                        ("k", 0, k.scratch["fox_qk"][bass.ds(h * HD + 256, HD), :]),
                                        ("k", HD, k.scratch["fox_k"][bass.ds(h * 2, 2), :])],
                          HD + 2, v2, y, 0)
                turn(k, "fox_turn", y[:, :, 0:256], k.ones[:, 0:2], fox_y, 2)
            matrix_lstm(k, vm, y)
            head_norm(k, "ml_rms", y[:, :, 0:256], H, HD, 1.0)
            turn(k, "ml_turn", y[:, :, 0:256], k.gain("mlstm_h_gain_2"), ml_y, 2)
            short_conv(k, conv_y, ml_y)
            biases = k.sb("biases", [P, 8, 2 * P], ctx=inner)
            sinks = k.sb("sinks", [P, 8], ctx=inner)
            window_bias(k, biases, sinks)
            y = k.sb("y_rows", [P, ST, 512], ctx=inner)
            for kv in range(2):
                attention(k, f"swa{kv}", 4,
                          lambda b, h: [("q", 0, k.scratch["swa_qk"][bass.ds(h * HD + kv * 4 * HD, HD), :]),
                                        ("k", 0, k.scratch["swa_qk"][512 + kv * HD:512 + (kv + 1) * HD, :])],
                          HD, v2, y, kv * 256, window=(kv * 4, 512 + kv * HD, biases, sinks))
            turn(k, "swa_turn", y[:, :, 0:512], k.ones[:, 0:4], swa_y, 4)
        merged = k.sb("merged", [P, KD, S], ctx=ctx)
        gated_merge(k, [("w_fox_out_2", fox_y, 2), ("w_conv_out_2", conv_y, 2), ("w_mlstm_out_2", ml_y, 2),
                        ("w_swa_out_2", swa_y, 4)], merged)
        project_residual(k, "merge_out", k.dram["w_merge_out_2"][0], merged, KD)


def split_values(k, v2, vm):
    nc = k.nc
    with k.phase() as ctx:
        (made,) = k.sems("split", "made")
        block = ctx.enter_context(nc.Block())

        @block.gpsimd
        def _(pool):
            link = k.own("pool", pool)
            link(nc.gpsimd.memset(k.causal[:], 0.0))
            link(nc.gpsimd.affine_select(out=k.causal[:, S - P:S], in_=k.causal[:, S - P:S], compare_op=ALU.is_ge,
                                         fill=NEG, base=0, pattern=[[-1, P]], channel_multiplier=1))

        @block.vector
        def _(dve):
            for t in range(ST):
                nc.vector.tensor_copy(vm[:, t, :, 0:HD], v2[:, t, 256:512].rearrange("p (h n) -> p h n", n=HD)
                                      ).then_inc(made, 1)
        k.chains["pool"].settle()


def store(k, view, tile):
    nc = k.nc
    with k.phase() as ctx:
        (stored,) = k.sems("store", "stored")
        block = ctx.enter_context(nc.Block())

        @block.sync
        def _(sp):
            sp.dma_start(view, tile).then_inc(stored, 16)
            sp.wait_ge(stored, 16)


def swiglu(k):
    norm_turn(k, "ffn2_norm", k.X, ST, k.gain("ffn_norm_2"), k.HT)
    with ExitStack() as ctx:
        hidden = k.sb("hidden", [P, FFC, S], ctx=ctx)
        swiglu_up(k, hidden)
        project_residual(k, "down", k.dram["w_down_2"][0], hidden, FFC)


def dump(k, tile):
    nc = k.nc
    with k.phase() as ctx:
        (stored,) = k.sems("dump", "stored")
        block = ctx.enter_context(nc.Block())

        @block.sync
        def _(sp):
            sp.dma_start(k.out.rearrange("a (t p) d -> p (a t) d", p=P), tile[:, :, :]).then_inc(stored, 16)
            sp.wait_ge(stored, 16)


def program(nc, dram, out):
    with ExitStack() as ctx:
        scratch = {name: nc.dram_tensor(f"scratch_{name}", shape, F32, kind="Internal").ap() for name, shape in (
            ("qk1", (2 * DIFF_QK, S)), ("qm", (MLA_HEADS * MLA_QK, S)), ("km", (MLA_HEADS * NOPE, S)),
            ("kpe", (ROPE, S)), ("ffn_rows", (S, D)), ("slot_token", (N_BLOCKS * BLK, 1)),
            ("expert_rows", (N_BLOCKS * BLK, D)), ("fox_qk", (512, S)), ("swa_qk", (640, S)), ("plain", (1280, S)),
            ("mo", (256, S)), ("fox_q", (8, S)), ("fox_k", (8, S)), ("mlstm_row", (4, S)), ("window_rows", (8, 3 * P)))}
        k = Core(nc, ctx, dram, out, scratch)
        setup(k)
        first_mixer(k)
        cross_mixer(k)
        expert_layer(k)
        final_norm(k)
        second_mixer(k)
        swiglu(k)
        store(k, out.rearrange("a (t p) d -> p (a t) d", p=P), k.X[:, :, :])


def build(nc, inputs):
    dram = {}
    for name, a in inputs.items():
        dram[name] = nc.dram_tensor(f"in_{name}_dram", a.shape, mybir.dt.from_np(a.dtype), kind="ExternalInput").ap()
    out = nc.dram_tensor("out_0_dram", (1, S, D), F32, kind="ExternalOutput").ap()
    program(nc, dram, out)


def kernel(**inputs):
    import numpy as _np
    import concourse.bacc as _bacc
    from concourse.bass_utils import run_bass_kernel_spmd as _run

    nc = _bacc.Bacc("TRN2", target_bir_lowering=False, num_devices=1)
    arrays = {name: _np.ascontiguousarray(a) for name, a in inputs.items()}
    build(nc, arrays)
    r = _run(nc, [{f"in_{name}_dram": a for name, a in arrays.items()}], core_ids=[0])
    return r.results[0]["out_0_dram"]
```

```python
from contextlib import ExitStack

import numpy as np

import concourse.bass as bass
from concourse import mybir

F32 = mybir.dt.float32
F32R = mybir.dt.float32r
I32 = mybir.dt.int32
U32 = mybir.dt.uint32
ALU = mybir.AluOpType
ACT = mybir.ActivationFunctionType
AX = mybir.AxisListType.X

P = 128
S = 1024
D = 1024
ST = S // P
KD = D // P
HALF = 512
EPS = 1e-6
NEG = -1e30

DIFF_HEADS, DIFF_HALF, DIFF_V = 8, 32, 64
DIFF_QK = DIFF_HEADS * 2 * DIFF_HALF
DIFF_W = DIFF_HEADS * DIFF_V
MLA_HEADS, MLA_QR, MLA_KVR, NOPE, ROPE, MLA_V = 8, 256, 128, 64, 32, 64
MLA_QK = NOPE + ROPE
MLA_W = MLA_HEADS * MLA_V
COL_VD = 2 * DIFF_QK
COL_CQ = COL_VD + DIFF_W
COL_KPE = COL_CQ + MLA_QR + MLA_KVR
LAMBDA_INIT = 0.8 - 0.6
MEM_T, MEM_HEADS, MEM_HD = 256, 4, 128
MEM_W = MEM_HEADS * MEM_HD

GROUPS, PER_GROUP = 4, 8
EXPERTS = GROUPS * PER_GROUP
FF = 256
BLK = 128
N_BLOCKS = -(-(2 * S + EXPERTS * (BLK - 1)) // BLK)

HD = 64
C_FQ, C_FF, C_CU, C_MQ, C_MI, C_MO, C_SQ = 0, 768, 772, 1540, 2308, 2316, 2572
C_FV, C_MV, C_SV, C_GATES = 512, 2052, 3212, 3340
D_FF = 2816
FFC = D_FF // P
WINDOW = 128

GAIN_ROWS = {}
_row = 0
for _name, _count in (("norm_mix_g", 8), ("norm_cross_g", 8), ("norm_mem_g", 8), ("norm_ffn_g", 8),
                      ("attn_norm_2", 8), ("ffn_norm_2", 8), ("mla_out_g", 4), ("mla_q_norm_g", 2),
                      ("mla_kv_norm_g", 1), ("mlstm_h_gain_2", 2), ("conv_w_2", 6)):
    GAIN_ROWS[_name] = (_row, _count)
    _row += _count
for _name in ("diff_out_g", "fox_q_gain_2", "fox_k_gain_2", "swa_q_gain_2", "swa_k_gain_2"):
    GAIN_ROWS[_name] = (_row, 1)
    _row += 1
N_GAINS = _row


SEMS = 24


class Chain:

    def __init__(self, sem):
        self.sem, self.total, self.start, self.count = sem, 0, 0, 0

    def enter(self, i, per):
        self.start, self.count, self.per = self.total + i * per, 0, per

    def leave(self, rounds):
        assert self.count == self.per, (self.count, self.per)
        self.total += rounds * self.per
        self.start, self.count = self.total, 0

    def step(self):
        self.count += 1
        return self.start + self.count

    def settle(self):
        self.total += self.count
        self.start, self.count = self.total, 0


class Core:

    def __init__(self, nc, ctx, dram, out, scratch):
        self.nc, self.ctx, self.dram, self.out = nc, ctx, dram, out
        self.scratch = scratch
        self.chains, self.names = {}, {}
        sb = self.sb
        self.banks = [[ctx.enter_context(nc.semaphore(f"bank{n}_{i}")) for i in range(SEMS)] for n in range(2)]
        self.bank, self.taken = 0, 0
        self.soft = {n: ctx.enter_context(nc.semaphore(n)) for n in (
            "token_numbers_scattered", "rows_gathered0", "rows_gathered1", "outputs_gathered0", "outputs_gathered1")}
        self.X = sb("X", [P, ST, D])
        self.ident = sb("ident", [P, P])
        self.ones = sb("ones", [P, P])
        self.ones64 = sb("ones64", [P, P])
        self.gains = sb("gains", [P, N_GAINS])
        self.ssq = sb("ssq", [P, ST])
        self.mean = sb("mean", [P, ST])
        self.root = sb("root", [P, ST])
        self.rstd = sb("rstd", [P, ST])
        for e in ("dve", "act", "pool"):
            self.chains[e] = Chain(ctx.enter_context(nc.semaphore(f"{e}_own")))

    def unused(self, name):
        self.names[name] = self.names.get(name, 0) + 1
        return name if self.names[name] == 1 else f"{name}_{self.names[name]}"

    def sb(self, name, shape, dt=F32, ctx=None):
        return (ctx or self.ctx).enter_context(self.nc.sbuf_tensor(self.unused(name), shape, dt))

    def ps(self, name, shape, ctx):
        return ctx.enter_context(self.nc.psum_tensor(self.unused(name), shape, F32))

    def phase(self):
        self.bank, self.taken = 1 - self.bank, 0
        other = [s.num for s in self.banks[1 - self.bank]]
        self.nc.gpsimd.sem_clear(range(min(other), max(other) + 1))
        return ExitStack()

    def sems(self, phase, names):
        n = len(names.split())
        got = self.banks[self.bank][self.taken:self.taken + n]
        assert len(got) == n, phase
        self.taken += n
        return got

    def gain(self, name, extra=0, count=None):
        row, n = GAIN_ROWS[name]
        return self.gains[:, row + extra:row + extra + (count or n)]

    def own(self, engine_name, engine):
        chain = self.chains[engine_name]

        def link(ins):
            value = chain.step()
            ins.then_inc(chain.sem, 1)
            engine.wait_ge(chain.sem, value)
        return link


def pair(k, name, shape, ctx):
    return k.sb(f"{name}_high", shape, F32R, ctx), k.sb(f"{name}_low", shape, F32R, ctx)


def add_product(nc, out, w, x, start, stop):
    if not isinstance(w, tuple):
        return nc.tensor.matmul(out, w, x, start=start, stop=stop)
    nc.tensor.matmul(out, w[0], x[0], start=start, stop=False)
    nc.tensor.matmul(out, w[0], x[1], start=False, stop=False)
    return nc.tensor.matmul(out, w[1], x[0], start=False, stop=stop)


def part(x, *index):
    return tuple(t[index] for t in x) if isinstance(x, tuple) else x[index]


def split_weights(nc, pool, j, b, loaded, raw, weights, products, split, passed):
    pool.wait_ge(*loaded)
    pool.wait_ge(products, j + 1)
    pool.sem_inc(passed, 1)
    nc.gpsimd.tensor_copy(weights[b][0][:], raw[b][:]).then_inc(split, 1)
    pool.wait_ge(split, 2 * j + 1 + 4)
    nc.gpsimd.tensor_tensor(weights[b][1][:], raw[b][:], weights[b][0][:], ALU.subtract).then_inc(split, 1)


def staged(engine, rounds, per_round, stages):
    def steps(i, count, before, own):
        for n in range(count):
            for lag, body in stages:
                if n >= lag and own:
                    body(i, n - lag, i * per_round + n - lag)
                elif n < lag and before:
                    body(i - 1, n - lag + per_round, i * per_round + n - lag)

    if len(stages) == 1:
        with engine.Fori(0, rounds) as i:
            steps(i, per_round, before=False, own=True)
        return
    steps(0, per_round, before=False, own=True)
    if rounds > 1:
        with engine.Fori(1, rounds) as i:
            steps(i, per_round, before=True, own=True)
    steps(rounds, max(lag for lag, _ in stages), before=True, own=False)


def setup(k):
    nc = k.nc
    with k.phase() as ctx:
        rows = k.sb("gain_rows", [N_GAINS, P], ctx=ctx)
        turned = k.ps("turned", [P, N_GAINS], ctx)
        x_in, gains_in, ident_made, gains_turned = k.sems("setup", "x_in gains_in ident_made gains_turned")
        block = ctx.enter_context(nc.Block())
        doubled = ("diff_out_g", "fox_q_gain_2", "fox_k_gain_2", "swa_q_gain_2", "swa_k_gain_2")
        n_loads = len(GAIN_ROWS) + len(doubled)

        @block.sync
        def _(sp):
            for name, (row, count) in GAIN_ROWS.items():
                if name in doubled:
                    for half in range(2):
                        sp.dma_start(rows[row:row + 1, half * 64:half * 64 + 64],
                                     k.dram[name]).then_inc(gains_in, 16)
                else:
                    flat = "l k c -> (l k c)" if name == "conv_w_2" else "l c -> (l c)"
                    src = k.dram[name].rearrange(flat).rearrange("(r c) -> r c", c=P)
                    sp.dma_start(rows[row:row + count, :], src).then_inc(gains_in, 16)

        @block.scalar
        def _(act):
            x = k.dram["x"].rearrange("a (t p) d -> p (a t) d", p=P)
            with act.Fori(0, ST) as t:
                act.dma_start(k.X[:, bass.ds(t, 1), :], x[:, bass.ds(t, 1), :]).then_inc(x_in, 16)
            act.wait_ge(x_in, 16 * ST)

        @block.gpsimd
        def _(pool):
            link = k.own("pool", pool)
            link(nc.gpsimd.memset(k.ident[:], 0.0))
            nc.gpsimd.affine_select(out=k.ident[:], in_=k.ident[:], compare_op=ALU.not_equal, fill=1.0,
                                    base=0, pattern=[[-1, P]], channel_multiplier=1).then_inc(ident_made, 1)
            link(nc.gpsimd.memset(k.ones64[:], 0.0))
            link(nc.gpsimd.memset(k.ones[:], 1.0))

        @block.vector
        def _(dve):
            link = k.own("dve", dve)
            dve.wait_ge(k.chains["pool"].sem, 3)
            link(nc.vector.memset(k.ones64[0:64, 0:64], 1.0))
            link(nc.vector.memset(k.ones64[64:128, 64:128], 1.0))
            dve.wait_ge(gains_turned, 1)
            link(nc.vector.tensor_copy(k.gains[:], turned[:, :]))

        @block.tensor
        def _(pe):
            pe.wait_ge(ident_made, 1)
            pe.wait_ge(gains_in, 16 * n_loads)
            nc.tensor.transpose(turned[:, :], rows[:, :], k.ident[0:N_GAINS, 0:N_GAINS]).then_inc(gains_turned, 1)

        for e in ("dve", "pool"):
            k.chains[e].settle()


def norm_turn(k, phase, X, tiles, gain, HT, rows_out=None):
    nc = k.nc
    pairs = tiles // 2
    with k.phase() as ctx:
        junk = [k.sb(f"{phase}_junk{b}", [P, D], ctx=ctx) for b in range(2)]
        scaled = [k.sb(f"{phase}_scaled{b}", [P, D], ctx=ctx) for b in range(2)]
        turned = [k.ps(f"{phase}_turned{b}", [P, KD, P], ctx) for b in range(2)]
        paired = isinstance(HT, tuple)
        plain = [tile[:].rearrange("p (c s) -> p c s", s=P) for tile in junk]
        even_squares, odd_squares, mean_ready, root_ready, rstd_ready, scaled_ready, turns, stored, kept0, kept1, highs, lows = k.sems(
            phase, "even_squares odd_squares mean_ready root_ready rstd_ready scaled_ready turns stored kept0 kept1 highs lows")
        kept = (kept0, kept1)
        block = ctx.enter_context(nc.Block())

        @block.scalar
        def _(act):
            act.sem_inc(kept0, 16)
            act.sem_inc(kept1, 16)
            for i in range(pairs):
                if i:
                    act.wait_ge(even_squares, i)
                nc.scalar.activation(junk[0][:], X[:, 2 * i, :], ACT.Square,
                                     accum_out=k.ssq[:, 2 * i:2 * i + 1]).then_inc(even_squares, 1)
            act.wait_ge(mean_ready, 1)
            nc.scalar.activation(k.root[:, 0:tiles], k.mean[:, 0:tiles], ACT.Sqrt).then_inc(root_ready, 1)
            act.wait_ge(rstd_ready, 1)

            def scale_rows(i, b, t):
                act.wait_ge(turns, t + 1)
                if rows_out is not None:
                    act.wait_ge(kept[b], 16 * i + 16)
                nc.scalar.activation(scaled[b][:], row_of(X, t), ACT.Copy,
                                     scale=k.rstd[:, bass.ds(t, 1)]).then_inc(scaled_ready, 1)

            def high_part(i, b, t):
                act.wait_ge(stored, t + 1 + 1)
                nc.scalar.activation(HT[0][:, :, bass.ds(t * P, P)], plain[b][:, :, :], ACT.Copy).then_inc(highs, 1)
            staged(act, pairs, 2, ((0, scale_rows), (1, high_part)) if paired else ((0, scale_rows),))

        @block.vector
        def _(dve):
            dve.sem_inc(stored, 1)
            link = k.own("dve", dve)
            for i in range(pairs):
                if i:
                    dve.wait_ge(odd_squares, i)
                nc.vector.tensor_tensor_reduce(out=junk[1][:], in0=X[:, 2 * i + 1, :], in1=X[:, 2 * i + 1, :],
                                               scale=1.0, scalar=0.0, op0=ALU.mult, op1=ALU.add,
                                               accum_out=k.ssq[:, 2 * i + 1:2 * i + 2]).then_inc(odd_squares, 1)
            dve.wait_ge(odd_squares, pairs)
            dve.wait_ge(even_squares, pairs)
            nc.vector.tensor_scalar(k.mean[:, 0:tiles], k.ssq[:, 0:tiles], 1.0 / D, EPS,
                                    ALU.mult, ALU.add).then_inc(mean_ready, 1)
            dve.wait_ge(root_ready, 1)
            nc.vector.reciprocal(k.rstd[:, 0:tiles], k.root[:, 0:tiles]).then_inc(rstd_ready, 1)

            def apply_gain(i, b, t):
                dve.wait_ge(turns, t + 1 + 2)
                if paired:
                    dve.wait_ge(lows, t + 1)
                target = plain[b][:, :, :] if paired else HT[:, :, bass.ds(t * P, P)]
                nc.vector.tensor_tensor(target, turned[b][:, :, :], gain.rearrange("p (c o) -> p c o", o=1).broadcast_to(
                    [P, KD, P]), ALU.mult).then_inc(stored, 1)

            def low_part(i, b, t):
                dve.wait_ge(highs, t + 1)
                nc.vector.tensor_tensor(HT[1][:, :, bass.ds(t * P, P)], plain[b][:, :, :], HT[0][:, :, bass.ds(t * P, P)],
                                        ALU.subtract).then_inc(lows, 1)
            dve.sem_inc(lows, 2)
            staged(dve, pairs, 2, ((0, apply_gain), (1, low_part)) if paired else ((0, apply_gain),))

        if rows_out is not None:
            @block.sync
            def _(sp):
                with sp.Fori(0, pairs) as i:
                    for b in range(2):
                        sp.wait_ge(scaled_ready, 2 * i + b + 1)
                        sp.dma_start(rows_out[bass.ds((2 * i + b) * P, P), :], scaled[b][:]).then_inc(kept[b], 16)
                sp.wait_ge(kept0, 16 * pairs + 16)
                sp.wait_ge(kept1, 16 * pairs + 16)

        @block.tensor
        def _(pe):
            pe.sem_inc(turns, 2)
            with pe.Fori(0, pairs) as i:
                for b in range(2):
                    pe.wait_ge(scaled_ready, 2 * i + b + 1)
                    if b == 0:
                        pe.wait_ge(stored, 2 * i + 1)
                    for c in range(KD):
                        last = nc.tensor.transpose(turned[b][:, c, :], scaled[b][:, c * P:(c + 1) * P], k.ident[:])
                    last.then_inc(turns, 1)


def row_of(X, t):
    return X[:, bass.ds(t, 1), :].rearrange("p a d -> p (a d)")


def project_rows(k, phase, w, n_chunks, src, kc, dest, scale=1.0, gain=None, tokens=S):
    nc = k.nc
    to_dram = not isinstance(dest, tuple)
    with k.phase() as ctx:
        raw = [k.sb(f"{phase}_w{b}", [P, kc, P], ctx=ctx) for b in range(2)]
        paired = isinstance(src, tuple)
        weights = [pair(k, f"{phase}_ws{b}", [P, kc, P], ctx) for b in range(2)] if paired else raw
        stage = [k.sb(f"{phase}_stage{b}", [P, tokens], ctx=ctx) for b in range(2)]
        acc = [k.ps(f"{phase}_acc{b}", [P, max(tokens, HALF)], ctx) for b in range(2)]
        if gain is not None:
            square = k.sb(f"{phase}_square", [P, S], ctx=ctx)
            norm = k.sb(f"{phase}_norm", [P, S], ctx=ctx)
            sums = k.ps(f"{phase}_sums", [P, S], ctx)
            squared, summed, meaned, rooted = k.sems(phase, "squared summed meaned rooted")
        w_in0, w_in1, products, split, passed, evacuated, stored0, stored1 = k.sems(
            phase, "w_in0 w_in1 products split passed evacuated stored0 stored1")
        w_in, stored = (w_in0, w_in1), (stored0, stored1)
        block = ctx.enter_context(nc.Block())
        pairs, tail = n_chunks // 2, n_chunks % 2
        w_view = w.rearrange("(c p) n -> p c n", p=P)

        def chunks(engine, body):
            with engine.Fori(0, pairs) as i:
                for b in range(2):
                    body(i * 2 + b, b, i)
            if tail:
                body(pairs * 2, 0, pairs)

        @block.sync
        def _(sp):
            def load(j, b, r):
                if paired:
                    sp.wait_ge(split, 2 * j + 2)
                else:
                    sp.wait_ge(products, j + 1)
                sp.dma_start(raw[b][:, :, :], w_view[:, :, bass.ds(j * P, P)]).then_inc(w_in[b], 16)
            chunks(sp, load)

        if paired:
            @block.gpsimd
            def _(pool):
                pool.sem_inc(split, 4)
                chunks(pool, lambda j, b, r: split_weights(nc, pool, j, b, (w_in[b], 16 * r + 16), raw, weights, products,
                                                           split, passed))

        @block.tensor
        def _(pe):
            if gain is not None:
                pe.sem_inc(summed, 1)
            pe.sem_inc(products, 2)

            def multiply(j, b, r):
                pe.wait_ge(*((split, 2 * j + 2 + 4) if paired else (w_in[b], 16 * r + 16)))
                pe.wait_ge(evacuated, j + 1)
                for c in range(kc):
                    for at in range(0, tokens, HALF):
                        to = min(at + HALF, tokens)
                        last = add_product(nc, acc[b][:, at:to], part(weights[b], slice(None), c, slice(None)),
                                           part(src, slice(None), c, slice(at, to)), c == 0, c == kc - 1)
                last.then_inc(products, 1)
                if gain is not None:
                    pe.wait_ge(squared, j + 1)
                    pe.wait_ge(meaned, j + 1)
                    for h in range(2):
                        last = nc.tensor.matmul(sums[:, h * HALF:(h + 1) * HALF], k.ones64[:],
                                                square[:, h * HALF:(h + 1) * HALF], start=True, stop=True)
                    last.then_inc(summed, 1)
            chunks(pe, multiply)

        @block.scalar
        def _(act):
            act.sem_inc(stored0, 16)
            act.sem_inc(stored1, 16)
            if gain is None:
                act.sem_inc(evacuated, 2)

            def leave(j, b, r):
                act.wait_ge(products, j + 1 + 2)
                if gain is not None:
                    act.wait_ge(summed, j + 1)
                    nc.scalar.activation(square[:], acc[b][:], ACT.Square).then_inc(squared, 1)
                    act.wait_ge(meaned, j + 1 + 1)
                    nc.scalar.activation(norm[:], norm[:], ACT.Sqrt).then_inc(rooted, 1)
                elif to_dram:
                    act.wait_ge(stored[b], 16 * r + 16)
                    nc.scalar.activation(stage[b][:], acc[b][:, 0:tokens], ACT.Copy, scale=scale).then_inc(evacuated, 1)
                else:
                    nc.scalar.activation(dest[0][:, bass.ds(j, 1), :].rearrange("p a s -> p (a s)"),
                                         acc[b][:, 0:tokens], ACT.Copy, scale=scale).then_inc(evacuated, 1)
                if to_dram:
                    act.wait_ge(evacuated, j + 1 + 2)
                    act.dma_start(dest.rearrange("(c p) s -> p c s", p=P)[:, bass.ds(j, 1), :].rearrange(
                        "p a s -> p (a s)"), stage[b][:]).then_inc(stored[b], 16)
            chunks(act, leave)
            if to_dram:
                act.wait_ge(stored0, 16 * (pairs + tail) + 16)
                act.wait_ge(stored1, 16 * pairs + 16)

        if gain is not None:
            @block.vector
            def _(dve):
                dve.sem_inc(meaned, 1)
                dve.sem_inc(evacuated, 2)
                link = k.own("dve", dve)
                chain = k.chains["dve"]

                def normalise(j, b, r):
                    dve.wait_ge(summed, j + 1 + 1)
                    nc.vector.tensor_scalar(norm[:], sums[:], 1.0 / HD, EPS, ALU.mult, ALU.add).then_inc(meaned, 1)
                    dve.wait_ge(rooted, j + 1)
                    link(nc.vector.reciprocal(norm[:], norm[:]))
                    dve.wait_ge(stored[b], 16 * r + 16)
                    nc.vector.scalar_tensor_tensor(out=stage[b][:], in0=acc[b][:], scalar=gain[:, bass.ds(j, 1)],
                                                   in1=norm[:], op0=ALU.mult, op1=ALU.mult).then_inc(evacuated, 1)
                with dve.Fori(0, pairs) as i:
                    chain.enter(i, 2)
                    for b in range(2):
                        normalise(i * 2 + b, b, i)
                    chain.leave(pairs)
                if tail:
                    normalise(pairs * 2, 0, pairs)
                    chain.settle()


def project_tokens(k, phase, loads, n_cols, src, kc, dest, tiles=ST):
    nc = k.nc
    pieces = [(c, min(HALF, n_cols - c)) for c in range(0, n_cols, HALF)]
    with k.phase() as ctx:
        weights = k.sb(f"{phase}_w", [P, kc, n_cols], ctx=ctx)
        tokens = [k.sb(f"{phase}_tokens{b}", [P, kc, P], ctx=ctx) for b in range(2)]
        acc = [k.ps(f"{phase}_acc{b}", [P, 2 * HALF], ctx) for b in range(2)]
        w_in, copied, products, evacuated, passed = k.sems(phase, "w_in copied products evacuated passed")
        block = ctx.enter_context(nc.Block())

        @block.sync
        def _(sp):
            for view, col, n in loads:
                into = weights[:, :, col:col + n]
                if kc == 1:
                    into = into.rearrange("p c (h n) -> p (c h) n", n=view.shape[-1])
                sp.dma_start(into, view).then_inc(w_in, 16)

        if isinstance(src, tuple):
            @block.gpsimd
            def _(pool):
                with pool.Fori(0, tiles // 2) as i:
                    for b in range(2):
                        pool.wait_ge(products, i * 2 + b + 1)
                        pool.sem_inc(passed, 1)
                        high, low = (x[:, 0:kc, bass.ds((i * 2 + b) * P, P)] for x in src)
                        nc.gpsimd.tensor_tensor(tokens[b][:, :, :], high, low, ALU.add).then_inc(copied, 1)
        else:
            @block.scalar
            def _(act):
                with act.Fori(0, tiles // 2) as i:
                    for b in range(2):
                        act.wait_ge(products, i * 2 + b + 1)
                        nc.scalar.activation(tokens[b][:, :, :], src[:, 0:kc, bass.ds((i * 2 + b) * P, P)],
                                             ACT.Copy).then_inc(copied, 1)

        @block.tensor
        def _(pe):
            pe.sem_inc(products, 2)
            pe.wait_ge(w_in, 16 * len(loads))
            with pe.Fori(0, tiles // 2) as i:
                for b in range(2):
                    pe.wait_ge(copied, i * 2 + b + 1)
                    pe.wait_ge(evacuated, i * 2 + b + 1)
                    for c in range(kc):
                        for at, n in pieces:
                            last = nc.tensor.matmul(acc[b][:, at:at + n], tokens[b][:, c, :],
                                                    weights[:, c, at:at + n], start=(c == 0), stop=(c == kc - 1))
                    last.then_inc(products, 1)

        @block.vector
        def _(dve):
            dve.sem_inc(evacuated, 2)
            with dve.Fori(0, tiles // 2) as i:
                for b in range(2):
                    dve.wait_ge(products, i * 2 + b + 1 + 2)
                    nc.vector.tensor_copy(row_of(dest, i * 2 + b), acc[b][:, 0:n_cols]).then_inc(evacuated, 1)


def project_residual(k, phase, w, src, kc):
    nc = k.nc
    with k.phase() as ctx:
        raw = [k.sb(f"{phase}_w{b}", [P, kc, P], ctx=ctx) for b in range(2)]
        paired = isinstance(src, tuple)
        weights = [pair(k, f"{phase}_ws{b}", [P, kc, P], ctx) for b in range(2)] if paired else raw
        rows = [k.sb(f"{phase}_rows{b}", [P, S], ctx=ctx) for b in range(2)]
        acc = [k.ps(f"{phase}_acc{b}", [P, S], ctx) for b in range(2)]
        turned = [k.ps(f"{phase}_turned{b}", [P, ST, P], ctx) for b in range(2)]
        w_in0, w_in1, products, split, passed, evacuated, turns, added = k.sems(
            phase, "w_in0 w_in1 products split passed evacuated turns added")
        w_in = (w_in0, w_in1)
        block = ctx.enter_context(nc.Block())
        w_view = w.rearrange("(c p) n -> p c n", p=P)

        @block.sync
        def _(sp):
            with sp.Fori(0, KD // 2) as i:
                for b in range(2):
                    sp.wait_ge(*((split, 2 * (2 * i + b) + 2) if paired else (products, i * 2 + b + 1)))
                    sp.dma_start(raw[b][:, :, :], w_view[:, :, bass.ds((i * 2 + b) * P, P)]).then_inc(w_in[b], 16)

        if paired:
            @block.gpsimd
            def _(pool):
                pool.sem_inc(split, 4)
                with pool.Fori(0, KD // 2) as i:
                    for b in range(2):
                        split_weights(nc, pool, 2 * i + b, b, (w_in[b], 16 * i + 16), raw, weights, products, split, passed)

        @block.tensor
        def _(pe):
            pe.sem_inc(turns, 1)
            pe.sem_inc(products, 2)
            with pe.Fori(0, KD // 2) as i:
                for b in range(2):
                    pe.wait_ge(*((split, 2 * (2 * i + b) + 2 + 4) if paired else (w_in[b], 16 * i + 16)))
                    pe.wait_ge(evacuated, i * 2 + 1)
                    for c in range(kc):
                        for h in range(2):
                            last = add_product(nc, acc[b][:, h * HALF:(h + 1) * HALF],
                                               part(weights[b], slice(None), c, slice(None)),
                                               part(src, slice(None), c, slice(h * HALF, (h + 1) * HALF)),
                                               c == 0, c == kc - 1)
                    last.then_inc(products, 1)
                for b in range(2):
                    pe.wait_ge(evacuated, i * 2 + b + 1 + 1)
                    pe.wait_ge(added, i * 2 + b + 1)
                    for t in range(ST):
                        last = nc.tensor.transpose(turned[b][:, t, :], rows[b][:, t * P:(t + 1) * P], k.ident[:])
                    last.then_inc(turns, 1)

        @block.scalar
        def _(act):
            act.sem_inc(evacuated, 1)
            with act.Fori(0, KD // 2) as i:
                for b in range(2):
                    act.wait_ge(products, i * 2 + b + 1 + 2)
                    act.wait_ge(turns, i * 2 + 1)
                    nc.scalar.activation(rows[b][:], acc[b][:], ACT.Copy).then_inc(evacuated, 1)

        @block.vector
        def _(dve):
            dve.sem_inc(added, 2)
            with dve.Fori(0, KD // 2) as i:
                for b in range(2):
                    dve.wait_ge(turns, i * 2 + b + 1 + 1)
                    x = k.X[:, :, bass.ds((i * 2 + b) * P, P)]
                    nc.vector.tensor_tensor(x, x, turned[b][:, :, :], ALU.add).then_inc(added, 1)



def tables(k):
    nc = k.nc
    with k.phase() as ctx:
        scale = MLA_QK ** -0.5
        pos_row_i = k.sb("pos_row_i", [P, S], I32, ctx=ctx)
        pos_row = k.sb("pos_row", [P, S], ctx=ctx)
        lams = k.sb("lams", [P, 4, DIFF_HALF], ctx=ctx)
        lam_junk = k.sb("lam_junk", [P, 2, DIFF_HALF], ctx=ctx)
        lam_dot = k.sb("lam_dot", [P, 4], ctx=ctx)
        consts = k.sb("consts", [1, 4, P], ctx=ctx)
        cols = k.sb("cols", [P, 4], ctx=ctx)
        turns = k.sb("turns", [P, S], ctx=ctx)
        angle = k.rot
        cols_ps = k.ps("cols_ps", [P, 4], ctx)
        pos_in, lams_in, consts_made, cols_turned, dots, lam_exp, angle_made = k.sems(
            "tables", "pos_in lams_in consts_made cols_turned dots lam_exp angle_made")
        block = ctx.enter_context(nc.Block())

        @block.sync
        def _(sp):
            sp.dma_start(pos_row_i[:], k.dram["positions"].broadcast_to([P, S])).then_inc(pos_in, 16)
            for n, name in enumerate(("diff_lambda_q1", "diff_lambda_k1", "diff_lambda_q2", "diff_lambda_k2")):
                sp.dma_start(lams[:, n, :], k.dram[name].broadcast_to([P, DIFF_HALF])).then_inc(lams_in, 16)

        @block.gpsimd
        def _(pool):
            link = k.own("pool", pool)
            quarters = consts[:, :, :].rearrange("a n (q c) -> a n q c", q=4)
            for f in range(ROPE // 2):
                inv = float(np.float32(10000.0) ** np.float32(-2.0 * f / ROPE))
                nc.gpsimd.memset(consts[:, 0, :].rearrange("a (q f) -> a q f", f=ROPE // 2)[:, :, f:f + 1],
                                 inv).then_inc(consts_made, 1)
            for q, (turn, radian) in enumerate(((0.25, np.pi / 2), (0.0, 0.0)) * 2):
                nc.gpsimd.memset(quarters[:, 1, q, :], turn).then_inc(consts_made, 1)
                nc.gpsimd.memset(quarters[:, 2, q, :], float(radian)).then_inc(consts_made, 1)
            for q, (low, high) in enumerate(((1.0, 1.0), (-1.0, 1.0), (scale, scale), (-scale, scale))):
                nc.gpsimd.memset(quarters[:, 3, q, 0:16], low).then_inc(consts_made, 1)
                nc.gpsimd.memset(quarters[:, 3, q, 16:32], high).then_inc(consts_made, 1)
            for h in range(DIFF_HEADS):
                nc.gpsimd.memset(k.slopes[:, h:h + 1], -(2.0 ** (-8.0 * (h + 1) / DIFF_HEADS)) * DIFF_HALF ** 0.5).then_inc(consts_made, 1)
            link(nc.gpsimd.memset(k.causal[:], 0.0))
            link(nc.gpsimd.affine_select(out=k.causal[:, S - P:S], in_=k.causal[:, S - P:S], compare_op=ALU.is_ge,
                                         fill=NEG, base=0, pattern=[[-1, P]], channel_multiplier=1))

        @block.tensor
        def _(pe):
            pe.wait_ge(consts_made, 32 + DIFF_HEADS)
            for n in range(4):
                last = nc.tensor.transpose(cols_ps[:, n:n + 1], consts[0:1, n, :], k.ident[0:1, 0:1])
            last.then_inc(cols_turned, 1)

        @block.vector
        def _(dve):
            link = k.own("dve", dve)
            dve.wait_ge(lams_in, 64)
            for n in range(2):
                nc.vector.tensor_tensor_reduce(out=lam_junk[:, n, :], in0=lams[:, 2 * n, :], in1=lams[:, 2 * n + 1, :],
                                               scale=1.0, scalar=0.0, op0=ALU.mult, op1=ALU.add,
                                               accum_out=lam_dot[:, n:n + 1]).then_inc(dots, 1)
            dve.wait_ge(pos_in, 16)
            link(nc.vector.tensor_copy(pos_row[:], pos_row_i[:]))
            dve.wait_ge(lam_exp, 1)
            link(nc.vector.tensor_tensor(lam_dot[:, 3:4], lam_dot[:, 3:4], lam_dot[:, 2:3], ALU.subtract))
            link(nc.vector.tensor_scalar(k.neg_lambda[:], lam_dot[:, 3:4], -LAMBDA_INIT, None, ALU.add))
            dve.wait_ge(cols_turned, 1)
            link(nc.vector.tensor_copy(cols[:], cols_ps[:]))
            link(nc.vector.tensor_scalar(angle[:], pos_row[:], cols[:, 0:1], None, ALU.mult))
            link(nc.vector.tensor_scalar(turns[:], angle[:], 1.0 / (2 * np.pi), cols[:, 1:2], ALU.mult, ALU.add))
            link(nc.vector.tensor_scalar(turns[:], turns[:], 12582912.0, None, ALU.add))
            link(nc.vector.tensor_scalar(turns[:], turns[:], -12582912.0, None, ALU.add))
            c1 = 6.28125
            c2 = float(np.float32(np.round((2 * np.pi - c1) * 2 ** 20) / 2 ** 20))
            c3 = float(2 * np.pi - c1 - c2)
            for part in (c1, c2, c3):
                link(nc.vector.scalar_tensor_tensor(out=angle[:], in0=turns[:], scalar=-part, in1=angle[:],
                                                    op0=ALU.mult, op1=ALU.add))
            link(nc.vector.tensor_scalar(angle[:], angle[:], cols[:, 2:3], 3.1415925, ALU.add, ALU.min))
            nc.vector.tensor_scalar(angle[:], angle[:], -3.1415925, None, ALU.max).then_inc(angle_made, 1)
            dve.wait_ge(angle_made, 2)
            link(nc.vector.tensor_scalar(k.rot[:], k.rot[:], cols[:, 3:4], None, ALU.mult))

        @block.scalar
        def _(act):
            act.wait_ge(dots, 2)
            nc.scalar.activation(lam_dot[:, 2:4], lam_dot[:, 0:2], ACT.Exp).then_inc(lam_exp, 1)
            act.wait_ge(angle_made, 1)
            nc.scalar.activation(k.rot[:], angle[:], ACT.Sin).then_inc(angle_made, 1)

        for e in ("dve", "pool"):
            k.chains[e].settle()


def distances(k):
    nc = k.nc
    with k.phase() as ctx:
        pos_row_i = k.sb("pos_row_i", [P, S], I32, ctx=ctx)
        pos_row = k.sb("pos_row", [P, S], ctx=ctx)
        pos_col_i = k.sb("pos_col_i", [P, ST], I32, ctx=ctx)
        pos_col = k.sb("pos_col", [P, ST], ctx=ctx)
        pos_in, dist_made, masked = k.sems("distances", "pos_in dist_made masked")
        block = ctx.enter_context(nc.Block())

        @block.sync
        def _(sp):
            sp.dma_start(pos_row_i[:], k.dram["positions"].broadcast_to([P, S])).then_inc(pos_in, 16)
            with nc.allow_non_contiguous_dma(reason="1024 positions, one to a descriptor"):
                sp.dma_start(pos_col_i[:], k.dram["positions"].rearrange("a (t p) -> p (a t)", p=P)).then_inc(pos_in, 16)

        @block.vector
        def _(dve):
            link = k.own("dve", dve)
            dve.wait_ge(pos_in, 32)
            link(nc.vector.tensor_copy(pos_row[:], pos_row_i[:]))
            link(nc.vector.tensor_copy(pos_col[:], pos_col_i[:]))
            for t in range(ST):
                link(nc.vector.tensor_scalar(k.dist[:, t, :], pos_row[:], pos_col[:, t:t + 1], None, ALU.subtract))
                nc.vector.scalar_tensor_tensor(out=k.dist[:, t, :], in0=k.dist[:, t, :], scalar=-1.0, in1=k.dist[:, t, :],
                                               op0=ALU.mult, op1=ALU.max).then_inc(dist_made, 1)

        @block.gpsimd
        def _(pool):
            for t in range(ST):
                pool.wait_ge(dist_made, t + 1)
                diag = k.dist[:, t, t * P:(t + 1) * P]
                nc.gpsimd.affine_select(out=diag, in_=diag, compare_op=ALU.is_ge, fill=-NEG, base=0,
                                        pattern=[[-1, P]], channel_multiplier=1).then_inc(masked, 1)
        k.chains["dve"].settle()


def latent_up(k, cq, HT):
    nc = k.nc
    with k.phase() as ctx:
        scale = MLA_QK ** -0.5
        W = 3 * ROPE
        wk = k.sb("kpe_w", [P, KD, W], ctx=ctx)
        wk_pair = pair(k, "kpe_ws", [P, KD, W], ctx)
        work = k.sb("lat_work", [P, 4, S], ctx=ctx)
        sq = work[:, 0:3, :]
        norm = k.sb("lat_norm", [P, 2, S], ctx=ctx)
        wq = [k.sb(f"lat_wq{b}", [P, 2, P], ctx=ctx) for b in range(2)]
        wn = [k.sb(f"lat_wn{b}", [P, NOPE], ctx=ctx) for b in range(2)]
        turned = [k.sb(f"lat_rot{b}", [P, S], ctx=ctx) for b in range(2)]
        qs = [work[:, b, :] for b in range(2)]
        ks = [work[0:NOPE, 2 + b, :] for b in range(2)]
        kpe = k.sb("kpe", [ROPE, S], ctx=ctx)
        qp = [k.ps(f"lat_qp{b}", [P, S], ctx) for b in range(2)]
        kp = [k.ps(f"lat_kp{b}", [P, S], ctx) for b in range(2)]
        (wk_in, wk_split, kpe_made, kpe_read, sq_made, sums_made, mean_made, root_made, lat_made, wq_in0, wq_in1, heads,
         nopes, q_made, turned_made, stored) = k.sems("lat", "wk_in wk_split kpe_made kpe_read sq_made sums_made mean_made root_made lat_made "
                                         "wq_in0 wq_in1 heads nopes q_made turned_made stored")
        w_in = (wq_in0, wq_in1)
        block = ctx.enter_context(nc.Block())
        w_uq = k.dram["w_mla_uq"].rearrange("l (c p) (h n) -> p (l c) h n", p=P, n=MLA_QK)
        w_ukv = k.dram["w_mla_ukv"].rearrange("l p (h n) -> p (l h) n", n=NOPE + MLA_V)
        w_pe = k.dram["w_in"][0].rearrange("(c p) n -> p c n", p=P)
        half = ROPE // 2

        def head(i, b):
            return i * 2 + b

        @block.sync
        def _(sp):
            for at, col, n in ((0, COL_KPE, ROPE), (ROPE, COL_KPE + half, half), (ROPE + half, COL_KPE, half),
                               (2 * ROPE, COL_KPE, ROPE)):
                sp.dma_start(wk[:, :, at:at + n], w_pe[:, :, col:col + n]).then_inc(wk_in, 16)
            with sp.Fori(0, MLA_HEADS // 2) as i:
                for b in range(2):
                    sp.wait_ge(heads, head(i, b) + 1)
                    for at, col, n in ((0, 0, MLA_QK), (MLA_QK, NOPE + half, half), (MLA_QK + half, NOPE, half)):
                        sp.dma_start(wq[b][:, :, at:at + n],
                                     w_uq[:, :, bass.ds(head(i, b), 1), col:col + n].rearrange(
                                         "p c h n -> p c (h n)")).then_inc(w_in[b], 16)
                    sp.dma_start(wn[b][:], w_ukv[:, bass.ds(head(i, b), 1), 0:NOPE].rearrange(
                        "p h n -> p (h n)")).then_inc(w_in[b], 16)

        @block.gpsimd
        def _(pool):
            pool.wait_ge(wk_in, 64)
            nc.gpsimd.tensor_copy(wk_pair[0][:], wk[:]).then_inc(wk_split, 1)
            pool.wait_ge(wk_split, 1)
            nc.gpsimd.tensor_tensor(wk_pair[1][:], wk[:], wk_pair[0][:], ALU.subtract).then_inc(wk_split, 1)

        @block.tensor
        def _(pe):
            pe.sem_inc(heads, 2)
            pe.wait_ge(wk_split, 2)
            for c in range(KD):
                for h in range(2):
                    last = add_product(nc, qp[0][0:W, h * HALF:(h + 1) * HALF],
                                       part(wk_pair, slice(None), c, slice(None)),
                                       part(HT, slice(None), c, slice(h * HALF, (h + 1) * HALF)), c == 0, c == KD - 1)
            last.then_inc(kpe_made, 1)
            pe.wait_ge(sq_made, 1)
            for n, chunks in ((0, (0, 1)), (1, (2,))):
                for c in chunks:
                    for h in range(2):
                        last = nc.tensor.matmul(kp[n][:, h * HALF:(h + 1) * HALF], k.ones[:],
                                                sq[:, c, h * HALF:(h + 1) * HALF],
                                                start=(c == chunks[0]), stop=(c == chunks[-1]))
            last.then_inc(sums_made, 1)
            pe.wait_ge(lat_made, 3)
            pe.wait_ge(kpe_read, 1)
            with pe.Fori(0, MLA_HEADS // 2) as i:
                for b in range(2):
                    pe.wait_ge(w_in[b], 64 * i + 64)
                    pe.wait_ge(q_made, head(i, b) + 1)
                    for c in range(2):
                        for h in range(2):
                            last = nc.tensor.matmul(qp[b][:, h * HALF:(h + 1) * HALF], wq[b][:, c, :],
                                                    cq[:, c, h * HALF:(h + 1) * HALF], start=(c == 0), stop=(c == 1))
                    for h in range(2):
                        last = nc.tensor.matmul(kp[b][0:NOPE, h * HALF:(h + 1) * HALF], wn[b][:],
                                                cq[:, 2, h * HALF:(h + 1) * HALF], start=True, stop=True)
                    last.then_inc(heads, 1)

        @block.scalar
        def _(act):
            act.sem_inc(stored, 16)
            nc.scalar.activation(sq[:, :, :], cq[:, :, :], ACT.Square).then_inc(sq_made, 1)
            act.wait_ge(mean_made, 2)
            nc.scalar.activation(norm[:, :, :], norm[:, :, :], ACT.Sqrt).then_inc(root_made, 1)
            act.sem_inc(nopes, 2 * 2)
            with act.Fori(0, MLA_HEADS // 2) as i:
                for b in range(2):
                    h = head(i, b)
                    act.wait_ge(heads, h + 1 + 2)
                    act.wait_ge(stored, 32 * h + 16)
                    nc.scalar.activation(qs[b][0:NOPE, :], qp[b][0:NOPE, :], ACT.Copy, scale=scale).then_inc(nopes, 1)
                    nc.scalar.activation(ks[b][:], kp[b][0:NOPE, :], ACT.Copy).then_inc(nopes, 1)
                    act.wait_ge(nopes, 2 * h + 2 + 4)
                    act.wait_ge(q_made, h + 1 + 2)
                    act.dma_start(k.scratch["qm"][bass.ds(h * MLA_QK, MLA_QK), :], qs[b][0:MLA_QK, :]).then_inc(stored, 16)
                    act.dma_start(k.scratch["km"][bass.ds(h * NOPE, NOPE), :], ks[b][:]).then_inc(stored, 16)
            act.dma_start(k.scratch["kpe"], kpe[:]).then_inc(stored, 16)
            act.wait_ge(stored, 32 * MLA_HEADS + 16 + 16)

        @block.vector
        def _(dve):
            link = k.own("dve", dve)
            dve.wait_ge(kpe_made, 1)
            link(nc.vector.tensor_tensor(turned[0][0:ROPE, :], qp[0][ROPE:2 * ROPE, :], k.rot[ROPE:2 * ROPE, :], ALU.mult))
            link(nc.vector.tensor_tensor(kpe[:], qp[0][0:ROPE, :], k.rot[0:ROPE, :], ALU.mult))
            nc.vector.tensor_tensor(kpe[:], kpe[:], turned[0][0:ROPE, :], ALU.add).then_inc(kpe_read, 1)
            dve.wait_ge(sums_made, 1)
            for n, width in ((0, MLA_QR), (1, MLA_KVR)):
                nc.vector.tensor_scalar(norm[:, n, :], kp[n][:], 1.0 / width, EPS, ALU.mult, ALU.add).then_inc(mean_made, 1)
            dve.wait_ge(root_made, 1)
            link(nc.vector.reciprocal(norm[:, :, :], norm[:, :, :]))
            gains = (k.gain("mla_q_norm_g", 0, 1), k.gain("mla_q_norm_g", 1, 1), k.gain("mla_kv_norm_g"))
            for c in range(3):
                nc.vector.scalar_tensor_tensor(out=cq[:, c, :], in0=cq[:, c, :], scalar=gains[c], in1=norm[:, c // 2, :],
                                               op0=ALU.mult, op1=ALU.mult).then_inc(lat_made, 1)
            dve.sem_inc(q_made, 2)
            dve.wait_ge(kpe_read, 1)
            pe_rows, swapped_rows = slice(NOPE, MLA_QK), slice(MLA_QK, P)
            chain = k.chains["dve"]
            chain.settle()
            with dve.Fori(0, MLA_HEADS // 2) as i:
                chain.enter(i, 4)
                for b in range(2):
                    h = head(i, b)
                    dve.wait_ge(heads, h + 1 + 2)
                    dve.wait_ge(stored, 32 * h + 16)
                    link(nc.vector.tensor_tensor(turned[b][pe_rows, :], qp[b][swapped_rows, :], k.rot[swapped_rows, :], ALU.mult))
                    link(nc.vector.tensor_tensor(qs[b][pe_rows, :], qp[b][pe_rows, :], k.rot[pe_rows, :], ALU.mult))
                    dve.wait_ge(nopes, 2 * h + 2 + 4)
                    nc.vector.tensor_tensor(qs[b][pe_rows, :], qs[b][pe_rows, :], turned[b][pe_rows, :],
                                            ALU.add).then_inc(q_made, 1)
                chain.leave(MLA_HEADS // 2)


TURN = 2


def attention(k, phase, heads, loads, rows, V, out, out_col, maps=1, alibi=False, scale=1.0,
              window=None):
    nc = k.nc
    with k.phase() as ctx:
        q = [k.sb(f"{phase}_q{b}", [P, S], ctx=ctx) for b in range(2)]
        kk = [k.sb(f"{phase}_k{b}", [P, S], ctx=ctx) for b in range(2)]
        probs = [[k.sb(f"{phase}_p{m}{b}", [P, S], ctx=ctx) for b in range(4)] for m in range(maps)]
        turned_sb = [k.sb(f"{phase}_pt{b}", [P, ST, P], ctx=ctx) for b in range(2)]
        slope = [k.sb(f"{phase}_slope{b}", [P, 1], ctx=ctx) for b in range(2)]
        bias = [k.sb(f"{phase}_bias{b}", [P, S], ctx=ctx) for b in range(2)] if alibi else None
        head_bias = [k.sb(f"{phase}_hbias{b}", [P, 2 * P], ctx=ctx) for b in range(2)] if window else None
        sink = [k.sb(f"{phase}_sink{b}", [P, 1], ctx=ctx) for b in range(2)] if window else None
        stats = [k.sb(f"{phase}_stats{n}", [P, 9], ctx=ctx) for n in range(8)]
        scores = [k.ps(f"{phase}_scores{n}", [P, S], ctx) for n in range(2)]
        turned = k.ps(f"{phase}_turned", [P, ST, P], ctx)
        outs = [k.ps(f"{phase}_out{b}", [P, HD], ctx) for b in range(2)]
        (head_in0, head_in1, products, biased, scored, maxed, exps, weighed, mixed, turns, copied, values, done,
         passed) = k.sems(phase, "head_in0 head_in1 products biased scored maxed exps weighed mixed turns copied "
                          "values done passed")
        head_in = (head_in0, head_in1)
        block = ctx.enter_context(nc.Block())
        per_round = 2 * ST
        n_loads = len(loads(0, 0))
        rounds = heads // 2
        ready = mixed if maps == 2 else exps

        def first(t):
            return max(t - 1, 0) if window else 0

        def parts(width):
            return [(c, min(HALF, width - c)) for c in range(0, width, HALF)]

        def value_cols(i, b):
            return slice(window[1], window[1] + HD) if window else bass.ds((i * 2 + b) * HD, HD)

        @block.sync
        def _(sp):
            with sp.Fori(0, rounds) as i:
                for b in range(2):
                    sp.wait_ge(products, (i * 2 + b) * ST * maps + 1)
                    for which, row, src in loads(b, i * 2 + b):
                        tile = q[b] if which == "q" else kk[b]
                        sp.dma_start(tile[row:row + src.shape[0], :], src).then_inc(head_in[b], 16)

        @block.tensor
        def _(pe):
            pe.sem_inc(products, 1 + ST * maps)
            pe.sem_inc(turns, 4)
            pe.sem_inc(values, 2)

            def score(i, n, g):
                b, t = n // ST, n % ST
                if t == 0:
                    pe.wait_ge(head_in[b], 16 * n_loads * i + 16 * n_loads)
                for m in range(maps):
                    pe.wait_ge(scored, g * maps + m + 1 + 1)
                    ps = scores[m if maps == 2 else n % 2]
                    r = slice(rows * m, rows * (m + 1))
                    for at, w in parts((t + 1 - first(t)) * P):
                        key = first(t) * P + at
                        last = nc.tensor.matmul(ps[:, at:at + w], q[b][r, t * P:(t + 1) * P],
                                                kk[b][r, key:key + w], start=True, stop=True)
                    last.then_inc(products, 1)

            def turn_probs(i, n, g):
                t = n % ST
                pe.wait_ge(ready, g + 1 + (maps == 1))
                pe.wait_ge(copied, g + 1)
                for c in range(t + 1 - first(t)):
                    last = nc.tensor.transpose(turned[:, c, :], probs[0][n % 4][:, c * P:(c + 1) * P], k.ident[:])
                last.then_inc(turns, 1)

            def multiply(i, n, g):
                b, t = n // ST, n % ST
                pe.wait_ge(copied, g + 1 + 1)
                pe.wait_ge(done, g + 1)
                for c in range(first(t), t + 1):
                    last = nc.tensor.matmul(outs[n % 2][:], turned_sb[n % 2][:, c - first(t), :],
                                            V[:, c, value_cols(i, b)], start=(c == first(t)), stop=(c == t))
                last.then_inc(values, 1)
            staged(pe, rounds, per_round, ((0, score), (TURN, turn_probs), (TURN + 1, multiply)))

        @block.vector
        def _(dve):
            dve.sem_inc(scored, 3)
            dve.sem_inc(done, 2)
            per_step = 2 if maps == 2 or window else 1

            def shift(i, n, g):
                t = n % ST
                w = (t + 1 - first(t)) * P
                st = stats[n % 8]
                dve.wait_ge(turns, g + 1)
                if alibi:
                    dve.wait_ge(biased, g + 2)
                if window and t == 0:
                    dve.wait_ge(biased, 2 * (i * 2 + n // ST) + 2)
                for m in range(maps):
                    dve.wait_ge(products, g * maps + m + 1 + ST * maps + 1)
                    dve.sem_inc(passed, 1)
                    ps = scores[m if maps == 2 else n % 2]
                    b_ap = (bias[n % 2][:, 0:w] if alibi else head_bias[n // ST][:, 2 * P - w:2 * P] if window
                            else k.causal[:, S - w:S])
                    least = sink[n // ST][:, 0:1] if window else -3e38
                    nc.vector.tensor_tensor_reduce(out=probs[m][n % 4][:, 0:w], in0=ps[:, 0:w], in1=b_ap,
                                                   scale=scale, scalar=least, op0=ALU.add, op1=ALU.max,
                                                   accum_out=st[:, m:m + 1]).then_inc(scored, 1)
                dve.wait_ge(scored, (g + 1) * maps + 2 + 1)
                nc.vector.tensor_scalar(st[:, 2:2 + maps], st[:, 0:maps], -1.0, None, ALU.mult).then_inc(maxed, 1)

            def weigh(i, n, g):
                t, st = n % ST, stats[n % 8]
                w = (t + 1 - first(t)) * P
                dve.wait_ge(exps, g + 1 + 1)
                if window:
                    nc.vector.tensor_tensor(st[:, 4:5], st[:, 4:5], st[:, 8:9], ALU.add).then_inc(weighed, 1)
                    dve.wait_ge(weighed, g * per_step + 1)
                nc.vector.reciprocal(st[:, 6:6 + maps], st[:, 4:4 + maps]).then_inc(weighed, 1)
                if maps == 2:
                    dve.wait_ge(weighed, g * per_step + 1)
                    nc.vector.scalar_tensor_tensor(out=st[:, 8:9], in0=st[:, 4:5], scalar=k.neg_lambda[:, 0:1],
                                                   in1=st[:, 7:8], op0=ALU.mult, op1=ALU.mult).then_inc(weighed, 1)
                    dve.wait_ge(weighed, g * per_step + 2)
                    nc.vector.scalar_tensor_tensor(out=probs[0][n % 4][:, 0:w], in0=probs[1][n % 4][:, 0:w],
                                                   scalar=st[:, 8:9], in1=probs[0][n % 4][:, 0:w],
                                                   op0=ALU.mult, op1=ALU.add).then_inc(mixed, 1)

            def scale_out(i, n, g):
                b, t = n // ST, n % ST
                dve.wait_ge(values, g + 1 + 2)
                dve.wait_ge(weighed, (g + 1) * per_step)
                nc.vector.tensor_scalar(out[:, t, bass.ds((i * 2 + b) * HD + out_col, HD)], outs[n % 2][:],
                                        stats[n % 8][:, 6:7], None, ALU.mult).then_inc(done, 1)
            staged(dve, rounds, per_round, ((0, shift), (TURN - 1, weigh), (TURN + 2, scale_out)))

        @block.scalar
        def _(act):
            act.sem_inc(exps, 1)
            act.sem_inc(copied, 1)

            def copy_turned(i, n, g):
                t = n % ST
                act.wait_ge(turns, g + 1 + 4)
                act.wait_ge(values, g + 1)
                nc.scalar.activation(turned_sb[n % 2][:, 0:t + 1 - first(t), :],
                                     turned[:, 0:t + 1 - first(t), :], ACT.Copy).then_inc(copied, 1)

            def exponentials(i, n, g):
                w, st = (n % ST + 1 - first(n % ST)) * P, stats[n % 8]
                act.wait_ge(maxed, g + 1)
                if window:
                    nc.scalar.activation(st[:, 8:9], sink[n // ST][:], ACT.Exp, bias=st[:, 2:3])
                for m in range(maps):
                    last = nc.scalar.activation(probs[m][n % 4][:, 0:w], probs[m][n % 4][:, 0:w], ACT.Exp,
                                                bias=st[:, 2 + m:3 + m], accum_out=st[:, 4 + m:5 + m])
                last.then_inc(exps, 1)
            staged(act, rounds, per_round, ((TURN, copy_turned), (0, exponentials)))

        if window:
            @block.gpsimd
            def _(pool):
                with pool.Fori(0, rounds) as i:
                    pool.wait_ge(scored, i * per_round + 2 + 1)
                    pool.wait_ge(exps, i * per_round + 1)
                    for b in range(2):
                        head = bass.ds(i * 2 + b + window[0], 1)
                        nc.gpsimd.tensor_copy(head_bias[b][:], window[2][:, head, :].rearrange("p h c -> p (h c)")
                                              ).then_inc(biased, 1)
                        nc.gpsimd.tensor_copy(sink[b][:], window[3][:, head]).then_inc(biased, 1)

        if alibi:
            @block.gpsimd
            def _(pool):
                pool.sem_inc(biased, 1)
                chain = k.chains["pool"]
                link = k.own("pool", pool)
                with pool.Fori(0, rounds) as i:
                    chain.enter(i, 2)
                    for n in range(per_round):
                        b, t = n // ST, n % ST
                        w = (t + 1) * P
                        if t == 0:
                            pool.wait_ge(biased, i * per_round + n + 1)
                            pool.sem_inc(passed, 1)
                            link(nc.gpsimd.tensor_copy(slope[b][:], k.slopes[:, bass.ds(i * 2 + b, 1)]))
                        pool.wait_ge(scored, (i * per_round + n) * 2 + 1)
                        pool.sem_inc(passed, 1)
                        nc.gpsimd.tensor_scalar(bias[n % 2][:, 0:w], k.dist[:, t, 0:w], slope[b][:], 1.0,
                                                ALU.mult, ALU.mult).then_inc(biased, 1)
                    chain.leave(rounds)


def head_norm(k, phase, Y, heads, width, factor):
    nc = k.nc
    with k.phase() as ctx:
        sq = k.sb(f"{phase}_sq", [P, ST, heads * width], ctx=ctx)
        norm = k.sb(f"{phase}_norm", [P, ST, heads], ctx=ctx)
        squared, mean_made, root_made, norm_made = k.sems(phase, "squared mean_made root_made norm_made")
        block = ctx.enter_context(nc.Block())
        n = ST * heads

        @block.scalar
        def _(act):
            nc.scalar.activation(sq[:, :, :], Y, ACT.Square).then_inc(squared, 1)
            act.wait_ge(mean_made, 1)
            nc.scalar.activation(norm[:, :, :], norm[:, :, :], ACT.Sqrt).then_inc(root_made, 1)

        @block.vector
        def _(dve):
            link = k.own("dve", dve)
            dve.wait_ge(squared, 1)
            link(nc.vector.tensor_reduce(norm[:, :, :], sq[:, :, :].rearrange("p t (h w) -> p t h w", w=width), AX, ALU.add))
            nc.vector.tensor_scalar(norm[:, :, :], norm[:, :, :], 1.0 / width / factor ** 2, EPS / factor ** 2,
                                    ALU.mult, ALU.add).then_inc(mean_made, 1)
            dve.wait_ge(root_made, 1)
            link(nc.vector.reciprocal(norm[:, :, :], norm[:, :, :]))
            for t in range(ST):
                link(nc.vector.tensor_tensor(Y[:, t, :].rearrange("p (h w) -> p h w", w=width),
                                             Y[:, t, :].rearrange("p (h w) -> p h w", w=width),
                                             norm[:, t, :].rearrange("p (h o) -> p h o", o=1).broadcast_to([P, heads, width]),
                                             ALU.mult))
        k.chains["dve"].settle()


def turn(k, phase, Y, gain, dest, chunks):
    nc = k.nc
    with k.phase() as ctx:
        tiles = [k.sb(f"{phase}_tile{b}", [P, chunks * P], ctx=ctx) for b in range(2)]
        turned = [k.ps(f"{phase}_turned{b}", [P, chunks, P], ctx) for b in range(2)]
        paired = isinstance(dest, tuple)
        plain = [k.sb(f"{phase}_plain{b}", [P, chunks, P], ctx=ctx) for b in range(2)] if paired else None
        copied, turns, stored, highs, lows = k.sems(phase, "copied turns stored highs lows")
        block = ctx.enter_context(nc.Block())

        @block.scalar
        def _(act):
            def copy_rows(i, b, t):
                act.wait_ge(turns, t + 1)
                nc.scalar.activation(tiles[b][:], row_of(Y, t), ACT.Copy).then_inc(copied, 1)

            def high_part(i, b, t):
                act.wait_ge(stored, t + 1 + 1)
                nc.scalar.activation(dest[0][:, 0:chunks, bass.ds(t * P, P)], plain[b][:, :, :], ACT.Copy).then_inc(highs, 1)
            staged(act, ST // 2, 2, ((0, copy_rows), (1, high_part)) if paired else ((0, copy_rows),))

        @block.tensor
        def _(pe):
            pe.sem_inc(turns, 2)
            with pe.Fori(0, ST // 2) as i:
                for b in range(2):
                    pe.wait_ge(copied, 2 * i + b + 1)
                    pe.wait_ge(stored, 2 * i + 1)
                    for c in range(chunks):
                        last = nc.tensor.transpose(turned[b][:, c, :], tiles[b][:, c * P:(c + 1) * P], k.ident[:])
                    last.then_inc(turns, 1)

        @block.vector
        def _(dve):
            dve.sem_inc(stored, 1)

            def apply_gain(i, b, t):
                dve.wait_ge(turns, t + 1 + 2)
                if paired:
                    dve.wait_ge(lows, t + 1)
                target = plain[b][:, :, :] if paired else dest[:, 0:chunks, bass.ds(t * P, P)]
                nc.vector.tensor_tensor(target, turned[b][:, :, :], gain.rearrange("p (c o) -> p c o", o=1).broadcast_to(
                    [P, chunks, P]), ALU.mult).then_inc(stored, 1)

            def low_part(i, b, t):
                dve.wait_ge(highs, t + 1)
                high, low = (x[:, 0:chunks, bass.ds(t * P, P)] for x in dest)
                nc.vector.tensor_tensor(low, plain[b][:, :, :], high, ALU.subtract).then_inc(lows, 1)
            dve.sem_inc(lows, 2)
            staged(dve, ST // 2, 2, ((0, apply_gain), (1, low_part)) if paired else ((0, apply_gain),))


def first_mixer(k):
    nc = k.nc
    w_in = k.dram["w_in"][0]
    with ExitStack() as ctx:
        vd = k.sb("vd", [P, ST, DIFF_W], ctx=ctx)
        vm = k.sb("vm", [P, ST, MLA_W], ctx=ctx)
        k.causal = k.sb("causal", [P, S], ctx=ctx)
        k.slopes = k.sb("slopes", [P, DIFF_HEADS], ctx=ctx)
        k.neg_lambda = k.sb("neg_lambda", [P, 1], ctx=ctx)
        with ExitStack() as early:
            cq = k.sb("cq", [P, 3, S], ctx=early)
            with ExitStack() as tab:
                k.rot = k.sb("rot", [P, S], ctx=tab)
                H = pair(k, "mix_h", [P, KD, S], tab)
                tables(k)
                norm_turn(k, "mix_norm", k.X, ST, k.gain("norm_mix_g"), H)
                project_rows(k, "diff_qk", w_in[:, 0:2 * DIFF_QK], 2 * DIFF_QK // P, H, KD, k.scratch["qk1"])
                project_rows(k, "latents", w_in[:, COL_CQ:COL_KPE], 3, H, KD, (cq,))
                project_tokens(k, "diff_v", [(w_in[:, COL_VD:COL_CQ].rearrange("(c p) n -> p c n", p=P), 0, DIFF_W)],
                               DIFF_W, H, KD, vd)
                latent_up(k, cq, H)
            w_ukv = k.dram["w_mla_ukv"].rearrange("l p (h n) -> p (l h) n", n=NOPE + MLA_V)
            project_tokens(k, "latent_v", [(w_ukv[:, :, NOPE:], 0, MLA_W)], MLA_W, cq[:, 2:3, :], 1, vm)
        mix = k.sb("mix", [P, ST, D], ctx=ctx)
        far = ctx.enter_context(ExitStack())
        k.dist = k.sb("dist", [P, ST, S], ctx=far)
        distances(k)
        attention(k, "diff", DIFF_HEADS,
                  lambda b, h: [("q", 0, k.scratch["qk1"][bass.ds(h * HD, HD), :]),
                                ("k", 0, k.scratch["qk1"][bass.ds(h * HD + DIFF_QK, HD), :])],
                  DIFF_HALF, vd, mix, 0, maps=2, alibi=True, scale=DIFF_HALF ** -0.5)
        attention(k, "latent", MLA_HEADS,
                  lambda b, h: [("q", 0, k.scratch["qm"][bass.ds(h * MLA_QK, MLA_QK), :]),
                                ("k", 0, k.scratch["km"][bass.ds(h * NOPE, NOPE), :]),
                                ("k", NOPE, k.scratch["kpe"])],
                  MLA_QK, vm, mix, DIFF_W)
        far.close()
        head_norm(k, "diff_rms", mix[:, :, 0:DIFF_W], DIFF_HEADS, DIFF_V, 1.0 - LAMBDA_INIT)
        head_norm(k, "latent_rms", mix[:, :, DIFF_W:D], 1, MLA_W, 1.0)
        H = pair(k, "mixed", [P, KD, S], ctx)
        diff_gain, latent_gain = k.gain("diff_out_g"), k.gain("mla_out_g")
        turn(k, "diff_turn", mix[:, :, 0:DIFF_W], diff_gain, part(H, slice(None), slice(0, 4)), 4)
        turn(k, "latent_turn", mix[:, :, DIFF_W:D], latent_gain, part(H, slice(None), slice(4, 8)), 4)
        project_residual(k, "mix_out", k.dram["w_out"][0], H, KD)


def memory_attention(k, q, km, vm, out):
    nc = k.nc
    with k.phase() as ctx:
        qt = [k.sb(f"mem_qt{b}", [P, MEM_HEADS, P], ctx=ctx) for b in range(2)]
        probs = [k.sb(f"mem_p{b}", [P, MEM_HEADS, MEM_T], ctx=ctx) for b in range(2)]
        turned_sb = [k.sb(f"mem_pt{b}", [P, 2 * MEM_HEADS, P], ctx=ctx) for b in range(2)]
        stats = [k.sb(f"mem_stats{b}", [P, 3, MEM_HEADS], ctx=ctx) for b in range(2)]
        scores = [k.ps(f"mem_scores{b}", [P, MEM_HEADS, MEM_T], ctx) for b in range(2)]
        turned = k.ps("mem_turned", [P, 2 * MEM_HEADS, P], ctx)
        outs = [k.ps(f"mem_out{b}", [P, MEM_HEADS, P], ctx) for b in range(2)]
        q_copied, products, shifted, exps, probs_ready, turns, copied, values, done = k.sems(
            "mem", "q_copied products shifted exps probs_ready turns copied values done")
        block = ctx.enter_context(nc.Block())

        def across(column):
            return column.rearrange("p (h o) -> p h o", o=1).broadcast_to([P, MEM_HEADS, MEM_T])

        @block.tensor
        def _(pe):
            pe.sem_inc(values, 1)
            pe.sem_inc(products, 1)
            pe.sem_inc(turns, 1)
            with pe.Fori(0, ST // 2) as i:
                for b in range(2):
                    pe.wait_ge(q_copied, 2 * i + b + 1)
                    pe.wait_ge(shifted, 2 * i + 1)
                    for h in range(MEM_HEADS):
                        last = nc.tensor.matmul(scores[b][:, h, :], qt[b][:, h, :], km[:, h, :], start=True, stop=True)
                    last.then_inc(products, 1)
                for b in range(2):
                    pe.wait_ge(probs_ready, 2 * i + b + 1)
                    pe.wait_ge(copied, 2 * i + b + 1)
                    for n in range(2 * MEM_HEADS):
                        last = nc.tensor.transpose(turned[:, n, :], probs[b][:, n // 2, (n % 2) * P:(n % 2 + 1) * P],
                                                   k.ident[:])
                    last.then_inc(turns, 1)
                for b in range(2):
                    pe.wait_ge(copied, 2 * i + b + 1 + 1)
                    pe.wait_ge(done, 2 * i + 1)
                    for h in range(MEM_HEADS):
                        for c in range(2):
                            last = nc.tensor.matmul(outs[b][:, h, :], vm[:, c, h * MEM_HD:(h + 1) * MEM_HD],
                                                    turned_sb[b][:, 2 * h + c, :], start=(c == 0), stop=(c == 1))
                    last.then_inc(values, 1)

        @block.vector
        def _(dve):
            dve.sem_inc(done, 1)
            dve.sem_inc(shifted, 1)
            link = k.own("dve", dve)
            chain = k.chains["dve"]
            with dve.Fori(0, ST // 2) as i:
                chain.enter(i, 6)
                for b in range(2):
                    dve.wait_ge(products, 2 * i + b + 1 + 1)
                    dve.wait_ge(turns, 2 * i + 1)
                    link(nc.vector.tensor_reduce(stats[b][:, 0, :], scores[b][:, :, :], AX, ALU.max))
                    nc.vector.tensor_tensor(probs[b][:, :, :], scores[b][:, :, :], across(stats[b][:, 0, :]),
                                            ALU.subtract).then_inc(shifted, 1)
                for b in range(2):
                    dve.wait_ge(exps, 2 * i + b + 1)
                    link(nc.vector.tensor_reduce(stats[b][:, 1, :], probs[b][:, :, :], AX, ALU.add))
                    link(nc.vector.reciprocal(stats[b][:, 2, :], stats[b][:, 1, :]))
                    nc.vector.tensor_tensor(probs[b][:, :, :], probs[b][:, :, :], across(stats[b][:, 2, :]),
                                            ALU.mult).then_inc(probs_ready, 1)
                for b in range(2):
                    dve.wait_ge(values, 2 * i + b + 1 + 1)
                    nc.vector.tensor_copy(out[:, :, bass.ds((2 * i + b) * P, P)], outs[b][:, :, :]).then_inc(done, 1)
                chain.leave(ST // 2)

        @block.scalar
        def _(act):
            act.sem_inc(copied, 1)
            with act.Fori(0, ST // 2) as i:
                for b in range(2):
                    act.wait_ge(products, 2 * i + 1)
                    nc.scalar.activation(qt[b][:, :, :], q[:, :, bass.ds((2 * i + b) * P, P)], ACT.Copy).then_inc(q_copied, 1)
                for b in range(2):
                    act.wait_ge(shifted, 2 * i + b + 1 + 1)
                    nc.scalar.activation(probs[b][:, :, :], probs[b][:, :, :], ACT.Exp).then_inc(exps, 1)
                for b in range(2):
                    act.wait_ge(turns, 2 * i + b + 1 + 1)
                    act.wait_ge(values, 2 * i + 1)
                    nc.scalar.activation(turned_sb[b][:, :, :], turned[:, :, :], ACT.Copy).then_inc(copied, 1)


def cross_mixer(k):
    nc = k.nc
    with ExitStack() as ctx:
        H = pair(k, "cross_h", [P, KD, S], ctx)
        norm_turn(k, "cross_norm", k.X, ST, k.gain("norm_cross_g"), H)
        out = k.sb("mem_mixed", [P, MEM_HEADS, S], ctx=ctx)
        with ExitStack() as inner:
            q = k.sb("mem_q", [P, MEM_HEADS, S], ctx=inner)
            km = k.sb("mem_k", [P, MEM_HEADS, MEM_T], ctx=inner)
            vm = k.sb("mem_v", [P, MEM_T // P, MEM_W], ctx=inner)
            mem = k.sb("mem_x", [P, MEM_T // P, D], ctx=inner)
            mem_t = k.sb("mem_t", [P, KD, MEM_T], ctx=inner)
            load_rows(k, k.dram["mem"].rearrange("a (t p) d -> p (a t) d", p=P), mem)
            norm_turn(k, "mem_norm", mem, MEM_T // P, k.gain("norm_mem_g"), mem_t)
            w_kv = k.dram["w_mem_kv"][0]
            project_rows(k, "mem_k", w_kv[:, 0:MEM_W], MEM_HEADS, mem_t, KD, (km,), tokens=MEM_T)
            project_tokens(k, "mem_v", [(w_kv[:, MEM_W:].rearrange("(c p) n -> p c n", p=P), 0, MEM_W)],
                           MEM_W, mem_t, KD, vm, tiles=MEM_T // P)
            project_rows(k, "mem_q", k.dram["w_mem_q"][0], MEM_HEADS, H, KD, (q,), scale=MEM_HD ** -0.5)
            memory_attention(k, q, km, vm, out)
        project_residual(k, "mem_out", k.dram["w_mem_o"][0], out, MEM_HEADS)


def load_rows(k, view, tile):
    nc = k.nc
    with k.phase() as ctx:
        (loaded,) = k.sems("load", "loaded")
        block = ctx.enter_context(nc.Block())

        @block.sync
        def _(sp):
            sp.dma_start(tile[:, :, :], view).then_inc(loaded, 16)
            sp.wait_ge(loaded, 16)


def route(k, logits, slots, weights, experts, slot_of_block):
    nc = k.nc
    E, G = EXPERTS, GROUPS
    with k.phase() as ctx:
        sb = lambda name, shape, dt=F32: k.sb(f"route_{name}", shape, dt, ctx=ctx)
        bias = sb("bias", [P, G + E])
        groups = sb("groups", [P, ST, 8])
        group_max, group_idx = sb("group_max", [P, ST, 8]), sb("group_idx", [P, ST, 8], U32)
        group_f, gate = sb("group_f", [P, ST]), sb("gate", [P, ST])
        e_sum = sb("e_sum", [P, ST, G])
        picked = sb("picked", [P, ST, E])
        top, top_idx = sb("top", [P, ST, 8]), sb("top_idx", [P, ST, 8], U32)
        choice = sb("choice", [P, 2, ST])
        ratio, total = sb("ratio", [P, ST]), sb("total", [P, ST])
        numbers, group_of = sb("numbers", [P, ST, E]), sb("group_of", [P, ST, E])
        hot = [sb(f"hot{c}", [P, ST, E]) for c in range(2)]
        both, before = sb("both", [P, ST, E]), sb("before", [P, ST + 1, E])
        earlier = sb("earlier", [P, P])
        steps, over = sb("steps", [P, E, ST]), sb("over", [P, E, ST])
        n_blocks, ends, starts = sb("n_blocks", [P, E]), sb("ends", [P, E]), sb("starts", [P, E])
        place = sb("place", [P, ST, E])
        slot_f = sb("slot_f", [P, 2, ST])
        block_no, passed = sb("block_no", [P, N_BLOCKS, E]), sb("passed", [P, N_BLOCKS, E])
        expert_f = sb("expert_f", [P, N_BLOCKS])
        tokens, clear = sb("tokens", [P, ST]), sb("clear", [N_BLOCKS, BLK])
        rows = sb("rows", [N_BLOCKS, BLK])
        ranks = k.ps("route_ranks", [P, ST, E], ctx)
        counts = k.ps("route_counts", [P, E], ctx)
        turned = k.ps("route_turned", [P, N_BLOCKS], ctx)
        bias_in, made, shifted, exped, hot_made, ranked, slots_made, cleared, rows_in, rows_turned = k.sems(
            "route", "bias_in made shifted exped hot_made ranked slots_made cleared rows_in rows_turned")
        scattered = k.soft["token_numbers_scattered"]
        block = ctx.enter_context(nc.Block())
        table = k.scratch["slot_token"]
        row_table = table.rearrange("(b s) o -> b (s o)", s=BLK)

        def over_experts(x):
            return x.rearrange("p (t o) -> p t o", o=1).broadcast_to([P, ST, E])

        def over_tiles(x):
            return x.rearrange("p (o e) -> p o e", o=1).broadcast_to([P, ST, x.shape[-1]])

        @block.sync
        def _(sp):
            sp.dma_start(bias[:, 0:G], k.dram["b_group_router"].broadcast_to([P, G])).then_inc(bias_in, 16)
            sp.dma_start(bias[:, G:], k.dram["b_expert_router"].broadcast_to([P, E])).then_inc(bias_in, 16)
            sp.wait_ge(made, 9)
            sp.dma_start(row_table, clear[:]).then_inc(cleared, 16)
            sp.wait_ge(scattered, 16 * 2 * ST)
            sp.dma_start(rows[:], row_table).then_inc(rows_in, 16)

        @block.gpsimd
        def _(pool):
            iota = dict(allow_small_or_imprecise_dtypes=True)
            nc.gpsimd.iota(numbers[:, :, :], [[0, ST], [1, E]], 0, 0, **iota).then_inc(made, 1)
            nc.gpsimd.iota(group_of[:, :, :], [[0, ST], [1, G], [0, PER_GROUP]], 0, 0, **iota).then_inc(made, 1)
            nc.gpsimd.iota(steps[:, :, :], [[0, E], [BLK, ST]], 0, 0, **iota).then_inc(made, 1)
            nc.gpsimd.iota(block_no[:, :, :], [[1, N_BLOCKS], [0, E]], 0, 0, **iota).then_inc(made, 1)
            nc.gpsimd.iota(tokens[:, :], [[P, ST]], 0, 1, **iota).then_inc(made, 1)
            nc.gpsimd.memset(earlier[:], 1.0).then_inc(made, 1)
            nc.gpsimd.memset(groups[:, :, :], -3e38).then_inc(made, 1)
            nc.gpsimd.memset(clear[:], 0.0).then_inc(made, 1)
            pool.wait_ge(made, 8)
            nc.gpsimd.affine_select(out=earlier[:], in_=earlier[:], compare_op=ALU.is_gt, fill=0.0, base=0,
                                    pattern=[[1, P]], channel_multiplier=-1).then_inc(made, 1)
            pool.wait_ge(slots_made, 2)
            pool.wait_ge(cleared, 16)
            for c in range(2):
                for t in range(ST):
                    nc.gpsimd.indirect_dma_start(
                        out=table, out_offset=bass.IndirectOffsetOnAxis(ap=slots[c][:, t:t + 1], axis=0),
                        in_=tokens[:, t:t + 1], in_offset=None).then_inc(scattered, 16)
            pool.wait_ge(scattered, 16 * 2 * ST)

        @block.scalar
        def _(act):
            act.wait_ge(shifted, 1)
            nc.scalar.activation(e_sum[:, :, :], e_sum[:, :, :], ACT.Exp).then_inc(exped, 1)
            act.wait_ge(shifted, 2)
            nc.scalar.activation(ratio[:], ratio[:], ACT.Exp).then_inc(exped, 1)

        @block.vector
        def _(dve):
            link = k.own("dve", dve)
            v = nc.vector
            dve.wait_ge(bias_in, 32)
            dve.wait_ge(made, 9)
            link(v.tensor_tensor(logits, logits, over_tiles(bias[:, :]), ALU.add))
            link(v.tensor_copy(groups[:, :, 0:G], logits[:, :, 0:G]))
            for t in range(ST):
                link(v.max(group_max[:, t, :], groups[:, t, :]))
                link(v.max_index(group_idx[:, t, :], group_max[:, t, :], groups[:, t, :]))
            v.tensor_tensor(e_sum[:, :, :], logits[:, :, 0:G], group_max[:, :, 0:1].broadcast_to([P, ST, G]),
                            ALU.subtract).then_inc(shifted, 1)
            link(v.tensor_copy(group_f[:], group_idx[:, :, 0:1].rearrange("p t o -> p (t o)")))
            dve.wait_ge(exped, 1)
            link(v.tensor_reduce(total[:], e_sum[:, :, :], AX, ALU.add))
            link(v.reciprocal(gate[:], total[:]))
            link(v.tensor_tensor(hot[0][:, :, :], group_of[:, :, :], over_experts(group_f[:]), ALU.is_equal))
            link(v.tensor_tensor(picked[:, :, :], logits[:, :, G:], hot[0][:, :, :], ALU.mult))
            link(v.tensor_scalar(hot[0][:, :, :], hot[0][:, :, :], -1.0, 3e38, ALU.add, ALU.mult))
            link(v.tensor_tensor(picked[:, :, :], picked[:, :, :], hot[0][:, :, :], ALU.add))
            for t in range(ST):
                link(v.max(top[:, t, :], picked[:, t, :]))
                link(v.max_index(top_idx[:, t, :], top[:, t, :], picked[:, t, :]))
            v.tensor_tensor(ratio[:], top[:, :, 1:2].rearrange("p t o -> p (t o)"),
                            top[:, :, 0:1].rearrange("p t o -> p (t o)"), ALU.subtract).then_inc(shifted, 1)
            for c in range(2):
                link(v.tensor_copy(choice[:, c, :], top_idx[:, :, c:c + 1].rearrange("p t o -> p (t o)")))
                link(v.tensor_tensor(hot[c][:, :, :], numbers[:, :, :], over_experts(choice[:, c, :]), ALU.is_equal))
            link(v.tensor_tensor(both[:, :, :], hot[0][:, :, :], hot[1][:, :, :], ALU.add))
            link(v.memset(before[:, 0, :], 0.0))
            for t in range(ST):
                link(v.tensor_tensor(before[:, t + 1, :], before[:, t, :], both[:, t, :], ALU.add))
            dve.sem_inc(hot_made, 1)
            dve.wait_ge(exped, 2)
            link(v.tensor_scalar(total[:], ratio[:], 1.0, None, ALU.add))
            link(v.reciprocal(total[:], total[:]))
            link(v.tensor_tensor(weights[:, 0, :], gate[:], total[:], ALU.mult))
            link(v.tensor_tensor(weights[:, 1, :], weights[:, 0, :], ratio[:], ALU.mult))
            dve.wait_ge(ranked, 1)
            link(v.tensor_tensor(over[:, :, :], counts[:, :].rearrange("p (e o) -> p e o", o=1).broadcast_to([P, E, ST]),
                                 steps[:, :, :], ALU.is_gt))
            link(v.tensor_reduce(n_blocks[:], over[:, :, :], AX, ALU.add))
            link(v.tensor_tensor_scan(ends[:], k.ones[:, 0:E], n_blocks[:], 0.0, ALU.mult, ALU.add))
            link(v.tensor_tensor(starts[:], ends[:], n_blocks[:], ALU.subtract))
            link(v.tensor_scalar(starts[:], starts[:], float(BLK), None, ALU.mult))
            link(v.tensor_tensor(place[:, :, :], ranks[:, :, :], over_tiles(starts[:, :]), ALU.add))
            for c in range(2):
                link(v.tensor_tensor(hot[c][:, :, :], hot[c][:, :, :], place[:, :, :], ALU.mult))
                link(v.tensor_reduce(slot_f[:, c, :], hot[c][:, :, :], AX, ALU.add))
                v.tensor_copy(slots[c][:], slot_f[:, c, :]).then_inc(slots_made, 1)
            link(v.tensor_tensor(passed[:, :, :], block_no[:, :, :],
                                 ends[:, :].rearrange("p (o e) -> p o e", o=1).broadcast_to([P, N_BLOCKS, E]), ALU.is_ge))
            link(v.tensor_reduce(expert_f[:], passed[:, :, :], AX, ALU.add))
            link(v.tensor_scalar(expert_f[:], expert_f[:], float(E - 1), None, ALU.min))
            link(v.tensor_copy(experts[:], expert_f[:]))
            dve.wait_ge(rows_turned, 1)
            link(v.tensor_copy(slot_of_block[:], turned[:]))

        @block.tensor
        def _(pe):
            pe.wait_ge(hot_made, 1)
            pe.wait_ge(made, 9)
            for t in range(ST):
                nc.tensor.matmul(ranks[:, t, :], earlier[:], both[:, t, :], start=True, stop=False)
                nc.tensor.matmul(ranks[:, t, :], k.ones[:], before[:, t, :], start=False, stop=True)
            nc.tensor.matmul(counts[:, :], k.ones[:], before[:, ST, :], start=True, stop=True).then_inc(ranked, 1)
            pe.wait_ge(rows_in, 16)
            nc.tensor.transpose(turned[:], rows[:], k.ident[0:N_BLOCKS, 0:N_BLOCKS]).then_inc(rows_turned, 1)
        k.chains["dve"].settle()


def run_experts(k, experts, slot_of_block):
    nc = k.nc
    with k.phase() as ctx:
        idx = [k.sb(f"moe_idx{b}", [P, 1], U32, ctx=ctx) for b in range(2)]
        rows = [k.sb(f"moe_rows{b}", [P, D], ctx=ctx) for b in range(2)]
        xt = [k.sb(f"moe_xt{b}", [P, KD, BLK], ctx=ctx) for b in range(2)]
        wgu = [k.sb(f"moe_wgu{b}", [P, 2, KD, FF], ctx=ctx) for b in range(2)]
        wd = [k.sb(f"moe_wd{b}", [P, FF // P, D], ctx=ctx) for b in range(2)]
        silu = [k.sb(f"moe_silu{b}", [P, 2, BLK], ctx=ctx) for b in range(2)]
        hidden = [k.sb(f"moe_hidden{b}", [P, 2, BLK], ctx=ctx) for b in range(2)]
        y = [k.sb(f"moe_y{b}", [P, D], ctx=ctx) for b in range(2)]
        turned = k.ps("moe_turned", [P, KD, BLK], ctx)
        up = [k.ps(f"moe_up{b}", [P, 2, 2, BLK], ctx) for b in range(2)]
        down = [k.ps(f"moe_down{b}", [P, D], ctx) for b in range(2)]
        (up_in0, up_in1, down_in0, down_in1, indexed, turns, x_ready, ups, silus, hiddens, downs, y_ready, stored0,
         stored1, passed) = k.sems("moe", "up_in0 up_in1 down_in0 down_in1 indexed turns x_ready ups silus hiddens "
                                   "downs y_ready stored0 stored1 passed")
        gathered = (k.soft["rows_gathered0"], k.soft["rows_gathered1"])
        up_in, down_in, stored = (up_in0, up_in1), (down_in0, down_in1), (stored0, stored1)
        block = ctx.enter_context(nc.Block())
        rounds = N_BLOCKS // 4
        gate_w = k.dram["w_expert_gate"][0].rearrange("e (c p) f -> p e c f", p=P)
        up_w = k.dram["w_expert_up"][0].rearrange("e (c p) f -> p e c f", p=P)
        down_w = k.dram["w_expert_down"][0].rearrange("e (c p) d -> p e c d", p=P)
        y_out = k.scratch["expert_rows"].rearrange("(n s) d -> s n d", s=BLK)
        ffn_gain = k.gain("norm_ffn_g")

        @block.sync
        def _(sp):
            with sp.Fori(0, rounds) as i:
                for n in range(4):
                    b, g = n % 2, 4 * i + n
                    e = sp.value_load(experts[0:1, bass.ds(g, 1)], min_val=0, max_val=EXPERTS - 1)
                    sp.wait_ge(ups, g + 1)
                    sp.dma_start(wgu[b][:, 0, :, :], gate_w[:, bass.ds(e, 1), :, :].rearrange("p e c f -> p (e c) f")
                                 ).then_inc(up_in[b], 16)
                    sp.dma_start(wgu[b][:, 1, :, :], up_w[:, bass.ds(e, 1), :, :].rearrange("p e c f -> p (e c) f")
                                 ).then_inc(up_in[b], 16)
                    sp.wait_ge(downs, g + 1)
                    sp.dma_start(wd[b][:, :, :], down_w[:, bass.ds(e, 1), :, :].rearrange("p e c d -> p (e c) d")
                                 ).then_inc(down_in[b], 16)

        @block.gpsimd
        def _(pool):
            with pool.Fori(0, rounds) as i:
                for n in range(4):
                    b, g = n % 2, 4 * i + n
                    pool.wait_ge(turns, g + 1)
                    nc.gpsimd.tensor_copy(idx[b][:], slot_of_block[:, bass.ds(g, 1)]).then_inc(indexed, 1)
                    pool.wait_ge(indexed, g + 1)
                    pool.sem_inc(passed, 1)
                    nc.gpsimd.indirect_dma_start(out=rows[b][:], out_offset=None, in_=k.scratch["ffn_rows"],
                                                 in_offset=bass.IndirectOffsetOnAxis(ap=idx[b][:, 0:1], axis=0)
                                                 ).then_inc(gathered[b], 16)

        @block.tensor
        def _(pe):
            pe.sem_inc(downs, 2)
            pe.sem_inc(turns, 2)
            pe.sem_inc(ups, 2)
            pe.sem_inc(x_ready, 1)

            def turn_rows(i, n):
                pe.wait_ge(gathered[n % 2], 16 * (2 * i + n // 2) + 16)
                pe.wait_ge(x_ready, 4 * i + n + 1)
                for c in range(KD):
                    last = nc.tensor.transpose(turned[:, c, :], rows[n % 2][:, c * P:(c + 1) * P], k.ident[:])
                last.then_inc(turns, 1)

            def round_(i, more):
                for n in range(4):
                    b, g = n % 2, 4 * i + n
                    pe.wait_ge(up_in[b], 32 * (2 * i + n // 2) + 32)
                    pe.wait_ge(x_ready, g + 1 + 1)
                    pe.wait_ge(hiddens, g + 1)
                    for m in range(2):
                        for f in range(2):
                            for c in range(KD):
                                last = nc.tensor.matmul(up[b][:, m, f, :], wgu[b][:, m, c, f * P:(f + 1) * P],
                                                        xt[b][:, c, :], start=(c == 0), stop=(c == KD - 1))
                    last.then_inc(ups, 1)
                    if n < 3 or more:
                        turn_rows(i, n + 1)
                    pe.wait_ge(down_in[b], 16 * (2 * i + n // 2) + 16)
                    pe.wait_ge(hiddens, g + 1 + 2)
                    pe.wait_ge(y_ready, g + 1)
                    for h in range(2):
                        for c in range(FF // P):
                            last = nc.tensor.matmul(down[b][:, h * HALF:(h + 1) * HALF], hidden[b][:, c, :],
                                                    wd[b][:, c, h * HALF:(h + 1) * HALF],
                                                    start=(c == 0), stop=(c == FF // P - 1))
                    last.then_inc(downs, 1)
            turn_rows(0, 0)
            with pe.Fori(0, rounds - 1) as i:
                round_(i, True)
            round_(rounds - 1, False)

        @block.vector
        def _(dve):
            dve.sem_inc(hiddens, 2)

            def apply_gain(i, n):
                g = 4 * i + n
                dve.wait_ge(turns, g + 1 + 2)
                dve.wait_ge(ups, g + 1)
                nc.vector.tensor_tensor(xt[n % 2][:, :, :], turned[:, :, :],
                                        ffn_gain.rearrange("p (c o) -> p c o", o=1).broadcast_to([P, KD, BLK]),
                                        ALU.mult).then_inc(x_ready, 1)

            def round_(i, more):
                for n in range(4):
                    b, g = n % 2, 4 * i + n
                    dve.wait_ge(silus, g + 1)
                    dve.wait_ge(downs, g + 1)
                    nc.vector.tensor_tensor(hidden[b][:, :, :], up[b][:, 1, :, :], silu[b][:, :, :],
                                            ALU.mult).then_inc(hiddens, 1)
                    if n < 3 or more:
                        apply_gain(i, n + 1)
            apply_gain(0, 0)
            with dve.Fori(0, rounds - 1) as i:
                round_(i, True)
            round_(rounds - 1, False)

        @block.scalar
        def _(act):
            act.sem_inc(stored0, 16)
            act.sem_inc(stored1, 16)
            act.sem_inc(y_ready, 2)
            with act.Fori(0, rounds) as i:
                for n in range(4):
                    b, g = n % 2, 4 * i + n
                    act.wait_ge(ups, g + 1 + 2)
                    act.wait_ge(hiddens, g + 1)
                    nc.scalar.activation(silu[b][:, :, :], up[b][:, 0, :, :], ACT.Silu).then_inc(silus, 1)
                    act.wait_ge(downs, g + 1 + 2)
                    act.wait_ge(stored[b], 16 * (2 * i + n // 2) + 16)
                    nc.scalar.activation(y[b][:], down[b][:], ACT.Copy).then_inc(y_ready, 1)
                    act.wait_ge(y_ready, g + 1 + 2)
                    act.dma_start(y_out[:, bass.ds(g, 1), :].rearrange("s n d -> s (n d)"),
                                  y[b][:]).then_inc(stored[b], 16)
            act.wait_ge(stored0, 16 * 2 * rounds + 16)
            act.wait_ge(stored1, 16 * 2 * rounds + 16)


def combine(k, slots, weights):
    nc = k.nc
    with k.phase() as ctx:
        idx = [[k.sb(f"comb_idx{c}{b}", [P, 1], U32, ctx=ctx) for b in range(2)] for c in range(2)]
        rows = [[k.sb(f"comb_rows{c}{b}", [P, D], ctx=ctx) for b in range(2)] for c in range(2)]
        indexed, added, passed = k.sems("comb", "indexed added passed")
        gathered = (k.soft["outputs_gathered0"], k.soft["outputs_gathered1"])
        block = ctx.enter_context(nc.Block())

        @block.gpsimd
        def _(pool):
            with pool.Fori(0, ST // 2) as i:
                for b in range(2):
                    pool.wait_ge(added, 4 * i + 1)
                    for c in range(2):
                        nc.gpsimd.tensor_copy(idx[c][b][:], slots[c][:, bass.ds(2 * i + b, 1)]).then_inc(indexed, 1)
                        pool.wait_ge(indexed, 2 * (2 * i + b) + c + 1)
                        pool.sem_inc(passed, 1)
                        nc.gpsimd.indirect_dma_start(out=rows[c][b][:], out_offset=None, in_=k.scratch["expert_rows"],
                                                     in_offset=bass.IndirectOffsetOnAxis(ap=idx[c][b][:, 0:1], axis=0)
                                                     ).then_inc(gathered[b], 16)

        @block.vector
        def _(dve):
            dve.sem_inc(added, 1)
            with dve.Fori(0, ST // 2) as i:
                for b in range(2):
                    dve.wait_ge(gathered[b], 32 * i + 32)
                    x = row_of(k.X, 2 * i + b)
                    for c in range(2):
                        nc.vector.scalar_tensor_tensor(out=x, in0=rows[c][b][:], scalar=weights[:, c, bass.ds(2 * i + b, 1)],
                                                       in1=x, op0=ALU.mult, op1=ALU.add).then_inc(added, 1)
                        dve.wait_ge(added, 2 * (2 * i + b) + c + 1 + 1)


def expert_layer(k):
    nc = k.nc
    with ExitStack() as ctx:
        logits = k.sb("logits", [P, ST, GROUPS + EXPERTS], ctx=ctx)
        slots = [k.sb(f"slots{c}", [P, ST], U32, ctx=ctx) for c in range(2)]
        weights = k.sb("route_w", [P, 2, ST], ctx=ctx)
        experts = k.sb("experts", [P, N_BLOCKS], I32, ctx=ctx)
        slot_of_block = k.sb("slot_of_block", [P, N_BLOCKS], U32, ctx=ctx)
        w_g = k.dram["w_group_router"][0].rearrange("(c p) n -> p c n", p=P)
        w_e = k.dram["w_expert_router"][0].rearrange("(c p) n -> p c n", p=P)
        with ExitStack() as inner:
            H = k.sb("ffn_h", [P, KD, S], ctx=inner)
            norm_turn(k, "ffn_norm", k.X, ST, k.gain("norm_ffn_g"), H, rows_out=k.scratch["ffn_rows"])
            project_tokens(k, "router", [(w_g, 0, GROUPS), (w_e, GROUPS, EXPERTS)], GROUPS + EXPERTS, H, KD, logits)
        route(k, logits[:, :, :], slots, weights, experts, slot_of_block)
        run_experts(k, experts, slot_of_block)
        combine(k, slots, weights)


def final_norm(k):
    nc = k.nc
    with k.phase() as ctx:
        gain = k.sb("final_gain", [P, D], ctx=ctx)
        junk = [k.sb(f"final_junk{b}", [P, D], ctx=ctx) for b in range(2)]
        gain_in, even, odd, mean_made, root_made, normed = k.sems("final", "gain_in even odd mean_made root_made normed")
        block = ctx.enter_context(nc.Block())

        @block.sync
        def _(sp):
            sp.dma_start(gain[:], k.dram["norm_final_g"].rearrange("(o d) -> o d", o=1).broadcast_to([P, D])
                         ).then_inc(gain_in, 16)

        @block.scalar
        def _(act):
            for t in range(0, ST, 2):
                if t:
                    act.wait_ge(even, t // 2)
                nc.scalar.activation(junk[0][:], k.X[:, t, :], ACT.Square, accum_out=k.ssq[:, t:t + 1]).then_inc(even, 1)
            act.wait_ge(mean_made, 1)
            nc.scalar.activation(k.root[:], k.mean[:], ACT.Sqrt).then_inc(root_made, 1)

        @block.vector
        def _(dve):
            link = k.own("dve", dve)
            for t in range(1, ST, 2):
                if t > 1:
                    dve.wait_ge(odd, t // 2)
                nc.vector.tensor_tensor_reduce(out=junk[1][:], in0=k.X[:, t, :], in1=k.X[:, t, :], scale=1.0, scalar=0.0,
                                               op0=ALU.mult, op1=ALU.add, accum_out=k.ssq[:, t:t + 1]).then_inc(odd, 1)
            dve.wait_ge(odd, ST // 2)
            dve.wait_ge(even, ST // 2)
            nc.vector.tensor_scalar(k.mean[:], k.ssq[:], 1.0 / D, EPS, ALU.mult, ALU.add).then_inc(mean_made, 1)
            dve.wait_ge(root_made, 1)
            link(nc.vector.reciprocal(k.rstd[:], k.root[:]))
            dve.wait_ge(gain_in, 16)
            with dve.Fori(0, ST) as t:
                nc.vector.scalar_tensor_tensor(out=row_of(k.X, t), in0=row_of(k.X, t), scalar=k.rstd[:, bass.ds(t, 1)],
                                               in1=gain[:], op0=ALU.mult, op1=ALU.mult).then_inc(normed, 1)
        k.chains["dve"].settle()


def gate_rows(k, vm, HT, spare):
    nc = k.nc
    H = 4
    with k.phase() as ctx:
        w = k.sb("gr_w", [P, KD, 96], ctx=ctx)
        w_pair = pair(k, "gr_ws", [P, KD, 96], ctx)
        bias = k.sb("gr_bias", [H, 3], ctx=ctx)
        rows = [tile[0:H, c, :] for tile, count in spare for c in range(count)]
        raw, logs, sums = rows[0:3], rows[3:5], rows[5:7]
        ones = k.sb("gr_ones", [H, S], ctx=ctx)
        a, top, floor, neg = (k.sb(f"gr_{n}", [H, S], ctx=ctx) for n in ("a", "top", "floor", "neg"))
        acc = k.ps("gr_acc", [P, S], ctx)
        cols = k.ps("gr_cols", [P, 2, ST, H], ctx)
        w_in, w_split, bias_in, cleared, products, copied, absed, logged, rows_made, turned, stored = k.sems(
            "gr", "w_in w_split bias_in cleared products copied absed logged rows_made turned stored")
        block = ctx.enter_context(nc.Block())
        w_view = k.dram["w_in_2"][0].rearrange("(c p) n -> p c n", p=P)

        @block.sync
        def _(sp):
            sp.wait_ge(cleared, 2)
            for n, col in enumerate((C_FF, C_MI, C_MI + H)):
                sp.dma_start(w[:, :, 32 * n:32 * n + H], w_view[:, :, col:col + H]).then_inc(w_in, 16)
            for n, name in enumerate(("fox_f_bias_2", "mlstm_i_bias_2", "mlstm_f_bias_2")):
                sp.dma_start(bias[:, n:n + 1], k.dram[name].rearrange("l h -> h l")).then_inc(bias_in, 16)
            fox_q = k.scratch["fox_q"].rearrange("(h n) s -> h n s", n=2)
            fox_k = k.scratch["fox_k"].rearrange("(h n) s -> h n s", n=2)
            sp.dma_start(fox_q[:, 0, :], ones[:]).then_inc(stored, 16)
            sp.dma_start(fox_k[:, 1, :], ones[:]).then_inc(stored, 16)
            sp.wait_ge(rows_made, 1)
            sp.dma_start(fox_q[:, 1, :], sums[0][:]).then_inc(stored, 16)
            sp.wait_ge(rows_made, 2)
            sp.dma_start(fox_k[:, 0, :], neg[:]).then_inc(stored, 16)
            sp.wait_ge(rows_made, 4)
            sp.dma_start(k.scratch["mlstm_row"], top[:]).then_inc(stored, 16)
            sp.wait_ge(stored, 16 * 5)

        @block.gpsimd
        def _(pool):
            nc.gpsimd.memset(w[:, :, :], 0.0).then_inc(cleared, 1)
            nc.gpsimd.memset(ones[:], 1.0).then_inc(cleared, 1)
            nc.gpsimd.memset(vm[:, :, :, HD:HD + 1], 1.0).then_inc(cleared, 1)
            pool.wait_ge(w_in, 48)
            nc.gpsimd.tensor_copy(w_pair[0][:], w[:]).then_inc(w_split, 1)
            pool.wait_ge(w_split, 1)
            nc.gpsimd.tensor_tensor(w_pair[1][:], w[:], w_pair[0][:], ALU.subtract).then_inc(w_split, 1)

        @block.tensor
        def _(pe):
            pe.wait_ge(w_split, 2)
            for c in range(KD):
                for h in range(2):
                    last = add_product(nc, acc[0:96, h * HALF:(h + 1) * HALF], part(w_pair, slice(None), c, slice(None)),
                                       part(HT, slice(None), c, slice(h * HALF, (h + 1) * HALF)), c == 0, c == KD - 1)
            last.then_inc(products, 1)
            pe.wait_ge(rows_made, 5)
            for n, row in enumerate((a, floor)):
                for t in range(ST):
                    last = nc.tensor.transpose(cols[:, n, t, :], row[:, t * P:(t + 1) * P], k.ident[0:H, 0:H])
            last.then_inc(turned, 1)

        @block.scalar
        def _(act):
            act.wait_ge(products, 1)
            for n in range(3):
                nc.scalar.activation(raw[n][:], acc[32 * n:32 * n + H, :], ACT.Copy).then_inc(copied, 1)
            for n, x in enumerate((raw[0], raw[2])):
                act.wait_ge(absed, n + 1)
                nc.scalar.activation(logs[n][:], x[:], ACT.Abs).then_inc(logged, 1)
                act.wait_ge(logged, 3 * n + 1)
                nc.scalar.activation(logs[n][:], logs[n][:], ACT.Exp, scale=-1.0).then_inc(logged, 1)
                act.wait_ge(logged, 3 * n + 2)
                nc.scalar.activation(logs[n][:], logs[n][:], ACT.Ln, bias=1.0).then_inc(logged, 1)
            act.wait_ge(turned, 1)
            nc.scalar.activation(k.a_col[:, :, :], cols[:, 0, :, :], ACT.Copy)
            nc.scalar.activation(k.floor_col[:, :, :], cols[:, 1, :, :], ACT.Exp, scale=-1.0)

        @block.vector
        def _(dve):
            link = k.own("dve", dve)
            v = nc.vector
            dve.wait_ge(bias_in, 48)
            dve.wait_ge(copied, 3)
            dve.wait_ge(cleared, 3)
            for n in (0, 2):
                v.tensor_scalar(raw[n][:], raw[n][:], bias[:, n:n + 1], None, ALU.add).then_inc(absed, 1)
            link(v.tensor_scalar(raw[1][:], raw[1][:], bias[:, 1:2], None, ALU.add))
            for n, x in enumerate((raw[0], raw[2])):
                dve.wait_ge(logged, 3 * n + 3)
                link(v.scalar_tensor_tensor(out=logs[n][:], in0=x[:], scalar=0.0, in1=logs[n][:],
                                            op0=ALU.min, op1=ALU.subtract))
                ins = v.tensor_tensor_scan(sums[n][:], ones[:], logs[n][:], 0.0, ALU.mult, ALU.add)
                if n == 0:
                    ins.then_inc(rows_made, 1)
                    dve.wait_ge(rows_made, 1)
                    v.tensor_scalar(neg[:], sums[0][:], -1.0, None, ALU.mult).then_inc(rows_made, 1)
                else:
                    link(ins)
            link(v.tensor_tensor(a[:], raw[1][:], sums[1][:], ALU.subtract))
            link(v.tensor_tensor_scan(top[:], ones[:], a[:], 0.0, ALU.mult, ALU.max))
            v.tensor_tensor(floor[:], top[:], sums[1][:], ALU.add).then_inc(rows_made, 1)
            dve.wait_ge(rows_made, 3)
            v.tensor_scalar(top[:], top[:], -1.0, None, ALU.mult).then_inc(rows_made, 1)
            dve.wait_ge(rows_made, 4)
            dve.sem_inc(rows_made, 1)
        k.chains["dve"].settle()


def matrix_lstm(k, V, out):
    nc = k.nc
    H = 4
    with k.phase() as ctx:
        q = [k.sb(f"ml_q{b}", [HD, S], ctx=ctx) for b in range(2)]
        kk = [k.sb(f"ml_k{b}", [HD, S], ctx=ctx) for b in range(2)]
        row = [k.sb(f"ml_row{b}", [P, S], ctx=ctx) for b in range(2)]
        a_col = [k.sb(f"ml_a{b}", [P, ST], ctx=ctx) for b in range(2)]
        decay = [k.sb(f"ml_decay{b}", [P, S], ctx=ctx) for b in range(2)]
        w = [[k.sb(f"ml_w{b}{t}", [P, S - t * P], ctx=ctx) for t in range(ST)] for b in range(2)]
        stats = [k.sb(f"ml_stats{b}", [P, ST, 2], ctx=ctx) for b in range(2)]
        values = [k.sb(f"ml_v{b}", [P, ST, HD + 1], ctx=ctx) for b in range(2)]
        before_mask = k.sb("ml_mask", [P, P], ctx=ctx)
        scores = [k.ps(f"ml_scores{b}", [P, S], ctx) for b in range(2)]
        acc = [k.ps(f"ml_acc{b}", [P, 2, HALF], ctx) for b in range(2)]
        (head_in0, head_in1, mask_made, a_ready, masked, decays, products, weighted, sums_made, done) = k.sems(
            "ml", "head_in0 head_in1 mask_made a_ready masked decays products weighted sums_made done")
        head_in = (head_in0, head_in1)
        block = ctx.enter_context(nc.Block())
        rounds = H // 2
        plain = k.scratch["plain"]
        q_row, k_row = C_MQ - C_CU, C_MQ + H * HD - C_CU

        def at(b, t):
            return acc[b][:, t // 4, (t % 4) * (HD + 1):(t % 4 + 1) * (HD + 1)]

        @block.sync
        def _(sp):
            with sp.Fori(0, rounds) as i:
                for b in range(2):
                    sp.wait_ge(done, 2 * i + 1)
                    h = i * 2 + b
                    sp.dma_start(q[b][:], plain[bass.ds(h * HD + q_row, HD), :]).then_inc(head_in[b], 16)
                    sp.dma_start(kk[b][:], plain[bass.ds(h * HD + k_row, HD), :]).then_inc(head_in[b], 16)
                    sp.dma_start(row[b][:], k.scratch["mlstm_row"][bass.ds(h, 1), :].broadcast_to([P, S])
                                 ).then_inc(head_in[b], 16)

        @block.gpsimd
        def _(pool):
            nc.gpsimd.memset(before_mask[:], 0.0).then_inc(mask_made, 1)
            pool.wait_ge(mask_made, 1)
            nc.gpsimd.affine_select(out=before_mask[:], in_=before_mask[:], compare_op=ALU.is_ge, fill=NEG, base=0,
                                    pattern=[[1, P]], channel_multiplier=-1).then_inc(mask_made, 1)
            with pool.Fori(0, rounds) as i:
                for b in range(2):
                    pool.wait_ge(done, 2 * i + 1)
                    h = i * 2 + b
                    nc.gpsimd.tensor_copy(a_col[b][:], k.a_col[:, :, bass.ds(h, 1)].rearrange("p t h -> p (t h)")
                                          ).then_inc(a_ready, 1)
                    nc.gpsimd.tensor_copy(values[b][:, :, :], V[:, :, bass.ds(h, 1), :].rearrange(
                        "p t h n -> p (t h) n")).then_inc(a_ready, 1)

        @block.tensor
        def _(pe):
            pe.sem_inc(sums_made, 1)
            with pe.Fori(0, rounds) as i:
                for b in range(2):
                    pe.wait_ge(head_in[b], 48 * i + 48)
                    for t in range(ST):
                        g = (i * 2 + b) * ST + t
                        pe.wait_ge(weighted, g + 1)
                        width = S - t * P
                        for c in range(0, width, HALF):
                            n = min(HALF, width - c)
                            last = nc.tensor.matmul(scores[t % 2][:, c:c + n], kk[b][:, t * P:(t + 1) * P],
                                                    q[b][:, t * P + c:t * P + c + n], start=True, stop=True)
                        last.then_inc(products, 1)
                for b in range(2):
                    pe.wait_ge(weighted, (i * 2 + b + 1) * ST + 2)
                    pe.wait_ge(a_ready, (i * 2 + b) * 2 + 2)
                    pe.wait_ge(done, 2 * i + 1)
                    for t in range(ST):
                        for c in range(t + 1):
                            last = nc.tensor.matmul(at(b, t), w[b][c][:, (t - c) * P:(t - c + 1) * P],
                                                    values[b][:, c, :], start=(c == 0), stop=(c == t))
                    last.then_inc(sums_made, 1)

        @block.scalar
        def _(act):
            with act.Fori(0, rounds) as i:
                for b in range(2):
                    act.wait_ge(head_in[b], 48 * i + 48)
                    act.wait_ge(a_ready, (i * 2 + b) * 2 + 2)
                    for t in range(ST):
                        g = (i * 2 + b) * ST + t
                        act.wait_ge(weighted, g + 1)
                        act.wait_ge(masked, g + 1)
                        nc.scalar.activation(decay[t % 2][:, 0:P], decay[t % 2][:, 0:P], ACT.Exp,
                                             bias=a_col[b][:, t:t + 1]).then_inc(decays, 1)
                        if t < ST - 1:
                            nc.scalar.activation(decay[t % 2][:, P:S - t * P], row[b][:, (t + 1) * P:S], ACT.Exp,
                                                 bias=a_col[b][:, t:t + 1]).then_inc(decays, 1)

        @block.vector
        def _(dve):
            dve.sem_inc(done, 1)
            link = k.own("dve", dve)
            chain = k.chains["dve"]
            dve.sem_inc(weighted, 2)
            dve.wait_ge(mask_made, 2)
            per = 2 * ST - 1
            with dve.Fori(0, rounds) as i:
                chain.enter(i, 2 * 3)
                for b in range(2):
                    dve.wait_ge(head_in[b], 48 * i + 48)
                    for t in range(ST + 1):
                        g = (i * 2 + b) * ST + t
                        if t < ST:
                            dve.wait_ge(weighted, g + 1)
                            nc.vector.tensor_tensor(decay[t % 2][:, 0:P], row[b][:, t * P:(t + 1) * P], before_mask[:],
                                                    ALU.add).then_inc(masked, 1)
                        if t:
                            dve.wait_ge(products, g)
                            dve.wait_ge(decays, (i * 2 + b) * per + min(2 * t, per))
                            dve.wait_ge(sums_made, 2 * i + 1)
                            width = S - (t - 1) * P
                            nc.vector.scalar_tensor_tensor(out=w[b][t - 1][:], in0=scores[(t - 1) % 2][:, 0:width],
                                                           scalar=HD ** -0.5, in1=decay[(t - 1) % 2][:, 0:width],
                                                           op0=ALU.mult, op1=ALU.mult).then_inc(weighted, 1)
                for b in range(2):
                    dve.wait_ge(sums_made, i * 2 + b + 1 + 1)
                    h = i * 2 + b
                    st = stats[b]
                    den = acc[b][:, :, 0:4 * (HD + 1)].rearrange("p a (t n) -> p a t n", n=HD + 1)[:, :, :, HD:HD + 1]
                    den = den.rearrange("p a t n -> p a (t n)")
                    one, two = (st[:, :, n:n + 1].rearrange("p (a t) n -> p a (t n)", a=2) for n in range(2))
                    link(nc.vector.tensor_copy(one, den))
                    link(nc.vector.scalar_tensor_tensor(
                        out=st[:, :, 1:2], in0=st[:, :, 0:1], scalar=-1.0, in1=k.floor_col[:, :, bass.ds(h, 1)],
                        op0=ALU.mult, op1=ALU.max))
                    link(nc.vector.tensor_tensor(st[:, :, 0:1], st[:, :, 0:1], st[:, :, 1:2], ALU.max))
                    nc.vector.reciprocal(st[:, :, 1:2], st[:, :, 0:1]).then_inc(mask_made, 1)
                    dve.wait_ge(mask_made, 2 + 5 * h + 1)
                    for t in range(ST):
                        ins = nc.vector.tensor_scalar(out[:, t, bass.ds(h * HD, HD)], at(b, t)[:, 0:HD], st[:, t, 1:2],
                                                      None, ALU.mult)
                    ins.then_inc(mask_made, 4)
                    dve.wait_ge(mask_made, 2 + 5 * h + 5)
                    dve.sem_inc(done, 1)
                chain.leave(rounds)


def short_conv(k, conv_out, ml_rows):
    nc = k.nc
    CH = 2
    with k.phase() as ctx:
        u, bg, cg, mo = (k.sb(f"conv_{n}", [P, CH, S], ctx=ctx) for n in ("u", "b", "c", "mo"))
        loaded, gated, chain_c = k.sems("conv", "loaded gated chain_c")
        block = ctx.enter_context(nc.Block())
        plain = k.scratch["plain"]

        @block.sync
        def _(sp):
            for n, tile in enumerate((u, bg, cg)):
                sp.dma_start(tile[:, :, :], plain[n * CH * P:(n + 1) * CH * P, :].rearrange("(c p) s -> p c s", p=P)
                             ).then_inc(loaded, 16)
            sp.dma_start(mo[:, :, :], k.scratch["mo"].rearrange("(c p) s -> p c s", p=P)).then_inc(gated, 16)

        @block.scalar
        def _(act):
            act.wait_ge(gated, 16)
            nc.scalar.activation(mo[:, :, :], mo[:, :, :], ACT.Sigmoid).then_inc(gated, 1)

        @block.vector
        def _(dve):
            link = k.own("dve", dve)
            dve.wait_ge(loaded, 48)
            link(nc.vector.tensor_tensor(u[:, :, :], u[:, :, :], cg[:, :, :], ALU.mult))
            for c in range(CH):
                taps = [k.gain("conv_w_2", n * CH + c, 1) for n in range(3)]
                link(nc.vector.tensor_scalar(conv_out[:, c, :], u[:, c, :], taps[2], None, ALU.mult))
                for back, tap in ((1, taps[1]), (2, taps[0])):
                    link(nc.vector.scalar_tensor_tensor(out=conv_out[:, c, back:], in0=u[:, c, 0:S - back], scalar=tap,
                                                        in1=conv_out[:, c, back:], op0=ALU.mult, op1=ALU.add))
            link(nc.vector.tensor_tensor(conv_out[:, :, :], conv_out[:, :, :], bg[:, :, :], ALU.mult))
            dve.wait_ge(gated, 17)
            link(nc.vector.tensor_tensor(ml_rows[:, :, :], ml_rows[:, :, :], mo[:, :, :], ALU.mult))
        k.chains["dve"].settle()


def t5_buckets(n):
    exact, most, buckets = 16, 128, 32
    out = []
    for d in range(n):
        if d < exact:
            out.append(d)
        else:
            large = exact + int(np.log(d / exact) / np.log(most / exact) * (buckets - exact))
            out.append(min(large, buckets - 1))
    return out


def window_bias(k, biases, sinks):
    nc = k.nc
    H, B, W2 = 8, 32, 3 * P
    with k.phase() as ctx:
        rel = k.sb("wb_rel", [B, H], ctx=ctx)
        hot = k.sb("wb_hot", [B, W2], ctx=ctx)
        index = k.sb("wb_index", [B, 1], ctx=ctx)
        bucket = k.sb("wb_bucket", [B, W2], ctx=ctx)
        rows = k.sb("wb_rows", [H, W2], ctx=ctx)
        flipped = k.sb("wb_flipped", [P, H, 2 * P], ctx=ctx)
        flip = k.sb("wb_flip", [P, P], ctx=ctx)
        acc = k.ps("wb_acc", [H, W2], ctx)
        turned = k.ps("wb_turned", [P, H, 2 * P], ctx)
        rel_in, bucketed, made, hot_made, product, rows_made, stored, loaded, upright = k.sems(
            "wb", "rel_in bucketed made hot_made product rows_made stored loaded upright")
        block = ctx.enter_context(nc.Block())
        buckets = t5_buckets(WINDOW)
        runs = []
        for j in range(P, 2 * P):
            value = buckets[2 * P - 1 - j]
            if runs and runs[-1][2] == value:
                runs[-1][1] = j + 1
            else:
                runs.append([j, j + 1, value])

        @block.sync
        def _(sp):
            sp.dma_start(rel[:], k.dram["rel_bias_2"]).then_inc(rel_in, 16)
            sp.dma_start(sinks[:], k.dram["swa_sinks_2"].broadcast_to([P, H])).then_inc(loaded, 16)
            sp.wait_ge(rows_made, 3)
            sp.dma_start(k.scratch["window_rows"], rows[:]).then_inc(stored, 16)
            sp.wait_ge(stored, 16)
            view = k.scratch["window_rows"]
            for h in range(H):
                skewed = bass.AP(view.tensor, view.offset + h * W2, [[1, P], [1, 2 * P]])
                sp.dma_start(flipped[:, h, :], skewed).then_inc(loaded, 16)

        @block.gpsimd
        def _(pool):
            nc.gpsimd.memset(bucket[:], -1.0).then_inc(made, 1)
            nc.gpsimd.iota(index[:], [[0, 1]], 0, 1, allow_small_or_imprecise_dtypes=True).then_inc(made, 1)
            nc.gpsimd.memset(flip[:], 0.0).then_inc(made, 1)
            pool.wait_ge(made, 3)
            nc.gpsimd.affine_select(out=flip[:], in_=flip[:], compare_op=ALU.not_equal, fill=1.0, base=1 - P,
                                    pattern=[[1, P]], channel_multiplier=1).then_inc(made, 1)
            for at, to, value in runs:
                nc.gpsimd.memset(bucket[:, at:to], float(value)).then_inc(bucketed, 1)

        @block.vector
        def _(dve):
            dve.wait_ge(bucketed, len(runs))
            nc.vector.tensor_scalar(hot[:], bucket[:], index[:], None, ALU.is_equal).then_inc(hot_made, 1)
            nc.vector.memset(rows[:, 0:P], NEG).then_inc(rows_made, 1)
            nc.vector.memset(rows[:, 2 * P:], NEG).then_inc(rows_made, 1)
            dve.wait_ge(product, 1)
            nc.vector.tensor_copy(rows[:, P:2 * P], acc[:, P:2 * P]).then_inc(rows_made, 1)
            dve.wait_ge(upright, 1)
            nc.vector.tensor_copy(biases[:, :, :], turned[:, :, :])

        @block.tensor
        def _(pe):
            pe.wait_ge(hot_made, 1)
            pe.wait_ge(rel_in, 16)
            nc.tensor.matmul(acc[:], rel[:], hot[:], start=True, stop=True).then_inc(product, 1)
            pe.wait_ge(made, 4)
            pe.wait_ge(loaded, 16 * (H + 1))
            for h in range(0, H, 2):
                last = nc.tensor.matmul(turned[:, h:h + 2, :], flip[:], flipped[:, h:h + 2, :], start=True, stop=True)
            last.then_inc(upright, 1)


def gated_merge(k, branches, merged, HT):
    nc = k.nc
    NB = len(branches)
    with k.phase() as ctx:
        wg_raw = [k.sb(f"gm_wg{b}", [P, KD, P], ctx=ctx) for b in range(2)]
        wg = [pair(k, f"gm_wgs{b}", [P, KD, P], ctx) for b in range(2)]
        wo = [k.sb(f"gm_wo{b}", [P, 4, P], ctx=ctx) for b in range(2)]
        gate = k.sb("gm_gate", [P, S], ctx=ctx)
        gated_part = k.sb("gm_part", [P, S], ctx=ctx)
        gate_ps = [k.ps(f"gm_gate_ps{b}", [P, S], ctx) for b in range(2)]
        out_ps = [k.ps(f"gm_out_ps{b}", [P, S], ctx) for b in range(2)]
        wg_in0, wg_in1, wo_in0, wo_in1, split, passed, products, gates, gated, totals = k.sems(
            "gm", "wg_in0 wg_in1 wo_in0 wo_in1 split passed products gates gated totals")
        wg_in, wo_in = (wg_in0, wg_in1), (wo_in0, wo_in1)
        block = ctx.enter_context(nc.Block())
        w_view = k.dram["w_in_2"][0].rearrange("(c p) n -> p c n", p=P)
        outs = [k.dram[name][0].rearrange("(c p) n -> p c n", p=P) for name, _, _ in branches]

        @block.sync
        def _(sp):
            with sp.Fori(0, KD) as i:
                for n in range(NB):
                    sp.wait_ge(split, 2 * (i * NB + n) + 2)
                    col = bass.ds(i * P + C_GATES + n * D, P)
                    sp.dma_start(wg_raw[n % 2][:, :, :], w_view[:, :, col]).then_inc(wg_in[n % 2], 16)
                    sp.wait_ge(products, i * NB + n + 1)
                    sp.sem_inc(passed, 1)
                    sp.dma_start(wo[n % 2][:, 0:branches[n][2], :], outs[n][:, :, bass.ds(i * P, P)]).then_inc(wo_in[n % 2], 16)

        @block.gpsimd
        def _(pool):
            pool.sem_inc(split, 4)
            with pool.Fori(0, KD) as i:
                for n in range(NB):
                    split_weights(nc, pool, i * NB + n, n % 2, (wg_in[n % 2], 16 * (i * (NB // 2) + n // 2) + 16), wg_raw, wg,
                                  products, split, passed)

        @block.tensor
        def _(pe):
            pe.sem_inc(products, 2)
            with pe.Fori(0, KD) as i:
                for n in range(NB):
                    b = n % 2
                    y, chunks = branches[n][1], branches[n][2]
                    pe.wait_ge(split, 2 * (i * NB + n) + 2 + 4)
                    pe.wait_ge(wo_in[b], 16 * (i * (NB // 2) + n // 2) + 16)
                    pe.wait_ge(gated, i * NB + n + 1)
                    for c in range(KD):
                        for h in range(2):
                            add_product(nc, gate_ps[b][:, h * HALF:(h + 1) * HALF], part(wg[b], slice(None), c, slice(None)),
                                        part(HT, slice(None), c, slice(h * HALF, (h + 1) * HALF)), c == 0, c == KD - 1)
                    for c in range(chunks):
                        for h in range(2):
                            last = nc.tensor.matmul(out_ps[b][:, h * HALF:(h + 1) * HALF], wo[b][:, c, :],
                                                    y[:, c, h * HALF:(h + 1) * HALF], start=(c == 0), stop=(c == chunks - 1))
                    last.then_inc(products, 1)

        @block.scalar
        def _(act):
            with act.Fori(0, KD) as i:
                for n in range(NB):
                    g = i * NB + n
                    act.wait_ge(products, g + 1 + 2)
                    act.wait_ge(gated, g + 2)
                    nc.scalar.activation(gate[:], gate_ps[n % 2][:], ACT.Sigmoid).then_inc(gates, 1)

        @block.vector
        def _(dve):
            dve.sem_inc(totals, 1)
            dve.sem_inc(gated, 2)
            with dve.Fori(0, KD) as i:
                total = merged[:, bass.ds(i, 1), :].rearrange("p c s -> p (c s)")
                for n in range(NB):
                    g = i * NB + n
                    dve.wait_ge(gates, g + 1)
                    if n == 0:
                        nc.vector.tensor_tensor(total, gate[:], out_ps[0][:], ALU.mult).then_inc(gated, 1)
                        dve.wait_ge(gated, g + 1 + 2)
                        dve.sem_inc(totals, 1)
                        continue
                    dve.wait_ge(totals, g + 1)
                    nc.vector.tensor_tensor(gated_part[:], gate[:], out_ps[n % 2][:], ALU.mult).then_inc(gated, 1)
                    dve.wait_ge(gated, g + 1 + 2)
                    nc.vector.tensor_tensor(total, total, gated_part[:], ALU.add).then_inc(totals, 1)


def swiglu_up(k, hidden, HT):
    nc = k.nc
    with k.phase() as ctx:
        raw = [k.X[:, 4 * b:4 * b + 2, :].rearrange("p m (c n) -> p m c n", n=P) for b in range(2)]
        silu = [k.X[:, 4 * b + 2, :] for b in range(2)]
        w = pair(k, "up_ws", [P, 2, KD, P], ctx)
        acc = [k.ps(f"up_acc{b}", [P, 2, S], ctx) for b in range(2)]
        x_saved, w_in0, w_in1, split, passed, products, silus, done = k.sems(
            "up", "x_saved w_in0 w_in1 split passed products silus done")
        w_in = (w_in0, w_in1)
        block = ctx.enter_context(nc.Block())
        views = [k.dram[name][0].rearrange("(c p) n -> p c n", p=P) for name in ("w_gate_2", "w_up_2")]

        @block.sync
        def _(sp):
            sp.dma_start(k.scratch["x_rows"].rearrange("(t p) d -> p t d", p=P), k.X[:, :, :]).then_inc(x_saved, 16)
            sp.wait_ge(x_saved, 16)
            with sp.Fori(0, FFC // 2) as i:
                for b in range(2):
                    sp.wait_ge(split, 4 * (2 * i + b) + 4)
                    for m in range(2):
                        sp.dma_start(raw[b][:, m, :, :], views[m][:, :, bass.ds((2 * i + b) * P, P)]).then_inc(w_in[b], 16)

        @block.gpsimd
        def _(pool):
            pool.sem_inc(split, 8)
            with pool.Fori(0, FFC // 2) as i:
                for b in range(2):
                    j = 2 * i + b
                    pool.wait_ge(w_in[b], 32 * i + 32)
                    for m in range(2):
                        pool.wait_ge(products, 2 * j + m + 1)
                        pool.sem_inc(passed, 1)
                        nc.gpsimd.tensor_copy(w[0][:, m, :, :], raw[b][:, m, :, :]).then_inc(split, 1)
                        pool.wait_ge(split, 4 * j + 2 * m + 1 + 8)
                        nc.gpsimd.tensor_tensor(w[1][:, m, :, :], raw[b][:, m, :, :], w[0][:, m, :, :],
                                                ALU.subtract).then_inc(split, 1)

        @block.tensor
        def _(pe):
            pe.sem_inc(products, 2)
            with pe.Fori(0, FFC // 2) as i:
                for b in range(2):
                    j = 2 * i + b
                    pe.wait_ge(done, j + 1)
                    for m in range(2):
                        pe.wait_ge(split, 4 * j + 2 * m + 2 + 8)
                        for c in range(KD):
                            for h in range(2):
                                last = add_product(nc, acc[b][:, m, h * HALF:(h + 1) * HALF],
                                                   part(w, slice(None), m, c, slice(None)),
                                                   part(HT, slice(None), c, slice(h * HALF, (h + 1) * HALF)),
                                                   c == 0, c == KD - 1)
                        last.then_inc(products, 1)

        @block.scalar
        def _(act):
            act.wait_ge(x_saved, 16)
            with act.Fori(0, FFC // 2) as i:
                for b in range(2):
                    act.wait_ge(products, 2 * (2 * i + b) + 2 + 2)
                    act.wait_ge(done, 2 * i + b + 1)
                    nc.scalar.activation(silu[b], acc[b][:, 0, :], ACT.Silu).then_inc(silus, 1)

        @block.vector
        def _(dve):
            dve.sem_inc(done, 2)
            with dve.Fori(0, FFC // 2) as i:
                for b in range(2):
                    dve.wait_ge(silus, 2 * i + b + 1)
                    nc.vector.tensor_tensor(hidden[:, bass.ds(2 * i + b, 1), :].rearrange("p c s -> p (c s)"),
                                            silu[b], acc[b][:, 1, :], ALU.mult).then_inc(done, 1)


def scaled_gains(k):
    nc = k.nc
    with k.phase() as ctx:
        (made,) = k.sems("gains", "made")
        block = ctx.enter_context(nc.Block())

        @block.vector
        def _(dve):
            for col, name, factor in (((0, 2), "fox_q_gain_2", HD ** -0.5), ((2, 4), "fox_k_gain_2", 1.0),
                                      ((4, 8), "swa_q_gain_2", HD ** -0.5), ((8, 9), "swa_k_gain_2", 1.0)):
                n = col[1] - col[0]
                nc.vector.tensor_scalar(k.head_gains[:, col[0]:col[1]], k.gain(name).broadcast_to([P, n]), factor, None,
                                        ALU.mult).then_inc(made, 1)


def second_mixer(k):
    nc = k.nc
    w_in = k.dram["w_in_2"][0]
    H = 4
    with ExitStack() as ctx:
        fox_y = k.sb("fox_y", [P, 2, S], ctx=ctx)
        conv_y = k.sb("conv_y", [P, 2, S], ctx=ctx)
        ml_y = k.sb("ml_y", [P, 2, S], ctx=ctx)
        swa_y = k.sb("swa_y", [P, 4, S], ctx=ctx)
        with ExitStack() as inner:
            k.head_gains = k.sb("head_gains", [P, 9], ctx=inner)
            k.a_col = k.sb("a_col", [P, ST, H], ctx=inner)
            k.floor_col = k.sb("floor_col", [P, ST, H], ctx=inner)
            v2 = k.sb("v2", [P, ST, 5 * P], ctx=inner)
            vm = k.sb("vm", [P, ST, H, HD + 1], ctx=inner)
            with ExitStack() as normed:
                HT = pair(k, "attn_h", [P, KD, S], normed)
                norm_turn(k, "attn_norm", k.X, ST, k.gain("attn_norm_2"), HT)
                scaled_gains(k)
                project_rows(k, "fox_qk", w_in[:, 0:512], 4, HT, KD, k.scratch["fox_qk"], gain=k.head_gains[:, 0:4])
                project_rows(k, "swa_qk", w_in[:, C_SQ:C_SQ + 640], 5, HT, KD, k.scratch["swa_qk"], gain=k.head_gains[:, 4:9])
                project_rows(k, "plain", w_in[:, C_CU:C_MV], 10, HT, KD, k.scratch["plain"])
                project_rows(k, "mo", w_in[:, C_MO:C_SQ], 2, HT, KD, k.scratch["mo"])
                views = [w_in[:, c:c + n].rearrange("(c p) n -> p c n", p=P) for c, n in ((C_FV, 256), (C_MV, 256), (C_SV, 128))]
                project_tokens(k, "v2", [(views[0], 0, 256), (views[1], 256, 256), (views[2], 512, 128)], 5 * P, HT, KD, v2)
                gate_rows(k, vm, HT, ((swa_y, 4), (conv_y, 2), (ml_y, 2)))
            y = swa_y[:, :, :].rearrange("p c (x n) -> p (c x) n", n=512)
            with ExitStack() as fox:
                k.causal = k.sb("causal", [P, S], ctx=fox)
                split_values(k, v2, vm)
                attention(k, "fox", H,
                          lambda b, h: [("q", 0, k.scratch["fox_qk"][bass.ds(h * HD, HD), :]),
                                        ("q", HD, k.scratch["fox_q"][bass.ds(h * 2, 2), :]),
                                        ("k", 0, k.scratch["fox_qk"][bass.ds(h * HD + 256, HD), :]),
                                        ("k", HD, k.scratch["fox_k"][bass.ds(h * 2, 2), :])],
                          HD + 2, v2, y, 0)
                turn(k, "fox_turn", y[:, :, 0:256], k.ones[:, 0:2], fox_y, 2)
            matrix_lstm(k, vm, y)
            head_norm(k, "ml_rms", y[:, :, 0:256], H, HD, 1.0)
            turn(k, "ml_turn", y[:, :, 0:256], k.gain("mlstm_h_gain_2"), ml_y, 2)
            short_conv(k, conv_y, ml_y)
            biases = k.sb("biases", [P, 8, 2 * P], ctx=inner)
            sinks = k.sb("sinks", [P, 8], ctx=inner)
            window_bias(k, biases, sinks)
            y = k.sb("y_rows", [P, ST, 512], ctx=inner)
            for kv in range(2):
                attention(k, f"swa{kv}", 4,
                          lambda b, h: [("q", 0, k.scratch["swa_qk"][bass.ds(h * HD + kv * 4 * HD, HD), :]),
                                        ("k", 0, k.scratch["swa_qk"][512 + kv * HD:512 + (kv + 1) * HD, :])],
                          HD, v2, y, kv * 256, window=(kv * 4, 512 + kv * HD, biases, sinks))
            turn(k, "swa_turn", y[:, :, 0:512], k.ones[:, 0:4], swa_y, 4)
        merged = k.sb("merged", [P, KD, S], ctx=ctx)
        with ExitStack() as normed:
            HT = pair(k, "attn_h", [P, KD, S], normed)
            norm_turn(k, "attn_norm", k.X, ST, k.gain("attn_norm_2"), HT)
            gated_merge(k, [("w_fox_out_2", fox_y, 2), ("w_conv_out_2", conv_y, 2), ("w_mlstm_out_2", ml_y, 2),
                        ("w_swa_out_2", swa_y, 4)], merged, HT)
        project_residual(k, "merge_out", k.dram["w_merge_out_2"][0], merged, KD)


def split_values(k, v2, vm):
    nc = k.nc
    with k.phase() as ctx:
        (made,) = k.sems("split", "made")
        block = ctx.enter_context(nc.Block())

        @block.gpsimd
        def _(pool):
            link = k.own("pool", pool)
            link(nc.gpsimd.memset(k.causal[:], 0.0))
            link(nc.gpsimd.affine_select(out=k.causal[:, S - P:S], in_=k.causal[:, S - P:S], compare_op=ALU.is_ge,
                                         fill=NEG, base=0, pattern=[[-1, P]], channel_multiplier=1))

        @block.vector
        def _(dve):
            for t in range(ST):
                nc.vector.tensor_copy(vm[:, t, :, 0:HD], v2[:, t, 256:512].rearrange("p (h n) -> p h n", n=HD)
                                      ).then_inc(made, 1)
        k.chains["pool"].settle()


def store(k, view, tile):
    nc = k.nc
    with k.phase() as ctx:
        (stored,) = k.sems("store", "stored")
        block = ctx.enter_context(nc.Block())

        @block.sync
        def _(sp):
            sp.dma_start(view, tile).then_inc(stored, 16)
            sp.wait_ge(stored, 16)


def swiglu(k):
    with ExitStack() as ctx:
        hidden = k.sb("hidden", [P, FFC, S], ctx=ctx)
        with ExitStack() as normed:
            H = pair(k, "ffn2_h", [P, KD, S], normed)
            norm_turn(k, "ffn2_norm", k.X, ST, k.gain("ffn_norm_2"), H)
            swiglu_up(k, hidden, H)
        load_rows(k, k.scratch["x_rows"].rearrange("(t p) d -> p t d", p=P), k.X)
        project_residual(k, "down", k.dram["w_down_2"][0], hidden, FFC)


def gate_rows(k, vm, HT, spare):
    nc = k.nc
    H = 4
    with k.phase() as ctx:
        w = k.sb("gr_w", [P, KD, 96], ctx=ctx)
        w_pair = pair(k, "gr_ws", [P, KD, 96], ctx)
        bias = k.sb("gr_bias", [H, 3], ctx=ctx)
        rows = [tile[0:H, c, :] for tile, count in spare for c in range(count)]
        raw, logs, sums = rows[0:3], rows[3:5], rows[5:7]
        ones = k.sb("gr_ones", [H, S], ctx=ctx)
        a, top, floor, neg = (k.sb(f"gr_{n}", [H, S], ctx=ctx) for n in ("a", "top", "floor", "neg"))
        acc = k.ps("gr_acc", [P, S], ctx)
        cols = k.ps("gr_cols", [P, 2, ST, H], ctx)
        w_in, w_split, bias_in, cleared, products, copied, absed, logged, rows_made, turned, stored = k.sems(
            "gr", "w_in w_split bias_in cleared products copied absed logged rows_made turned stored")
        block = ctx.enter_context(nc.Block())
        w_view = k.dram["w_in_2"][0].rearrange("(c p) n -> p c n", p=P)

        @block.sync
        def _(sp):
            sp.wait_ge(cleared, 2)
            for n, col in enumerate((C_FF, C_MI, C_MI + H)):
                sp.dma_start(w[:, :, 32 * n:32 * n + H], w_view[:, :, col:col + H]).then_inc(w_in, 16)
            for n, name in enumerate(("fox_f_bias_2", "mlstm_i_bias_2", "mlstm_f_bias_2")):
                sp.dma_start(bias[:, n:n + 1], k.dram[name].rearrange("l h -> h l")).then_inc(bias_in, 16)
            fox_q = k.scratch["fox_q"].rearrange("(h n) s -> h n s", n=2)
            fox_k = k.scratch["fox_k"].rearrange("(h n) s -> h n s", n=2)
            sp.dma_start(fox_q[:, 0, :], ones[:]).then_inc(stored, 16)
            sp.dma_start(fox_k[:, 1, :], ones[:]).then_inc(stored, 16)
            sp.wait_ge(rows_made, 1)
            sp.dma_start(fox_q[:, 1, :], sums[0][:]).then_inc(stored, 16)
            sp.wait_ge(rows_made, 2)
            sp.dma_start(fox_k[:, 0, :], neg[:]).then_inc(stored, 16)
            sp.wait_ge(rows_made, 4)
            sp.dma_start(k.scratch["mlstm_row"], top[:]).then_inc(stored, 16)
            sp.wait_ge(stored, 16 * 5)

        @block.gpsimd
        def _(pool):
            nc.gpsimd.memset(w[:, :, :], 0.0).then_inc(cleared, 1)
            nc.gpsimd.memset(ones[:], 1.0).then_inc(cleared, 1)
            nc.gpsimd.memset(vm[:, :, :, HD:HD + 1], 1.0).then_inc(cleared, 1)
            pool.wait_ge(w_in, 48)
            nc.gpsimd.tensor_copy(w_pair[0][:], w[:]).then_inc(w_split, 1)
            pool.wait_ge(w_split, 1)
            nc.gpsimd.tensor_tensor(w_pair[1][:], w[:], w_pair[0][:], ALU.subtract).then_inc(w_split, 1)

        @block.tensor
        def _(pe):
            pe.wait_ge(w_split, 2)
            for c in range(KD):
                for h in range(2):
                    last = add_product(nc, acc[0:96, h * HALF:(h + 1) * HALF], part(w_pair, slice(None), c, slice(None)),
                                       part(HT, slice(None), c, slice(h * HALF, (h + 1) * HALF)), c == 0, c == KD - 1)
            last.then_inc(products, 1)
            pe.wait_ge(rows_made, 5)
            for n, row in enumerate((a, floor)):
                for t in range(ST):
                    last = nc.tensor.transpose(cols[:, n, t, :], row[:, t * P:(t + 1) * P], k.ident[0:H, 0:H])
            last.then_inc(turned, 1)

        @block.scalar
        def _(act):
            act.wait_ge(products, 1)
            for n in range(3):
                nc.scalar.activation(raw[n][:], acc[32 * n:32 * n + H, :], ACT.Copy).then_inc(copied, 1)
            for n, x in enumerate((raw[0], raw[2])):
                act.wait_ge(absed, n + 1)
                nc.scalar.activation(logs[n][:], x[:], ACT.Abs).then_inc(logged, 1)
                act.wait_ge(logged, 3 * n + 1)
                nc.scalar.activation(logs[n][:], logs[n][:], ACT.Exp, scale=-1.0).then_inc(logged, 1)
                act.wait_ge(logged, 3 * n + 2)
                nc.scalar.activation(logs[n][:], logs[n][:], ACT.Ln, bias=1.0).then_inc(logged, 1)
            act.wait_ge(turned, 1)
            nc.scalar.activation(k.a_col[:, :, :], cols[:, 0, :, :], ACT.Copy)
            nc.scalar.activation(k.floor_col[:, :, :], cols[:, 1, :, :], ACT.Exp, scale=-1.0)

        @block.vector
        def _(dve):
            link = k.own("dve", dve)
            v = nc.vector
            dve.wait_ge(bias_in, 48)
            dve.wait_ge(copied, 3)
            dve.wait_ge(cleared, 3)
            for n in (0, 2):
                v.tensor_scalar(raw[n][:], raw[n][:], bias[:, n:n + 1], None, ALU.add).then_inc(absed, 1)
            link(v.tensor_scalar(raw[1][:], raw[1][:], bias[:, 1:2], None, ALU.add))
            for n, x in enumerate((raw[0], raw[2])):
                dve.wait_ge(logged, 3 * n + 3)
                link(v.scalar_tensor_tensor(out=logs[n][:], in0=x[:], scalar=0.0, in1=logs[n][:],
                                            op0=ALU.min, op1=ALU.subtract))
                ins = v.tensor_tensor_scan(sums[n][:], ones[:], logs[n][:], 0.0, ALU.mult, ALU.add)
                if n == 0:
                    ins.then_inc(rows_made, 1)
                    dve.wait_ge(rows_made, 1)
                    v.tensor_scalar(neg[:], sums[0][:], -1.0, None, ALU.mult).then_inc(rows_made, 1)
                else:
                    link(ins)
            link(v.tensor_tensor(a[:], raw[1][:], sums[1][:], ALU.subtract))
            link(v.tensor_tensor_scan(top[:], ones[:], a[:], 0.0, ALU.mult, ALU.max))
            v.tensor_tensor(floor[:], top[:], sums[1][:], ALU.add).then_inc(rows_made, 1)
            dve.wait_ge(rows_made, 3)
            v.tensor_scalar(top[:], top[:], -1.0, None, ALU.mult).then_inc(rows_made, 1)
            dve.wait_ge(rows_made, 4)
            dve.sem_inc(rows_made, 1)
        k.chains["dve"].settle()


def matrix_lstm(k, V, out):
    nc = k.nc
    H = 4
    with k.phase() as ctx:
        q = [k.sb(f"ml_q{b}", [HD, S], ctx=ctx) for b in range(2)]
        kk = [k.sb(f"ml_k{b}", [HD, S], ctx=ctx) for b in range(2)]
        row = [k.sb(f"ml_row{b}", [P, S], ctx=ctx) for b in range(2)]
        a_col = [k.sb(f"ml_a{b}", [P, ST], ctx=ctx) for b in range(2)]
        decay = [k.sb(f"ml_decay{b}", [P, S], ctx=ctx) for b in range(2)]
        w = [[k.sb(f"ml_w{b}{t}", [P, S - t * P], ctx=ctx) for t in range(ST)] for b in range(2)]
        stats = [k.sb(f"ml_stats{b}", [P, ST, 2], ctx=ctx) for b in range(2)]
        values = [k.sb(f"ml_v{b}", [P, ST, HD + 1], ctx=ctx) for b in range(2)]
        before_mask = k.sb("ml_mask", [P, P], ctx=ctx)
        scores = [k.ps(f"ml_scores{b}", [P, S], ctx) for b in range(2)]
        acc = [k.ps(f"ml_acc{b}", [P, 2, HALF], ctx) for b in range(2)]
        (head_in0, head_in1, mask_made, a_ready, masked, decays, products, weighted, sums_made, done) = k.sems(
            "ml", "head_in0 head_in1 mask_made a_ready masked decays products weighted sums_made done")
        head_in = (head_in0, head_in1)
        block = ctx.enter_context(nc.Block())
        rounds = H // 2
        plain = k.scratch["plain"]
        q_row, k_row = C_MQ - C_CU, C_MQ + H * HD - C_CU

        def at(b, t):
            return acc[b][:, t // 4, (t % 4) * (HD + 1):(t % 4 + 1) * (HD + 1)]

        @block.sync
        def _(sp):
            with sp.Fori(0, rounds) as i:
                for b in range(2):
                    sp.wait_ge(done, 2 * i + 1)
                    h = i * 2 + b
                    sp.dma_start(q[b][:], plain[bass.ds(h * HD + q_row, HD), :]).then_inc(head_in[b], 16)
                    sp.dma_start(kk[b][:], plain[bass.ds(h * HD + k_row, HD), :]).then_inc(head_in[b], 16)
                    sp.dma_start(row[b][:], k.scratch["mlstm_row"][bass.ds(h, 1), :].broadcast_to([P, S])
                                 ).then_inc(head_in[b], 16)

        @block.gpsimd
        def _(pool):
            nc.gpsimd.memset(before_mask[:], 0.0).then_inc(mask_made, 1)
            pool.wait_ge(mask_made, 1)
            nc.gpsimd.affine_select(out=before_mask[:], in_=before_mask[:], compare_op=ALU.is_ge, fill=NEG, base=0,
                                    pattern=[[1, P]], channel_multiplier=-1).then_inc(mask_made, 1)
            with pool.Fori(0, rounds) as i:
                for b in range(2):
                    pool.wait_ge(done, 2 * i + 1)
                    h = i * 2 + b
                    nc.gpsimd.tensor_copy(a_col[b][:], k.a_col[:, :, bass.ds(h, 1)].rearrange("p t h -> p (t h)")
                                          ).then_inc(a_ready, 1)
                    nc.gpsimd.tensor_copy(values[b][:, :, :], V[:, :, bass.ds(h, 1), :].rearrange(
                        "p t h n -> p (t h) n")).then_inc(a_ready, 1)

        @block.tensor
        def _(pe):
            pe.sem_inc(sums_made, 1)
            with pe.Fori(0, rounds) as i:
                for b in range(2):
                    pe.wait_ge(head_in[b], 48 * i + 48)
                    for t in range(ST):
                        g = (i * 2 + b) * ST + t
                        pe.wait_ge(weighted, g + 1)
                        width = S - t * P
                        for c in range(0, width, HALF):
                            n = min(HALF, width - c)
                            last = nc.tensor.matmul(scores[t % 2][:, c:c + n], kk[b][:, t * P:(t + 1) * P],
                                                    q[b][:, t * P + c:t * P + c + n], start=True, stop=True)
                        last.then_inc(products, 1)
                for b in range(2):
                    pe.wait_ge(weighted, (i * 2 + b + 1) * ST + 2)
                    pe.wait_ge(a_ready, (i * 2 + b) * 2 + 2)
                    pe.wait_ge(done, 2 * i + 1)
                    for t in range(ST):
                        for c in range(t + 1):
                            last = nc.tensor.matmul(at(b, t), w[b][c][:, (t - c) * P:(t - c + 1) * P],
                                                    values[b][:, c, :], start=(c == 0), stop=(c == t))
                    last.then_inc(sums_made, 1)

        @block.scalar
        def _(act):
            with act.Fori(0, rounds) as i:
                for b in range(2):
                    act.wait_ge(head_in[b], 48 * i + 48)
                    act.wait_ge(a_ready, (i * 2 + b) * 2 + 2)
                    for t in range(ST):
                        g = (i * 2 + b) * ST + t
                        act.wait_ge(weighted, g + 1)
                        act.wait_ge(masked, g + 1)
                        nc.scalar.activation(decay[t % 2][:, 0:P], decay[t % 2][:, 0:P], ACT.Exp,
                                             bias=a_col[b][:, t:t + 1]).then_inc(decays, 1)
                        if t < ST - 1:
                            nc.scalar.activation(decay[t % 2][:, P:S - t * P], row[b][:, (t + 1) * P:S], ACT.Exp,
                                                 bias=a_col[b][:, t:t + 1]).then_inc(decays, 1)

        @block.vector
        def _(dve):
            dve.sem_inc(done, 1)
            link = k.own("dve", dve)
            chain = k.chains["dve"]
            dve.sem_inc(weighted, 2)
            dve.wait_ge(mask_made, 2)
            per = 2 * ST - 1
            with dve.Fori(0, rounds) as i:
                chain.enter(i, 2 * 3)
                for b in range(2):
                    dve.wait_ge(head_in[b], 48 * i + 48)
                    for t in range(ST + 1):
                        g = (i * 2 + b) * ST + t
                        if t < ST:
                            dve.wait_ge(weighted, g + 1)
                            nc.vector.tensor_tensor(decay[t % 2][:, 0:P], row[b][:, t * P:(t + 1) * P], before_mask[:],
                                                    ALU.add).then_inc(masked, 1)
                        if t:
                            dve.wait_ge(products, g)
                            dve.wait_ge(decays, (i * 2 + b) * per + min(2 * t, per))
                            dve.wait_ge(sums_made, 2 * i + 1)
                            width = S - (t - 1) * P
                            nc.vector.scalar_tensor_tensor(out=w[b][t - 1][:], in0=scores[(t - 1) % 2][:, 0:width],
                                                           scalar=HD ** -0.5, in1=decay[(t - 1) % 2][:, 0:width],
                                                           op0=ALU.mult, op1=ALU.mult).then_inc(weighted, 1)
                for b in range(2):
                    dve.wait_ge(sums_made, i * 2 + b + 1 + 1)
                    h = i * 2 + b
                    st = stats[b]
                    den = acc[b][:, :, 0:4 * (HD + 1)].rearrange("p a (t n) -> p a t n", n=HD + 1)[:, :, :, HD:HD + 1]
                    den = den.rearrange("p a t n -> p a (t n)")
                    one, two = (st[:, :, n:n + 1].rearrange("p (a t) n -> p a (t n)", a=2) for n in range(2))
                    link(nc.vector.tensor_copy(one, den))
                    link(nc.vector.scalar_tensor_tensor(
                        out=st[:, :, 1:2], in0=st[:, :, 0:1], scalar=-1.0, in1=k.floor_col[:, :, bass.ds(h, 1)],
                        op0=ALU.mult, op1=ALU.max))
                    link(nc.vector.tensor_tensor(st[:, :, 0:1], st[:, :, 0:1], st[:, :, 1:2], ALU.max))
                    nc.vector.reciprocal(st[:, :, 1:2], st[:, :, 0:1]).then_inc(mask_made, 1)
                    dve.wait_ge(mask_made, 2 + 5 * h + 1)
                    for t in range(ST):
                        ins = nc.vector.tensor_scalar(out[:, t, bass.ds(h * HD, HD)], at(b, t)[:, 0:HD], st[:, t, 1:2],
                                                      None, ALU.mult)
                    ins.then_inc(mask_made, 4)
                    dve.wait_ge(mask_made, 2 + 5 * h + 5)
                    dve.sem_inc(done, 1)
                chain.leave(rounds)


def short_conv(k, conv_out, ml_rows):
    nc = k.nc
    CH = 2
    with k.phase() as ctx:
        u, bg, cg, mo = (k.sb(f"conv_{n}", [P, CH, S], ctx=ctx) for n in ("u", "b", "c", "mo"))
        loaded, gated, chain_c = k.sems("conv", "loaded gated chain_c")
        block = ctx.enter_context(nc.Block())
        plain = k.scratch["plain"]

        @block.sync
        def _(sp):
            for n, tile in enumerate((u, bg, cg)):
                sp.dma_start(tile[:, :, :], plain[n * CH * P:(n + 1) * CH * P, :].rearrange("(c p) s -> p c s", p=P)
                             ).then_inc(loaded, 16)
            sp.dma_start(mo[:, :, :], k.scratch["mo"].rearrange("(c p) s -> p c s", p=P)).then_inc(gated, 16)

        @block.scalar
        def _(act):
            act.wait_ge(gated, 16)
            nc.scalar.activation(mo[:, :, :], mo[:, :, :], ACT.Sigmoid).then_inc(gated, 1)

        @block.vector
        def _(dve):
            link = k.own("dve", dve)
            dve.wait_ge(loaded, 48)
            link(nc.vector.tensor_tensor(u[:, :, :], u[:, :, :], cg[:, :, :], ALU.mult))
            for c in range(CH):
                taps = [k.gain("conv_w_2", n * CH + c, 1) for n in range(3)]
                link(nc.vector.tensor_scalar(conv_out[:, c, :], u[:, c, :], taps[2], None, ALU.mult))
                for back, tap in ((1, taps[1]), (2, taps[0])):
                    link(nc.vector.scalar_tensor_tensor(out=conv_out[:, c, back:], in0=u[:, c, 0:S - back], scalar=tap,
                                                        in1=conv_out[:, c, back:], op0=ALU.mult, op1=ALU.add))
            link(nc.vector.tensor_tensor(conv_out[:, :, :], conv_out[:, :, :], bg[:, :, :], ALU.mult))
            dve.wait_ge(gated, 17)
            link(nc.vector.tensor_tensor(ml_rows[:, :, :], ml_rows[:, :, :], mo[:, :, :], ALU.mult))
        k.chains["dve"].settle()


def t5_buckets(n):
    exact, most, buckets = 16, 128, 32
    out = []
    for d in range(n):
        if d < exact:
            out.append(d)
        else:
            large = exact + int(np.log(d / exact) / np.log(most / exact) * (buckets - exact))
            out.append(min(large, buckets - 1))
    return out


def window_bias(k, biases, sinks):
    nc = k.nc
    H, B, W2 = 8, 32, 3 * P
    with k.phase() as ctx:
        rel = k.sb("wb_rel", [B, H], ctx=ctx)
        hot = k.sb("wb_hot", [B, W2], ctx=ctx)
        index = k.sb("wb_index", [B, 1], ctx=ctx)
        bucket = k.sb("wb_bucket", [B, W2], ctx=ctx)
        rows = k.sb("wb_rows", [H, W2], ctx=ctx)
        flipped = k.sb("wb_flipped", [P, H, 2 * P], ctx=ctx)
        flip = k.sb("wb_flip", [P, P], ctx=ctx)
        acc = k.ps("wb_acc", [H, W2], ctx)
        turned = k.ps("wb_turned", [P, H, 2 * P], ctx)
        rel_in, bucketed, made, hot_made, product, rows_made, stored, loaded, upright = k.sems(
            "wb", "rel_in bucketed made hot_made product rows_made stored loaded upright")
        block = ctx.enter_context(nc.Block())
        buckets = t5_buckets(WINDOW)
        runs = []
        for j in range(P, 2 * P):
            value = buckets[2 * P - 1 - j]
            if runs and runs[-1][2] == value:
                runs[-1][1] = j + 1
            else:
                runs.append([j, j + 1, value])

        @block.sync
        def _(sp):
            sp.dma_start(rel[:], k.dram["rel_bias_2"]).then_inc(rel_in, 16)
            sp.dma_start(sinks[:], k.dram["swa_sinks_2"].broadcast_to([P, H])).then_inc(loaded, 16)
            sp.wait_ge(rows_made, 3)
            sp.dma_start(k.scratch["window_rows"], rows[:]).then_inc(stored, 16)
            sp.wait_ge(stored, 16)
            view = k.scratch["window_rows"]
            for h in range(H):
                skewed = bass.AP(view.tensor, view.offset + h * W2, [[1, P], [1, 2 * P]])
                sp.dma_start(flipped[:, h, :], skewed).then_inc(loaded, 16)

        @block.gpsimd
        def _(pool):
            nc.gpsimd.memset(bucket[:], -1.0).then_inc(made, 1)
            nc.gpsimd.iota(index[:], [[0, 1]], 0, 1, allow_small_or_imprecise_dtypes=True).then_inc(made, 1)
            nc.gpsimd.memset(flip[:], 0.0).then_inc(made, 1)
            pool.wait_ge(made, 3)
            nc.gpsimd.affine_select(out=flip[:], in_=flip[:], compare_op=ALU.not_equal, fill=1.0, base=1 - P,
                                    pattern=[[1, P]], channel_multiplier=1).then_inc(made, 1)
            for at, to, value in runs:
                nc.gpsimd.memset(bucket[:, at:to], float(value)).then_inc(bucketed, 1)

        @block.vector
        def _(dve):
            dve.wait_ge(bucketed, len(runs))
            nc.vector.tensor_scalar(hot[:], bucket[:], index[:], None, ALU.is_equal).then_inc(hot_made, 1)
            nc.vector.memset(rows[:, 0:P], NEG).then_inc(rows_made, 1)
            nc.vector.memset(rows[:, 2 * P:], NEG).then_inc(rows_made, 1)
            dve.wait_ge(product, 1)
            nc.vector.tensor_copy(rows[:, P:2 * P], acc[:, P:2 * P]).then_inc(rows_made, 1)
            dve.wait_ge(upright, 1)
            nc.vector.tensor_copy(biases[:, :, :], turned[:, :, :])

        @block.tensor
        def _(pe):
            pe.wait_ge(hot_made, 1)
            pe.wait_ge(rel_in, 16)
            nc.tensor.matmul(acc[:], rel[:], hot[:], start=True, stop=True).then_inc(product, 1)
            pe.wait_ge(made, 4)
            pe.wait_ge(loaded, 16 * (H + 1))
            for h in range(0, H, 2):
                last = nc.tensor.matmul(turned[:, h:h + 2, :], flip[:], flipped[:, h:h + 2, :], start=True, stop=True)
            last.then_inc(upright, 1)


def gated_merge(k, branches, merged, HT):
    nc = k.nc
    NB = len(branches)
    with k.phase() as ctx:
        wg_raw = [k.sb(f"gm_wg{b}", [P, KD, P], ctx=ctx) for b in range(2)]
        wg = [pair(k, f"gm_wgs{b}", [P, KD, P], ctx) for b in range(2)]
        wo = [k.sb(f"gm_wo{b}", [P, 4, P], ctx=ctx) for b in range(2)]
        gate = k.sb("gm_gate", [P, S], ctx=ctx)
        gated_part = k.sb("gm_part", [P, S], ctx=ctx)
        gate_ps = [k.ps(f"gm_gate_ps{b}", [P, S], ctx) for b in range(2)]
        out_ps = [k.ps(f"gm_out_ps{b}", [P, S], ctx) for b in range(2)]
        wg_in0, wg_in1, wo_in0, wo_in1, split, passed, products, gates, gated, totals = k.sems(
            "gm", "wg_in0 wg_in1 wo_in0 wo_in1 split passed products gates gated totals")
        wg_in, wo_in = (wg_in0, wg_in1), (wo_in0, wo_in1)
        block = ctx.enter_context(nc.Block())
        w_view = k.dram["w_in_2"][0].rearrange("(c p) n -> p c n", p=P)
        outs = [k.dram[name][0].rearrange("(c p) n -> p c n", p=P) for name, _, _ in branches]

        @block.sync
        def _(sp):
            with sp.Fori(0, KD) as i:
                for n in range(NB):
                    sp.wait_ge(split, 2 * (i * NB + n) + 2)
                    col = bass.ds(i * P + C_GATES + n * D, P)
                    sp.dma_start(wg_raw[n % 2][:, :, :], w_view[:, :, col]).then_inc(wg_in[n % 2], 16)
                    sp.wait_ge(products, i * NB + n + 1)
                    sp.sem_inc(passed, 1)
                    sp.dma_start(wo[n % 2][:, 0:branches[n][2], :], outs[n][:, :, bass.ds(i * P, P)]).then_inc(wo_in[n % 2], 16)

        @block.gpsimd
        def _(pool):
            pool.sem_inc(split, 4)
            with pool.Fori(0, KD) as i:
                for n in range(NB):
                    split_weights(nc, pool, i * NB + n, n % 2, (wg_in[n % 2], 16 * (i * (NB // 2) + n // 2) + 16), wg_raw, wg,
                                  products, split, passed)

        @block.tensor
        def _(pe):
            pe.sem_inc(products, 2)
            with pe.Fori(0, KD) as i:
                for n in range(NB):
                    b = n % 2
                    y, chunks = branches[n][1], branches[n][2]
                    pe.wait_ge(split, 2 * (i * NB + n) + 2 + 4)
                    pe.wait_ge(wo_in[b], 16 * (i * (NB // 2) + n // 2) + 16)
                    pe.wait_ge(gated, i * NB + n + 1)
                    for c in range(KD):
                        for h in range(2):
                            add_product(nc, gate_ps[b][:, h * HALF:(h + 1) * HALF], part(wg[b], slice(None), c, slice(None)),
                                        part(HT, slice(None), c, slice(h * HALF, (h + 1) * HALF)), c == 0, c == KD - 1)
                    for c in range(chunks):
                        for h in range(2):
                            last = nc.tensor.matmul(out_ps[b][:, h * HALF:(h + 1) * HALF], wo[b][:, c, :],
                                                    y[:, c, h * HALF:(h + 1) * HALF], start=(c == 0), stop=(c == chunks - 1))
                    last.then_inc(products, 1)

        @block.scalar
        def _(act):
            with act.Fori(0, KD) as i:
                for n in range(NB):
                    g = i * NB + n
                    act.wait_ge(products, g + 1 + 2)
                    act.wait_ge(gated, g + 2)
                    nc.scalar.activation(gate[:], gate_ps[n % 2][:], ACT.Sigmoid).then_inc(gates, 1)

        @block.vector
        def _(dve):
            dve.sem_inc(totals, 1)
            dve.sem_inc(gated, 2)
            with dve.Fori(0, KD) as i:
                total = merged[:, bass.ds(i, 1), :].rearrange("p c s -> p (c s)")
                for n in range(NB):
                    g = i * NB + n
                    dve.wait_ge(gates, g + 1)
                    if n == 0:
                        nc.vector.tensor_tensor(total, gate[:], out_ps[0][:], ALU.mult).then_inc(gated, 1)
                        dve.wait_ge(gated, g + 1 + 2)
                        dve.sem_inc(totals, 1)
                        continue
                    dve.wait_ge(totals, g + 1)
                    nc.vector.tensor_tensor(gated_part[:], gate[:], out_ps[n % 2][:], ALU.mult).then_inc(gated, 1)
                    dve.wait_ge(gated, g + 1 + 2)
                    nc.vector.tensor_tensor(total, total, gated_part[:], ALU.add).then_inc(totals, 1)


def swiglu_up(k, hidden, HT):
    nc = k.nc
    with k.phase() as ctx:
        raw = [k.X[:, 4 * b:4 * b + 2, :].rearrange("p m (c n) -> p m c n", n=P) for b in range(2)]
        silu = [k.X[:, 4 * b + 2, :] for b in range(2)]
        w = pair(k, "up_ws", [P, 2, KD, P], ctx)
        acc = [k.ps(f"up_acc{b}", [P, 2, S], ctx) for b in range(2)]
        x_saved, w_in0, w_in1, split, passed, products, silus, done = k.sems(
            "up", "x_saved w_in0 w_in1 split passed products silus done")
        w_in = (w_in0, w_in1)
        block = ctx.enter_context(nc.Block())
        views = [k.dram[name][0].rearrange("(c p) n -> p c n", p=P) for name in ("w_gate_2", "w_up_2")]

        @block.sync
        def _(sp):
            sp.dma_start(k.scratch["x_rows"].rearrange("(t p) d -> p t d", p=P), k.X[:, :, :]).then_inc(x_saved, 16)
            sp.wait_ge(x_saved, 16)
            with sp.Fori(0, FFC // 2) as i:
                for b in range(2):
                    sp.wait_ge(split, 4 * (2 * i + b) + 4)
                    for m in range(2):
                        sp.dma_start(raw[b][:, m, :, :], views[m][:, :, bass.ds((2 * i + b) * P, P)]).then_inc(w_in[b], 16)

        @block.gpsimd
        def _(pool):
            pool.sem_inc(split, 8)
            with pool.Fori(0, FFC // 2) as i:
                for b in range(2):
                    j = 2 * i + b
                    pool.wait_ge(w_in[b], 32 * i + 32)
                    for m in range(2):
                        pool.wait_ge(products, 2 * j + m + 1)
                        pool.sem_inc(passed, 1)
                        nc.gpsimd.tensor_copy(w[0][:, m, :, :], raw[b][:, m, :, :]).then_inc(split, 1)
                        pool.wait_ge(split, 4 * j + 2 * m + 1 + 8)
                        nc.gpsimd.tensor_tensor(w[1][:, m, :, :], raw[b][:, m, :, :], w[0][:, m, :, :],
                                                ALU.subtract).then_inc(split, 1)

        @block.tensor
        def _(pe):
            pe.sem_inc(products, 2)
            with pe.Fori(0, FFC // 2) as i:
                for b in range(2):
                    j = 2 * i + b
                    pe.wait_ge(done, j + 1)
                    for m in range(2):
                        pe.wait_ge(split, 4 * j + 2 * m + 2 + 8)
                        for c in range(KD):
                            for h in range(2):
                                last = add_product(nc, acc[b][:, m, h * HALF:(h + 1) * HALF],
                                                   part(w, slice(None), m, c, slice(None)),
                                                   part(HT, slice(None), c, slice(h * HALF, (h + 1) * HALF)),
                                                   c == 0, c == KD - 1)
                        last.then_inc(products, 1)

        @block.scalar
        def _(act):
            act.wait_ge(x_saved, 16)
            with act.Fori(0, FFC // 2) as i:
                for b in range(2):
                    act.wait_ge(products, 2 * (2 * i + b) + 2 + 2)
                    act.wait_ge(done, 2 * i + b + 1)
                    nc.scalar.activation(silu[b], acc[b][:, 0, :], ACT.Silu).then_inc(silus, 1)

        @block.vector
        def _(dve):
            dve.sem_inc(done, 2)
            with dve.Fori(0, FFC // 2) as i:
                for b in range(2):
                    dve.wait_ge(silus, 2 * i + b + 1)
                    nc.vector.tensor_tensor(hidden[:, bass.ds(2 * i + b, 1), :].rearrange("p c s -> p (c s)"),
                                            silu[b], acc[b][:, 1, :], ALU.mult).then_inc(done, 1)


def scaled_gains(k):
    nc = k.nc
    with k.phase() as ctx:
        (made,) = k.sems("gains", "made")
        block = ctx.enter_context(nc.Block())

        @block.vector
        def _(dve):
            for col, name, factor in (((0, 2), "fox_q_gain_2", HD ** -0.5), ((2, 4), "fox_k_gain_2", 1.0),
                                      ((4, 8), "swa_q_gain_2", HD ** -0.5), ((8, 9), "swa_k_gain_2", 1.0)):
                n = col[1] - col[0]
                nc.vector.tensor_scalar(k.head_gains[:, col[0]:col[1]], k.gain(name).broadcast_to([P, n]), factor, None,
                                        ALU.mult).then_inc(made, 1)


def second_mixer(k):
    nc = k.nc
    w_in = k.dram["w_in_2"][0]
    H = 4
    with ExitStack() as ctx:
        fox_y = k.sb("fox_y", [P, 2, S], ctx=ctx)
        conv_y = k.sb("conv_y", [P, 2, S], ctx=ctx)
        ml_y = k.sb("ml_y", [P, 2, S], ctx=ctx)
        swa_y = k.sb("swa_y", [P, 4, S], ctx=ctx)
        with ExitStack() as inner:
            k.head_gains = k.sb("head_gains", [P, 9], ctx=inner)
            k.a_col = k.sb("a_col", [P, ST, H], ctx=inner)
            k.floor_col = k.sb("floor_col", [P, ST, H], ctx=inner)
            v2 = k.sb("v2", [P, ST, 5 * P], ctx=inner)
            vm = k.sb("vm", [P, ST, H, HD + 1], ctx=inner)
            with ExitStack() as normed:
                HT = pair(k, "attn_h", [P, KD, S], normed)
                norm_turn(k, "attn_norm", k.X, ST, k.gain("attn_norm_2"), HT)
                scaled_gains(k)
                project_rows(k, "fox_qk", w_in[:, 0:512], 4, HT, KD, k.scratch["fox_qk"], gain=k.head_gains[:, 0:4])
                project_rows(k, "swa_qk", w_in[:, C_SQ:C_SQ + 640], 5, HT, KD, k.scratch["swa_qk"], gain=k.head_gains[:, 4:9])
                project_rows(k, "plain", w_in[:, C_CU:C_MV], 10, HT, KD, k.scratch["plain"])
                project_rows(k, "mo", w_in[:, C_MO:C_SQ], 2, HT, KD, k.scratch["mo"])
                views = [w_in[:, c:c + n].rearrange("(c p) n -> p c n", p=P) for c, n in ((C_FV, 256), (C_MV, 256), (C_SV, 128))]
                project_tokens(k, "v2", [(views[0], 0, 256), (views[1], 256, 256), (views[2], 512, 128)], 5 * P, HT, KD, v2)
                gate_rows(k, vm, HT, ((swa_y, 4), (conv_y, 2), (ml_y, 2)))
            y = swa_y[:, :, :].rearrange("p c (x n) -> p (c x) n", n=512)
            with ExitStack() as fox:
                k.causal = k.sb("causal", [P, S], ctx=fox)
                split_values(k, v2, vm)
                attention(k, "fox", H,
                          lambda b, h: [("q", 0, k.scratch["fox_qk"][bass.ds(h * HD, HD), :]),
                                        ("q", HD, k.scratch["fox_q"][bass.ds(h * 2, 2), :]),
                                        ("k", 0, k.scratch["fox_qk"][bass.ds(h * HD + 256, HD), :]),
                                        ("k", HD, k.scratch["fox_k"][bass.ds(h * 2, 2), :])],
                          HD + 2, v2, y, 0)
                turn(k, "fox_turn", y[:, :, 0:256], k.ones[:, 0:2], fox_y, 2)
            matrix_lstm(k, vm, y)
            head_norm(k, "ml_rms", y[:, :, 0:256], H, HD, 1.0)
            turn(k, "ml_turn", y[:, :, 0:256], k.gain("mlstm_h_gain_2"), ml_y, 2)
            short_conv(k, conv_y, ml_y)
            biases = k.sb("biases", [P, 8, 2 * P], ctx=inner)
            sinks = k.sb("sinks", [P, 8], ctx=inner)
            window_bias(k, biases, sinks)
            y = k.sb("y_rows", [P, ST, 512], ctx=inner)
            for kv in range(2):
                attention(k, f"swa{kv}", 4,
                          lambda b, h: [("q", 0, k.scratch["swa_qk"][bass.ds(h * HD + kv * 4 * HD, HD), :]),
                                        ("k", 0, k.scratch["swa_qk"][512 + kv * HD:512 + (kv + 1) * HD, :])],
                          HD, v2, y, kv * 256, window=(kv * 4, 512 + kv * HD, biases, sinks))
            turn(k, "swa_turn", y[:, :, 0:512], k.ones[:, 0:4], swa_y, 4)
        merged = k.sb("merged", [P, KD, S], ctx=ctx)
        with ExitStack() as normed:
            HT = pair(k, "attn_h", [P, KD, S], normed)
            norm_turn(k, "attn_norm", k.X, ST, k.gain("attn_norm_2"), HT)
            gated_merge(k, [("w_fox_out_2", fox_y, 2), ("w_conv_out_2", conv_y, 2), ("w_mlstm_out_2", ml_y, 2),
                        ("w_swa_out_2", swa_y, 4)], merged, HT)
        project_residual(k, "merge_out", k.dram["w_merge_out_2"][0], merged, KD)


def split_values(k, v2, vm):
    nc = k.nc
    with k.phase() as ctx:
        (made,) = k.sems("split", "made")
        block = ctx.enter_context(nc.Block())

        @block.gpsimd
        def _(pool):
            link = k.own("pool", pool)
            link(nc.gpsimd.memset(k.causal[:], 0.0))
            link(nc.gpsimd.affine_select(out=k.causal[:, S - P:S], in_=k.causal[:, S - P:S], compare_op=ALU.is_ge,
                                         fill=NEG, base=0, pattern=[[-1, P]], channel_multiplier=1))

        @block.vector
        def _(dve):
            for t in range(ST):
                nc.vector.tensor_copy(vm[:, t, :, 0:HD], v2[:, t, 256:512].rearrange("p (h n) -> p h n", n=HD)
                                      ).then_inc(made, 1)
        k.chains["pool"].settle()


def store(k, view, tile):
    nc = k.nc
    with k.phase() as ctx:
        (stored,) = k.sems("store", "stored")
        block = ctx.enter_context(nc.Block())

        @block.sync
        def _(sp):
            sp.dma_start(view, tile).then_inc(stored, 16)
            sp.wait_ge(stored, 16)


def swiglu(k):
    with ExitStack() as ctx:
        hidden = k.sb("hidden", [P, FFC, S], ctx=ctx)
        with ExitStack() as normed:
            H = pair(k, "ffn2_h", [P, KD, S], normed)
            norm_turn(k, "ffn2_norm", k.X, ST, k.gain("ffn_norm_2"), H)
            swiglu_up(k, hidden, H)
        load_rows(k, k.scratch["x_rows"].rearrange("(t p) d -> p t d", p=P), k.X)
        project_residual(k, "down", k.dram["w_down_2"][0], hidden, FFC)


def dump(k, tile):
    nc = k.nc
    with k.phase() as ctx:
        (stored,) = k.sems("dump", "stored")
        block = ctx.enter_context(nc.Block())

        @block.sync
        def _(sp):
            sp.dma_start(k.out.rearrange("a (t p) d -> p (a t) d", p=P), tile[:, :, :]).then_inc(stored, 16)
            sp.wait_ge(stored, 16)


def program(nc, dram, out):
    with ExitStack() as ctx:
        scratch = {name: nc.dram_tensor(f"scratch_{name}", shape, F32, kind="Internal").ap() for name, shape in (
            ("qk1", (2 * DIFF_QK, S)), ("qm", (MLA_HEADS * MLA_QK, S)), ("km", (MLA_HEADS * NOPE, S)),
            ("kpe", (ROPE, S)), ("ffn_rows", (S, D)), ("slot_token", (N_BLOCKS * BLK, 1)),
            ("expert_rows", (N_BLOCKS * BLK, D)), ("fox_qk", (512, S)), ("swa_qk", (640, S)), ("plain", (1280, S)),
            ("mo", (256, S)), ("fox_q", (8, S)), ("fox_k", (8, S)), ("mlstm_row", (4, S)), ("window_rows", (8, 3 * P)),
            ("x_rows", (S, D)), ("debug", (1280, S)))}
        k = Core(nc, ctx, dram, out, scratch)
        setup(k)
        first_mixer(k)
        cross_mixer(k)
        expert_layer(k)
        final_norm(k)
        second_mixer(k)
        swiglu(k)
        store(k, out.rearrange("a (t p) d -> p (a t) d", p=P), k.X[:, :, :])


def build(nc, inputs):
    dram = {}
    for name, a in inputs.items():
        dram[name] = nc.dram_tensor(f"in_{name}_dram", a.shape, mybir.dt.from_np(a.dtype), kind="ExternalInput").ap()
    out = nc.dram_tensor("out_0_dram", (1, S, D), F32, kind="ExternalOutput").ap()
    program(nc, dram, out)


def kernel(**inputs):
    import numpy as _np
    import concourse.bacc as _bacc
    from concourse.bass_utils import run_bass_kernel_spmd as _run

    nc = _bacc.Bacc("TRN2", target_bir_lowering=False, num_devices=1)
    arrays = {name: _np.ascontiguousarray(a) for name, a in inputs.items()}
    build(nc, arrays)
    r = _run(nc, [{f"in_{name}_dram": a for name, a in arrays.items()}], core_ids=[0])
    return r.results[0]["out_0_dram"]
```

```python
from contextlib import ExitStack

import numpy as np

import concourse.bass as bass
from concourse import mybir

F32 = mybir.dt.float32
F32R = mybir.dt.float32r
I32 = mybir.dt.int32
U32 = mybir.dt.uint32
ALU = mybir.AluOpType
ACT = mybir.ActivationFunctionType
AX = mybir.AxisListType.X

P = 128
S = 1024
D = 1024
ST = S // P
KD = D // P
HALF = 512
EPS = 1e-6
NEG = -1e30

DIFF_HEADS, DIFF_HALF, DIFF_V = 8, 32, 64
DIFF_QK = DIFF_HEADS * 2 * DIFF_HALF
DIFF_W = DIFF_HEADS * DIFF_V
MLA_HEADS, MLA_QR, MLA_KVR, NOPE, ROPE, MLA_V = 8, 256, 128, 64, 32, 64
MLA_QK = NOPE + ROPE
MLA_W = MLA_HEADS * MLA_V
COL_VD = 2 * DIFF_QK
COL_CQ = COL_VD + DIFF_W
COL_KPE = COL_CQ + MLA_QR + MLA_KVR
LAMBDA_INIT = 0.8 - 0.6
MEM_T, MEM_HEADS, MEM_HD = 256, 4, 128
MEM_W = MEM_HEADS * MEM_HD

GROUPS, PER_GROUP = 4, 8
EXPERTS = GROUPS * PER_GROUP
FF = 256
BLK = 128
N_BLOCKS = -(-(2 * S + EXPERTS * (BLK - 1)) // BLK)

HD = 64
C_FQ, C_FF, C_CU, C_MQ, C_MI, C_MO, C_SQ = 0, 768, 772, 1540, 2308, 2316, 2572
C_FV, C_MV, C_SV, C_GATES = 512, 2052, 3212, 3340
D_FF = 2816
FFC = D_FF // P
WINDOW = 128

GAIN_ROWS = {}
_row = 0
for _name, _count in (("norm_mix_g", 8), ("norm_cross_g", 8), ("norm_mem_g", 8), ("norm_ffn_g", 8),
                      ("attn_norm_2", 8), ("ffn_norm_2", 8), ("mla_out_g", 4), ("mla_q_norm_g", 2),
                      ("mla_kv_norm_g", 1), ("mlstm_h_gain_2", 2), ("conv_w_2", 6)):
    GAIN_ROWS[_name] = (_row, _count)
    _row += _count
for _name in ("diff_out_g", "fox_q_gain_2", "fox_k_gain_2", "swa_q_gain_2", "swa_k_gain_2"):
    GAIN_ROWS[_name] = (_row, 1)
    _row += 1
N_GAINS = _row


SEMS = 24


class Chain:

    def __init__(self, sem):
        self.sem, self.total, self.start, self.count = sem, 0, 0, 0

    def enter(self, i, per):
        self.start, self.count, self.per = self.total + i * per, 0, per

    def leave(self, rounds):
        assert self.count == self.per, (self.count, self.per)
        self.total += rounds * self.per
        self.start, self.count = self.total, 0

    def step(self):
        self.count += 1
        return self.start + self.count

    def settle(self):
        self.total += self.count
        self.start, self.count = self.total, 0


class Core:

    def __init__(self, nc, ctx, dram, out, scratch):
        self.nc, self.ctx, self.dram, self.out = nc, ctx, dram, out
        self.scratch = scratch
        self.chains, self.names = {}, {}
        sb = self.sb
        self.banks = [[ctx.enter_context(nc.semaphore(f"bank{n}_{i}")) for i in range(SEMS)] for n in range(2)]
        self.bank, self.taken = 0, 0
        self.soft = {n: ctx.enter_context(nc.semaphore(n)) for n in (
            "token_numbers_scattered", "rows_gathered0", "rows_gathered1", *(f"outputs_gathered{b}" for b in range(4)))}
        self.X = sb("X", [P, ST, D])
        self.ident = sb("ident", [P, P])
        self.ones = sb("ones", [P, P])
        self.ones64 = sb("ones64", [P, P])
        self.gains = sb("gains", [P, N_GAINS])
        self.ssq = sb("ssq", [P, ST])
        self.mean = sb("mean", [P, ST])
        self.root = sb("root", [P, ST])
        self.rstd = sb("rstd", [P, ST])
        for e in ("dve", "act", "pool"):
            self.chains[e] = Chain(ctx.enter_context(nc.semaphore(f"{e}_own")))

    def unused(self, name):
        self.names[name] = self.names.get(name, 0) + 1
        return name if self.names[name] == 1 else f"{name}_{self.names[name]}"

    def sb(self, name, shape, dt=F32, ctx=None):
        return (ctx or self.ctx).enter_context(self.nc.sbuf_tensor(self.unused(name), shape, dt))

    def ps(self, name, shape, ctx):
        return ctx.enter_context(self.nc.psum_tensor(self.unused(name), shape, F32))

    def phase(self):
        self.bank, self.taken = 1 - self.bank, 0
        other = [s.num for s in self.banks[1 - self.bank]]
        self.nc.gpsimd.sem_clear(range(min(other), max(other) + 1))
        return ExitStack()

    def sems(self, phase, names):
        n = len(names.split())
        got = self.banks[self.bank][self.taken:self.taken + n]
        assert len(got) == n, phase
        self.taken += n
        return got

    def gain(self, name, extra=0, count=None):
        row, n = GAIN_ROWS[name]
        return self.gains[:, row + extra:row + extra + (count or n)]

    def own(self, engine_name, engine):
        chain = self.chains[engine_name]

        def link(ins):
            value = chain.step()
            ins.then_inc(chain.sem, 1)
            engine.wait_ge(chain.sem, value)
        return link


def pair(k, name, shape, ctx):
    return k.sb(f"{name}_high", shape, F32R, ctx), k.sb(f"{name}_low", shape, F32R, ctx)


def add_product(nc, out, w, x, start, stop):
    if not isinstance(w, tuple):
        return nc.tensor.matmul(out, w, x, start=start, stop=stop)
    nc.tensor.matmul(out, w[0], x[0], start=start, stop=False)
    nc.tensor.matmul(out, w[0], x[1], start=False, stop=False)
    return nc.tensor.matmul(out, w[1], x[0], start=False, stop=stop)


def part(x, *index):
    return tuple(t[index] for t in x) if isinstance(x, tuple) else x[index]


def split_weights(nc, pool, j, b, loaded, raw, weights, products, split, passed):
    pool.wait_ge(*loaded)
    pool.wait_ge(products, j + 1)
    pool.sem_inc(passed, 1)
    nc.gpsimd.tensor_copy(weights[b][0][:], raw[b][:]).then_inc(split, 1)
    pool.wait_ge(split, 2 * j + 1 + 4)
    nc.gpsimd.tensor_tensor(weights[b][1][:], raw[b][:], weights[b][0][:], ALU.subtract).then_inc(split, 1)


def split_first(nc, engine, loaded, raw, weights, split):
    for b in range(2):
        if engine is nc.scalar:
            engine.wait_ge(loaded[b], 16)
            engine.wait_ge(split, 4 + 2 * b)
            nc.scalar.activation(weights[b][0][:], raw[b][:], ACT.Copy).then_inc(split, 1)
        else:
            engine.wait_ge(split, 4 + 2 * b + 1)
            nc.vector.tensor_tensor(weights[b][1][:], raw[b][:], weights[b][0][:], ALU.subtract).then_inc(split, 1)


def staged(engine, rounds, per_round, stages):
    def steps(i, count, before, own):
        for n in range(count):
            for lag, body in stages:
                if n >= lag and own:
                    body(i, n - lag, i * per_round + n - lag)
                elif n < lag and before:
                    body(i - 1, n - lag + per_round, i * per_round + n - lag)

    if len(stages) == 1:
        with engine.Fori(0, rounds) as i:
            steps(i, per_round, before=False, own=True)
        return
    steps(0, per_round, before=False, own=True)
    if rounds > 1:
        with engine.Fori(1, rounds) as i:
            steps(i, per_round, before=True, own=True)
    steps(rounds, max(lag for lag, _ in stages), before=True, own=False)


def setup(k):
    nc = k.nc
    with k.phase() as ctx:
        rows = k.sb("gain_rows", [N_GAINS, P], ctx=ctx)
        turned = k.ps("turned", [P, N_GAINS], ctx)
        x_in, gains_in, ident_made, gains_turned = k.sems("setup", "x_in gains_in ident_made gains_turned")
        block = ctx.enter_context(nc.Block())
        doubled = ("diff_out_g", "fox_q_gain_2", "fox_k_gain_2", "swa_q_gain_2", "swa_k_gain_2")
        n_loads = len(GAIN_ROWS) + len(doubled)

        @block.sync
        def _(sp):
            for name, (row, count) in GAIN_ROWS.items():
                if name in doubled:
                    for half in range(2):
                        sp.dma_start(rows[row:row + 1, half * 64:half * 64 + 64],
                                     k.dram[name]).then_inc(gains_in, 16)
                else:
                    flat = "l k c -> (l k c)" if name == "conv_w_2" else "l c -> (l c)"
                    src = k.dram[name].rearrange(flat).rearrange("(r c) -> r c", c=P)
                    sp.dma_start(rows[row:row + count, :], src).then_inc(gains_in, 16)

        @block.scalar
        def _(act):
            x = k.dram["x"].rearrange("a (t p) d -> p (a t) d", p=P)
            with act.Fori(0, ST) as t:
                act.dma_start(k.X[:, bass.ds(t, 1), :], x[:, bass.ds(t, 1), :]).then_inc(x_in, 16)
            act.wait_ge(x_in, 16 * ST)

        @block.gpsimd
        def _(pool):
            link = k.own("pool", pool)
            link(nc.gpsimd.memset(k.ident[:], 0.0))
            nc.gpsimd.affine_select(out=k.ident[:], in_=k.ident[:], compare_op=ALU.not_equal, fill=1.0,
                                    base=0, pattern=[[-1, P]], channel_multiplier=1).then_inc(ident_made, 1)
            link(nc.gpsimd.memset(k.ones64[:], 0.0))
            link(nc.gpsimd.memset(k.ones[:], 1.0))

        @block.vector
        def _(dve):
            link = k.own("dve", dve)
            dve.wait_ge(k.chains["pool"].sem, 3)
            link(nc.vector.memset(k.ones64[0:64, 0:64], 1.0))
            link(nc.vector.memset(k.ones64[64:128, 64:128], 1.0))
            dve.wait_ge(gains_turned, 1)
            link(nc.vector.tensor_copy(k.gains[:], turned[:, :]))

        @block.tensor
        def _(pe):
            pe.wait_ge(ident_made, 1)
            pe.wait_ge(gains_in, 16 * n_loads)
            nc.tensor.transpose(turned[:, :], rows[:, :], k.ident[0:N_GAINS, 0:N_GAINS]).then_inc(gains_turned, 1)

        for e in ("dve", "pool"):
            k.chains[e].settle()


def norm_turn(k, phase, X, tiles, gain, HT, rows_out=None, save=None):
    nc = k.nc
    pairs = tiles // 2
    with k.phase() as ctx:
        junk = [k.sb(f"{phase}_junk{b}", [P, D], ctx=ctx) for b in range(2)]
        scaled = [k.sb(f"{phase}_scaled{b}", [P, D], ctx=ctx) for b in range(2)]
        turned = [k.ps(f"{phase}_turned{b}", [P, KD, P], ctx) for b in range(2)]
        paired = isinstance(HT, tuple)
        plain = [tile[:].rearrange("p (c s) -> p c s", s=P) for tile in junk]
        even_squares, odd_squares, mean_ready, root_ready, rstd_ready, scaled_ready, turns, stored, kept0, kept1, highs, lows0, lows1, passed = k.sems(
            phase, "even_squares odd_squares mean_ready root_ready rstd_ready scaled_ready turns stored kept0 kept1 highs lows0 lows1 passed")
        kept, lows = (kept0, kept1), (lows0, lows1)
        block = ctx.enter_context(nc.Block())

        @block.scalar
        def _(act):
            act.sem_inc(kept0, 16)
            act.sem_inc(kept1, 16)
            for i in range(pairs):
                if i:
                    act.wait_ge(even_squares, i)
                nc.scalar.activation(junk[0][:], X[:, 2 * i, :], ACT.Square,
                                     accum_out=k.ssq[:, 2 * i:2 * i + 1]).then_inc(even_squares, 1)
            act.wait_ge(mean_ready, 1)
            nc.scalar.activation(k.root[:, 0:tiles], k.mean[:, 0:tiles], ACT.Sqrt).then_inc(root_ready, 1)
            act.wait_ge(rstd_ready, 1)

            def scale_rows(i, b, t):
                act.wait_ge(turns, t + 1)
                if rows_out is not None:
                    act.wait_ge(kept[b], 16 * i + 16)
                nc.scalar.activation(scaled[b][:], row_of(X, t), ACT.Copy,
                                     scale=k.rstd[:, bass.ds(t, 1)]).then_inc(scaled_ready, 1)

            def high_part(i, b, t):
                act.wait_ge(stored, t + 1 + 1)
                nc.scalar.activation(HT[0][:, :, bass.ds(t * P, P)], plain[b][:, :, :], ACT.Copy).then_inc(highs, 1)
            staged(act, pairs, 2, ((0, scale_rows), (1, high_part)) if paired else ((0, scale_rows),))

        @block.vector
        def _(dve):
            dve.sem_inc(stored, 1)
            link = k.own("dve", dve)
            for i in range(pairs):
                if i:
                    dve.wait_ge(odd_squares, i)
                nc.vector.tensor_tensor_reduce(out=junk[1][:], in0=X[:, 2 * i + 1, :], in1=X[:, 2 * i + 1, :],
                                               scale=1.0, scalar=0.0, op0=ALU.mult, op1=ALU.add,
                                               accum_out=k.ssq[:, 2 * i + 1:2 * i + 2]).then_inc(odd_squares, 1)
            dve.wait_ge(odd_squares, pairs)
            dve.wait_ge(even_squares, pairs)
            nc.vector.tensor_scalar(k.mean[:, 0:tiles], k.ssq[:, 0:tiles], 1.0 / D, EPS,
                                    ALU.mult, ALU.add).then_inc(mean_ready, 1)
            dve.wait_ge(root_ready, 1)
            nc.vector.reciprocal(k.rstd[:, 0:tiles], k.root[:, 0:tiles]).then_inc(rstd_ready, 1)

            def apply_gain(i, b, t):
                dve.wait_ge(turns, t + 1 + 2)
                if paired:
                    dve.wait_ge(lows[b], i + 1)
                target = plain[b][:, :, :] if paired else HT[:, :, bass.ds(t * P, P)]
                nc.vector.tensor_tensor(target, turned[b][:, :, :], gain.rearrange("p (c o) -> p c o", o=1).broadcast_to(
                    [P, KD, P]), ALU.mult).then_inc(stored, 1)

            def low_part(i, b, t):
                if b:
                    return
                dve.wait_ge(highs, t + 1)
                nc.vector.tensor_tensor(HT[1][:, :, bass.ds(t * P, P)], plain[b][:, :, :], HT[0][:, :, bass.ds(t * P, P)],
                                        ALU.subtract).then_inc(lows0, 1)
            dve.sem_inc(lows0, 1)
            staged(dve, pairs, 2, ((0, apply_gain), (1, low_part)) if paired else ((0, apply_gain),))

        if paired:
            @block.gpsimd
            def _(pool):
                pool.sem_inc(lows1, 1)
                with pool.Fori(0, pairs) as i:
                    pool.wait_ge(highs, 2 * i + 2)
                    pool.sem_inc(passed, 1)
                    cols = bass.ds((2 * i + 1) * P, P)
                    nc.gpsimd.tensor_tensor(HT[1][:, :, cols], plain[1][:, :, :], HT[0][:, :, cols],
                                            ALU.subtract).then_inc(lows1, 1)

        if save is not None:
            @block.sync
            def _(sp):
                sp.dma_start(save, X[:, :, :]).then_inc(kept0, 16)
                sp.wait_ge(kept0, 16 + 16)

        if rows_out is not None:
            @block.sync
            def _(sp):
                with sp.Fori(0, pairs) as i:
                    for b in range(2):
                        sp.wait_ge(scaled_ready, 2 * i + b + 1)
                        sp.dma_start(rows_out[bass.ds((2 * i + b) * P, P), :], scaled[b][:]).then_inc(kept[b], 16)
                sp.wait_ge(kept0, 16 * pairs + 16)
                sp.wait_ge(kept1, 16 * pairs + 16)

        @block.tensor
        def _(pe):
            pe.sem_inc(turns, 2)
            with pe.Fori(0, pairs) as i:
                for b in range(2):
                    pe.wait_ge(scaled_ready, 2 * i + b + 1)
                    if b == 0:
                        pe.wait_ge(stored, 2 * i + 1)
                    for c in range(KD):
                        last = nc.tensor.transpose(turned[b][:, c, :], scaled[b][:, c * P:(c + 1) * P], k.ident[:])
                    last.then_inc(turns, 1)


def row_of(X, t):
    return X[:, bass.ds(t, 1), :].rearrange("p a d -> p (a d)")


def project_rows(k, phase, w, n_chunks, src, kc, dest, scale=1.0, gain=None, tokens=S, low=None):
    nc = k.nc
    to_dram = not isinstance(dest, tuple)
    with k.phase() as ctx:
        raw = [k.sb(f"{phase}_w{b}", [P, kc, P], ctx=ctx) for b in range(2)]
        paired = isinstance(src, tuple)
        weights = [pair(k, f"{phase}_ws{b}", [P, kc, P], ctx) for b in range(2)] if paired else raw
        stage = [k.sb(f"{phase}_stage{b}", [P, tokens], F32R if low is not None else F32, ctx) for b in range(2)]
        low_stage = [k.sb(f"{phase}_low{b}", [P, tokens], F32R, ctx) for b in range(2)] if low is not None else None
        acc = [k.ps(f"{phase}_acc{b}", [P, max(tokens, HALF)], ctx) for b in range(2)]
        if gain is not None:
            square = k.sb(f"{phase}_square", [P, S], ctx=ctx)
            norm = k.sb(f"{phase}_norm", [P, S], ctx=ctx)
            sums = k.ps(f"{phase}_sums", [P, S], ctx)
            squared, summed, meaned, rooted = k.sems(phase, "squared summed meaned rooted")
        w_in0, w_in1, products, split, passed, evacuated, stored0, stored1, highs = k.sems(
            phase, "w_in0 w_in1 products split passed evacuated stored0 stored1 highs")
        stores = 1 if low is None else 2
        w_in, stored = (w_in0, w_in1), (stored0, stored1)
        block = ctx.enter_context(nc.Block())
        pairs, tail = n_chunks // 2, n_chunks % 2
        w_view = w.rearrange("(c p) n -> p c n", p=P)

        def chunks(engine, body, start=0):
            if start < pairs:
                with engine.Fori(start, pairs) as i:
                    for b in range(2):
                        body(i * 2 + b, b, i)
            if tail:
                body(pairs * 2, 0, pairs)

        @block.sync
        def _(sp):
            def load(j, b, r):
                if paired:
                    sp.wait_ge(split, 2 * j + 2)
                else:
                    sp.wait_ge(products, j + 1)
                sp.dma_start(raw[b][:, :, :], w_view[:, :, bass.ds(j * P, P)]).then_inc(w_in[b], 16)
            chunks(sp, load)

        if paired:
            @block.gpsimd
            def _(pool):
                pool.sem_inc(split, 4)
                pool.wait_ge(split, 4 + 4)
                chunks(pool, lambda j, b, r: split_weights(nc, pool, j, b, (w_in[b], 16 * r + 16), raw, weights, products,
                                                           split, passed), start=1)

        @block.tensor
        def _(pe):
            if gain is not None:
                pe.sem_inc(summed, 1)
            pe.sem_inc(products, 2)

            def multiply(j, b, r, sum_last):
                pe.wait_ge(*((split, 2 * j + 2 + 4) if paired else (w_in[b], 16 * r + 16)))
                pe.wait_ge(evacuated, j + 1)
                for c in range(kc):
                    if c == 2 and sum_last:
                        sum_squares(j - 1)
                    for at in range(0, tokens, HALF):
                        to = min(at + HALF, tokens)
                        last = add_product(nc, acc[b][:, at:to], part(weights[b], slice(None), c, slice(None)),
                                           part(src, slice(None), c, slice(at, to)), c == 0, c == kc - 1)
                last.then_inc(products, 1)

            def sum_squares(j):
                pe.wait_ge(squared, j + 1)
                pe.wait_ge(meaned, j + 1)
                for h in range(2):
                    last = nc.tensor.matmul(sums[:, h * HALF:(h + 1) * HALF], k.ones64[:],
                                            square[:, h * HALF:(h + 1) * HALF], start=True, stop=True)
                last.then_inc(summed, 1)

            if gain is None:
                chunks(pe, lambda j, b, r: multiply(j, b, r, False))
            else:
                multiply(0, 0, 0, False)
                multiply(1, 1, 0, True)
                chunks(pe, lambda j, b, r: multiply(j, b, r, True), start=1)
                sum_squares(n_chunks - 1)

        @block.scalar
        def _(act):
            act.sem_inc(stored0, 16)
            act.sem_inc(stored1, 16)
            if paired:
                split_first(nc, act, w_in, raw, weights, split)
            if gain is None:
                act.sem_inc(evacuated, 2)

            def leave(j, b, r):
                act.wait_ge(products, j + 1 + 2)
                if gain is not None:
                    act.wait_ge(summed, j + 1)
                    nc.scalar.activation(square[:], acc[b][:], ACT.Square).then_inc(squared, 1)
                    act.wait_ge(meaned, j + 1 + 1)
                    nc.scalar.activation(norm[:], norm[:], ACT.Ln).then_inc(rooted, 1)
                    act.wait_ge(rooted, 2 * j + 1)
                    nc.scalar.activation(norm[:], norm[:], ACT.Exp, scale=-0.5).then_inc(rooted, 1)
                elif low is not None:
                    act.wait_ge(stored[b], 32 * r + 16)
                    nc.scalar.activation(stage[b][:], acc[b][:, 0:tokens], ACT.Copy, scale=scale).then_inc(highs, 1)
                elif to_dram:
                    act.wait_ge(stored[b], 16 * r + 16)
                    nc.scalar.activation(stage[b][:], acc[b][:, 0:tokens], ACT.Copy, scale=scale).then_inc(evacuated, 1)
                else:
                    nc.scalar.activation(dest[0][:, bass.ds(j, 1), :].rearrange("p a s -> p (a s)"),
                                         acc[b][:, 0:tokens], ACT.Copy, scale=scale).then_inc(evacuated, 1)
                if to_dram:
                    act.wait_ge(evacuated, j + 1 + 2)
                    for target, source in ((dest, stage), (low, low_stage))[0:stores]:
                        act.dma_start(target.rearrange("(c p) s -> p c s", p=P)[:, bass.ds(j, 1), :].rearrange(
                            "p a s -> p (a s)"), source[b][:].bitcast(F32)).then_inc(stored[b], 16)
            chunks(act, leave)
            if to_dram:
                act.wait_ge(stored0, 16 * stores * (pairs + tail) + 16)
                act.wait_ge(stored1, 16 * stores * pairs + 16)

        if low is not None:
            @block.vector
            def _(dve):
                split_first(nc, dve, w_in, raw, weights, split)

                def low_part(j, b, r):
                    dve.wait_ge(highs, j + 1)
                    dve.wait_ge(stored[b], 32 * r + 16)
                    nc.vector.scalar_tensor_tensor(out=low_stage[b][:], in0=acc[b][:, 0:tokens], scalar=scale,
                                                   in1=stage[b][:], op0=ALU.mult, op1=ALU.subtract).then_inc(evacuated, 1)
                chunks(dve, low_part)

        if paired and low is None and gain is None:
            @block.vector
            def _(dve):
                split_first(nc, dve, w_in, raw, weights, split)

        if gain is not None:
            @block.vector
            def _(dve):
                dve.sem_inc(meaned, 1)
                if paired:
                    split_first(nc, dve, w_in, raw, weights, split)
                dve.sem_inc(evacuated, 2)

                def normalise(j, b, r):
                    dve.wait_ge(summed, j + 1 + 1)
                    nc.vector.tensor_scalar(norm[:], sums[:], 1.0 / HD, EPS, ALU.mult, ALU.add).then_inc(meaned, 1)
                    dve.wait_ge(rooted, 2 * j + 2)
                    dve.wait_ge(stored[b], 16 * r + 16)
                    nc.vector.scalar_tensor_tensor(out=stage[b][:], in0=acc[b][:], scalar=gain[:, bass.ds(j, 1)],
                                                   in1=norm[:], op0=ALU.mult, op1=ALU.mult).then_inc(evacuated, 1)
                chunks(dve, normalise)


def project_tokens(k, phase, loads, n_cols, src, kc, dest, tiles=ST):
    nc = k.nc
    pieces = [(c, min(HALF, n_cols - c)) for c in range(0, n_cols, HALF)]
    with k.phase() as ctx:
        weights = k.sb(f"{phase}_w", [P, kc, n_cols], ctx=ctx)
        tokens = [k.sb(f"{phase}_tokens{b}", [P, kc, P], ctx=ctx) for b in range(2)]
        acc = [k.ps(f"{phase}_acc{b}", [P, 2 * HALF], ctx) for b in range(2)]
        w_in, copied, products, evacuated, passed = k.sems(phase, "w_in copied products evacuated passed")
        block = ctx.enter_context(nc.Block())

        @block.sync
        def _(sp):
            for view, col, n in loads:
                into = weights[:, :, col:col + n]
                if kc == 1:
                    into = into.rearrange("p c (h n) -> p (c h) n", n=view.shape[-1])
                sp.dma_start(into, view).then_inc(w_in, 16)

        if isinstance(src, tuple):
            @block.gpsimd
            def _(pool):
                with pool.Fori(0, tiles // 2) as i:
                    for b in range(2):
                        pool.wait_ge(products, i * 2 + b + 1)
                        pool.sem_inc(passed, 1)
                        high, low = (x[:, 0:kc, bass.ds((i * 2 + b) * P, P)] for x in src)
                        nc.gpsimd.tensor_tensor(tokens[b][:, :, :], high, low, ALU.add).then_inc(copied, 1)
        else:
            @block.scalar
            def _(act):
                with act.Fori(0, tiles // 2) as i:
                    for b in range(2):
                        act.wait_ge(products, i * 2 + b + 1)
                        nc.scalar.activation(tokens[b][:, :, :], src[:, 0:kc, bass.ds((i * 2 + b) * P, P)],
                                             ACT.Copy).then_inc(copied, 1)

        @block.tensor
        def _(pe):
            pe.sem_inc(products, 2)
            pe.wait_ge(w_in, 16 * len(loads))
            with pe.Fori(0, tiles // 2) as i:
                for b in range(2):
                    pe.wait_ge(copied, i * 2 + b + 1)
                    pe.wait_ge(evacuated, i * 2 + b + 1)
                    for c in range(kc):
                        for at, n in pieces:
                            last = nc.tensor.matmul(acc[b][:, at:at + n], tokens[b][:, c, :],
                                                    weights[:, c, at:at + n], start=(c == 0), stop=(c == kc - 1))
                    last.then_inc(products, 1)

        @block.vector
        def _(dve):
            dve.sem_inc(evacuated, 2)
            with dve.Fori(0, tiles // 2) as i:
                for b in range(2):
                    dve.wait_ge(products, i * 2 + b + 1 + 2)
                    nc.vector.tensor_copy(row_of(dest, i * 2 + b), acc[b][:, 0:n_cols]).then_inc(evacuated, 1)


def project_residual(k, phase, w, src, kc, split_src=False, out=None, saved=None):
    nc = k.nc
    with k.phase() as ctx:
        raw = [k.sb(f"{phase}_w{b}", [P, kc, P], ctx=ctx) for b in range(2)]
        plain_src = src
        if split_src:
            src = pair(k, f"{phase}_src", [P, kc, S], ctx)
        paired = isinstance(src, tuple)
        weights = [pair(k, f"{phase}_ws{b}", [P, kc, P], ctx) for b in range(2)] if paired else raw
        rows = [k.sb(f"{phase}_rows{b}", [P, S], ctx=ctx) for b in range(2)]
        acc = [k.ps(f"{phase}_acc{b}", [P, S], ctx) for b in range(2)]
        turned = [k.ps(f"{phase}_turned{b}", [P, ST, P], ctx) for b in range(2)]
        w_in0, w_in1, products, split, src_split, passed, evacuated, turns, added, stored, x_in = k.sems(
            phase, "w_in0 w_in1 products split src_split passed evacuated turns added stored x_in")
        w_in = (w_in0, w_in1)
        block = ctx.enter_context(nc.Block())
        w_view = w.rearrange("(c p) n -> p c n", p=P)

        @block.sync
        def _(sp):
            with sp.Fori(0, KD // 2) as i:
                for b in range(2):
                    sp.wait_ge(*((split, 2 * (2 * i + b) + 2) if paired else (products, i * 2 + b + 1)))
                    sp.dma_start(raw[b][:, :, :], w_view[:, :, bass.ds((i * 2 + b) * P, P)]).then_inc(w_in[b], 16)

        if paired:
            @block.gpsimd
            def _(pool):
                pool.sem_inc(split, 4)
                pool.wait_ge(split, 4 + 4)
                with pool.Fori(1, KD // 2) as i:
                    for b in range(2):
                        split_weights(nc, pool, 2 * i + b, b, (w_in[b], 16 * i + 16), raw, weights, products, split, passed)

        @block.tensor
        def _(pe):
            pe.sem_inc(turns, 1)
            pe.sem_inc(products, 2)
            with pe.Fori(0, KD // 2) as i:
                for b in range(2):
                    pe.wait_ge(*((split, 2 * (2 * i + b) + 2 + 4) if paired else (w_in[b], 16 * i + 16)))
                    pe.wait_ge(evacuated, i * 2 + 1)
                    for c in range(kc):
                        if split_src:
                            pe.wait_ge(src_split, 2 * c + 2)
                        for h in range(2):
                            last = add_product(nc, acc[b][:, h * HALF:(h + 1) * HALF],
                                               part(weights[b], slice(None), c, slice(None)),
                                               part(src, slice(None), c, slice(h * HALF, (h + 1) * HALF)),
                                               c == 0, c == kc - 1)
                    last.then_inc(products, 1)
                for b in range(2):
                    pe.wait_ge(evacuated, i * 2 + b + 1 + 1)
                    pe.wait_ge(added, i * 2 + b + 1)
                    for t in range(ST):
                        last = nc.tensor.transpose(turned[b][:, t, :], rows[b][:, t * P:(t + 1) * P], k.ident[:])
                    last.then_inc(turns, 1)

        @block.scalar
        def _(act):
            act.sem_inc(evacuated, 1)
            if saved is not None:
                act.dma_start(k.X[:, :, :], saved).then_inc(x_in, 16)
            if paired:
                split_first(nc, act, w_in, raw, weights, split)
            if split_src:
                for c in range(kc):
                    if c:
                        act.wait_ge(src_split, 2 * c)
                    nc.scalar.activation(src[0][:, c, :], plain_src[:, c, :], ACT.Copy).then_inc(src_split, 1)
            with act.Fori(0, KD // 2) as i:
                for b in range(2):
                    act.wait_ge(products, i * 2 + b + 1 + 2)
                    act.wait_ge(turns, i * 2 + 1)
                    nc.scalar.activation(rows[b][:], acc[b][:], ACT.Copy).then_inc(evacuated, 1)
                if out is not None:
                    for b in range(2):
                        act.wait_ge(added, i * 2 + b + 1 + 2)
                        col = bass.ds((i * 2 + b) * P, P)
                        act.dma_start(out[:, :, col], k.X[:, :, col]).then_inc(stored, 16)
            if out is not None:
                act.wait_ge(stored, 16 * KD)

        @block.vector
        def _(dve):
            dve.sem_inc(added, 2)
            if saved is not None:
                dve.wait_ge(x_in, 16)
            if paired:
                split_first(nc, dve, w_in, raw, weights, split)
            if split_src:
                for c in range(kc):
                    dve.wait_ge(src_split, 2 * c + 1)
                    nc.vector.tensor_tensor(src[1][:, c, :], plain_src[:, c, :], src[0][:, c, :],
                                            ALU.subtract).then_inc(src_split, 1)
            with dve.Fori(0, KD // 2) as i:
                for b in range(2):
                    dve.wait_ge(turns, i * 2 + b + 1 + 1)
                    x = k.X[:, :, bass.ds((i * 2 + b) * P, P)]
                    nc.vector.tensor_tensor(x, x, turned[b][:, :, :], ALU.add).then_inc(added, 1)


def tables(k):
    nc = k.nc
    with k.phase() as ctx:
        scale = MLA_QK ** -0.5
        pos_row_i = k.sb("pos_row_i", [P, S], I32, ctx=ctx)
        pos_row = k.sb("pos_row", [P, S], ctx=ctx)
        lams = k.sb("lams", [P, 4, DIFF_HALF], ctx=ctx)
        lam_junk = k.sb("lam_junk", [P, 2, DIFF_HALF], ctx=ctx)
        lam_dot = k.sb("lam_dot", [P, 4], ctx=ctx)
        consts = k.sb("consts", [1, 4, P], ctx=ctx)
        cols = k.sb("cols", [P, 4], ctx=ctx)
        turns = k.sb("turns", [P, S], ctx=ctx)
        angle = k.rot
        cols_ps = k.ps("cols_ps", [P, 4], ctx)
        pos_in, lams_in, consts_made, cols_turned, dots, lam_exp, angle_made = k.sems(
            "tables", "pos_in lams_in consts_made cols_turned dots lam_exp angle_made")
        block = ctx.enter_context(nc.Block())

        @block.sync
        def _(sp):
            sp.dma_start(pos_row_i[:], k.dram["positions"].broadcast_to([P, S])).then_inc(pos_in, 16)
            for n, name in enumerate(("diff_lambda_q1", "diff_lambda_k1", "diff_lambda_q2", "diff_lambda_k2")):
                sp.dma_start(lams[:, n, :], k.dram[name].broadcast_to([P, DIFF_HALF])).then_inc(lams_in, 16)

        @block.gpsimd
        def _(pool):
            link = k.own("pool", pool)
            quarters = consts[:, :, :].rearrange("a n (q c) -> a n q c", q=4)
            for f in range(ROPE // 2):
                inv = float(np.float32(10000.0) ** np.float32(-2.0 * f / ROPE))
                nc.gpsimd.memset(consts[:, 0, :].rearrange("a (q f) -> a q f", f=ROPE // 2)[:, :, f:f + 1],
                                 inv).then_inc(consts_made, 1)
            for q, (turn, radian) in enumerate(((0.25, np.pi / 2), (0.0, 0.0)) * 2):
                nc.gpsimd.memset(quarters[:, 1, q, :], turn).then_inc(consts_made, 1)
                nc.gpsimd.memset(quarters[:, 2, q, :], float(radian)).then_inc(consts_made, 1)
            for q, (low, high) in enumerate(((1.0, 1.0), (-1.0, 1.0), (scale, scale), (-scale, scale))):
                nc.gpsimd.memset(quarters[:, 3, q, 0:16], low).then_inc(consts_made, 1)
                nc.gpsimd.memset(quarters[:, 3, q, 16:32], high).then_inc(consts_made, 1)
            for h in range(DIFF_HEADS):
                nc.gpsimd.memset(k.slopes[:, h:h + 1], -(2.0 ** (-8.0 * (h + 1) / DIFF_HEADS)) * DIFF_HALF ** 0.5).then_inc(consts_made, 1)
            link(nc.gpsimd.memset(k.causal[:], 0.0))
            link(nc.gpsimd.affine_select(out=k.causal[:, S - P:S], in_=k.causal[:, S - P:S], compare_op=ALU.is_ge,
                                         fill=NEG, base=0, pattern=[[-1, P]], channel_multiplier=1))

        @block.tensor
        def _(pe):
            pe.wait_ge(consts_made, 32 + DIFF_HEADS)
            for n in range(4):
                last = nc.tensor.transpose(cols_ps[:, n:n + 1], consts[0:1, n, :], k.ident[0:1, 0:1])
            last.then_inc(cols_turned, 1)

        @block.vector
        def _(dve):
            link = k.own("dve", dve)
            dve.wait_ge(lams_in, 64)
            for n in range(2):
                nc.vector.tensor_tensor_reduce(out=lam_junk[:, n, :], in0=lams[:, 2 * n, :], in1=lams[:, 2 * n + 1, :],
                                               scale=1.0, scalar=0.0, op0=ALU.mult, op1=ALU.add,
                                               accum_out=lam_dot[:, n:n + 1]).then_inc(dots, 1)
            dve.wait_ge(pos_in, 16)
            link(nc.vector.tensor_copy(pos_row[:], pos_row_i[:]))
            dve.wait_ge(lam_exp, 1)
            link(nc.vector.tensor_tensor(lam_dot[:, 3:4], lam_dot[:, 3:4], lam_dot[:, 2:3], ALU.subtract))
            link(nc.vector.tensor_scalar(k.neg_lambda[:], lam_dot[:, 3:4], -LAMBDA_INIT, None, ALU.add))
            dve.wait_ge(cols_turned, 1)
            link(nc.vector.tensor_copy(cols[:], cols_ps[:]))
            link(nc.vector.tensor_scalar(angle[:], pos_row[:], cols[:, 0:1], None, ALU.mult))
            link(nc.vector.tensor_scalar(turns[:], angle[:], 1.0 / (2 * np.pi), cols[:, 1:2], ALU.mult, ALU.add))
            link(nc.vector.tensor_scalar(turns[:], turns[:], 12582912.0, None, ALU.add))
            link(nc.vector.tensor_scalar(turns[:], turns[:], -12582912.0, None, ALU.add))
            c1 = 6.28125
            c2 = float(np.float32(np.round((2 * np.pi - c1) * 2 ** 20) / 2 ** 20))
            c3 = float(2 * np.pi - c1 - c2)
            for part in (c1, c2, c3):
                link(nc.vector.scalar_tensor_tensor(out=angle[:], in0=turns[:], scalar=-part, in1=angle[:],
                                                    op0=ALU.mult, op1=ALU.add))
            link(nc.vector.tensor_scalar(angle[:], angle[:], cols[:, 2:3], 3.1415925, ALU.add, ALU.min))
            nc.vector.tensor_scalar(angle[:], angle[:], -3.1415925, None, ALU.max).then_inc(angle_made, 1)
            dve.wait_ge(angle_made, 2)
            link(nc.vector.tensor_scalar(k.rot[:], k.rot[:], cols[:, 3:4], None, ALU.mult))

        @block.scalar
        def _(act):
            act.wait_ge(dots, 2)
            nc.scalar.activation(lam_dot[:, 2:4], lam_dot[:, 0:2], ACT.Exp).then_inc(lam_exp, 1)
            act.wait_ge(angle_made, 1)
            nc.scalar.activation(k.rot[:], angle[:], ACT.Sin).then_inc(angle_made, 1)

        for e in ("dve", "pool"):
            k.chains[e].settle()


def distances(k):
    nc = k.nc
    with k.phase() as ctx:
        pos_row_i = k.sb("pos_row_i", [P, S], I32, ctx=ctx)
        pos_row = k.sb("pos_row", [P, S], ctx=ctx)
        pos_col_i = k.sb("pos_col_i", [P, ST], I32, ctx=ctx)
        pos_col = k.sb("pos_col", [P, ST], ctx=ctx)
        pos_in, dist_made, masked = k.sems("distances", "pos_in dist_made masked")
        block = ctx.enter_context(nc.Block())

        @block.sync
        def _(sp):
            sp.dma_start(pos_row_i[:], k.dram["positions"].broadcast_to([P, S])).then_inc(pos_in, 16)
            with nc.allow_non_contiguous_dma(reason="1024 positions, one to a descriptor"):
                sp.dma_start(pos_col_i[:], k.dram["positions"].rearrange("a (t p) -> p (a t)", p=P)).then_inc(pos_in, 16)

        @block.vector
        def _(dve):
            link = k.own("dve", dve)
            dve.wait_ge(pos_in, 32)
            link(nc.vector.tensor_copy(pos_row[:], pos_row_i[:]))
            link(nc.vector.tensor_copy(pos_col[:], pos_col_i[:]))
            for t in range(ST):
                link(nc.vector.tensor_scalar(k.dist[:, t, :], pos_row[:], pos_col[:, t:t + 1], None, ALU.subtract))
                nc.vector.scalar_tensor_tensor(out=k.dist[:, t, :], in0=k.dist[:, t, :], scalar=-1.0, in1=k.dist[:, t, :],
                                               op0=ALU.mult, op1=ALU.max).then_inc(dist_made, 1)

        @block.gpsimd
        def _(pool):
            for t in range(ST):
                pool.wait_ge(dist_made, t + 1)
                diag = k.dist[:, t, t * P:(t + 1) * P]
                nc.gpsimd.affine_select(out=diag, in_=diag, compare_op=ALU.is_ge, fill=-NEG, base=0,
                                        pattern=[[-1, P]], channel_multiplier=1).then_inc(masked, 1)
        k.chains["dve"].settle()


def latent_up(k, cq, HT):
    nc = k.nc
    with k.phase() as ctx:
        scale = MLA_QK ** -0.5
        W = 3 * ROPE
        wk = k.sb("kpe_w", [P, KD, W], ctx=ctx)
        wk_pair = pair(k, "kpe_ws", [P, KD, W], ctx)
        work = k.sb("lat_work", [P, 4, S], ctx=ctx)
        sq = work[:, 0:3, :]
        norm = k.sb("lat_norm", [P, 2, S], ctx=ctx)
        wq = [k.sb(f"lat_wq{b}", [P, 2, P], ctx=ctx) for b in range(2)]
        wn = [k.sb(f"lat_wn{b}", [P, NOPE], ctx=ctx) for b in range(2)]
        turned = [k.sb(f"lat_rot{b}", [P, S], ctx=ctx) for b in range(2)]
        qs = [work[:, b, :] for b in range(2)]
        ks = [work[0:NOPE, 2 + b, :] for b in range(2)]
        kpe = k.sb("kpe", [ROPE, S], ctx=ctx)
        qp = [k.ps(f"lat_qp{b}", [P, S], ctx) for b in range(2)]
        kp = [k.ps(f"lat_kp{b}", [P, S], ctx) for b in range(2)]
        (wk_in, wk_split, kpe_made, kpe_read, sq_made, sums_made, mean_made, root_made, lat_made, wq_in0, wq_in1, heads,
         nopes, q_made, turned_made, stored) = k.sems("lat", "wk_in wk_split kpe_made kpe_read sq_made sums_made mean_made root_made lat_made "
                                         "wq_in0 wq_in1 heads nopes q_made turned_made stored")
        w_in = (wq_in0, wq_in1)
        block = ctx.enter_context(nc.Block())
        w_uq = k.dram["w_mla_uq"].rearrange("l (c p) (h n) -> p (l c) h n", p=P, n=MLA_QK)
        w_ukv = k.dram["w_mla_ukv"].rearrange("l p (h n) -> p (l h) n", n=NOPE + MLA_V)
        w_pe = k.dram["w_in"][0].rearrange("(c p) n -> p c n", p=P)
        half = ROPE // 2

        def head(i, b):
            return i * 2 + b

        @block.sync
        def _(sp):
            for at, col, n in ((0, COL_KPE, ROPE), (ROPE, COL_KPE + half, half), (ROPE + half, COL_KPE, half),
                               (2 * ROPE, COL_KPE, ROPE)):
                sp.dma_start(wk[:, :, at:at + n], w_pe[:, :, col:col + n]).then_inc(wk_in, 16)
            with sp.Fori(0, MLA_HEADS // 2) as i:
                for b in range(2):
                    sp.wait_ge(heads, head(i, b) + 1)
                    for at, col, n in ((0, 0, MLA_QK), (MLA_QK, NOPE + half, half), (MLA_QK + half, NOPE, half)):
                        sp.dma_start(wq[b][:, :, at:at + n],
                                     w_uq[:, :, bass.ds(head(i, b), 1), col:col + n].rearrange(
                                         "p c h n -> p c (h n)")).then_inc(w_in[b], 16)
                    sp.dma_start(wn[b][:], w_ukv[:, bass.ds(head(i, b), 1), 0:NOPE].rearrange(
                        "p h n -> p (h n)")).then_inc(w_in[b], 16)

        @block.gpsimd
        def _(pool):
            pool.wait_ge(wk_in, 64)
            nc.gpsimd.tensor_copy(wk_pair[0][:], wk[:]).then_inc(wk_split, 1)
            pool.wait_ge(wk_split, 1)
            nc.gpsimd.tensor_tensor(wk_pair[1][:], wk[:], wk_pair[0][:], ALU.subtract).then_inc(wk_split, 1)

        @block.tensor
        def _(pe):
            pe.sem_inc(heads, 2)
            pe.wait_ge(wk_split, 2)
            for c in range(KD):
                for h in range(2):
                    last = add_product(nc, qp[0][0:W, h * HALF:(h + 1) * HALF],
                                       part(wk_pair, slice(None), c, slice(None)),
                                       part(HT, slice(None), c, slice(h * HALF, (h + 1) * HALF)), c == 0, c == KD - 1)
            last.then_inc(kpe_made, 1)
            pe.wait_ge(sq_made, 1)
            for n, chunks in ((0, (0, 1)), (1, (2,))):
                for c in chunks:
                    for h in range(2):
                        last = nc.tensor.matmul(kp[n][:, h * HALF:(h + 1) * HALF], k.ones[:],
                                                sq[:, c, h * HALF:(h + 1) * HALF],
                                                start=(c == chunks[0]), stop=(c == chunks[-1]))
            last.then_inc(sums_made, 1)
            pe.wait_ge(lat_made, 3)
            pe.wait_ge(kpe_read, 1)
            with pe.Fori(0, MLA_HEADS // 2) as i:
                for b in range(2):
                    pe.wait_ge(w_in[b], 64 * i + 64)
                    pe.wait_ge(q_made, head(i, b) + 1)
                    for c in range(2):
                        for h in range(2):
                            last = nc.tensor.matmul(qp[b][:, h * HALF:(h + 1) * HALF], wq[b][:, c, :],
                                                    cq[:, c, h * HALF:(h + 1) * HALF], start=(c == 0), stop=(c == 1))
                    for h in range(2):
                        last = nc.tensor.matmul(kp[b][0:NOPE, h * HALF:(h + 1) * HALF], wn[b][:],
                                                cq[:, 2, h * HALF:(h + 1) * HALF], start=True, stop=True)
                    last.then_inc(heads, 1)

        @block.scalar
        def _(act):
            act.sem_inc(stored, 16)
            nc.scalar.activation(sq[:, :, :], cq[:, :, :], ACT.Square).then_inc(sq_made, 1)
            act.wait_ge(mean_made, 2)
            nc.scalar.activation(norm[:, :, :], norm[:, :, :], ACT.Ln).then_inc(root_made, 1)
            act.wait_ge(root_made, 1)
            nc.scalar.activation(norm[:, :, :], norm[:, :, :], ACT.Exp, scale=-0.5).then_inc(root_made, 1)
            act.sem_inc(nopes, 2 * 2)
            with act.Fori(0, MLA_HEADS // 2) as i:
                for b in range(2):
                    h = head(i, b)
                    act.wait_ge(heads, h + 1 + 2)
                    act.wait_ge(stored, 32 * h + 16)
                    nc.scalar.activation(qs[b][0:NOPE, :], qp[b][0:NOPE, :], ACT.Copy, scale=scale).then_inc(nopes, 1)
                    nc.scalar.activation(ks[b][:], kp[b][0:NOPE, :], ACT.Copy).then_inc(nopes, 1)
                    act.wait_ge(nopes, 2 * h + 2 + 4)
                    act.wait_ge(q_made, h + 1 + 2)
                    act.dma_start(k.scratch["qm"][bass.ds(h * MLA_QK, MLA_QK), :], qs[b][0:MLA_QK, :]).then_inc(stored, 16)
                    act.dma_start(k.scratch["km"][bass.ds(h * NOPE, NOPE), :], ks[b][:]).then_inc(stored, 16)
            act.dma_start(k.scratch["kpe"], kpe[:]).then_inc(stored, 16)
            act.wait_ge(stored, 32 * MLA_HEADS + 16 + 16)

        @block.vector
        def _(dve):
            link = k.own("dve", dve)
            dve.wait_ge(kpe_made, 1)
            link(nc.vector.tensor_tensor(turned[0][0:ROPE, :], qp[0][ROPE:2 * ROPE, :], k.rot[ROPE:2 * ROPE, :], ALU.mult))
            link(nc.vector.tensor_tensor(kpe[:], qp[0][0:ROPE, :], k.rot[0:ROPE, :], ALU.mult))
            nc.vector.tensor_tensor(kpe[:], kpe[:], turned[0][0:ROPE, :], ALU.add).then_inc(kpe_read, 1)
            dve.wait_ge(sums_made, 1)
            for n, width in ((0, MLA_QR), (1, MLA_KVR)):
                nc.vector.tensor_scalar(norm[:, n, :], kp[n][:], 1.0 / width, EPS, ALU.mult, ALU.add).then_inc(mean_made, 1)
            dve.wait_ge(root_made, 2)
            gains = (k.gain("mla_q_norm_g", 0, 1), k.gain("mla_q_norm_g", 1, 1), k.gain("mla_kv_norm_g"))
            for c in range(3):
                nc.vector.scalar_tensor_tensor(out=cq[:, c, :], in0=cq[:, c, :], scalar=gains[c], in1=norm[:, c // 2, :],
                                               op0=ALU.mult, op1=ALU.mult).then_inc(lat_made, 1)
            dve.sem_inc(q_made, 2)
            dve.wait_ge(kpe_read, 1)
            pe_rows, swapped_rows = slice(NOPE, MLA_QK), slice(MLA_QK, P)
            chain = k.chains["dve"]
            chain.settle()
            with dve.Fori(0, MLA_HEADS // 2) as i:
                chain.enter(i, 4)
                for b in range(2):
                    h = head(i, b)
                    dve.wait_ge(heads, h + 1 + 2)
                    dve.wait_ge(stored, 32 * h + 16)
                    link(nc.vector.tensor_tensor(turned[b][pe_rows, :], qp[b][swapped_rows, :], k.rot[swapped_rows, :], ALU.mult))
                    link(nc.vector.tensor_tensor(qs[b][pe_rows, :], qp[b][pe_rows, :], k.rot[pe_rows, :], ALU.mult))
                    dve.wait_ge(nopes, 2 * h + 2 + 4)
                    nc.vector.tensor_tensor(qs[b][pe_rows, :], qs[b][pe_rows, :], turned[b][pe_rows, :],
                                            ALU.add).then_inc(q_made, 1)
                chain.leave(MLA_HEADS // 2)


TURN = 2


def attention(k, phase, heads, loads, rows, V, out, out_col, maps=1, packed=False, alibi=False, scale=1.0,
              window=None):
    nc = k.nc
    with k.phase() as ctx:
        kind = F32R if packed else F32
        q = [[k.sb(f"{phase}_q{m}{b}", [P, S], kind, ctx) for m in range(maps)] for b in range(2)]
        kk = [[k.sb(f"{phase}_k{m}{b}", [P, S], kind, ctx) for m in range(maps)] for b in range(2)]
        probs = [[k.sb(f"{phase}_p{m}{b}", [P, S], ctx=ctx) for b in range(4 - 2 * m)] for m in range(maps)]
        turned_sb = [k.sb(f"{phase}_pt{b}", [P, ST, P], ctx=ctx) for b in range(2)]
        slope = [k.sb(f"{phase}_slope{b}", [P, 1], ctx=ctx) for b in range(2)]
        bias = [k.sb(f"{phase}_bias{b}", [P, S], ctx=ctx) for b in range(2)] if alibi else None
        head_bias = [k.sb(f"{phase}_hbias{b}", [P, 2 * P], ctx=ctx) for b in range(2)] if window else None
        sink = [k.sb(f"{phase}_sink{b}", [P, 1], ctx=ctx) for b in range(2)] if window else None
        stats = [k.sb(f"{phase}_stats{n}", [P, 9], ctx=ctx) for n in range(8)]
        scores = [k.ps(f"{phase}_scores{n}", [P, S], ctx) for n in range(2)]
        turned = k.ps(f"{phase}_turned", [P, ST, P], ctx)
        outs = [k.ps(f"{phase}_out{b}", [P, HD], ctx) for b in range(2)]
        (head_in0, head_in1, products, biased, scored, maxed, exps, weighed, mixed, turns, copied, values, done,
         passed) = k.sems(phase, "head_in0 head_in1 products biased scored maxed exps weighed mixed turns copied "
                          "values done passed")
        head_in = (head_in0, head_in1)
        block = ctx.enter_context(nc.Block())
        per_round = 2 * ST
        n_loads = len(loads(0, 0))
        rounds = heads // 2
        ready = mixed if maps == 2 else exps

        def first(t):
            return max(t - 1, 0) if window else 0

        def parts(width):
            return [(c, min(HALF, width - c)) for c in range(0, width, HALF)]

        def value_cols(i, b):
            return slice(window[1], window[1] + HD) if window else bass.ds((i * 2 + b) * HD, HD)

        @block.sync
        def _(sp):
            with sp.Fori(0, rounds) as i:
                for b in range(2):
                    sp.wait_ge(products, (i * 2 + b) * ST * maps + 1)
                    for which, m, row, src in loads(b, i * 2 + b):
                        tile = (q if which == "q" else kk)[b][m]
                        sp.dma_start(tile[row:row + src.shape[0], :].bitcast(F32), src).then_inc(head_in[b], 16)

        @block.tensor
        def _(pe):
            pe.sem_inc(products, 1 + ST * maps)
            pe.sem_inc(turns, 4)
            pe.sem_inc(values, 2)

            def score(i, n, g):
                b, t = n // ST, n % ST
                if t == 0:
                    pe.wait_ge(head_in[b], 16 * n_loads * i + 16 * n_loads)
                for m in range(maps):
                    pe.wait_ge(scored, g * maps + m + 1 + 1)
                    ps = scores[m if maps == 2 else n % 2]
                    for at, w in parts((t + 1 - first(t)) * P):
                        key = first(t) * P + at
                        last = nc.tensor.matmul(ps[:, at:at + w], q[b][m][0:rows, t * P:(t + 1) * P],
                                                kk[b][m][0:rows, key:key + w], start=True, stop=True)
                    last.then_inc(products, 1)

            def turn_probs(i, n, g):
                t = n % ST
                pe.wait_ge(ready, g + 1 + maps)
                pe.wait_ge(copied, g + 1)
                for c in range(t + 1 - first(t)):
                    last = nc.tensor.transpose(turned[:, c, :], probs[0][n % 4][:, c * P:(c + 1) * P], k.ident[:])
                last.then_inc(turns, 1)

            def multiply(i, n, g):
                b, t = n // ST, n % ST
                pe.wait_ge(copied, g + 1 + 1)
                pe.wait_ge(done, g + 1)
                for c in range(first(t), t + 1):
                    last = nc.tensor.matmul(outs[n % 2][:], turned_sb[n % 2][:, c - first(t), :],
                                            V[:, c, value_cols(i, b)], start=(c == first(t)), stop=(c == t))
                last.then_inc(values, 1)
            staged(pe, rounds, per_round, ((0, score), (TURN, turn_probs), (TURN + 1, multiply)))

        @block.vector
        def _(dve):
            dve.sem_inc(scored, 3)
            if maps == 2:
                dve.sem_inc(mixed, 2)
            dve.sem_inc(done, 2)
            per_step = 2 if maps == 2 or window else 1

            def shift(i, n, g):
                t = n % ST
                w = (t + 1 - first(t)) * P
                st = stats[n % 8]
                if maps == 2:
                    dve.wait_ge(mixed, g + 1)
                dve.wait_ge(turns, g + 1)
                if alibi:
                    dve.wait_ge(biased, g + 2)
                if window and t == 0:
                    dve.wait_ge(biased, 2 * (i * 2 + n // ST) + 2)
                for m in range(maps):
                    dve.wait_ge(products, g * maps + m + 1 + ST * maps + 1)
                    dve.sem_inc(passed, 1)
                    ps = scores[m if maps == 2 else n % 2]
                    b_ap = (bias[n % 2][:, 0:w] if alibi else head_bias[n // ST][:, 2 * P - w:2 * P] if window
                            else k.causal[:, S - w:S])
                    least = sink[n // ST][:, 0:1] if window else -3e38
                    nc.vector.tensor_tensor_reduce(out=probs[m][n % (4 - 2 * m)][:, 0:w], in0=ps[:, 0:w], in1=b_ap,
                                                   scale=scale, scalar=least, op0=ALU.add, op1=ALU.max,
                                                   accum_out=st[:, m:m + 1]).then_inc(scored, 1)
                dve.wait_ge(scored, (g + 1) * maps + 2 + 1)
                nc.vector.tensor_scalar(st[:, 2:2 + maps], st[:, 0:maps], -1.0, None, ALU.mult).then_inc(maxed, 1)

            def weigh(i, n, g):
                t, st = n % ST, stats[n % 8]
                w = (t + 1 - first(t)) * P
                dve.wait_ge(exps, g + 1 + 1)
                if window:
                    nc.vector.tensor_tensor(st[:, 4:5], st[:, 4:5], st[:, 8:9], ALU.add).then_inc(weighed, 1)
                    dve.wait_ge(weighed, g * per_step + 1)
                nc.vector.reciprocal(st[:, 6:6 + maps], st[:, 4:4 + maps]).then_inc(weighed, 1)
                if maps == 2:
                    dve.wait_ge(weighed, g * per_step + 1)
                    nc.vector.scalar_tensor_tensor(out=st[:, 8:9], in0=st[:, 4:5], scalar=k.neg_lambda[:, 0:1],
                                                   in1=st[:, 7:8], op0=ALU.mult, op1=ALU.mult).then_inc(weighed, 1)
                    dve.wait_ge(weighed, g * per_step + 2)
                    nc.vector.scalar_tensor_tensor(out=probs[0][n % 4][:, 0:w], in0=probs[1][n % 2][:, 0:w],
                                                   scalar=st[:, 8:9], in1=probs[0][n % 4][:, 0:w],
                                                   op0=ALU.mult, op1=ALU.add).then_inc(mixed, 1)

            def scale_out(i, n, g):
                b, t = n // ST, n % ST
                dve.wait_ge(values, g + 1 + 2)
                dve.wait_ge(weighed, (g + 1) * per_step)
                nc.vector.tensor_scalar(out[:, t, bass.ds((i * 2 + b) * HD + out_col, HD)], outs[n % 2][:],
                                        stats[n % 8][:, 6:7], None, ALU.mult).then_inc(done, 1)
            staged(dve, rounds, per_round, ((0, shift), (TURN - 1, weigh), (TURN + 2, scale_out)))

        @block.scalar
        def _(act):
            act.sem_inc(exps, 1)
            act.sem_inc(copied, 1)

            def copy_turned(i, n, g):
                t = n % ST
                act.wait_ge(turns, g + 1 + 4)
                act.wait_ge(values, g + 1)
                nc.scalar.activation(turned_sb[n % 2][:, 0:t + 1 - first(t), :],
                                     turned[:, 0:t + 1 - first(t), :], ACT.Copy).then_inc(copied, 1)

            def exponentials(i, n, g):
                w, st = (n % ST + 1 - first(n % ST)) * P, stats[n % 8]
                act.wait_ge(maxed, g + 1)
                if window:
                    nc.scalar.activation(st[:, 8:9], sink[n // ST][:], ACT.Exp, bias=st[:, 2:3])
                for m in range(maps):
                    p = probs[m][n % (4 - 2 * m)][:, 0:w]
                    last = nc.scalar.activation(p, p, ACT.Exp,
                                                bias=st[:, 2 + m:3 + m], accum_out=st[:, 4 + m:5 + m])
                last.then_inc(exps, 1)
            staged(act, rounds, per_round, ((TURN, copy_turned), (0, exponentials)))

        if window:
            @block.gpsimd
            def _(pool):
                with pool.Fori(0, rounds) as i:
                    pool.wait_ge(scored, i * per_round + 2 + 1)
                    pool.wait_ge(exps, i * per_round + 1)
                    for b in range(2):
                        head = bass.ds(i * 2 + b + window[0], 1)
                        nc.gpsimd.tensor_copy(head_bias[b][:], window[2][:, head, :].rearrange("p h c -> p (h c)")
                                              ).then_inc(biased, 1)
                        nc.gpsimd.tensor_copy(sink[b][:], window[3][:, head]).then_inc(biased, 1)

        if alibi:
            @block.gpsimd
            def _(pool):
                pool.sem_inc(biased, 1)
                chain = k.chains["pool"]
                link = k.own("pool", pool)
                with pool.Fori(0, rounds) as i:
                    chain.enter(i, 2)
                    for n in range(per_round):
                        b, t = n // ST, n % ST
                        w = (t + 1) * P
                        if t == 0:
                            pool.wait_ge(biased, i * per_round + n + 1)
                            pool.sem_inc(passed, 1)
                            link(nc.gpsimd.tensor_copy(slope[b][:], k.slopes[:, bass.ds(i * 2 + b, 1)]))
                        pool.wait_ge(scored, (i * per_round + n) * 2 + 1)
                        pool.sem_inc(passed, 1)
                        nc.gpsimd.tensor_scalar(bias[n % 2][:, 0:w], k.dist[:, t, 0:w], slope[b][:], 1.0,
                                                ALU.mult, ALU.mult).then_inc(biased, 1)
                    chain.leave(rounds)


def head_norm(k, phase, Y, heads, width, factor):
    nc = k.nc
    with k.phase() as ctx:
        sq = k.sb(f"{phase}_sq", [P, ST, heads * width], ctx=ctx)
        norm = k.sb(f"{phase}_norm", [P, ST, heads], ctx=ctx)
        squared, mean_made, root_made, norm_made = k.sems(phase, "squared mean_made root_made norm_made")
        block = ctx.enter_context(nc.Block())
        n = ST * heads

        @block.scalar
        def _(act):
            nc.scalar.activation(sq[:, :, :], Y, ACT.Square).then_inc(squared, 1)
            act.wait_ge(mean_made, 1)
            nc.scalar.activation(norm[:, :, :], norm[:, :, :], ACT.Sqrt).then_inc(root_made, 1)

        @block.vector
        def _(dve):
            link = k.own("dve", dve)
            dve.wait_ge(squared, 1)
            link(nc.vector.tensor_reduce(norm[:, :, :], sq[:, :, :].rearrange("p t (h w) -> p t h w", w=width), AX, ALU.add))
            nc.vector.tensor_scalar(norm[:, :, :], norm[:, :, :], 1.0 / width / factor ** 2, EPS / factor ** 2,
                                    ALU.mult, ALU.add).then_inc(mean_made, 1)
            dve.wait_ge(root_made, 1)
            link(nc.vector.reciprocal(norm[:, :, :], norm[:, :, :]))
            for t in range(ST):
                link(nc.vector.tensor_tensor(Y[:, t, :].rearrange("p (h w) -> p h w", w=width),
                                             Y[:, t, :].rearrange("p (h w) -> p h w", w=width),
                                             norm[:, t, :].rearrange("p (h o) -> p h o", o=1).broadcast_to([P, heads, width]),
                                             ALU.mult))
        k.chains["dve"].settle()


def turn(k, phase, Y, gain, dest, chunks):
    nc = k.nc
    with k.phase() as ctx:
        tiles = [k.sb(f"{phase}_tile{b}", [P, chunks * P], ctx=ctx) for b in range(2)]
        turned = [k.ps(f"{phase}_turned{b}", [P, chunks, P], ctx) for b in range(2)]
        paired = isinstance(dest, tuple)
        plain = [k.sb(f"{phase}_plain{b}", [P, chunks, P], ctx=ctx) for b in range(2)] if paired else None
        copied, turns, stored, highs, lows = k.sems(phase, "copied turns stored highs lows")
        block = ctx.enter_context(nc.Block())

        @block.scalar
        def _(act):
            def copy_rows(i, b, t):
                act.wait_ge(turns, t + 1)
                nc.scalar.activation(tiles[b][:], row_of(Y, t), ACT.Copy).then_inc(copied, 1)

            def high_part(i, b, t):
                act.wait_ge(stored, t + 1 + 1)
                nc.scalar.activation(dest[0][:, 0:chunks, bass.ds(t * P, P)], plain[b][:, :, :], ACT.Copy).then_inc(highs, 1)
            staged(act, ST // 2, 2, ((0, copy_rows), (1, high_part)) if paired else ((0, copy_rows),))

        @block.tensor
        def _(pe):
            pe.sem_inc(turns, 2)
            with pe.Fori(0, ST // 2) as i:
                for b in range(2):
                    pe.wait_ge(copied, 2 * i + b + 1)
                    pe.wait_ge(stored, 2 * i + 1)
                    for c in range(chunks):
                        last = nc.tensor.transpose(turned[b][:, c, :], tiles[b][:, c * P:(c + 1) * P], k.ident[:])
                    last.then_inc(turns, 1)

        @block.vector
        def _(dve):
            dve.sem_inc(stored, 1)

            def apply_gain(i, b, t):
                dve.wait_ge(turns, t + 1 + 2)
                if paired:
                    dve.wait_ge(lows, t + 1)
                target = plain[b][:, :, :] if paired else dest[:, 0:chunks, bass.ds(t * P, P)]
                nc.vector.tensor_tensor(target, turned[b][:, :, :], gain.rearrange("p (c o) -> p c o", o=1).broadcast_to(
                    [P, chunks, P]), ALU.mult).then_inc(stored, 1)

            def low_part(i, b, t):
                dve.wait_ge(highs, t + 1)
                high, low = (x[:, 0:chunks, bass.ds(t * P, P)] for x in dest)
                nc.vector.tensor_tensor(low, plain[b][:, :, :], high, ALU.subtract).then_inc(lows, 1)
            dve.sem_inc(lows, 2)
            staged(dve, ST // 2, 2, ((0, apply_gain), (1, low_part)) if paired else ((0, apply_gain),))


def first_mixer(k):
    nc = k.nc
    w_in = k.dram["w_in"][0]
    with ExitStack() as ctx:
        vd = k.sb("vd", [P, ST, DIFF_W], ctx=ctx)
        vm = k.sb("vm", [P, ST, MLA_W], ctx=ctx)
        k.causal = k.sb("causal", [P, S], ctx=ctx)
        k.slopes = k.sb("slopes", [P, DIFF_HEADS], ctx=ctx)
        k.neg_lambda = k.sb("neg_lambda", [P, 1], ctx=ctx)
        with ExitStack() as early:
            cq = k.sb("cq", [P, 3, S], ctx=early)
            with ExitStack() as tab:
                k.rot = k.sb("rot", [P, S], ctx=tab)
                H = pair(k, "mix_h", [P, KD, S], tab)
                tables(k)
                norm_turn(k, "mix_norm", k.X, ST, k.gain("norm_mix_g"), H)
                project_rows(k, "diff_qk", w_in[:, 0:2 * DIFF_QK], 2 * DIFF_QK // P, H, KD, k.scratch["qk1"],
                             low=k.scratch["qk1_low"])
                project_rows(k, "latents", w_in[:, COL_CQ:COL_KPE], 3, H, KD, (cq,))
                project_tokens(k, "diff_v", [(w_in[:, COL_VD:COL_CQ].rearrange("(c p) n -> p c n", p=P), 0, DIFF_W)],
                               DIFF_W, H, KD, vd)
                latent_up(k, cq, H)
            w_ukv = k.dram["w_mla_ukv"].rearrange("l p (h n) -> p (l h) n", n=NOPE + MLA_V)
            project_tokens(k, "latent_v", [(w_ukv[:, :, NOPE:], 0, MLA_W)], MLA_W, cq[:, 2:3, :], 1, vm)
        mix = k.sb("mix", [P, ST, D], ctx=ctx)
        far = ctx.enter_context(ExitStack())
        k.dist = k.sb("dist", [P, ST, S], ctx=far)
        distances(k)
        high, low = k.scratch["qk1"], k.scratch["qk1_low"]
        attention(k, "diff", DIFF_HEADS,
                  lambda b, h: [(which, m, part_row * DIFF_HALF, src[bass.ds(h * HD + (m * DIFF_HALF + first), DIFF_HALF), :])
                                for which, first, parts in (("q", 0, (high, high, low)), ("k", DIFF_QK, (high, low, high)))
                                for m in range(2) for part_row, src in enumerate(parts)],
                  3 * DIFF_HALF, vd, mix, 0, maps=2, packed=True, alibi=True, scale=DIFF_HALF ** -0.5)
        attention(k, "latent", MLA_HEADS,
                  lambda b, h: [("q", 0, 0, k.scratch["qm"][bass.ds(h * MLA_QK, MLA_QK), :]),
                                ("k", 0, 0, k.scratch["km"][bass.ds(h * NOPE, NOPE), :]),
                                ("k", 0, NOPE, k.scratch["kpe"])],
                  MLA_QK, vm, mix, DIFF_W)
        far.close()
        head_norm(k, "diff_rms", mix[:, :, 0:DIFF_W], DIFF_HEADS, DIFF_V, 1.0 - LAMBDA_INIT)
        head_norm(k, "latent_rms", mix[:, :, DIFF_W:D], 1, MLA_W, 1.0)
        H = pair(k, "mixed", [P, KD, S], ctx)
        diff_gain, latent_gain = k.gain("diff_out_g"), k.gain("mla_out_g")
        turn(k, "diff_turn", mix[:, :, 0:DIFF_W], diff_gain, part(H, slice(None), slice(0, 4)), 4)
        turn(k, "latent_turn", mix[:, :, DIFF_W:D], latent_gain, part(H, slice(None), slice(4, 8)), 4)
        project_residual(k, "mix_out", k.dram["w_out"][0], H, KD)


def memory_attention(k, q, km, vm, out):
    nc = k.nc
    with k.phase() as ctx:
        qt = [k.sb(f"mem_qt{b}", [P, MEM_HEADS, P], ctx=ctx) for b in range(2)]
        probs = [k.sb(f"mem_p{b}", [P, MEM_HEADS, MEM_T], ctx=ctx) for b in range(4)]
        turned_sb = [k.sb(f"mem_pt{b}", [P, 2 * MEM_HEADS, P], ctx=ctx) for b in range(2)]
        stats = [k.sb(f"mem_stats{b}", [P, 3, MEM_HEADS], ctx=ctx) for b in range(4)]
        scores = [k.ps(f"mem_scores{b}", [P, MEM_HEADS, MEM_T], ctx) for b in range(2)]
        turned = k.ps("mem_turned", [P, 2 * MEM_HEADS, P], ctx)
        outs = [k.ps(f"mem_out{b}", [P, MEM_HEADS, P], ctx) for b in range(2)]
        q_copied, products, maxed, shifted, exps, summed, probs_ready, turns, copied, values, done = k.sems(
            "mem", "q_copied products maxed shifted exps summed probs_ready turns copied values done")
        block = ctx.enter_context(nc.Block())

        def across(column):
            return column.rearrange("p (h o) -> p h o", o=1).broadcast_to([P, MEM_HEADS, MEM_T])

        rounds, per_round = 2, ST // 2

        @block.tensor
        def _(pe):
            pe.sem_inc(products, 2)
            pe.sem_inc(turns, 4)
            pe.sem_inc(values, 2)

            def score(i, n, g):
                pe.wait_ge(q_copied, g + 1)
                pe.wait_ge(shifted, g + 1)
                for h in range(MEM_HEADS):
                    last = nc.tensor.matmul(scores[n % 2][:, h, :], qt[n % 2][:, h, :], km[:, h, :], start=True, stop=True)
                last.then_inc(products, 1)

            def turn_probs(i, n, g):
                pe.wait_ge(probs_ready, g + 1)
                pe.wait_ge(copied, g + 1)
                for c in range(2 * MEM_HEADS):
                    last = nc.tensor.transpose(turned[:, c, :], probs[n % 4][:, c // 2, (c % 2) * P:(c % 2 + 1) * P],
                                               k.ident[:])
                last.then_inc(turns, 1)

            def multiply(i, n, g):
                pe.wait_ge(copied, g + 1 + 1)
                pe.wait_ge(done, g + 1)
                for h in range(MEM_HEADS):
                    for c in range(2):
                        last = nc.tensor.matmul(outs[n % 2][:, h, :], vm[:, c, h * MEM_HD:(h + 1) * MEM_HD],
                                                turned_sb[n % 2][:, 2 * h + c, :], start=(c == 0), stop=(c == 1))
                last.then_inc(values, 1)
            staged(pe, rounds, per_round, ((0, score), (2, turn_probs), (3, multiply)))

        @block.vector
        def _(dve):
            dve.sem_inc(done, 2)
            dve.sem_inc(shifted, 2)

            def shift(i, n, g):
                dve.wait_ge(products, g + 1 + 2)
                dve.wait_ge(turns, g + 1)
                ps, p, st = scores[n % 2], probs[n % 4], stats[n % 4]
                nc.vector.tensor_reduce(st[:, 0, :], ps[:, :, :], AX, ALU.max).then_inc(maxed, 1)
                dve.wait_ge(maxed, g + 1)
                nc.vector.tensor_tensor(p[:, :, :], ps[:, :, :], across(st[:, 0, :]), ALU.subtract).then_inc(shifted, 1)

            def weigh(i, n, g):
                dve.wait_ge(exps, g + 1)
                p, st = probs[n % 4], stats[n % 4]
                nc.vector.tensor_reduce(st[:, 1, :], p[:, :, :], AX, ALU.add).then_inc(summed, 1)
                dve.wait_ge(summed, 2 * g + 1)
                nc.vector.reciprocal(st[:, 2, :], st[:, 1, :]).then_inc(summed, 1)
                dve.wait_ge(summed, 2 * g + 2)
                nc.vector.tensor_tensor(p[:, :, :], p[:, :, :], across(st[:, 2, :]), ALU.mult).then_inc(probs_ready, 1)

            def leave(i, n, g):
                dve.wait_ge(values, g + 1 + 2)
                nc.vector.tensor_copy(out[:, :, bass.ds((i * per_round + n) * P, P)], outs[n % 2][:, :, :]).then_inc(done, 1)
            staged(dve, rounds, per_round, ((0, shift), (1, weigh), (4, leave)))

        @block.scalar
        def _(act):
            act.sem_inc(copied, 1)

            def copy_queries(i, n, g):
                act.wait_ge(products, g + 1)
                nc.scalar.activation(qt[n % 2][:, :, :], q[:, :, bass.ds((i * per_round + n) * P, P)],
                                     ACT.Copy).then_inc(q_copied, 1)

            def exponentials(i, n, g):
                act.wait_ge(shifted, g + 1 + 2)
                nc.scalar.activation(probs[n % 4][:, :, :], probs[n % 4][:, :, :], ACT.Exp).then_inc(exps, 1)

            def copy_turned(i, n, g):
                act.wait_ge(turns, g + 1 + 4)
                act.wait_ge(values, g + 1)
                nc.scalar.activation(turned_sb[n % 2][:, :, :], turned[:, :, :], ACT.Copy).then_inc(copied, 1)
            staged(act, rounds, per_round, ((3, copy_turned), (1, exponentials), (0, copy_queries)))


def cross_mixer(k):
    nc = k.nc
    with ExitStack() as ctx:
        H = pair(k, "cross_h", [P, KD, S], ctx)
        norm_turn(k, "cross_norm", k.X, ST, k.gain("norm_cross_g"), H)
        out = k.sb("mem_mixed", [P, MEM_HEADS, S], ctx=ctx)
        with ExitStack() as inner:
            q = k.sb("mem_q", [P, MEM_HEADS, S], ctx=inner)
            km = k.sb("mem_k", [P, MEM_HEADS, MEM_T], ctx=inner)
            vm = k.sb("mem_v", [P, MEM_T // P, MEM_W], ctx=inner)
            mem = k.sb("mem_x", [P, MEM_T // P, D], ctx=inner)
            mem_t = k.sb("mem_t", [P, KD, MEM_T], ctx=inner)
            load_rows(k, k.dram["mem"].rearrange("a (t p) d -> p (a t) d", p=P), mem)
            norm_turn(k, "mem_norm", mem, MEM_T // P, k.gain("norm_mem_g"), mem_t)
            w_kv = k.dram["w_mem_kv"][0]
            project_rows(k, "mem_k", w_kv[:, 0:MEM_W], MEM_HEADS, mem_t, KD, (km,), tokens=MEM_T)
            project_tokens(k, "mem_v", [(w_kv[:, MEM_W:].rearrange("(c p) n -> p c n", p=P), 0, MEM_W)],
                           MEM_W, mem_t, KD, vm, tiles=MEM_T // P)
            project_rows(k, "mem_q", k.dram["w_mem_q"][0], MEM_HEADS, H, KD, (q,), scale=MEM_HD ** -0.5)
            memory_attention(k, q, km, vm, out)
        project_residual(k, "mem_out", k.dram["w_mem_o"][0], out, MEM_HEADS, split_src=True)


def load_rows(k, view, tile):
    nc = k.nc
    with k.phase() as ctx:
        (loaded,) = k.sems("load", "loaded")
        block = ctx.enter_context(nc.Block())

        @block.sync
        def _(sp):
            sp.dma_start(tile[:, :, :], view).then_inc(loaded, 16)
            sp.wait_ge(loaded, 16)


def route(k, logits, slots, weights, experts, slot_of_block):
    nc = k.nc
    E, G = EXPERTS, GROUPS
    with k.phase() as ctx:
        sb = lambda name, shape, dt=F32: k.sb(f"route_{name}", shape, dt, ctx=ctx)
        bias = sb("bias", [P, G + E])
        groups = sb("groups", [P, ST, 8])
        group_max, group_idx = sb("group_max", [P, ST, 8]), sb("group_idx", [P, ST, 8], U32)
        group_f, gate = sb("group_f", [P, ST]), sb("gate", [P, ST])
        e_sum = sb("e_sum", [P, ST, G])
        picked = sb("picked", [P, ST, E])
        top, top_idx = sb("top", [P, ST, 8]), sb("top_idx", [P, ST, 8], U32)
        choice = sb("choice", [P, 2, ST])
        ratio, total = sb("ratio", [P, ST]), sb("total", [P, ST])
        numbers, group_of = sb("numbers", [P, ST, E]), sb("group_of", [P, ST, E])
        hot = [sb(f"hot{c}", [P, ST, E]) for c in range(2)]
        both, before = sb("both", [P, ST, E]), sb("before", [P, ST + 1, E])
        earlier = sb("earlier", [P, P])
        steps, over = sb("steps", [P, E, ST]), sb("over", [P, E, ST])
        n_blocks, ends, starts = sb("n_blocks", [P, E]), sb("ends", [P, E]), sb("starts", [P, E])
        place = sb("place", [P, ST, E])
        slot_f = sb("slot_f", [P, 2, ST])
        block_no, passed = sb("block_no", [P, N_BLOCKS, E]), sb("passed", [P, N_BLOCKS, E])
        expert_f = sb("expert_f", [P, N_BLOCKS])
        tokens, clear = sb("tokens", [P, ST]), sb("clear", [N_BLOCKS, BLK])
        rows = sb("rows", [N_BLOCKS, BLK])
        ranks = k.ps("route_ranks", [P, ST, E], ctx)
        counts = k.ps("route_counts", [P, E], ctx)
        turned = k.ps("route_turned", [P, N_BLOCKS], ctx)
        bias_in, made, shifted, exped, hot_made, ranked, slots_made, cleared, rows_in, rows_turned = k.sems(
            "route", "bias_in made shifted exped hot_made ranked slots_made cleared rows_in rows_turned")
        scattered = k.soft["token_numbers_scattered"]
        block = ctx.enter_context(nc.Block())
        table = k.scratch["slot_token"]
        row_table = table.rearrange("(b s) o -> b (s o)", s=BLK)

        def over_experts(x):
            return x.rearrange("p (t o) -> p t o", o=1).broadcast_to([P, ST, E])

        def over_tiles(x):
            return x.rearrange("p (o e) -> p o e", o=1).broadcast_to([P, ST, x.shape[-1]])

        @block.sync
        def _(sp):
            sp.dma_start(bias[:, 0:G], k.dram["b_group_router"].broadcast_to([P, G])).then_inc(bias_in, 16)
            sp.dma_start(bias[:, G:], k.dram["b_expert_router"].broadcast_to([P, E])).then_inc(bias_in, 16)
            sp.wait_ge(made, 9)
            sp.dma_start(row_table, clear[:]).then_inc(cleared, 16)
            sp.wait_ge(scattered, 16 * 2 * ST)
            sp.dma_start(rows[:], row_table).then_inc(rows_in, 16)

        @block.gpsimd
        def _(pool):
            iota = dict(allow_small_or_imprecise_dtypes=True)
            nc.gpsimd.iota(numbers[:, :, :], [[0, ST], [1, E]], 0, 0, **iota).then_inc(made, 1)
            nc.gpsimd.iota(group_of[:, :, :], [[0, ST], [1, G], [0, PER_GROUP]], 0, 0, **iota).then_inc(made, 1)
            nc.gpsimd.iota(steps[:, :, :], [[0, E], [BLK, ST]], 0, 0, **iota).then_inc(made, 1)
            nc.gpsimd.iota(block_no[:, :, :], [[1, N_BLOCKS], [0, E]], 0, 0, **iota).then_inc(made, 1)
            nc.gpsimd.iota(tokens[:, :], [[P, ST]], 0, 1, **iota).then_inc(made, 1)
            nc.gpsimd.memset(earlier[:], 1.0).then_inc(made, 1)
            nc.gpsimd.memset(groups[:, :, :], -3e38).then_inc(made, 1)
            nc.gpsimd.memset(clear[:], 0.0).then_inc(made, 1)
            pool.wait_ge(made, 8)
            nc.gpsimd.affine_select(out=earlier[:], in_=earlier[:], compare_op=ALU.is_gt, fill=0.0, base=0,
                                    pattern=[[1, P]], channel_multiplier=-1).then_inc(made, 1)
            pool.wait_ge(slots_made, 2)
            pool.wait_ge(cleared, 16)
            for c in range(2):
                for t in range(ST):
                    nc.gpsimd.indirect_dma_start(
                        out=table, out_offset=bass.IndirectOffsetOnAxis(ap=slots[c][:, t:t + 1], axis=0),
                        in_=tokens[:, t:t + 1], in_offset=None).then_inc(scattered, 16)
            pool.wait_ge(scattered, 16 * 2 * ST)

        @block.scalar
        def _(act):
            act.wait_ge(shifted, 1)
            nc.scalar.activation(e_sum[:, :, :], e_sum[:, :, :], ACT.Exp).then_inc(exped, 1)
            act.wait_ge(shifted, 2)
            nc.scalar.activation(ratio[:], ratio[:], ACT.Exp).then_inc(exped, 1)

        @block.vector
        def _(dve):
            link = k.own("dve", dve)
            v = nc.vector
            dve.wait_ge(bias_in, 32)
            dve.wait_ge(made, 9)
            link(v.tensor_tensor(logits, logits, over_tiles(bias[:, :]), ALU.add))
            link(v.tensor_copy(groups[:, :, 0:G], logits[:, :, 0:G]))
            for t in range(ST):
                link(v.max(group_max[:, t, :], groups[:, t, :]))
                link(v.max_index(group_idx[:, t, :], group_max[:, t, :], groups[:, t, :]))
            v.tensor_tensor(e_sum[:, :, :], logits[:, :, 0:G], group_max[:, :, 0:1].broadcast_to([P, ST, G]),
                            ALU.subtract).then_inc(shifted, 1)
            link(v.tensor_copy(group_f[:], group_idx[:, :, 0:1].rearrange("p t o -> p (t o)")))
            dve.wait_ge(exped, 1)
            link(v.tensor_reduce(total[:], e_sum[:, :, :], AX, ALU.add))
            link(v.reciprocal(gate[:], total[:]))
            link(v.tensor_tensor(hot[0][:, :, :], group_of[:, :, :], over_experts(group_f[:]), ALU.is_equal))
            link(v.tensor_tensor(picked[:, :, :], logits[:, :, G:], hot[0][:, :, :], ALU.mult))
            link(v.tensor_scalar(hot[0][:, :, :], hot[0][:, :, :], -1.0, 3e38, ALU.add, ALU.mult))
            link(v.tensor_tensor(picked[:, :, :], picked[:, :, :], hot[0][:, :, :], ALU.add))
            for t in range(ST):
                link(v.max(top[:, t, :], picked[:, t, :]))
                link(v.max_index(top_idx[:, t, :], top[:, t, :], picked[:, t, :]))
            v.tensor_tensor(ratio[:], top[:, :, 1:2].rearrange("p t o -> p (t o)"),
                            top[:, :, 0:1].rearrange("p t o -> p (t o)"), ALU.subtract).then_inc(shifted, 1)
            for c in range(2):
                link(v.tensor_copy(choice[:, c, :], top_idx[:, :, c:c + 1].rearrange("p t o -> p (t o)")))
                link(v.tensor_tensor(hot[c][:, :, :], numbers[:, :, :], over_experts(choice[:, c, :]), ALU.is_equal))
            link(v.tensor_tensor(both[:, :, :], hot[0][:, :, :], hot[1][:, :, :], ALU.add))
            link(v.memset(before[:, 0, :], 0.0))
            for t in range(ST):
                link(v.tensor_tensor(before[:, t + 1, :], before[:, t, :], both[:, t, :], ALU.add))
            dve.sem_inc(hot_made, 1)
            dve.wait_ge(exped, 2)
            link(v.tensor_scalar(total[:], ratio[:], 1.0, None, ALU.add))
            link(v.reciprocal(total[:], total[:]))
            link(v.tensor_tensor(weights[:, 0, :], gate[:], total[:], ALU.mult))
            link(v.tensor_tensor(weights[:, 1, :], weights[:, 0, :], ratio[:], ALU.mult))
            dve.wait_ge(ranked, 1)
            link(v.tensor_tensor(over[:, :, :], counts[:, :].rearrange("p (e o) -> p e o", o=1).broadcast_to([P, E, ST]),
                                 steps[:, :, :], ALU.is_gt))
            link(v.tensor_reduce(n_blocks[:], over[:, :, :], AX, ALU.add))
            link(v.tensor_tensor_scan(ends[:], k.ones[:, 0:E], n_blocks[:], 0.0, ALU.mult, ALU.add))
            link(v.tensor_tensor(starts[:], ends[:], n_blocks[:], ALU.subtract))
            link(v.tensor_scalar(starts[:], starts[:], float(BLK), None, ALU.mult))
            link(v.tensor_tensor(place[:, :, :], ranks[:, :, :], over_tiles(starts[:, :]), ALU.add))
            for c in range(2):
                link(v.tensor_tensor(hot[c][:, :, :], hot[c][:, :, :], place[:, :, :], ALU.mult))
                link(v.tensor_reduce(slot_f[:, c, :], hot[c][:, :, :], AX, ALU.add))
                v.tensor_copy(slots[c][:], slot_f[:, c, :]).then_inc(slots_made, 1)
            link(v.tensor_tensor(passed[:, :, :], block_no[:, :, :],
                                 ends[:, :].rearrange("p (o e) -> p o e", o=1).broadcast_to([P, N_BLOCKS, E]), ALU.is_ge))
            link(v.tensor_reduce(expert_f[:], passed[:, :, :], AX, ALU.add))
            link(v.tensor_scalar(expert_f[:], expert_f[:], float(E - 1), None, ALU.min))
            link(v.tensor_copy(experts[:], expert_f[:]))
            dve.wait_ge(rows_turned, 1)
            link(v.tensor_copy(slot_of_block[:], turned[:]))

        @block.tensor
        def _(pe):
            pe.wait_ge(hot_made, 1)
            pe.wait_ge(made, 9)
            for t in range(ST):
                nc.tensor.matmul(ranks[:, t, :], earlier[:], both[:, t, :], start=True, stop=False)
                nc.tensor.matmul(ranks[:, t, :], k.ones[:], before[:, t, :], start=False, stop=True)
            nc.tensor.matmul(counts[:, :], k.ones[:], before[:, ST, :], start=True, stop=True).then_inc(ranked, 1)
            pe.wait_ge(rows_in, 16)
            nc.tensor.transpose(turned[:], rows[:], k.ident[0:N_BLOCKS, 0:N_BLOCKS]).then_inc(rows_turned, 1)
        k.chains["dve"].settle()


def run_experts(k, experts, slot_of_block):
    nc = k.nc
    with k.phase() as ctx:
        idx = [k.sb(f"moe_idx{b}", [P, 1], U32, ctx=ctx) for b in range(2)]
        rows = [k.sb(f"moe_rows{b}", [P, D], ctx=ctx) for b in range(2)]
        xt = [k.sb(f"moe_xt{b}", [P, KD, BLK], ctx=ctx) for b in range(2)]
        wgu = [k.sb(f"moe_wgu{b}", [P, 2, KD, FF], ctx=ctx) for b in range(2)]
        wd = [k.sb(f"moe_wd{b}", [P, FF // P, D], ctx=ctx) for b in range(2)]
        silu = [k.sb(f"moe_silu{b}", [P, 2, BLK], ctx=ctx) for b in range(2)]
        hidden = [k.sb(f"moe_hidden{b}", [P, 2, BLK], ctx=ctx) for b in range(2)]
        y = [k.sb(f"moe_y{b}", [P, D], ctx=ctx) for b in range(2)]
        turned = k.ps("moe_turned", [P, KD, BLK], ctx)
        up = [k.ps(f"moe_up{b}", [P, 2, 2, BLK], ctx) for b in range(2)]
        down = [k.ps(f"moe_down{b}", [P, D], ctx) for b in range(2)]
        (up_in0, up_in1, down_in0, down_in1, indexed, turns, x_ready, ups, silus, hiddens, downs, y_ready, stored0,
         stored1, passed) = k.sems("moe", "up_in0 up_in1 down_in0 down_in1 indexed turns x_ready ups silus hiddens "
                                   "downs y_ready stored0 stored1 passed")
        gathered = (k.soft["rows_gathered0"], k.soft["rows_gathered1"])
        up_in, down_in, stored = (up_in0, up_in1), (down_in0, down_in1), (stored0, stored1)
        block = ctx.enter_context(nc.Block())
        rounds = N_BLOCKS // 4
        gate_w = k.dram["w_expert_gate"][0].rearrange("e (c p) f -> p e c f", p=P)
        up_w = k.dram["w_expert_up"][0].rearrange("e (c p) f -> p e c f", p=P)
        down_w = k.dram["w_expert_down"][0].rearrange("e (c p) d -> p e c d", p=P)
        y_out = k.scratch["expert_rows"].rearrange("(n s) d -> s n d", s=BLK)
        ffn_gain = k.gain("norm_ffn_g")

        @block.sync
        def _(sp):
            with sp.Fori(0, rounds) as i:
                for n in range(4):
                    b, g = n % 2, 4 * i + n
                    e = sp.value_load(experts[0:1, bass.ds(g, 1)], min_val=0, max_val=EXPERTS - 1)
                    sp.wait_ge(ups, g + 1)
                    sp.dma_start(wgu[b][:, 0, :, :], gate_w[:, bass.ds(e, 1), :, :].rearrange("p e c f -> p (e c) f")
                                 ).then_inc(up_in[b], 16)
                    sp.dma_start(wgu[b][:, 1, :, :], up_w[:, bass.ds(e, 1), :, :].rearrange("p e c f -> p (e c) f")
                                 ).then_inc(up_in[b], 16)
                    sp.wait_ge(downs, g + 1)
                    sp.dma_start(wd[b][:, :, :], down_w[:, bass.ds(e, 1), :, :].rearrange("p e c d -> p (e c) d")
                                 ).then_inc(down_in[b], 16)

        @block.gpsimd
        def _(pool):
            with pool.Fori(0, rounds) as i:
                for n in range(4):
                    b, g = n % 2, 4 * i + n
                    pool.wait_ge(turns, g + 1)
                    nc.gpsimd.tensor_copy(idx[b][:], slot_of_block[:, bass.ds(g, 1)]).then_inc(indexed, 1)
                    pool.wait_ge(indexed, g + 1)
                    pool.sem_inc(passed, 1)
                    nc.gpsimd.indirect_dma_start(out=rows[b][:], out_offset=None, in_=k.scratch["ffn_rows"],
                                                 in_offset=bass.IndirectOffsetOnAxis(ap=idx[b][:, 0:1], axis=0)
                                                 ).then_inc(gathered[b], 16)

        @block.tensor
        def _(pe):
            pe.sem_inc(downs, 2)
            pe.sem_inc(turns, 2)
            pe.sem_inc(ups, 2)
            pe.sem_inc(x_ready, 1)

            def turn_rows(i, n):
                pe.wait_ge(gathered[n % 2], 16 * (2 * i + n // 2) + 16)
                pe.wait_ge(x_ready, 4 * i + n + 1)
                for c in range(KD):
                    last = nc.tensor.transpose(turned[:, c, :], rows[n % 2][:, c * P:(c + 1) * P], k.ident[:])
                last.then_inc(turns, 1)

            def round_(i, more):
                for n in range(4):
                    b, g = n % 2, 4 * i + n
                    pe.wait_ge(up_in[b], 32 * (2 * i + n // 2) + 32)
                    pe.wait_ge(x_ready, g + 1 + 1)
                    pe.wait_ge(hiddens, g + 1)
                    for m in range(2):
                        for f in range(2):
                            for c in range(KD):
                                last = nc.tensor.matmul(up[b][:, m, f, :], wgu[b][:, m, c, f * P:(f + 1) * P],
                                                        xt[b][:, c, :], start=(c == 0), stop=(c == KD - 1))
                    last.then_inc(ups, 1)
                    if n < 3 or more:
                        turn_rows(i, n + 1)
                    pe.wait_ge(down_in[b], 16 * (2 * i + n // 2) + 16)
                    pe.wait_ge(hiddens, g + 1 + 2)
                    pe.wait_ge(y_ready, g + 1)
                    for h in range(2):
                        for c in range(FF // P):
                            last = nc.tensor.matmul(down[b][:, h * HALF:(h + 1) * HALF], hidden[b][:, c, :],
                                                    wd[b][:, c, h * HALF:(h + 1) * HALF],
                                                    start=(c == 0), stop=(c == FF // P - 1))
                    last.then_inc(downs, 1)
            turn_rows(0, 0)
            with pe.Fori(0, rounds - 1) as i:
                round_(i, True)
            round_(rounds - 1, False)

        @block.vector
        def _(dve):
            dve.sem_inc(hiddens, 2)

            def apply_gain(i, n):
                g = 4 * i + n
                dve.wait_ge(turns, g + 1 + 2)
                dve.wait_ge(ups, g + 1)
                nc.vector.tensor_tensor(xt[n % 2][:, :, :], turned[:, :, :],
                                        ffn_gain.rearrange("p (c o) -> p c o", o=1).broadcast_to([P, KD, BLK]),
                                        ALU.mult).then_inc(x_ready, 1)

            def round_(i, more):
                for n in range(4):
                    b, g = n % 2, 4 * i + n
                    dve.wait_ge(silus, g + 1)
                    dve.wait_ge(downs, g + 1)
                    nc.vector.tensor_tensor(hidden[b][:, :, :], up[b][:, 1, :, :], silu[b][:, :, :],
                                            ALU.mult).then_inc(hiddens, 1)
                    if n < 3 or more:
                        apply_gain(i, n + 1)
            apply_gain(0, 0)
            with dve.Fori(0, rounds - 1) as i:
                round_(i, True)
            round_(rounds - 1, False)

        @block.scalar
        def _(act):
            act.sem_inc(stored0, 16)
            act.sem_inc(stored1, 16)
            act.sem_inc(y_ready, 2)
            with act.Fori(0, rounds) as i:
                for n in range(4):
                    b, g = n % 2, 4 * i + n
                    act.wait_ge(ups, g + 1 + 2)
                    act.wait_ge(hiddens, g + 1)
                    nc.scalar.activation(silu[b][:, :, :], up[b][:, 0, :, :], ACT.Silu).then_inc(silus, 1)
                    act.wait_ge(downs, g + 1 + 2)
                    act.wait_ge(stored[b], 16 * (2 * i + n // 2) + 16)
                    nc.scalar.activation(y[b][:], down[b][:], ACT.Copy).then_inc(y_ready, 1)
                    act.wait_ge(y_ready, g + 1 + 2)
                    act.dma_start(y_out[:, bass.ds(g, 1), :].rearrange("s n d -> s (n d)"),
                                  y[b][:]).then_inc(stored[b], 16)
            act.wait_ge(stored0, 16 * 2 * rounds + 16)
            act.wait_ge(stored1, 16 * 2 * rounds + 16)


def combine(k, slots, weights):
    nc = k.nc
    with k.phase() as ctx:
        idx = [[k.sb(f"comb_idx{c}{b}", [P, 1], U32, ctx=ctx) for b in range(4)] for c in range(2)]
        rows = [[k.sb(f"comb_rows{c}{b}", [P, D], ctx=ctx) for b in range(4)] for c in range(2)]
        indexed, added, passed = k.sems("comb", "indexed added passed")
        gathered = [k.soft[f"outputs_gathered{b}"] for b in range(4)]
        block = ctx.enter_context(nc.Block())

        @block.gpsimd
        def _(pool):
            with pool.Fori(0, ST // 4) as i:
                for b in range(4):
                    pool.wait_ge(added, 2 * (4 * i + b) + 2)
                    for c in range(2):
                        nc.gpsimd.tensor_copy(idx[c][b][:], slots[c][:, bass.ds(4 * i + b, 1)]).then_inc(indexed, 1)
                        pool.wait_ge(indexed, 2 * (4 * i + b) + c + 1)
                        pool.sem_inc(passed, 1)
                        nc.gpsimd.indirect_dma_start(out=rows[c][b][:], out_offset=None, in_=k.scratch["expert_rows"],
                                                     in_offset=bass.IndirectOffsetOnAxis(ap=idx[c][b][:, 0:1], axis=0)
                                                     ).then_inc(gathered[b], 16)

        @block.vector
        def _(dve):
            dve.sem_inc(added, 8)
            with dve.Fori(0, ST // 4) as i:
                for b in range(4):
                    dve.wait_ge(gathered[b], 32 * i + 32)
                    x = row_of(k.X, 4 * i + b)
                    for c in range(2):
                        nc.vector.scalar_tensor_tensor(out=x, in0=rows[c][b][:], scalar=weights[:, c, bass.ds(4 * i + b, 1)],
                                                       in1=x, op0=ALU.mult, op1=ALU.add).then_inc(added, 1)
                        dve.wait_ge(added, 2 * (4 * i + b) + c + 1 + 8)


def expert_layer(k):
    nc = k.nc
    with ExitStack() as ctx:
        logits = k.sb("logits", [P, ST, GROUPS + EXPERTS], ctx=ctx)
        slots = [k.sb(f"slots{c}", [P, ST], U32, ctx=ctx) for c in range(2)]
        weights = k.sb("route_w", [P, 2, ST], ctx=ctx)
        experts = k.sb("experts", [P, N_BLOCKS], I32, ctx=ctx)
        slot_of_block = k.sb("slot_of_block", [P, N_BLOCKS], U32, ctx=ctx)
        w_g = k.dram["w_group_router"][0].rearrange("(c p) n -> p c n", p=P)
        w_e = k.dram["w_expert_router"][0].rearrange("(c p) n -> p c n", p=P)
        with ExitStack() as inner:
            H = k.sb("ffn_h", [P, KD, S], ctx=inner)
            norm_turn(k, "ffn_norm", k.X, ST, k.gain("norm_ffn_g"), H, rows_out=k.scratch["ffn_rows"])
            project_tokens(k, "router", [(w_g, 0, GROUPS), (w_e, GROUPS, EXPERTS)], GROUPS + EXPERTS, H, KD, logits)
        route(k, logits[:, :, :], slots, weights, experts, slot_of_block)
        run_experts(k, experts, slot_of_block)
        combine(k, slots, weights)


def final_norm(k):
    nc = k.nc
    with k.phase() as ctx:
        gain = k.sb("final_gain", [P, D], ctx=ctx)
        junk = [k.sb(f"final_junk{b}", [P, D], ctx=ctx) for b in range(2)]
        gain_in, even, odd, mean_made, root_made, normed = k.sems("final", "gain_in even odd mean_made root_made normed")
        block = ctx.enter_context(nc.Block())

        @block.sync
        def _(sp):
            sp.dma_start(gain[:], k.dram["norm_final_g"].rearrange("(o d) -> o d", o=1).broadcast_to([P, D])
                         ).then_inc(gain_in, 16)

        @block.scalar
        def _(act):
            for t in range(0, ST, 2):
                if t:
                    act.wait_ge(even, t // 2)
                nc.scalar.activation(junk[0][:], k.X[:, t, :], ACT.Square, accum_out=k.ssq[:, t:t + 1]).then_inc(even, 1)
            act.wait_ge(mean_made, 1)
            nc.scalar.activation(k.root[:], k.mean[:], ACT.Sqrt).then_inc(root_made, 1)

        @block.vector
        def _(dve):
            link = k.own("dve", dve)
            for t in range(1, ST, 2):
                if t > 1:
                    dve.wait_ge(odd, t // 2)
                nc.vector.tensor_tensor_reduce(out=junk[1][:], in0=k.X[:, t, :], in1=k.X[:, t, :], scale=1.0, scalar=0.0,
                                               op0=ALU.mult, op1=ALU.add, accum_out=k.ssq[:, t:t + 1]).then_inc(odd, 1)
            dve.wait_ge(odd, ST // 2)
            dve.wait_ge(even, ST // 2)
            nc.vector.tensor_scalar(k.mean[:], k.ssq[:], 1.0 / D, EPS, ALU.mult, ALU.add).then_inc(mean_made, 1)
            dve.wait_ge(root_made, 1)
            link(nc.vector.reciprocal(k.rstd[:], k.root[:]))
            dve.wait_ge(gain_in, 16)
            with dve.Fori(0, ST) as t:
                nc.vector.scalar_tensor_tensor(out=row_of(k.X, t), in0=row_of(k.X, t), scalar=k.rstd[:, bass.ds(t, 1)],
                                               in1=gain[:], op0=ALU.mult, op1=ALU.mult).then_inc(normed, 1)
        k.chains["dve"].settle()


def gate_rows(k, vm, HT, spare):
    nc = k.nc
    H = 4
    with k.phase() as ctx:
        w = k.sb("gr_w", [P, KD, 96], ctx=ctx)
        w_pair = pair(k, "gr_ws", [P, KD, 96], ctx)
        bias = k.sb("gr_bias", [H, 3], ctx=ctx)
        rows = [tile[0:H, c, :] for tile, count in spare for c in range(count)]
        raw, logs, sums = rows[0:3], rows[3:5], rows[5:7]
        ones = k.sb("gr_ones", [H, S], ctx=ctx)
        a, top, floor, neg = (k.sb(f"gr_{n}", [H, S], ctx=ctx) for n in ("a", "top", "floor", "neg"))
        acc = k.ps("gr_acc", [P, S], ctx)
        cols = k.ps("gr_cols", [P, 2, ST, H], ctx)
        w_in, w_split, bias_in, cleared, products, copied, absed, logged, rows_made, turned, stored = k.sems(
            "gr", "w_in w_split bias_in cleared products copied absed logged rows_made turned stored")
        block = ctx.enter_context(nc.Block())
        w_view = k.dram["w_in_2"][0].rearrange("(c p) n -> p c n", p=P)

        @block.sync
        def _(sp):
            sp.wait_ge(cleared, 2)
            for n, col in enumerate((C_FF, C_MI, C_MI + H)):
                sp.dma_start(w[:, :, 32 * n:32 * n + H], w_view[:, :, col:col + H]).then_inc(w_in, 16)
            for n, name in enumerate(("fox_f_bias_2", "mlstm_i_bias_2", "mlstm_f_bias_2")):
                sp.dma_start(bias[:, n:n + 1], k.dram[name].rearrange("l h -> h l")).then_inc(bias_in, 16)
            fox_q = k.scratch["fox_q"].rearrange("(h n) s -> h n s", n=2)
            fox_k = k.scratch["fox_k"].rearrange("(h n) s -> h n s", n=2)
            sp.dma_start(fox_q[:, 0, :], ones[:]).then_inc(stored, 16)
            sp.dma_start(fox_k[:, 1, :], ones[:]).then_inc(stored, 16)
            sp.wait_ge(rows_made, 1)
            sp.dma_start(fox_q[:, 1, :], sums[0][:]).then_inc(stored, 16)
            sp.wait_ge(rows_made, 2)
            sp.dma_start(fox_k[:, 0, :], neg[:]).then_inc(stored, 16)
            sp.wait_ge(rows_made, 4)
            sp.dma_start(k.scratch["mlstm_row"], top[:]).then_inc(stored, 16)
            sp.wait_ge(stored, 16 * 5)

        @block.gpsimd
        def _(pool):
            nc.gpsimd.memset(w[:, :, :], 0.0).then_inc(cleared, 1)
            nc.gpsimd.memset(ones[:], 1.0).then_inc(cleared, 1)
            nc.gpsimd.memset(vm[:, :, :, HD:HD + 1], 1.0).then_inc(cleared, 1)
            pool.wait_ge(w_in, 48)
            nc.gpsimd.tensor_copy(w_pair[0][:], w[:]).then_inc(w_split, 1)
            pool.wait_ge(w_split, 1)
            nc.gpsimd.tensor_tensor(w_pair[1][:], w[:], w_pair[0][:], ALU.subtract).then_inc(w_split, 1)

        @block.tensor
        def _(pe):
            pe.wait_ge(w_split, 2)
            for c in range(KD):
                for h in range(2):
                    last = add_product(nc, acc[0:96, h * HALF:(h + 1) * HALF], part(w_pair, slice(None), c, slice(None)),
                                       part(HT, slice(None), c, slice(h * HALF, (h + 1) * HALF)), c == 0, c == KD - 1)
            last.then_inc(products, 1)
            pe.wait_ge(rows_made, 5)
            for n, row in enumerate((a, floor)):
                for t in range(ST):
                    last = nc.tensor.transpose(cols[:, n, t, :], row[:, t * P:(t + 1) * P], k.ident[0:H, 0:H])
            last.then_inc(turned, 1)

        @block.scalar
        def _(act):
            act.wait_ge(products, 1)
            for n in range(3):
                nc.scalar.activation(raw[n][:], acc[32 * n:32 * n + H, :], ACT.Copy).then_inc(copied, 1)
            for n, x in enumerate((raw[0], raw[2])):
                act.wait_ge(absed, n + 1)
                nc.scalar.activation(logs[n][:], x[:], ACT.Abs).then_inc(logged, 1)
                act.wait_ge(logged, 3 * n + 1)
                nc.scalar.activation(logs[n][:], logs[n][:], ACT.Exp, scale=-1.0).then_inc(logged, 1)
                act.wait_ge(logged, 3 * n + 2)
                nc.scalar.activation(logs[n][:], logs[n][:], ACT.Ln, bias=1.0).then_inc(logged, 1)
            act.wait_ge(turned, 1)
            nc.scalar.activation(k.a_col[:, :, :], cols[:, 0, :, :], ACT.Copy)
            nc.scalar.activation(k.floor_col[:, :, :], cols[:, 1, :, :], ACT.Exp, scale=-1.0)

        @block.vector
        def _(dve):
            link = k.own("dve", dve)
            v = nc.vector
            dve.wait_ge(bias_in, 48)
            dve.wait_ge(copied, 3)
            dve.wait_ge(cleared, 3)
            for n in (0, 2):
                v.tensor_scalar(raw[n][:], raw[n][:], bias[:, n:n + 1], None, ALU.add).then_inc(absed, 1)
            link(v.tensor_scalar(raw[1][:], raw[1][:], bias[:, 1:2], None, ALU.add))
            for n, x in enumerate((raw[0], raw[2])):
                dve.wait_ge(logged, 3 * n + 3)
                link(v.scalar_tensor_tensor(out=logs[n][:], in0=x[:], scalar=0.0, in1=logs[n][:],
                                            op0=ALU.min, op1=ALU.subtract))
                ins = v.tensor_tensor_scan(sums[n][:], ones[:], logs[n][:], 0.0, ALU.mult, ALU.add)
                if n == 0:
                    ins.then_inc(rows_made, 1)
                    dve.wait_ge(rows_made, 1)
                    v.tensor_scalar(neg[:], sums[0][:], -1.0, None, ALU.mult).then_inc(rows_made, 1)
                else:
                    link(ins)
            link(v.tensor_tensor(a[:], raw[1][:], sums[1][:], ALU.subtract))
            link(v.tensor_tensor_scan(top[:], ones[:], a[:], 0.0, ALU.mult, ALU.max))
            v.tensor_tensor(floor[:], top[:], sums[1][:], ALU.add).then_inc(rows_made, 1)
            dve.wait_ge(rows_made, 3)
            v.tensor_scalar(top[:], top[:], -1.0, None, ALU.mult).then_inc(rows_made, 1)
            dve.wait_ge(rows_made, 4)
            dve.sem_inc(rows_made, 1)
        k.chains["dve"].settle()


def matrix_lstm(k, V, out):
    nc = k.nc
    H = 4
    with k.phase() as ctx:
        q = [k.sb(f"ml_q{b}", [HD, S], ctx=ctx) for b in range(2)]
        kk = [k.sb(f"ml_k{b}", [HD, S], ctx=ctx) for b in range(2)]
        row = [k.sb(f"ml_row{b}", [P, S], ctx=ctx) for b in range(2)]
        a_col = [k.sb(f"ml_a{b}", [P, ST], ctx=ctx) for b in range(2)]
        decay = [k.sb(f"ml_decay{b}", [P, S], ctx=ctx) for b in range(2)]
        w = [[k.sb(f"ml_w{b}{t}", [P, S - t * P], ctx=ctx) for t in range(ST)] for b in range(2)]
        stats = [k.sb(f"ml_stats{b}", [P, ST, 2], ctx=ctx) for b in range(2)]
        values = [k.sb(f"ml_v{b}", [P, ST, HD + 1], ctx=ctx) for b in range(2)]
        before_mask = k.sb("ml_mask", [P, P], ctx=ctx)
        scores = [k.ps(f"ml_scores{b}", [P, S], ctx) for b in range(2)]
        acc = [k.ps(f"ml_acc{b}", [P, 2, HALF], ctx) for b in range(2)]
        (head_in0, head_in1, mask_made, a_ready, v_ready, masked, decays, products, weighted, sums_made, linked,
         done) = k.sems("ml", "head_in0 head_in1 mask_made a_ready v_ready masked decays products weighted sums_made "
                        "linked done")
        head_in = (head_in0, head_in1)
        block = ctx.enter_context(nc.Block())
        rounds = H // 2
        plain = k.scratch["plain"]
        q_row, k_row = C_MQ - C_CU, C_MQ + H * HD - C_CU

        def at(b, t):
            return acc[b][:, t // 4, (t % 4) * (HD + 1):(t % 4 + 1) * (HD + 1)]

        @block.sync
        def _(sp):
            with sp.Fori(0, rounds) as i:
                for b in range(2):
                    sp.wait_ge(weighted, (2 * i + b) * ST + 2)
                    h = i * 2 + b
                    sp.dma_start(q[b][:], plain[bass.ds(h * HD + q_row, HD), :]).then_inc(head_in[b], 16)
                    sp.dma_start(kk[b][:], plain[bass.ds(h * HD + k_row, HD), :]).then_inc(head_in[b], 16)
                    sp.dma_start(row[b][:], k.scratch["mlstm_row"][bass.ds(h, 1), :].broadcast_to([P, S])
                                 ).then_inc(head_in[b], 16)

        @block.gpsimd
        def _(pool):
            nc.gpsimd.memset(before_mask[:], 0.0).then_inc(mask_made, 1)
            pool.wait_ge(mask_made, 1)
            nc.gpsimd.affine_select(out=before_mask[:], in_=before_mask[:], compare_op=ALU.is_ge, fill=NEG, base=0,
                                    pattern=[[1, P]], channel_multiplier=-1).then_inc(mask_made, 1)
            with pool.Fori(0, rounds) as i:
                for b in range(2):
                    pool.wait_ge(weighted, (2 * i + b) * ST + 2)
                    h = i * 2 + b
                    nc.gpsimd.tensor_copy(a_col[b][:], k.a_col[:, :, bass.ds(h, 1)].rearrange("p t h -> p (t h)")
                                          ).then_inc(a_ready, 1)
                    pool.wait_ge(sums_made, (2 * i + b) * ST + 1)
                    h = i * 2 + b
                    nc.gpsimd.tensor_copy(values[b][:, :, :], V[:, :, bass.ds(h, 1), :].rearrange(
                        "p t h n -> p (t h) n")).then_inc(v_ready, 1)

        @block.tensor
        def _(pe):
            pe.sem_inc(sums_made, 1 + ST)

            def score(i, n, g):
                b, t = n // ST, n % ST
                if t == 0:
                    pe.wait_ge(head_in[b], 48 * i + 48)
                pe.wait_ge(weighted, g + 1 + 8)
                width = S - t * P
                for c in range(0, width, HALF):
                    w_c = min(HALF, width - c)
                    last = nc.tensor.matmul(scores[t % 2][:, c:c + w_c], kk[b][:, t * P:(t + 1) * P],
                                            q[b][:, t * P + c:t * P + c + w_c], start=True, stop=True)
                last.then_inc(products, 1)

            def add_up(i, n, g):
                b, t = n // ST, n % ST
                pe.wait_ge(weighted, g + 1 + 10)
                if t == 0:
                    pe.wait_ge(v_ready, i * 2 + b + 1)
                    pe.wait_ge(done, i * 2 + b + 1)
                for c in range(t + 1):
                    last = nc.tensor.matmul(at(b, t), w[b][c][:, (t - c) * P:(t - c + 1) * P],
                                            values[b][:, c, :], start=(c == 0), stop=(c == t))
                last.then_inc(sums_made, 1)
            staged(pe, rounds, 2 * ST, ((0, score), (ST, add_up)))

        @block.scalar
        def _(act):
            def decay_from(i, n, g):
                b, t = n // ST, n % ST
                if t == 0:
                    act.wait_ge(head_in[b], 48 * i + 48)
                    act.wait_ge(a_ready, i * 2 + b + 1)
                act.wait_ge(weighted, g + 1 + 8)
                act.wait_ge(masked, g + 1)
                nc.scalar.activation(decay[t % 2][:, 0:P], decay[t % 2][:, 0:P], ACT.Exp,
                                     bias=a_col[b][:, t:t + 1]).then_inc(decays, 1)
                if t < ST - 1:
                    nc.scalar.activation(decay[t % 2][:, P:S - t * P], row[b][:, (t + 1) * P:S], ACT.Exp,
                                         bias=a_col[b][:, t:t + 1]).then_inc(decays, 1)
            staged(act, rounds, 2 * ST, ((0, decay_from),))

        @block.vector
        def _(dve):
            dve.sem_inc(done, 2)
            dve.sem_inc(weighted, 2 + ST)
            dve.wait_ge(mask_made, 2)
            per = 2 * ST - 1

            def mask(i, n, g):
                b, t = n // ST, n % ST
                if t == 0:
                    dve.wait_ge(head_in[b], 48 * i + 48)
                dve.wait_ge(weighted, g + 1 + 8)
                nc.vector.tensor_tensor(decay[t % 2][:, 0:P], row[b][:, t * P:(t + 1) * P], before_mask[:],
                                        ALU.add).then_inc(masked, 1)

            def weigh(i, n, g):
                b, t = n // ST, n % ST
                dve.wait_ge(products, g + 1)
                dve.wait_ge(decays, (i * 2 + b) * per + min(2 * (t + 1), per))
                dve.wait_ge(sums_made, (2 * i + b) * ST + 1)
                width = S - t * P
                nc.vector.scalar_tensor_tensor(out=w[b][t][:], in0=scores[t % 2][:, 0:width],
                                               scalar=HD ** -0.5, in1=decay[t % 2][:, 0:width],
                                               op0=ALU.mult, op1=ALU.mult).then_inc(weighted, 1)

            def divide(i, n, g):
                b, t = n // ST, n % ST
                if t < ST - 1:
                    return
                h = i * 2 + b
                dve.wait_ge(sums_made, h * ST + 2 * ST + 1)
                st = stats[b]
                den = acc[b][:, :, 0:4 * (HD + 1)].rearrange("p a (t n) -> p a t n", n=HD + 1)[:, :, :, HD:HD + 1]
                den = den.rearrange("p a t n -> p a (t n)")
                one = st[:, :, 0:1].rearrange("p (a t) n -> p a (t n)", a=2)
                nc.vector.tensor_copy(one, den).then_inc(linked, 1)
                dve.wait_ge(linked, 5 * h + 1)
                nc.vector.scalar_tensor_tensor(
                    out=st[:, :, 1:2], in0=st[:, :, 0:1], scalar=-1.0, in1=k.floor_col[:, :, bass.ds(h, 1)],
                    op0=ALU.mult, op1=ALU.max).then_inc(linked, 1)
                dve.wait_ge(linked, 5 * h + 2)
                nc.vector.tensor_tensor(st[:, :, 0:1], st[:, :, 0:1], st[:, :, 1:2], ALU.max).then_inc(linked, 1)
                dve.wait_ge(linked, 5 * h + 3)
                nc.vector.reciprocal(st[:, :, 1:2], st[:, :, 0:1]).then_inc(linked, 1)
                dve.wait_ge(linked, 5 * h + 4)
                for tile in range(ST):
                    ins = nc.vector.tensor_scalar(out[:, tile, bass.ds(h * HD, HD)], at(b, tile)[:, 0:HD],
                                                  st[:, tile, 1:2], None, ALU.mult)
                ins.then_inc(linked, 1)
                dve.wait_ge(linked, 5 * h + 5)
                dve.sem_inc(done, 1)
            staged(dve, rounds, 2 * ST, ((0, mask), (1, weigh), (ST + 1, divide)))


def short_conv(k, conv_out, ml_rows):
    nc = k.nc
    CH = 2
    with k.phase() as ctx:
        u, bg, cg, mo = (k.sb(f"conv_{n}", [P, CH, S], ctx=ctx) for n in ("u", "b", "c", "mo"))
        loaded, gated, chain_c = k.sems("conv", "loaded gated chain_c")
        block = ctx.enter_context(nc.Block())
        plain = k.scratch["plain"]

        @block.sync
        def _(sp):
            for n, tile in enumerate((u, bg, cg)):
                sp.dma_start(tile[:, :, :], plain[n * CH * P:(n + 1) * CH * P, :].rearrange("(c p) s -> p c s", p=P)
                             ).then_inc(loaded, 16)
            sp.dma_start(mo[:, :, :], k.scratch["mo"].rearrange("(c p) s -> p c s", p=P)).then_inc(gated, 16)

        @block.scalar
        def _(act):
            act.wait_ge(gated, 16)
            nc.scalar.activation(mo[:, :, :], mo[:, :, :], ACT.Sigmoid).then_inc(gated, 1)

        @block.vector
        def _(dve):
            link = k.own("dve", dve)
            dve.wait_ge(loaded, 48)
            link(nc.vector.tensor_tensor(u[:, :, :], u[:, :, :], cg[:, :, :], ALU.mult))
            for c in range(CH):
                taps = [k.gain("conv_w_2", n * CH + c, 1) for n in range(3)]
                link(nc.vector.tensor_scalar(conv_out[:, c, :], u[:, c, :], taps[2], None, ALU.mult))
                for back, tap in ((1, taps[1]), (2, taps[0])):
                    link(nc.vector.scalar_tensor_tensor(out=conv_out[:, c, back:], in0=u[:, c, 0:S - back], scalar=tap,
                                                        in1=conv_out[:, c, back:], op0=ALU.mult, op1=ALU.add))
            link(nc.vector.tensor_tensor(conv_out[:, :, :], conv_out[:, :, :], bg[:, :, :], ALU.mult))
            dve.wait_ge(gated, 17)
            link(nc.vector.tensor_tensor(ml_rows[:, :, :], ml_rows[:, :, :], mo[:, :, :], ALU.mult))
        k.chains["dve"].settle()


def t5_buckets(n):
    exact, most, buckets = 16, 128, 32
    out = []
    for d in range(n):
        if d < exact:
            out.append(d)
        else:
            large = exact + int(np.log(d / exact) / np.log(most / exact) * (buckets - exact))
            out.append(min(large, buckets - 1))
    return out


def window_bias(k, biases, sinks):
    nc = k.nc
    H, B, W2 = 8, 32, 3 * P
    with k.phase() as ctx:
        rel = k.sb("wb_rel", [B, H], ctx=ctx)
        hot = k.sb("wb_hot", [B, W2], ctx=ctx)
        index = k.sb("wb_index", [B, 1], ctx=ctx)
        bucket = k.sb("wb_bucket", [B, W2], ctx=ctx)
        rows = k.sb("wb_rows", [H, W2], ctx=ctx)
        flipped = k.sb("wb_flipped", [P, H, 2 * P], ctx=ctx)
        flip = k.sb("wb_flip", [P, P], ctx=ctx)
        acc = k.ps("wb_acc", [H, W2], ctx)
        turned = k.ps("wb_turned", [P, H, 2 * P], ctx)
        rel_in, bucketed, made, hot_made, product, rows_made, stored, loaded, upright = k.sems(
            "wb", "rel_in bucketed made hot_made product rows_made stored loaded upright")
        block = ctx.enter_context(nc.Block())
        buckets = t5_buckets(WINDOW)
        runs = []
        for j in range(P, 2 * P):
            value = buckets[2 * P - 1 - j]
            if runs and runs[-1][2] == value:
                runs[-1][1] = j + 1
            else:
                runs.append([j, j + 1, value])

        @block.sync
        def _(sp):
            sp.dma_start(rel[:], k.dram["rel_bias_2"]).then_inc(rel_in, 16)
            sp.dma_start(sinks[:], k.dram["swa_sinks_2"].broadcast_to([P, H])).then_inc(loaded, 16)
            sp.wait_ge(rows_made, 3)
            sp.dma_start(k.scratch["window_rows"], rows[:]).then_inc(stored, 16)
            sp.wait_ge(stored, 16)
            view = k.scratch["window_rows"]
            for h in range(H):
                skewed = bass.AP(view.tensor, view.offset + h * W2, [[1, P], [1, 2 * P]])
                sp.dma_start(flipped[:, h, :], skewed).then_inc(loaded, 16)

        @block.gpsimd
        def _(pool):
            nc.gpsimd.memset(bucket[:], -1.0).then_inc(made, 1)
            nc.gpsimd.iota(index[:], [[0, 1]], 0, 1, allow_small_or_imprecise_dtypes=True).then_inc(made, 1)
            nc.gpsimd.memset(flip[:], 0.0).then_inc(made, 1)
            pool.wait_ge(made, 3)
            nc.gpsimd.affine_select(out=flip[:], in_=flip[:], compare_op=ALU.not_equal, fill=1.0, base=1 - P,
                                    pattern=[[1, P]], channel_multiplier=1).then_inc(made, 1)
            for at, to, value in runs:
                nc.gpsimd.memset(bucket[:, at:to], float(value)).then_inc(bucketed, 1)

        @block.vector
        def _(dve):
            dve.wait_ge(bucketed, len(runs))
            nc.vector.tensor_scalar(hot[:], bucket[:], index[:], None, ALU.is_equal).then_inc(hot_made, 1)
            nc.vector.memset(rows[:, 0:P], NEG).then_inc(rows_made, 1)
            nc.vector.memset(rows[:, 2 * P:], NEG).then_inc(rows_made, 1)
            dve.wait_ge(product, 1)
            nc.vector.tensor_copy(rows[:, P:2 * P], acc[:, P:2 * P]).then_inc(rows_made, 1)
            dve.wait_ge(upright, 1)
            nc.vector.tensor_copy(biases[:, :, :], turned[:, :, :])

        @block.tensor
        def _(pe):
            pe.wait_ge(hot_made, 1)
            pe.wait_ge(rel_in, 16)
            nc.tensor.matmul(acc[:], rel[:], hot[:], start=True, stop=True).then_inc(product, 1)
            pe.wait_ge(made, 4)
            pe.wait_ge(loaded, 16 * (H + 1))
            for h in range(0, H, 2):
                last = nc.tensor.matmul(turned[:, h:h + 2, :], flip[:], flipped[:, h:h + 2, :], start=True, stop=True)
            last.then_inc(upright, 1)


def gated_merge(k, branches, merged, HT):
    nc = k.nc
    NB = len(branches)
    with k.phase() as ctx:
        wg_raw = [k.sb(f"gm_wg{b}", [P, KD, P], ctx=ctx) for b in range(2)]
        wg = [pair(k, f"gm_wgs{b}", [P, KD, P], ctx) for b in range(2)]
        wo = [k.sb(f"gm_wo{b}", [P, 4, P], ctx=ctx) for b in range(2)]
        gate = k.sb("gm_gate", [P, S], ctx=ctx)
        gated_part = k.sb("gm_part", [P, S], ctx=ctx)
        gate_ps = [k.ps(f"gm_gate_ps{b}", [P, S], ctx) for b in range(2)]
        out_ps = [k.ps(f"gm_out_ps{b}", [P, S], ctx) for b in range(2)]
        wg_in0, wg_in1, wo_in0, wo_in1, split, passed, products, gates, gated, totals = k.sems(
            "gm", "wg_in0 wg_in1 wo_in0 wo_in1 split passed products gates gated totals")
        wg_in, wo_in = (wg_in0, wg_in1), (wo_in0, wo_in1)
        block = ctx.enter_context(nc.Block())
        w_view = k.dram["w_in_2"][0].rearrange("(c p) n -> p c n", p=P)
        outs = [k.dram[name][0].rearrange("(c p) n -> p c n", p=P) for name, _, _ in branches]

        @block.sync
        def _(sp):
            with sp.Fori(0, KD) as i:
                for n in range(NB):
                    sp.wait_ge(split, 2 * (i * NB + n) + 2)
                    col = bass.ds(i * P + C_GATES + n * D, P)
                    sp.dma_start(wg_raw[n % 2][:, :, :], w_view[:, :, col]).then_inc(wg_in[n % 2], 16)
                    sp.wait_ge(products, i * NB + n + 1)
                    sp.sem_inc(passed, 1)
                    sp.dma_start(wo[n % 2][:, 0:branches[n][2], :], outs[n][:, :, bass.ds(i * P, P)]).then_inc(wo_in[n % 2], 16)

        @block.gpsimd
        def _(pool):
            pool.sem_inc(split, 4)
            pool.wait_ge(split, 4 + 4)

            def split_round(i, start):
                for n in range(start, NB):
                    split_weights(nc, pool, i * NB + n, n % 2, (wg_in[n % 2], 16 * (i * (NB // 2) + n // 2) + 16), wg_raw, wg,
                                  products, split, passed)
            split_round(0, 2)
            with pool.Fori(1, KD) as i:
                split_round(i, 0)

        @block.tensor
        def _(pe):
            pe.sem_inc(products, 2)
            with pe.Fori(0, KD) as i:
                for n in range(NB):
                    b = n % 2
                    y, chunks = branches[n][1], branches[n][2]
                    pe.wait_ge(split, 2 * (i * NB + n) + 2 + 4)
                    pe.wait_ge(wo_in[b], 16 * (i * (NB // 2) + n // 2) + 16)
                    pe.wait_ge(gated, i * NB + n + 1)
                    for c in range(KD):
                        for h in range(2):
                            add_product(nc, gate_ps[b][:, h * HALF:(h + 1) * HALF], part(wg[b], slice(None), c, slice(None)),
                                        part(HT, slice(None), c, slice(h * HALF, (h + 1) * HALF)), c == 0, c == KD - 1)
                    for c in range(chunks):
                        for h in range(2):
                            last = nc.tensor.matmul(out_ps[b][:, h * HALF:(h + 1) * HALF], wo[b][:, c, :],
                                                    y[:, c, h * HALF:(h + 1) * HALF], start=(c == 0), stop=(c == chunks - 1))
                    last.then_inc(products, 1)

        @block.scalar
        def _(act):
            split_first(nc, act, wg_in, wg_raw, wg, split)
            with act.Fori(0, KD) as i:
                for n in range(NB):
                    g = i * NB + n
                    act.wait_ge(products, g + 1 + 2)
                    act.wait_ge(gated, g + 2)
                    nc.scalar.activation(gate[:], gate_ps[n % 2][:], ACT.Sigmoid).then_inc(gates, 1)

        @block.vector
        def _(dve):
            dve.sem_inc(totals, 1)
            dve.sem_inc(gated, 2)
            split_first(nc, dve, wg_in, wg_raw, wg, split)
            with dve.Fori(0, KD) as i:
                total = merged[:, bass.ds(i, 1), :].rearrange("p c s -> p (c s)")
                for n in range(NB):
                    g = i * NB + n
                    dve.wait_ge(gates, g + 1)
                    if n == 0:
                        nc.vector.tensor_tensor(total, gate[:], out_ps[0][:], ALU.mult).then_inc(gated, 1)
                        dve.wait_ge(gated, g + 1 + 2)
                        dve.sem_inc(totals, 1)
                        continue
                    dve.wait_ge(totals, g + 1)
                    nc.vector.tensor_tensor(gated_part[:], gate[:], out_ps[n % 2][:], ALU.mult).then_inc(gated, 1)
                    dve.wait_ge(gated, g + 1 + 2)
                    nc.vector.tensor_tensor(total, total, gated_part[:], ALU.add).then_inc(totals, 1)


def swiglu_up(k, hidden, HT):
    nc = k.nc
    with k.phase() as ctx:
        raw = [k.X[:, 4 * b:4 * b + 2, :].rearrange("p m (c n) -> p m c n", n=P) for b in range(2)]
        silu = [k.X[:, 4 * b + 2, :] for b in range(2)]
        w = pair(k, "up_ws", [P, 2, KD, P], ctx)
        acc = [k.ps(f"up_acc{b}", [P, 2, S], ctx) for b in range(2)]
        w_in0, w_in1, split, passed, products, silus, done = k.sems(
            "up", "w_in0 w_in1 split passed products silus done")
        w_in = (w_in0, w_in1)
        block = ctx.enter_context(nc.Block())
        views = [k.dram[name][0].rearrange("(c p) n -> p c n", p=P) for name in ("w_gate_2", "w_up_2")]

        @block.sync
        def _(sp):
            with sp.Fori(0, FFC // 2) as i:
                for b in range(2):
                    sp.wait_ge(split, 4 * (2 * i + b) + 4)
                    for m in range(2):
                        sp.dma_start(raw[b][:, m, :, :], views[m][:, :, bass.ds((2 * i + b) * P, P)]).then_inc(w_in[b], 16)

        @block.gpsimd
        def _(pool):
            pool.sem_inc(split, 8)
            pool.wait_ge(split, 8 + 4)

            def split_chunk(i, b):
                j = 2 * i + b
                pool.wait_ge(w_in[b], 32 * i + 32)
                for m in range(2):
                    pool.wait_ge(products, 2 * j + m + 1)
                    pool.sem_inc(passed, 1)
                    nc.gpsimd.tensor_copy(w[0][:, m, :, :], raw[b][:, m, :, :]).then_inc(split, 1)
                    pool.wait_ge(split, 4 * j + 2 * m + 1 + 8)
                    nc.gpsimd.tensor_tensor(w[1][:, m, :, :], raw[b][:, m, :, :], w[0][:, m, :, :],
                                            ALU.subtract).then_inc(split, 1)
            split_chunk(0, 1)
            with pool.Fori(1, FFC // 2) as i:
                for b in range(2):
                    split_chunk(i, b)

        @block.tensor
        def _(pe):
            pe.sem_inc(products, 2)
            with pe.Fori(0, FFC // 2) as i:
                for b in range(2):
                    j = 2 * i + b
                    pe.wait_ge(done, j + 1)
                    for m in range(2):
                        pe.wait_ge(split, 4 * j + 2 * m + 2 + 8)
                        for c in range(KD):
                            for h in range(2):
                                last = add_product(nc, acc[b][:, m, h * HALF:(h + 1) * HALF],
                                                   part(w, slice(None), m, c, slice(None)),
                                                   part(HT, slice(None), c, slice(h * HALF, (h + 1) * HALF)),
                                                   c == 0, c == KD - 1)
                        last.then_inc(products, 1)

        @block.scalar
        def _(act):
            act.wait_ge(w_in0, 32)
            for m in range(2):
                act.wait_ge(split, 8 + 2 * m)
                nc.scalar.activation(w[0][:, m, :, :], raw[0][:, m, :, :], ACT.Copy).then_inc(split, 1)
            with act.Fori(0, FFC // 2) as i:
                for b in range(2):
                    act.wait_ge(products, 2 * (2 * i + b) + 2 + 2)
                    act.wait_ge(done, 2 * i + b + 1)
                    nc.scalar.activation(silu[b], acc[b][:, 0, :], ACT.Silu).then_inc(silus, 1)

        @block.vector
        def _(dve):
            dve.sem_inc(done, 2)
            for m in range(2):
                dve.wait_ge(split, 8 + 2 * m + 1)
                nc.vector.tensor_tensor(w[1][:, m, :, :], raw[0][:, m, :, :], w[0][:, m, :, :], ALU.subtract).then_inc(split, 1)
            with dve.Fori(0, FFC // 2) as i:
                for b in range(2):
                    dve.wait_ge(silus, 2 * i + b + 1)
                    nc.vector.tensor_tensor(hidden[:, bass.ds(2 * i + b, 1), :].rearrange("p c s -> p (c s)"),
                                            silu[b], acc[b][:, 1, :], ALU.mult).then_inc(done, 1)


def scaled_gains(k):
    nc = k.nc
    with k.phase() as ctx:
        (made,) = k.sems("gains", "made")
        block = ctx.enter_context(nc.Block())

        @block.vector
        def _(dve):
            for col, name, factor in (((0, 2), "fox_q_gain_2", HD ** -0.5), ((2, 4), "fox_k_gain_2", 1.0),
                                      ((4, 8), "swa_q_gain_2", HD ** -0.5), ((8, 9), "swa_k_gain_2", 1.0)):
                n = col[1] - col[0]
                nc.vector.tensor_scalar(k.head_gains[:, col[0]:col[1]], k.gain(name).broadcast_to([P, n]), factor, None,
                                        ALU.mult).then_inc(made, 1)


def second_mixer(k):
    nc = k.nc
    w_in = k.dram["w_in_2"][0]
    H = 4
    with ExitStack() as ctx:
        fox_y = k.sb("fox_y", [P, 2, S], ctx=ctx)
        conv_y = k.sb("conv_y", [P, 2, S], ctx=ctx)
        ml_y = k.sb("ml_y", [P, 2, S], ctx=ctx)
        swa_y = k.sb("swa_y", [P, 4, S], ctx=ctx)
        with ExitStack() as inner:
            k.head_gains = k.sb("head_gains", [P, 9], ctx=inner)
            k.a_col = k.sb("a_col", [P, ST, H], ctx=inner)
            k.floor_col = k.sb("floor_col", [P, ST, H], ctx=inner)
            v2 = k.sb("v2", [P, ST, 5 * P], ctx=inner)
            vm = k.sb("vm", [P, ST, H, HD + 1], ctx=inner)
            with ExitStack() as normed:
                HT = pair(k, "attn_h", [P, KD, S], normed)
                norm_turn(k, "attn_norm", k.X, ST, k.gain("attn_norm_2"), HT)
                scaled_gains(k)
                project_rows(k, "fox_qk", w_in[:, 0:512], 4, HT, KD, k.scratch["fox_qk"], gain=k.head_gains[:, 0:4])
                project_rows(k, "swa_qk", w_in[:, C_SQ:C_SQ + 640], 5, HT, KD, k.scratch["swa_qk"], gain=k.head_gains[:, 4:9])
                project_rows(k, "plain", w_in[:, C_CU:C_MV], 10, HT, KD, k.scratch["plain"])
                project_rows(k, "mo", w_in[:, C_MO:C_SQ], 2, HT, KD, k.scratch["mo"])
                views = [w_in[:, c:c + n].rearrange("(c p) n -> p c n", p=P) for c, n in ((C_FV, 256), (C_MV, 256), (C_SV, 128))]
                project_tokens(k, "v2", [(views[0], 0, 256), (views[1], 256, 256), (views[2], 512, 128)], 5 * P, HT, KD, v2)
                gate_rows(k, vm, HT, ((swa_y, 4), (conv_y, 2), (ml_y, 2)))
            y = swa_y[:, :, :].rearrange("p c (x n) -> p (c x) n", n=512)
            with ExitStack() as fox:
                k.causal = k.sb("causal", [P, S], ctx=fox)
                split_values(k, v2, vm)
                attention(k, "fox", H,
                          lambda b, h: [("q", 0, 0, k.scratch["fox_qk"][bass.ds(h * HD, HD), :]),
                                        ("q", 0, HD, k.scratch["fox_q"][bass.ds(h * 2, 2), :]),
                                        ("k", 0, 0, k.scratch["fox_qk"][bass.ds(h * HD + 256, HD), :]),
                                        ("k", 0, HD, k.scratch["fox_k"][bass.ds(h * 2, 2), :])],
                          HD + 2, v2, y, 0)
                turn(k, "fox_turn", y[:, :, 0:256], k.ones[:, 0:2], fox_y, 2)
            matrix_lstm(k, vm, y)
            head_norm(k, "ml_rms", y[:, :, 0:256], H, HD, 1.0)
            turn(k, "ml_turn", y[:, :, 0:256], k.gain("mlstm_h_gain_2"), ml_y, 2)
            short_conv(k, conv_y, ml_y)
            biases = k.sb("biases", [P, 8, 2 * P], ctx=inner)
            sinks = k.sb("sinks", [P, 8], ctx=inner)
            window_bias(k, biases, sinks)
            y = k.sb("y_rows", [P, ST, 512], ctx=inner)
            for kv in range(2):
                attention(k, f"swa{kv}", 4,
                          lambda b, h: [("q", 0, 0, k.scratch["swa_qk"][bass.ds(h * HD + kv * 4 * HD, HD), :]),
                                        ("k", 0, 0, k.scratch["swa_qk"][512 + kv * HD:512 + (kv + 1) * HD, :])],
                          HD, v2, y, kv * 256, window=(kv * 4, 512 + kv * HD, biases, sinks))
            turn(k, "swa_turn", y[:, :, 0:512], k.ones[:, 0:4], swa_y, 4)
        merged = k.sb("merged", [P, KD, S], ctx=ctx)
        with ExitStack() as normed:
            HT = pair(k, "attn_h", [P, KD, S], normed)
            norm_turn(k, "attn_norm", k.X, ST, k.gain("attn_norm_2"), HT)
            gated_merge(k, [("w_fox_out_2", fox_y, 2), ("w_conv_out_2", conv_y, 2), ("w_mlstm_out_2", ml_y, 2),
                        ("w_swa_out_2", swa_y, 4)], merged, HT)
        project_residual(k, "merge_out", k.dram["w_merge_out_2"][0], merged, KD, split_src=True)


def split_values(k, v2, vm):
    nc = k.nc
    with k.phase() as ctx:
        (made,) = k.sems("split", "made")
        block = ctx.enter_context(nc.Block())

        @block.gpsimd
        def _(pool):
            link = k.own("pool", pool)
            link(nc.gpsimd.memset(k.causal[:], 0.0))
            link(nc.gpsimd.affine_select(out=k.causal[:, S - P:S], in_=k.causal[:, S - P:S], compare_op=ALU.is_ge,
                                         fill=NEG, base=0, pattern=[[-1, P]], channel_multiplier=1))

        @block.vector
        def _(dve):
            for t in range(ST):
                nc.vector.tensor_copy(vm[:, t, :, 0:HD], v2[:, t, 256:512].rearrange("p (h n) -> p h n", n=HD)
                                      ).then_inc(made, 1)
        k.chains["pool"].settle()


def store(k, view, tile):
    nc = k.nc
    with k.phase() as ctx:
        (stored,) = k.sems("store", "stored")
        block = ctx.enter_context(nc.Block())

        @block.sync
        def _(sp):
            sp.dma_start(view, tile).then_inc(stored, 16)
            sp.wait_ge(stored, 16)


def swiglu(k):
    x_rows = k.scratch["x_rows"].rearrange("(t p) d -> p t d", p=P)
    with ExitStack() as ctx:
        hidden = k.sb("hidden", [P, FFC, S], ctx=ctx)
        with ExitStack() as normed:
            H = pair(k, "ffn2_h", [P, KD, S], normed)
            norm_turn(k, "ffn2_norm", k.X, ST, k.gain("ffn_norm_2"), H, save=x_rows)
            swiglu_up(k, hidden, H)
        project_residual(k, "down", k.dram["w_down_2"][0], hidden, FFC, saved=x_rows,
                         out=k.out.rearrange("a (t p) d -> p (a t) d", p=P))


def gate_rows(k, vm, HT, spare):
    nc = k.nc
    H = 4
    with k.phase() as ctx:
        w = k.sb("gr_w", [P, KD, 96], ctx=ctx)
        w_pair = pair(k, "gr_ws", [P, KD, 96], ctx)
        bias = k.sb("gr_bias", [H, 3], ctx=ctx)
        rows = [tile[0:H, c, :] for tile, count in spare for c in range(count)]
        raw, logs, sums = rows[0:3], rows[3:5], rows[5:7]
        ones = k.sb("gr_ones", [H, S], ctx=ctx)
        a, top, floor, neg = (k.sb(f"gr_{n}", [H, S], ctx=ctx) for n in ("a", "top", "floor", "neg"))
        acc = k.ps("gr_acc", [P, S], ctx)
        cols = k.ps("gr_cols", [P, 2, ST, H], ctx)
        w_in, w_split, bias_in, cleared, products, copied, absed, logged, rows_made, turned, stored = k.sems(
            "gr", "w_in w_split bias_in cleared products copied absed logged rows_made turned stored")
        block = ctx.enter_context(nc.Block())
        w_view = k.dram["w_in_2"][0].rearrange("(c p) n -> p c n", p=P)

        @block.sync
        def _(sp):
            sp.wait_ge(cleared, 2)
            for n, col in enumerate((C_FF, C_MI, C_MI + H)):
                sp.dma_start(w[:, :, 32 * n:32 * n + H], w_view[:, :, col:col + H]).then_inc(w_in, 16)
            for n, name in enumerate(("fox_f_bias_2", "mlstm_i_bias_2", "mlstm_f_bias_2")):
                sp.dma_start(bias[:, n:n + 1], k.dram[name].rearrange("l h -> h l")).then_inc(bias_in, 16)
            fox_q = k.scratch["fox_q"].rearrange("(h n) s -> h n s", n=2)
            fox_k = k.scratch["fox_k"].rearrange("(h n) s -> h n s", n=2)
            sp.dma_start(fox_q[:, 0, :], ones[:]).then_inc(stored, 16)
            sp.dma_start(fox_k[:, 1, :], ones[:]).then_inc(stored, 16)
            sp.wait_ge(rows_made, 1)
            sp.dma_start(fox_q[:, 1, :], sums[0][:]).then_inc(stored, 16)
            sp.wait_ge(rows_made, 2)
            sp.dma_start(fox_k[:, 0, :], neg[:]).then_inc(stored, 16)
            sp.wait_ge(rows_made, 4)
            sp.dma_start(k.scratch["mlstm_row"], top[:]).then_inc(stored, 16)
            sp.wait_ge(stored, 16 * 5)

        @block.gpsimd
        def _(pool):
            nc.gpsimd.memset(w[:, :, :], 0.0).then_inc(cleared, 1)
            nc.gpsimd.memset(ones[:], 1.0).then_inc(cleared, 1)
            nc.gpsimd.memset(vm[:, :, :, HD:HD + 1], 1.0).then_inc(cleared, 1)
            pool.wait_ge(w_in, 48)
            nc.gpsimd.tensor_copy(w_pair[0][:], w[:]).then_inc(w_split, 1)
            pool.wait_ge(w_split, 1)
            nc.gpsimd.tensor_tensor(w_pair[1][:], w[:], w_pair[0][:], ALU.subtract).then_inc(w_split, 1)

        @block.tensor
        def _(pe):
            pe.wait_ge(w_split, 2)
            for c in range(KD):
                for h in range(2):
                    last = add_product(nc, acc[0:96, h * HALF:(h + 1) * HALF], part(w_pair, slice(None), c, slice(None)),
                                       part(HT, slice(None), c, slice(h * HALF, (h + 1) * HALF)), c == 0, c == KD - 1)
            last.then_inc(products, 1)
            pe.wait_ge(rows_made, 5)
            for n, row in enumerate((a, floor)):
                for t in range(ST):
                    last = nc.tensor.transpose(cols[:, n, t, :], row[:, t * P:(t + 1) * P], k.ident[0:H, 0:H])
            last.then_inc(turned, 1)

        @block.scalar
        def _(act):
            act.wait_ge(products, 1)
            for n in range(3):
                nc.scalar.activation(raw[n][:], acc[32 * n:32 * n + H, :], ACT.Copy).then_inc(copied, 1)
            for n, x in enumerate((raw[0], raw[2])):
                act.wait_ge(absed, n + 1)
                nc.scalar.activation(logs[n][:], x[:], ACT.Abs).then_inc(logged, 1)
                act.wait_ge(logged, 3 * n + 1)
                nc.scalar.activation(logs[n][:], logs[n][:], ACT.Exp, scale=-1.0).then_inc(logged, 1)
                act.wait_ge(logged, 3 * n + 2)
                nc.scalar.activation(logs[n][:], logs[n][:], ACT.Ln, bias=1.0).then_inc(logged, 1)
            act.wait_ge(turned, 1)
            nc.scalar.activation(k.a_col[:, :, :], cols[:, 0, :, :], ACT.Copy)
            nc.scalar.activation(k.floor_col[:, :, :], cols[:, 1, :, :], ACT.Exp, scale=-1.0)

        @block.vector
        def _(dve):
            link = k.own("dve", dve)
            v = nc.vector
            dve.wait_ge(bias_in, 48)
            dve.wait_ge(copied, 3)
            dve.wait_ge(cleared, 3)
            for n in (0, 2):
                v.tensor_scalar(raw[n][:], raw[n][:], bias[:, n:n + 1], None, ALU.add).then_inc(absed, 1)
            link(v.tensor_scalar(raw[1][:], raw[1][:], bias[:, 1:2], None, ALU.add))
            for n, x in enumerate((raw[0], raw[2])):
                dve.wait_ge(logged, 3 * n + 3)
                link(v.scalar_tensor_tensor(out=logs[n][:], in0=x[:], scalar=0.0, in1=logs[n][:],
                                            op0=ALU.min, op1=ALU.subtract))
                ins = v.tensor_tensor_scan(sums[n][:], ones[:], logs[n][:], 0.0, ALU.mult, ALU.add)
                if n == 0:
                    ins.then_inc(rows_made, 1)
                    dve.wait_ge(rows_made, 1)
                    v.tensor_scalar(neg[:], sums[0][:], -1.0, None, ALU.mult).then_inc(rows_made, 1)
                else:
                    link(ins)
            link(v.tensor_tensor(a[:], raw[1][:], sums[1][:], ALU.subtract))
            link(v.tensor_tensor_scan(top[:], ones[:], a[:], 0.0, ALU.mult, ALU.max))
            v.tensor_tensor(floor[:], top[:], sums[1][:], ALU.add).then_inc(rows_made, 1)
            dve.wait_ge(rows_made, 3)
            v.tensor_scalar(top[:], top[:], -1.0, None, ALU.mult).then_inc(rows_made, 1)
            dve.wait_ge(rows_made, 4)
            dve.sem_inc(rows_made, 1)
        k.chains["dve"].settle()


def matrix_lstm(k, V, out):
    nc = k.nc
    H = 4
    with k.phase() as ctx:
        q = [k.sb(f"ml_q{b}", [HD, S], ctx=ctx) for b in range(2)]
        kk = [k.sb(f"ml_k{b}", [HD, S], ctx=ctx) for b in range(2)]
        row = [k.sb(f"ml_row{b}", [P, S], ctx=ctx) for b in range(2)]
        a_col = [k.sb(f"ml_a{b}", [P, ST], ctx=ctx) for b in range(2)]
        decay = [k.sb(f"ml_decay{b}", [P, S], ctx=ctx) for b in range(2)]
        w = [[k.sb(f"ml_w{b}{t}", [P, S - t * P], ctx=ctx) for t in range(ST)] for b in range(2)]
        stats = [k.sb(f"ml_stats{b}", [P, ST, 2], ctx=ctx) for b in range(2)]
        values = [k.sb(f"ml_v{b}", [P, ST, HD + 1], ctx=ctx) for b in range(2)]
        before_mask = k.sb("ml_mask", [P, P], ctx=ctx)
        scores = [k.ps(f"ml_scores{b}", [P, S], ctx) for b in range(2)]
        acc = [k.ps(f"ml_acc{b}", [P, 2, HALF], ctx) for b in range(2)]
        (head_in0, head_in1, mask_made, a_ready, v_ready, masked, decays, products, weighted, sums_made, linked,
         done) = k.sems("ml", "head_in0 head_in1 mask_made a_ready v_ready masked decays products weighted sums_made "
                        "linked done")
        head_in = (head_in0, head_in1)
        block = ctx.enter_context(nc.Block())
        rounds = H // 2
        plain = k.scratch["plain"]
        q_row, k_row = C_MQ - C_CU, C_MQ + H * HD - C_CU

        def at(b, t):
            return acc[b][:, t // 4, (t % 4) * (HD + 1):(t % 4 + 1) * (HD + 1)]

        @block.sync
        def _(sp):
            with sp.Fori(0, rounds) as i:
                for b in range(2):
                    sp.wait_ge(weighted, (2 * i + b) * ST + 2)
                    h = i * 2 + b
                    sp.dma_start(q[b][:], plain[bass.ds(h * HD + q_row, HD), :]).then_inc(head_in[b], 16)
                    sp.dma_start(kk[b][:], plain[bass.ds(h * HD + k_row, HD), :]).then_inc(head_in[b], 16)
                    sp.dma_start(row[b][:], k.scratch["mlstm_row"][bass.ds(h, 1), :].broadcast_to([P, S])
                                 ).then_inc(head_in[b], 16)

        @block.gpsimd
        def _(pool):
            nc.gpsimd.memset(before_mask[:], 0.0).then_inc(mask_made, 1)
            pool.wait_ge(mask_made, 1)
            nc.gpsimd.affine_select(out=before_mask[:], in_=before_mask[:], compare_op=ALU.is_ge, fill=NEG, base=0,
                                    pattern=[[1, P]], channel_multiplier=-1).then_inc(mask_made, 1)
            with pool.Fori(0, rounds) as i:
                for b in range(2):
                    pool.wait_ge(weighted, (2 * i + b) * ST + 2)
                    h = i * 2 + b
                    nc.gpsimd.tensor_copy(a_col[b][:], k.a_col[:, :, bass.ds(h, 1)].rearrange("p t h -> p (t h)")
                                          ).then_inc(a_ready, 1)
                    pool.wait_ge(sums_made, (2 * i + b) * ST + 1)
                    h = i * 2 + b
                    nc.gpsimd.tensor_copy(values[b][:, :, :], V[:, :, bass.ds(h, 1), :].rearrange(
                        "p t h n -> p (t h) n")).then_inc(v_ready, 1)

        @block.tensor
        def _(pe):
            pe.sem_inc(sums_made, 1 + ST)

            def score(i, n, g):
                b, t = n // ST, n % ST
                if t == 0:
                    pe.wait_ge(head_in[b], 48 * i + 48)
                pe.wait_ge(weighted, g + 1 + 8)
                width = S - t * P
                for c in range(0, width, HALF):
                    w_c = min(HALF, width - c)
                    last = nc.tensor.matmul(scores[t % 2][:, c:c + w_c], kk[b][:, t * P:(t + 1) * P],
                                            q[b][:, t * P + c:t * P + c + w_c], start=True, stop=True)
                last.then_inc(products, 1)

            def add_up(i, n, g):
                b, t = n // ST, n % ST
                pe.wait_ge(weighted, g + 1 + 10)
                if t == 0:
                    pe.wait_ge(v_ready, i * 2 + b + 1)
                    pe.wait_ge(done, i * 2 + b + 1)
                for c in range(t + 1):
                    last = nc.tensor.matmul(at(b, t), w[b][c][:, (t - c) * P:(t - c + 1) * P],
                                            values[b][:, c, :], start=(c == 0), stop=(c == t))
                last.then_inc(sums_made, 1)
            staged(pe, rounds, 2 * ST, ((0, score), (ST, add_up)))

        @block.scalar
        def _(act):
            def decay_from(i, n, g):
                b, t = n // ST, n % ST
                if t == 0:
                    act.wait_ge(head_in[b], 48 * i + 48)
                    act.wait_ge(a_ready, i * 2 + b + 1)
                act.wait_ge(weighted, g + 1 + 8)
                act.wait_ge(masked, g + 1)
                nc.scalar.activation(decay[t % 2][:, 0:P], decay[t % 2][:, 0:P], ACT.Exp,
                                     bias=a_col[b][:, t:t + 1]).then_inc(decays, 1)
                if t < ST - 1:
                    nc.scalar.activation(decay[t % 2][:, P:S - t * P], row[b][:, (t + 1) * P:S], ACT.Exp,
                                         bias=a_col[b][:, t:t + 1]).then_inc(decays, 1)
            staged(act, rounds, 2 * ST, ((0, decay_from),))

        @block.vector
        def _(dve):
            dve.sem_inc(done, 2)
            dve.sem_inc(weighted, 2 + ST)
            dve.wait_ge(mask_made, 2)
            per = 2 * ST - 1

            def mask(i, n, g):
                b, t = n // ST, n % ST
                if t == 0:
                    dve.wait_ge(head_in[b], 48 * i + 48)
                dve.wait_ge(weighted, g + 1 + 8)
                nc.vector.tensor_tensor(decay[t % 2][:, 0:P], row[b][:, t * P:(t + 1) * P], before_mask[:],
                                        ALU.add).then_inc(masked, 1)

            def weigh(i, n, g):
                b, t = n // ST, n % ST
                dve.wait_ge(products, g + 1)
                dve.wait_ge(decays, (i * 2 + b) * per + min(2 * (t + 1), per))
                dve.wait_ge(sums_made, (2 * i + b) * ST + 1)
                width = S - t * P
                nc.vector.scalar_tensor_tensor(out=w[b][t][:], in0=scores[t % 2][:, 0:width],
                                               scalar=HD ** -0.5, in1=decay[t % 2][:, 0:width],
                                               op0=ALU.mult, op1=ALU.mult).then_inc(weighted, 1)

            def divide(i, n, g):
                b, t = n // ST, n % ST
                if t < ST - 1:
                    return
                h = i * 2 + b
                dve.wait_ge(sums_made, h * ST + 2 * ST + 1)
                st = stats[b]
                den = acc[b][:, :, 0:4 * (HD + 1)].rearrange("p a (t n) -> p a t n", n=HD + 1)[:, :, :, HD:HD + 1]
                den = den.rearrange("p a t n -> p a (t n)")
                one = st[:, :, 0:1].rearrange("p (a t) n -> p a (t n)", a=2)
                nc.vector.tensor_copy(one, den).then_inc(linked, 1)
                dve.wait_ge(linked, 5 * h + 1)
                nc.vector.scalar_tensor_tensor(
                    out=st[:, :, 1:2], in0=st[:, :, 0:1], scalar=-1.0, in1=k.floor_col[:, :, bass.ds(h, 1)],
                    op0=ALU.mult, op1=ALU.max).then_inc(linked, 1)
                dve.wait_ge(linked, 5 * h + 2)
                nc.vector.tensor_tensor(st[:, :, 0:1], st[:, :, 0:1], st[:, :, 1:2], ALU.max).then_inc(linked, 1)
                dve.wait_ge(linked, 5 * h + 3)
                nc.vector.reciprocal(st[:, :, 1:2], st[:, :, 0:1]).then_inc(linked, 1)
                dve.wait_ge(linked, 5 * h + 4)
                for tile in range(ST):
                    ins = nc.vector.tensor_scalar(out[:, tile, bass.ds(h * HD, HD)], at(b, tile)[:, 0:HD],
                                                  st[:, tile, 1:2], None, ALU.mult)
                ins.then_inc(linked, 1)
                dve.wait_ge(linked, 5 * h + 5)
                dve.sem_inc(done, 1)
            staged(dve, rounds, 2 * ST, ((0, mask), (1, weigh), (ST + 1, divide)))


def short_conv(k, conv_out, ml_rows):
    nc = k.nc
    CH = 2
    with k.phase() as ctx:
        u, bg, cg, mo = (k.sb(f"conv_{n}", [P, CH, S], ctx=ctx) for n in ("u", "b", "c", "mo"))
        loaded, gated, chain_c = k.sems("conv", "loaded gated chain_c")
        block = ctx.enter_context(nc.Block())
        plain = k.scratch["plain"]

        @block.sync
        def _(sp):
            for n, tile in enumerate((u, bg, cg)):
                sp.dma_start(tile[:, :, :], plain[n * CH * P:(n + 1) * CH * P, :].rearrange("(c p) s -> p c s", p=P)
                             ).then_inc(loaded, 16)
            sp.dma_start(mo[:, :, :], k.scratch["mo"].rearrange("(c p) s -> p c s", p=P)).then_inc(gated, 16)

        @block.scalar
        def _(act):
            act.wait_ge(gated, 16)
            nc.scalar.activation(mo[:, :, :], mo[:, :, :], ACT.Sigmoid).then_inc(gated, 1)

        @block.vector
        def _(dve):
            link = k.own("dve", dve)
            dve.wait_ge(loaded, 48)
            link(nc.vector.tensor_tensor(u[:, :, :], u[:, :, :], cg[:, :, :], ALU.mult))
            for c in range(CH):
                taps = [k.gain("conv_w_2", n * CH + c, 1) for n in range(3)]
                link(nc.vector.tensor_scalar(conv_out[:, c, :], u[:, c, :], taps[2], None, ALU.mult))
                for back, tap in ((1, taps[1]), (2, taps[0])):
                    link(nc.vector.scalar_tensor_tensor(out=conv_out[:, c, back:], in0=u[:, c, 0:S - back], scalar=tap,
                                                        in1=conv_out[:, c, back:], op0=ALU.mult, op1=ALU.add))
            link(nc.vector.tensor_tensor(conv_out[:, :, :], conv_out[:, :, :], bg[:, :, :], ALU.mult))
            dve.wait_ge(gated, 17)
            link(nc.vector.tensor_tensor(ml_rows[:, :, :], ml_rows[:, :, :], mo[:, :, :], ALU.mult))
        k.chains["dve"].settle()


def t5_buckets(n):
    exact, most, buckets = 16, 128, 32
    out = []
    for d in range(n):
        if d < exact:
            out.append(d)
        else:
            large = exact + int(np.log(d / exact) / np.log(most / exact) * (buckets - exact))
            out.append(min(large, buckets - 1))
    return out


def window_bias(k, biases, sinks):
    nc = k.nc
    H, B, W2 = 8, 32, 3 * P
    with k.phase() as ctx:
        rel = k.sb("wb_rel", [B, H], ctx=ctx)
        hot = k.sb("wb_hot", [B, W2], ctx=ctx)
        index = k.sb("wb_index", [B, 1], ctx=ctx)
        bucket = k.sb("wb_bucket", [B, W2], ctx=ctx)
        rows = k.sb("wb_rows", [H, W2], ctx=ctx)
        flipped = k.sb("wb_flipped", [P, H, 2 * P], ctx=ctx)
        flip = k.sb("wb_flip", [P, P], ctx=ctx)
        acc = k.ps("wb_acc", [H, W2], ctx)
        turned = k.ps("wb_turned", [P, H, 2 * P], ctx)
        rel_in, bucketed, made, hot_made, product, rows_made, stored, loaded, upright = k.sems(
            "wb", "rel_in bucketed made hot_made product rows_made stored loaded upright")
        block = ctx.enter_context(nc.Block())
        buckets = t5_buckets(WINDOW)
        runs = []
        for j in range(P, 2 * P):
            value = buckets[2 * P - 1 - j]
            if runs and runs[-1][2] == value:
                runs[-1][1] = j + 1
            else:
                runs.append([j, j + 1, value])

        @block.sync
        def _(sp):
            sp.dma_start(rel[:], k.dram["rel_bias_2"]).then_inc(rel_in, 16)
            sp.dma_start(sinks[:], k.dram["swa_sinks_2"].broadcast_to([P, H])).then_inc(loaded, 16)
            sp.wait_ge(rows_made, 3)
            sp.dma_start(k.scratch["window_rows"], rows[:]).then_inc(stored, 16)
            sp.wait_ge(stored, 16)
            view = k.scratch["window_rows"]
            for h in range(H):
                skewed = bass.AP(view.tensor, view.offset + h * W2, [[1, P], [1, 2 * P]])
                sp.dma_start(flipped[:, h, :], skewed).then_inc(loaded, 16)

        @block.gpsimd
        def _(pool):
            nc.gpsimd.memset(bucket[:], -1.0).then_inc(made, 1)
            nc.gpsimd.iota(index[:], [[0, 1]], 0, 1, allow_small_or_imprecise_dtypes=True).then_inc(made, 1)
            nc.gpsimd.memset(flip[:], 0.0).then_inc(made, 1)
            pool.wait_ge(made, 3)
            nc.gpsimd.affine_select(out=flip[:], in_=flip[:], compare_op=ALU.not_equal, fill=1.0, base=1 - P,
                                    pattern=[[1, P]], channel_multiplier=1).then_inc(made, 1)
            for at, to, value in runs:
                nc.gpsimd.memset(bucket[:, at:to], float(value)).then_inc(bucketed, 1)

        @block.vector
        def _(dve):
            dve.wait_ge(bucketed, len(runs))
            nc.vector.tensor_scalar(hot[:], bucket[:], index[:], None, ALU.is_equal).then_inc(hot_made, 1)
            nc.vector.memset(rows[:, 0:P], NEG).then_inc(rows_made, 1)
            nc.vector.memset(rows[:, 2 * P:], NEG).then_inc(rows_made, 1)
            dve.wait_ge(product, 1)
            nc.vector.tensor_copy(rows[:, P:2 * P], acc[:, P:2 * P]).then_inc(rows_made, 1)
            dve.wait_ge(upright, 1)
            nc.vector.tensor_copy(biases[:, :, :], turned[:, :, :])

        @block.tensor
        def _(pe):
            pe.wait_ge(hot_made, 1)
            pe.wait_ge(rel_in, 16)
            nc.tensor.matmul(acc[:], rel[:], hot[:], start=True, stop=True).then_inc(product, 1)
            pe.wait_ge(made, 4)
            pe.wait_ge(loaded, 16 * (H + 1))
            for h in range(0, H, 2):
                last = nc.tensor.matmul(turned[:, h:h + 2, :], flip[:], flipped[:, h:h + 2, :], start=True, stop=True)
            last.then_inc(upright, 1)


def gated_merge(k, branches, merged, HT):
    nc = k.nc
    NB = len(branches)
    with k.phase() as ctx:
        wg_raw = [k.sb(f"gm_wg{b}", [P, KD, P], ctx=ctx) for b in range(2)]
        wg = [pair(k, f"gm_wgs{b}", [P, KD, P], ctx) for b in range(2)]
        wo = [k.sb(f"gm_wo{b}", [P, 4, P], ctx=ctx) for b in range(2)]
        gate = k.sb("gm_gate", [P, S], ctx=ctx)
        gated_part = k.sb("gm_part", [P, S], ctx=ctx)
        gate_ps = [k.ps(f"gm_gate_ps{b}", [P, S], ctx) for b in range(2)]
        out_ps = [k.ps(f"gm_out_ps{b}", [P, S], ctx) for b in range(2)]
        wg_in0, wg_in1, wo_in0, wo_in1, split, passed, products, gates, gated, totals = k.sems(
            "gm", "wg_in0 wg_in1 wo_in0 wo_in1 split passed products gates gated totals")
        wg_in, wo_in = (wg_in0, wg_in1), (wo_in0, wo_in1)
        block = ctx.enter_context(nc.Block())
        w_view = k.dram["w_in_2"][0].rearrange("(c p) n -> p c n", p=P)
        outs = [k.dram[name][0].rearrange("(c p) n -> p c n", p=P) for name, _, _ in branches]

        @block.sync
        def _(sp):
            with sp.Fori(0, KD) as i:
                for n in range(NB):
                    sp.wait_ge(split, 2 * (i * NB + n) + 2)
                    col = bass.ds(i * P + C_GATES + n * D, P)
                    sp.dma_start(wg_raw[n % 2][:, :, :], w_view[:, :, col]).then_inc(wg_in[n % 2], 16)
                    sp.wait_ge(products, i * NB + n + 1)
                    sp.sem_inc(passed, 1)
                    sp.dma_start(wo[n % 2][:, 0:branches[n][2], :], outs[n][:, :, bass.ds(i * P, P)]).then_inc(wo_in[n % 2], 16)

        @block.gpsimd
        def _(pool):
            pool.sem_inc(split, 4)
            pool.wait_ge(split, 4 + 4)

            def split_round(i, start):
                for n in range(start, NB):
                    split_weights(nc, pool, i * NB + n, n % 2, (wg_in[n % 2], 16 * (i * (NB // 2) + n // 2) + 16), wg_raw, wg,
                                  products, split, passed)
            split_round(0, 2)
            with pool.Fori(1, KD) as i:
                split_round(i, 0)

        @block.tensor
        def _(pe):
            pe.sem_inc(products, 2)
            with pe.Fori(0, KD) as i:
                for n in range(NB):
                    b = n % 2
                    y, chunks = branches[n][1], branches[n][2]
                    pe.wait_ge(split, 2 * (i * NB + n) + 2 + 4)
                    pe.wait_ge(wo_in[b], 16 * (i * (NB // 2) + n // 2) + 16)
                    pe.wait_ge(gated, i * NB + n + 1)
                    for c in range(KD):
                        for h in range(2):
                            add_product(nc, gate_ps[b][:, h * HALF:(h + 1) * HALF], part(wg[b], slice(None), c, slice(None)),
                                        part(HT, slice(None), c, slice(h * HALF, (h + 1) * HALF)), c == 0, c == KD - 1)
                    for c in range(chunks):
                        for h in range(2):
                            last = nc.tensor.matmul(out_ps[b][:, h * HALF:(h + 1) * HALF], wo[b][:, c, :],
                                                    y[:, c, h * HALF:(h + 1) * HALF], start=(c == 0), stop=(c == chunks - 1))
                    last.then_inc(products, 1)

        @block.scalar
        def _(act):
            split_first(nc, act, wg_in, wg_raw, wg, split)
            with act.Fori(0, KD) as i:
                for n in range(NB):
                    g = i * NB + n
                    act.wait_ge(products, g + 1 + 2)
                    act.wait_ge(gated, g + 2)
                    nc.scalar.activation(gate[:], gate_ps[n % 2][:], ACT.Sigmoid).then_inc(gates, 1)

        @block.vector
        def _(dve):
            dve.sem_inc(totals, 1)
            dve.sem_inc(gated, 2)
            split_first(nc, dve, wg_in, wg_raw, wg, split)
            with dve.Fori(0, KD) as i:
                total = merged[:, bass.ds(i, 1), :].rearrange("p c s -> p (c s)")
                for n in range(NB):
                    g = i * NB + n
                    dve.wait_ge(gates, g + 1)
                    if n == 0:
                        nc.vector.tensor_tensor(total, gate[:], out_ps[0][:], ALU.mult).then_inc(gated, 1)
                        dve.wait_ge(gated, g + 1 + 2)
                        dve.sem_inc(totals, 1)
                        continue
                    dve.wait_ge(totals, g + 1)
                    nc.vector.tensor_tensor(gated_part[:], gate[:], out_ps[n % 2][:], ALU.mult).then_inc(gated, 1)
                    dve.wait_ge(gated, g + 1 + 2)
                    nc.vector.tensor_tensor(total, total, gated_part[:], ALU.add).then_inc(totals, 1)


def swiglu_up(k, hidden, HT):
    nc = k.nc
    with k.phase() as ctx:
        raw = [k.X[:, 4 * b:4 * b + 2, :].rearrange("p m (c n) -> p m c n", n=P) for b in range(2)]
        silu = [k.X[:, 4 * b + 2, :] for b in range(2)]
        w = pair(k, "up_ws", [P, 2, KD, P], ctx)
        acc = [k.ps(f"up_acc{b}", [P, 2, S], ctx) for b in range(2)]
        w_in0, w_in1, split, passed, products, silus, done = k.sems(
            "up", "w_in0 w_in1 split passed products silus done")
        w_in = (w_in0, w_in1)
        block = ctx.enter_context(nc.Block())
        views = [k.dram[name][0].rearrange("(c p) n -> p c n", p=P) for name in ("w_gate_2", "w_up_2")]

        @block.sync
        def _(sp):
            with sp.Fori(0, FFC // 2) as i:
                for b in range(2):
                    sp.wait_ge(split, 4 * (2 * i + b) + 4)
                    for m in range(2):
                        sp.dma_start(raw[b][:, m, :, :], views[m][:, :, bass.ds((2 * i + b) * P, P)]).then_inc(w_in[b], 16)

        @block.gpsimd
        def _(pool):
            pool.sem_inc(split, 8)
            pool.wait_ge(split, 8 + 4)

            def split_chunk(i, b):
                j = 2 * i + b
                pool.wait_ge(w_in[b], 32 * i + 32)
                for m in range(2):
                    pool.wait_ge(products, 2 * j + m + 1)
                    pool.sem_inc(passed, 1)
                    nc.gpsimd.tensor_copy(w[0][:, m, :, :], raw[b][:, m, :, :]).then_inc(split, 1)
                    pool.wait_ge(split, 4 * j + 2 * m + 1 + 8)
                    nc.gpsimd.tensor_tensor(w[1][:, m, :, :], raw[b][:, m, :, :], w[0][:, m, :, :],
                                            ALU.subtract).then_inc(split, 1)
            split_chunk(0, 1)
            with pool.Fori(1, FFC // 2) as i:
                for b in range(2):
                    split_chunk(i, b)

        @block.tensor
        def _(pe):
            pe.sem_inc(products, 2)
            with pe.Fori(0, FFC // 2) as i:
                for b in range(2):
                    j = 2 * i + b
                    pe.wait_ge(done, j + 1)
                    for m in range(2):
                        pe.wait_ge(split, 4 * j + 2 * m + 2 + 8)
                        for c in range(KD):
                            for h in range(2):
                                last = add_product(nc, acc[b][:, m, h * HALF:(h + 1) * HALF],
                                                   part(w, slice(None), m, c, slice(None)),
                                                   part(HT, slice(None), c, slice(h * HALF, (h + 1) * HALF)),
                                                   c == 0, c == KD - 1)
                        last.then_inc(products, 1)

        @block.scalar
        def _(act):
            act.wait_ge(w_in0, 32)
            for m in range(2):
                act.wait_ge(split, 8 + 2 * m)
                nc.scalar.activation(w[0][:, m, :, :], raw[0][:, m, :, :], ACT.Copy).then_inc(split, 1)
            with act.Fori(0, FFC // 2) as i:
                for b in range(2):
                    act.wait_ge(products, 2 * (2 * i + b) + 2 + 2)
                    act.wait_ge(done, 2 * i + b + 1)
                    nc.scalar.activation(silu[b], acc[b][:, 0, :], ACT.Silu).then_inc(silus, 1)

        @block.vector
        def _(dve):
            dve.sem_inc(done, 2)
            for m in range(2):
                dve.wait_ge(split, 8 + 2 * m + 1)
                nc.vector.tensor_tensor(w[1][:, m, :, :], raw[0][:, m, :, :], w[0][:, m, :, :], ALU.subtract).then_inc(split, 1)
            with dve.Fori(0, FFC // 2) as i:
                for b in range(2):
                    dve.wait_ge(silus, 2 * i + b + 1)
                    nc.vector.tensor_tensor(hidden[:, bass.ds(2 * i + b, 1), :].rearrange("p c s -> p (c s)"),
                                            silu[b], acc[b][:, 1, :], ALU.mult).then_inc(done, 1)


def scaled_gains(k):
    nc = k.nc
    with k.phase() as ctx:
        (made,) = k.sems("gains", "made")
        block = ctx.enter_context(nc.Block())

        @block.vector
        def _(dve):
            for col, name, factor in (((0, 2), "fox_q_gain_2", HD ** -0.5), ((2, 4), "fox_k_gain_2", 1.0),
                                      ((4, 8), "swa_q_gain_2", HD ** -0.5), ((8, 9), "swa_k_gain_2", 1.0)):
                n = col[1] - col[0]
                nc.vector.tensor_scalar(k.head_gains[:, col[0]:col[1]], k.gain(name).broadcast_to([P, n]), factor, None,
                                        ALU.mult).then_inc(made, 1)


def second_mixer(k):
    nc = k.nc
    w_in = k.dram["w_in_2"][0]
    H = 4
    with ExitStack() as ctx:
        fox_y = k.sb("fox_y", [P, 2, S], ctx=ctx)
        conv_y = k.sb("conv_y", [P, 2, S], ctx=ctx)
        ml_y = k.sb("ml_y", [P, 2, S], ctx=ctx)
        swa_y = k.sb("swa_y", [P, 4, S], ctx=ctx)
        with ExitStack() as inner:
            k.head_gains = k.sb("head_gains", [P, 9], ctx=inner)
            k.a_col = k.sb("a_col", [P, ST, H], ctx=inner)
            k.floor_col = k.sb("floor_col", [P, ST, H], ctx=inner)
            v2 = k.sb("v2", [P, ST, 5 * P], ctx=inner)
            vm = k.sb("vm", [P, ST, H, HD + 1], ctx=inner)
            with ExitStack() as normed:
                HT = pair(k, "attn_h", [P, KD, S], normed)
                norm_turn(k, "attn_norm", k.X, ST, k.gain("attn_norm_2"), HT)
                scaled_gains(k)
                project_rows(k, "fox_qk", w_in[:, 0:512], 4, HT, KD, k.scratch["fox_qk"], gain=k.head_gains[:, 0:4])
                project_rows(k, "swa_qk", w_in[:, C_SQ:C_SQ + 640], 5, HT, KD, k.scratch["swa_qk"], gain=k.head_gains[:, 4:9])
                project_rows(k, "plain", w_in[:, C_CU:C_MV], 10, HT, KD, k.scratch["plain"])
                project_rows(k, "mo", w_in[:, C_MO:C_SQ], 2, HT, KD, k.scratch["mo"])
                views = [w_in[:, c:c + n].rearrange("(c p) n -> p c n", p=P) for c, n in ((C_FV, 256), (C_MV, 256), (C_SV, 128))]
                project_tokens(k, "v2", [(views[0], 0, 256), (views[1], 256, 256), (views[2], 512, 128)], 5 * P, HT, KD, v2)
                gate_rows(k, vm, HT, ((swa_y, 4), (conv_y, 2), (ml_y, 2)))
            y = swa_y[:, :, :].rearrange("p c (x n) -> p (c x) n", n=512)
            with ExitStack() as fox:
                k.causal = k.sb("causal", [P, S], ctx=fox)
                split_values(k, v2, vm)
                attention(k, "fox", H,
                          lambda b, h: [("q", 0, 0, k.scratch["fox_qk"][bass.ds(h * HD, HD), :]),
                                        ("q", 0, HD, k.scratch["fox_q"][bass.ds(h * 2, 2), :]),
                                        ("k", 0, 0, k.scratch["fox_qk"][bass.ds(h * HD + 256, HD), :]),
                                        ("k", 0, HD, k.scratch["fox_k"][bass.ds(h * 2, 2), :])],
                          HD + 2, v2, y, 0)
                turn(k, "fox_turn", y[:, :, 0:256], k.ones[:, 0:2], fox_y, 2)
            matrix_lstm(k, vm, y)
            head_norm(k, "ml_rms", y[:, :, 0:256], H, HD, 1.0)
            turn(k, "ml_turn", y[:, :, 0:256], k.gain("mlstm_h_gain_2"), ml_y, 2)
            short_conv(k, conv_y, ml_y)
            biases = k.sb("biases", [P, 8, 2 * P], ctx=inner)
            sinks = k.sb("sinks", [P, 8], ctx=inner)
            window_bias(k, biases, sinks)
            y = k.sb("y_rows", [P, ST, 512], ctx=inner)
            for kv in range(2):
                attention(k, f"swa{kv}", 4,
                          lambda b, h: [("q", 0, 0, k.scratch["swa_qk"][bass.ds(h * HD + kv * 4 * HD, HD), :]),
                                        ("k", 0, 0, k.scratch["swa_qk"][512 + kv * HD:512 + (kv + 1) * HD, :])],
                          HD, v2, y, kv * 256, window=(kv * 4, 512 + kv * HD, biases, sinks))
            turn(k, "swa_turn", y[:, :, 0:512], k.ones[:, 0:4], swa_y, 4)
        merged = k.sb("merged", [P, KD, S], ctx=ctx)
        with ExitStack() as normed:
            HT = pair(k, "attn_h", [P, KD, S], normed)
            norm_turn(k, "attn_norm", k.X, ST, k.gain("attn_norm_2"), HT)
            gated_merge(k, [("w_fox_out_2", fox_y, 2), ("w_conv_out_2", conv_y, 2), ("w_mlstm_out_2", ml_y, 2),
                        ("w_swa_out_2", swa_y, 4)], merged, HT)
        project_residual(k, "merge_out", k.dram["w_merge_out_2"][0], merged, KD, split_src=True)


def split_values(k, v2, vm):
    nc = k.nc
    with k.phase() as ctx:
        (made,) = k.sems("split", "made")
        block = ctx.enter_context(nc.Block())

        @block.gpsimd
        def _(pool):
            link = k.own("pool", pool)
            link(nc.gpsimd.memset(k.causal[:], 0.0))
            link(nc.gpsimd.affine_select(out=k.causal[:, S - P:S], in_=k.causal[:, S - P:S], compare_op=ALU.is_ge,
                                         fill=NEG, base=0, pattern=[[-1, P]], channel_multiplier=1))

        @block.vector
        def _(dve):
            for t in range(ST):
                nc.vector.tensor_copy(vm[:, t, :, 0:HD], v2[:, t, 256:512].rearrange("p (h n) -> p h n", n=HD)
                                      ).then_inc(made, 1)
        k.chains["pool"].settle()


def store(k, view, tile):
    nc = k.nc
    with k.phase() as ctx:
        (stored,) = k.sems("store", "stored")
        block = ctx.enter_context(nc.Block())

        @block.sync
        def _(sp):
            sp.dma_start(view, tile).then_inc(stored, 16)
            sp.wait_ge(stored, 16)


def swiglu(k):
    x_rows = k.scratch["x_rows"].rearrange("(t p) d -> p t d", p=P)
    with ExitStack() as ctx:
        hidden = k.sb("hidden", [P, FFC, S], ctx=ctx)
        with ExitStack() as normed:
            H = pair(k, "ffn2_h", [P, KD, S], normed)
            norm_turn(k, "ffn2_norm", k.X, ST, k.gain("ffn_norm_2"), H, save=x_rows)
            swiglu_up(k, hidden, H)
        project_residual(k, "down", k.dram["w_down_2"][0], hidden, FFC, saved=x_rows,
                         out=k.out.rearrange("a (t p) d -> p (a t) d", p=P))


def dump(k, tile):
    nc = k.nc
    with k.phase() as ctx:
        (stored,) = k.sems("dump", "stored")
        block = ctx.enter_context(nc.Block())

        @block.sync
        def _(sp):
            sp.dma_start(k.out.rearrange("a (t p) d -> p (a t) d", p=P), tile[:, :, :]).then_inc(stored, 16)
            sp.wait_ge(stored, 16)


def program(nc, dram, out):
    with ExitStack() as ctx:
        scratch = {name: nc.dram_tensor(f"scratch_{name}", shape, F32, kind="Internal").ap() for name, shape in (
            ("qk1", (2 * DIFF_QK, S)), ("qk1_low", (2 * DIFF_QK, S)), ("qm", (MLA_HEADS * MLA_QK, S)), ("km", (MLA_HEADS * NOPE, S)),
            ("kpe", (ROPE, S)), ("ffn_rows", (S, D)), ("slot_token", (N_BLOCKS * BLK, 1)),
            ("expert_rows", (N_BLOCKS * BLK, D)), ("fox_qk", (512, S)), ("swa_qk", (640, S)), ("plain", (1280, S)),
            ("mo", (256, S)), ("fox_q", (8, S)), ("fox_k", (8, S)), ("mlstm_row", (4, S)), ("window_rows", (8, 3 * P)),
            ("x_rows", (S, D)), ("debug", (1280, S)))}
        k = Core(nc, ctx, dram, out, scratch)
        setup(k)
        first_mixer(k)
        cross_mixer(k)
        expert_layer(k)
        final_norm(k)
        second_mixer(k)
        swiglu(k)


def build(nc, inputs):
    dram = {}
    for name, a in inputs.items():
        dram[name] = nc.dram_tensor(f"in_{name}_dram", a.shape, mybir.dt.from_np(a.dtype), kind="ExternalInput").ap()
    out = nc.dram_tensor("out_0_dram", (1, S, D), F32, kind="ExternalOutput").ap()
    program(nc, dram, out)


def kernel(**inputs):
    import numpy as _np
    import concourse.bacc as _bacc
    from concourse.bass_utils import run_bass_kernel_spmd as _run

    nc = _bacc.Bacc("TRN2", target_bir_lowering=False, num_devices=1)
    arrays = {name: _np.ascontiguousarray(a) for name, a in inputs.items()}
    build(nc, arrays)
    r = _run(nc, [{f"in_{name}_dram": a for name, a in arrays.items()}], core_ids=[0])
    return r.results[0]["out_0_dram"]
```
